# Optimizing a Trainium2 kernel written in Bass

```python
import jax, jax.numpy as jnp
from jax import lax
import numpy as np
import jax
import jax.numpy as jnp

D_MODEL = 1024
BATCH = 1
SEQ = 512
DEPTH = 2

HEAD_DIM = 64
Q_BLOCK = 128
EPS = 1e-6
NEG_INF = -1e30
A_HEADS = 8
A_PATTERNS = ((128, 1), (512, 4), (2048, 16))
B_HEADS = 4
B_DK = 64
B_DV = 128
B_GATE_RANK = 16
B_GATE_TAU = 16.0
B_CHUNK = 64
C_HEADS = 8
C_KV_HEADS = 2
C_WINDOW = 128
D_HEADS = 8
D_Q_RANK = 384
D_KV_RANK = 256
D_NOPE = 64
D_ROPE = 32
D_V = 64
ROPE_BASE = 10000.0
D_FF = -(-8 * D_MODEL // (3 * 256)) * 256

L0_IN_SIZES = (A_HEADS * HEAD_DIM, A_HEADS * HEAD_DIM, A_HEADS * HEAD_DIM,
               B_HEADS * B_DK, B_HEADS * B_DK, B_HEADS * B_DV, B_HEADS * B_DV, B_GATE_RANK)
L0_IN = sum(L0_IN_SIZES)
L0_MIX = A_HEADS * HEAD_DIM + B_HEADS * B_DV
L1_IN_SIZES = (C_HEADS * HEAD_DIM, C_KV_HEADS * HEAD_DIM, C_KV_HEADS * HEAD_DIM,
               D_Q_RANK, D_KV_RANK, D_ROPE)
L1_IN = sum(L1_IN_SIZES)
L1_MIX = C_HEADS * HEAD_DIM + D_HEADS * D_V
N_EVEN = (DEPTH + 1) // 2
N_ODD = DEPTH // 2


def rmsnorm(x, g):
    xf = x.astype(jnp.float32)
    y = xf * lax.rsqrt(jnp.mean(xf * xf, axis=-1, keepdims=True) + EPS)
    return (y * g.astype(jnp.float32)).astype(x.dtype)

def alibi_slopes(n):
    return jnp.asarray(np.array([2.0 ** (-8.0 * (i + 1) / n) for i in range(n)], dtype=np.float32))

def split_cols(t, sizes):
    return jnp.split(t, [int(c) for c in np.cumsum(sizes)[:-1]], axis=-1)

def with_prev_block(t, blk):
    lead = t.shape[:-2]
    L, dh = t.shape[-2:]
    tb = t.reshape(*lead, L // blk, blk, dh)
    prev = jnp.concatenate([jnp.zeros_like(tb[..., :1, :, :]), tb[..., :-1, :, :]], axis=-3)
    return jnp.concatenate([prev, tb], axis=-2)

def band_geometry(nb, blk, max_rel):
    i = jnp.arange(blk)[:, None]
    j = jnp.arange(2 * blk)[None, :]
    rel = i + blk - j
    key_pos = jnp.arange(nb)[:, None, None] * blk + j - blk
    valid = (rel >= 0) & (rel <= max_rel) & (key_pos >= 0)
    return rel.astype(jnp.float32), valid

def rope(t, pos):
    half = t.shape[-1] // 2
    freqs = ROPE_BASE ** (-jnp.arange(half, dtype=jnp.float32) / half)
    ang = pos.astype(jnp.float32)[:, None] * freqs[None, :]
    cos, sin = jnp.cos(ang)[:, None, :], jnp.sin(ang)[:, None, :]
    tf = t.astype(jnp.float32)
    t1, t2 = tf[..., :half], tf[..., half:]
    return jnp.concatenate([t1 * cos - t2 * sin, t2 * cos + t1 * sin], axis=-1).astype(t.dtype)

def dilated_branch(q, k, v, slopes, window, dilation):
    B_, H, S, dh = q.shape
    L = S // dilation
    Lp = -(-L // Q_BLOCK) * Q_BLOCK
    nb = Lp // Q_BLOCK

    def by_residue(t):
        t = t.reshape(B_, H, L, dilation, dh).transpose(0, 1, 3, 2, 4)
        return jnp.pad(t, ((0, 0), (0, 0), (0, 0), (0, Lp - L), (0, 0)))

    qb = by_residue(q).reshape(B_, H, dilation, nb, Q_BLOCK, dh)
    kb = with_prev_block(by_residue(k), Q_BLOCK)
    vb = with_prev_block(by_residue(v), Q_BLOCK).astype(jnp.float32)
    rel, valid = band_geometry(nb, Q_BLOCK, window // dilation)
    s = jnp.einsum('bhrnid,bhrnjd->bhrnij', qb, kb, preferred_element_type=jnp.float32) * dh ** -0.5
    s = s - slopes[:, None, None, None, None] * (rel * dilation)
    s = jnp.where(valid, s, NEG_INF)
    m = s.max(-1)
    p = jnp.exp(s - m[..., None])
    den = p.sum(-1)
    o = jnp.einsum('bhrnij,bhrnjd->bhrnid', p, vb) / den[..., None]

    def back(t):
        t = t.reshape(B_, H, dilation, Lp, *t.shape[5:])[:, :, :, :L]
        t = jnp.moveaxis(t, 2, 3)
        return t.reshape(B_, H, S, *t.shape[4:])

    return back(o), back(m), back(den)

def dilated_attention(q, k, v):
    slopes = alibi_slopes(A_HEADS)
    outs, maxes, dens = zip(*[dilated_branch(q, k, v, slopes, w, d) for (w, d) in A_PATTERNS])
    m_all = jnp.stack(maxes)
    wts = jnp.stack(dens) * jnp.exp(m_all - m_all.max(0))
    return jnp.einsum('pbhs,pbhsd->bhsd', wts, jnp.stack(outs)) / wts.sum(0)[..., None]

def gla(q, k, v, r, g_low, w_gate_up, b_gate, norm_g):
    B_, S, _ = q.shape
    C = B_CHUNK
    nc = S // C
    log_a = jax.nn.log_sigmoid((g_low @ w_gate_up + b_gate).astype(jnp.float32)) / B_GATE_TAU

    def chunks(t, dh):
        return t.reshape(B_, nc, C, B_HEADS, dh).transpose(0, 3, 1, 2, 4).astype(jnp.float32)

    qc = chunks(q, B_DK) * B_DK ** -0.5
    kc = chunks(k, B_DK)
    vc = chunks(v, B_DV)
    bcum = jnp.cumsum(chunks(log_a, B_DK), axis=-2)
    b_last = bcum[..., -1:, :]
    b_mid = bcum[..., C // 2 - 1:C // 2, :]
    att = jnp.einsum('bhncd,bhnsd->bhncs', qc * jnp.exp(bcum - b_mid), kc * jnp.exp(b_mid - bcum))
    att = jnp.where(jnp.tril(jnp.ones((C, C), dtype=bool)), att, 0.0)
    o_intra = jnp.einsum('bhncs,bhnse->bhnce', att, vc)
    dS = jnp.einsum('bhnsd,bhnse->bhnde', kc * jnp.exp(b_last - bcum), vc)
    decay = jnp.exp(b_last[..., 0, :])

    def step(state, inp):
        dS_n, dec_n = inp
        return dec_n[..., None] * state + dS_n, state

    init = jnp.zeros((B_, B_HEADS, B_DK, B_DV), jnp.float32)
    _, s_prev = lax.scan(step, init, (jnp.moveaxis(dS, 2, 0), jnp.moveaxis(decay, 2, 0)))
    s_prev = jnp.moveaxis(s_prev, 0, 2)
    o_inter = jnp.einsum('bhncd,bhnde->bhnce', qc * jnp.exp(bcum), s_prev)
    o = (o_intra + o_inter).transpose(0, 2, 3, 1, 4).reshape(B_, S, B_HEADS, B_DV)
    o = rmsnorm(o, norm_g)
    o = o * jax.nn.silu(r.astype(jnp.float32)).reshape(B_, S, B_HEADS, B_DV)
    return o.reshape(B_, S, B_HEADS * B_DV)

def swa_sink_attention(q, k, v, sinks):
    B_, S, _ = q.shape
    G = C_HEADS // C_KV_HEADS
    nb = S // Q_BLOCK
    qb = q.reshape(B_, nb, Q_BLOCK, C_KV_HEADS, G, HEAD_DIM).transpose(0, 3, 4, 1, 2, 5)
    kt = k.reshape(B_, S, C_KV_HEADS, HEAD_DIM).transpose(0, 2, 1, 3)
    vt = v.reshape(B_, S, C_KV_HEADS, HEAD_DIM).transpose(0, 2, 1, 3)
    kb = with_prev_block(kt, Q_BLOCK)
    vb = with_prev_block(vt, Q_BLOCK).astype(jnp.float32)
    rel, valid = band_geometry(nb, Q_BLOCK, C_WINDOW - 1)
    slopes = alibi_slopes(C_HEADS).reshape(C_KV_HEADS, G)[:, :, None, None, None]
    s = jnp.einsum('bkgnid,bknjd->bkgnij', qb, kb, preferred_element_type=jnp.float32) * HEAD_DIM ** -0.5
    s = jnp.where(valid, s - slopes * rel, NEG_INF)
    sink = sinks.astype(jnp.float32).reshape(C_KV_HEADS, G)[:, :, None, None, None]
    m = jnp.maximum(s.max(-1, keepdims=True), sink)
    p = jnp.exp(s - m)
    den = p.sum(-1, keepdims=True) + jnp.exp(sink - m)
    o = jnp.einsum('bkgnij,bknjd->bkgnid', p / den, vb)
    return o.transpose(0, 3, 4, 1, 2, 5).reshape(B_, S, C_HEADS * HEAD_DIM)

def mla(c_q, c_kv, k_rope, q_norm, w_uq, kv_norm, w_ukv):
    B_, S, _ = c_q.shape
    pos = jnp.arange(S)
    q = (rmsnorm(c_q, q_norm) @ w_uq).reshape(B_, S, D_HEADS, D_NOPE + D_ROPE)
    kv = (rmsnorm(c_kv, kv_norm) @ w_ukv).reshape(B_, S, D_HEADS, D_NOPE + D_V)
    q_nope, q_pe = q[..., :D_NOPE], rope(q[..., D_NOPE:], pos)
    k_nope, v = kv[..., :D_NOPE], kv[..., D_NOPE:].astype(jnp.float32)
    k_pe = rope(k_rope[:, :, None, :], pos)[:, :, 0, :]
    scale = (D_NOPE + D_ROPE) ** -0.5
    nb = S // Q_BLOCK
    qn_b = q_nope.reshape(B_, nb, Q_BLOCK, D_HEADS, D_NOPE).transpose(1, 0, 2, 3, 4)
    qp_b = q_pe.reshape(B_, nb, Q_BLOCK, D_HEADS, D_ROPE).transpose(1, 0, 2, 3, 4)
    kpos = jnp.arange(S)

    def block(args):
        qn, qp, n = args
        s = (jnp.einsum('bihd,bjhd->bhij', qn, k_nope, preferred_element_type=jnp.float32)
             + jnp.einsum('bihd,bjd->bhij', qp, k_pe, preferred_element_type=jnp.float32)) * scale
        qpos = n * Q_BLOCK + jnp.arange(Q_BLOCK)
        s = jnp.where(qpos[:, None] >= kpos[None, :], s, NEG_INF)
        return jnp.einsum('bhij,bjhd->bihd', jax.nn.softmax(s, axis=-1), v)

    o = lax.map(block, (qn_b, qp_b, jnp.arange(nb)))
    return o.transpose(1, 0, 2, 3, 4).reshape(B_, S, D_HEADS * D_V)

def mix_even(h, w_in, w_out, gla_w_gate_up, gla_b_gate, gla_norm):
    B_, S, _ = h.shape
    qa, ka, va, qb, kb, vb, rb, gb = split_cols(h @ w_in, L0_IN_SIZES)
    heads = lambda t: t.reshape(B_, S, A_HEADS, HEAD_DIM).transpose(0, 2, 1, 3)
    o_a = dilated_attention(heads(qa), heads(ka), heads(va))
    o_a = o_a.transpose(0, 2, 1, 3).reshape(B_, S, A_HEADS * HEAD_DIM)
    o_b = gla(qb, kb, vb, rb, gb, gla_w_gate_up, gla_b_gate, gla_norm)
    return jnp.concatenate([o_a, o_b], axis=-1).astype(h.dtype) @ w_out

def mix_odd(h, w_in, w_out, sinks, q_norm, w_uq, kv_norm, w_ukv):
    qc, kc, vc, c_q, c_kv, k_rope = split_cols(h @ w_in, L1_IN_SIZES)
    o_c = swa_sink_attention(qc, kc, vc, sinks)
    o_d = mla(c_q, c_kv, k_rope, q_norm, w_uq, kv_norm, w_ukv)
    return jnp.concatenate([o_c, o_d], axis=-1).astype(h.dtype) @ w_out

def swiglu(h, w_gate, w_up, w_down):
    return (jax.nn.silu(h @ w_gate) * (h @ w_up)) @ w_down

def first_inputs(seed: int = 0) -> dict:
    key = jax.random.key(seed)
    ks = jax.random.split(key, 24)
    nrm = lambda k, shape, fan_in: jax.random.normal(k, shape, jnp.float32) * fan_in ** -0.5
    gain = lambda k, shape: 1.0 + 0.02 * jax.random.normal(k, shape, jnp.float32)
    return {
        "x": jax.random.normal(ks[0], (BATCH, SEQ, D_MODEL), jnp.float32),
        "norm_mix_pre": gain(ks[1], (DEPTH, D_MODEL)),
        "norm_mix_post": gain(ks[2], (DEPTH, D_MODEL)),
        "norm_ffn_pre": gain(ks[3], (DEPTH, D_MODEL)),
        "norm_ffn_post": gain(ks[4], (DEPTH, D_MODEL)),
        "ffn_w_gate": nrm(ks[5], (DEPTH, D_MODEL, D_FF), D_MODEL),
        "ffn_w_up": nrm(ks[6], (DEPTH, D_MODEL, D_FF), D_MODEL),
        "ffn_w_down": nrm(ks[7], (DEPTH, D_FF, D_MODEL), D_FF),
        "ab_w_in": nrm(ks[8], (N_EVEN, D_MODEL, L0_IN), D_MODEL),
        "ab_w_out": nrm(ks[9], (N_EVEN, L0_MIX, D_MODEL), L0_MIX),
        "gla_w_gate_up": nrm(ks[10], (N_EVEN, B_GATE_RANK, B_HEADS * B_DK), B_GATE_RANK),
        "gla_b_gate": 0.1 * jax.random.normal(ks[11], (N_EVEN, B_HEADS * B_DK), jnp.float32),
        "gla_norm": gain(ks[12], (N_EVEN, B_DV)),
        "cd_w_in": nrm(ks[13], (N_ODD, D_MODEL, L1_IN), D_MODEL),
        "cd_w_out": nrm(ks[14], (N_ODD, L1_MIX, D_MODEL), L1_MIX),
        "swa_sinks": jax.random.normal(ks[15], (N_ODD, C_HEADS), jnp.float32),
        "mla_q_norm": gain(ks[16], (N_ODD, D_Q_RANK)),
        "mla_w_uq": nrm(ks[17], (N_ODD, D_Q_RANK, D_HEADS * (D_NOPE + D_ROPE)), D_Q_RANK),
        "mla_kv_norm": gain(ks[18], (N_ODD, D_KV_RANK)),
        "mla_w_ukv": nrm(ks[19], (N_ODD, D_KV_RANK, D_HEADS * (D_NOPE + D_V)), D_KV_RANK),
    }

def first_block(x, norm_mix_pre, norm_mix_post, norm_ffn_pre, norm_ffn_post,
              ffn_w_gate, ffn_w_up, ffn_w_down,
              ab_w_in, ab_w_out, gla_w_gate_up, gla_b_gate, gla_norm,
              cd_w_in, cd_w_out, swa_sinks, mla_q_norm, mla_w_uq, mla_kv_norm, mla_w_ukv):
    for layer in range(DEPTH):
        i = layer // 2
        h = rmsnorm(x, norm_mix_pre[layer])
        if layer % 2 == 0:
            y = mix_even(h, ab_w_in[i], ab_w_out[i], gla_w_gate_up[i], gla_b_gate[i], gla_norm[i])
        else:
            y = mix_odd(h, cd_w_in[i], cd_w_out[i], swa_sinks[i], mla_q_norm[i], mla_w_uq[i],
                        mla_kv_norm[i], mla_w_ukv[i])
        x = x + rmsnorm(y, norm_mix_post[layer]).astype(x.dtype)
        h = rmsnorm(x, norm_ffn_pre[layer])
        f = swiglu(h, ffn_w_gate[layer], ffn_w_up[layer], ffn_w_down[layer])
        x = x + rmsnorm(f, norm_ffn_post[layer]).astype(x.dtype)
    return x


GRID_W = 64
CTX_LEN = 256
N_MIXERS = 2
N_LAYERS_A = (DEPTH + N_MIXERS - 1) // N_MIXERS
N_LAYERS_B = DEPTH // N_MIXERS
N_MOD = 6
NORM_EPS = 1e-6
CHUNK = 128
GMLP_WIDTH = 2 * D_MODEL
GMLP_GROUP_CH = 128
GMLP_GROUPS = GMLP_WIDTH // GMLP_GROUP_CH
LN_EPS = 1e-5
RWKV_HEAD = 64
RWKV_HEADS = D_MODEL // RWKV_HEAD
DECAY_LORA = 64
AAA_LORA = 64
GATE_LORA = 160
GN_EPS = 64e-5
N_DIR = 2
N_GROUPS = 4
EXPERTS_PER_GROUP = 8
N_EXPERTS = N_GROUPS * EXPERTS_PER_GROUP
EXPERT_HIDDEN = 512
TOP_K = 2
MOE_BLOCK = 128


def rmsnorm_2(x, g):
    xf = x.astype(jnp.float32)
    y = xf * lax.rsqrt(jnp.mean(xf * xf, axis=-1, keepdims=True) + NORM_EPS)
    return y.astype(x.dtype) * g

def layernorm(x, g, b, eps):
    xf = x.astype(jnp.float32)
    mu = jnp.mean(xf, axis=-1, keepdims=True)
    var = jnp.mean(jnp.square(xf - mu), axis=-1, keepdims=True)
    return ((xf - mu) * lax.rsqrt(var + eps)).astype(x.dtype) * g + b

def gmlp_mixer(h, w_in, b_in, ln_g, ln_b, w_s, b_s, w_out, b_out):
    bsz, n, _ = h.shape
    z = jax.nn.gelu(h @ w_in + b_in, approximate=False)
    u, v = jnp.split(z, 2, axis=-1)
    v = layernorm(v, ln_g, ln_b, LN_EPS)
    v = v.reshape(bsz, n // CHUNK, CHUNK, GMLP_GROUPS, GMLP_GROUP_CH)
    v = jnp.einsum('gpq,bcqgd->bcpgd', w_s, v) + b_s.T[:, :, None]
    return (u * v.reshape(bsz, n, GMLP_WIDTH)) @ w_out + b_out

def qshift_grid(h, rows):
    bsz, n, d = h.shape
    q = d // 4
    g = h.reshape(bsz, rows, GRID_W, d)
    left = jnp.pad(g[:, :, :-1, :q], ((0, 0), (0, 0), (1, 0), (0, 0)))
    right = jnp.pad(g[:, :, 1:, q:2 * q], ((0, 0), (0, 0), (0, 1), (0, 0)))
    up = jnp.pad(g[:, :-1, :, 2 * q:3 * q], ((0, 0), (1, 0), (0, 0), (0, 0)))
    down = jnp.pad(g[:, 1:, :, 3 * q:], ((0, 0), (0, 1), (0, 0), (0, 0)))
    return jnp.concatenate([left, right, up, down], axis=-1).reshape(bsz, n, d)

def bishift_1d(h):
    half = h.shape[-1] // 2
    prev = jnp.pad(h[:, :-1, :half], ((0, 0), (1, 0), (0, 0)))
    nxt = jnp.pad(h[:, 1:, half:], ((0, 0), (0, 1), (0, 0)))
    return jnp.concatenate([prev, nxt], axis=-1)

def _heads(z):
    return z.reshape(*z.shape[:-1], RWKV_HEADS, RWKV_HEAD)

def _both_dirs(z):
    return jnp.stack([z, z[:, ::-1]])

def _rev_dir1(z):
    return jnp.stack([z[0], z[1][:, ::-1]])

def _scan_layout(z):
    return jnp.moveaxis(_heads(z), 2, 0).astype(jnp.float32)

def rwkv_prepare(h, h_shift, mu, wr, wk, wv, w0, w1, w2, a0, a1, a2, k_k, k_a):
    xx = h_shift - h
    xr, xw, xk, xv, xa = [h + xx * mu[j] for j in range(5)]
    r = xr @ wr
    k = xk @ wk
    v = xv @ wv
    lw = jnp.einsum('zbtr,zrd->zbtd', jnp.tanh(jnp.einsum('btd,zdr->zbtr', xw, w1)), w2)
    w_log = -jax.nn.softplus(-(w0[:, None, None, :] + lw).astype(jnp.float32)) - 0.5
    decay = jnp.exp(-jnp.exp(w_log))
    la = jnp.einsum('zbtr,zrd->zbtd', jnp.einsum('btd,zdr->zbtr', xa, a1), a2)
    a = jax.nn.sigmoid((a0[:, None, None, :] + la).astype(jnp.float32))
    kk = _heads(k * k_k).astype(jnp.float32)
    kk = (kk * lax.rsqrt(jnp.sum(kk * kk, axis=-1, keepdims=True) + 1e-12)).reshape(k.shape)
    k_mod = k[None] * (1 + (a - 1) * k_a)
    scan_in = (_scan_layout(_both_dirs(r)), _scan_layout(_rev_dir1(decay)), _scan_layout(_rev_dir1(k_mod)),
               _scan_layout(_both_dirs(v)), _scan_layout(_both_dirs(-kk)), _scan_layout(_rev_dir1(kk[None] * a)))
    return scan_in, r, k_mod, v, xx

def _wkv_step(S, inp):
    r_t, w_t, k_t, v_t, a_t, b_t = inp
    sa = jnp.einsum('zbhvk,zbhk->zbhv', S, a_t)
    S = S * w_t[..., None, :] + sa[..., :, None] * b_t[..., None, :] + v_t[..., :, None] * k_t[..., None, :]
    return S, jnp.einsum('zbhvk,zbhk->zbhv', S, r_t)

def wkv_bidir(state0, scan_in):
    state, ys = lax.scan(_wkv_step, state0, scan_in)
    ys = jnp.moveaxis(ys, 0, 2)
    return state, ys[0] + ys[1][:, ::-1]

def rwkv_out(y, h, xx, r, k_mod, v, mu, ln_g, ln_b, r_k, g1, g2, wo):
    bsz, n, d = r.shape
    y = layernorm(y, ln_g.reshape(RWKV_HEADS, RWKV_HEAD), ln_b.reshape(RWKV_HEADS, RWKV_HEAD), GN_EPS)
    bonus = jnp.einsum('bthk,zbthk->bth', _heads(r) * r_k, _heads(k_mod))
    y = y.astype(r.dtype) + bonus[..., None] * _heads(v)
    xg = h + xx * mu[5]
    gate = jax.nn.sigmoid(xg @ g1) @ g2
    return (y.reshape(bsz, n, d) * gate) @ wo

def rwkv_mixer(hc, hl, rows, need_ctx_out, mu, wr, wk, wv, wo, w0, w1, w2, a0, a1, a2, g1, g2,
               k_k, k_a, r_k, ln_g, ln_b):
    proj = (mu, wr, wk, wv, w0, w1, w2, a0, a1, a2, k_k, k_a)
    scan_c, r_c, km_c, v_c, xx_c = rwkv_prepare(hc, bishift_1d(hc), *proj)
    scan_l, r_l, km_l, v_l, xx_l = rwkv_prepare(hl, qshift_grid(hl, rows), *proj)
    state0 = jnp.zeros((N_DIR, hc.shape[0], RWKV_HEADS, RWKV_HEAD, RWKV_HEAD), jnp.float32)
    state_c, y_c = wkv_bidir(state0, scan_c)
    _, y_l = wkv_bidir(state_c, scan_l)
    outp = (mu, ln_g, ln_b, r_k, g1, g2, wo)
    out_l = rwkv_out(y_l, hl, xx_l, r_l, km_l, v_l, *outp)
    out_c = rwkv_out(y_c, hc, xx_c, r_c, km_c, v_c, *outp) if need_ctx_out else None
    return out_c, out_l

def hier_moe(h, w_grp, b_grp, w_exp, b_exp, w_gate, w_up, w_down):
    n_tok, d = h.shape
    hf = h.astype(jnp.float32)
    grp_logits = hf @ w_grp.astype(jnp.float32) + b_grp.astype(jnp.float32)
    grp_prob = jax.nn.softmax(grp_logits, axis=-1)
    grp = jnp.argmax(grp_logits, axis=-1)
    p_grp = jnp.take_along_axis(grp_prob, grp[:, None], axis=-1)
    exp_logits = (hf @ w_exp.astype(jnp.float32) + b_exp.astype(jnp.float32)).reshape(n_tok, N_GROUPS, EXPERTS_PER_GROUP)
    exp_logits = jnp.take_along_axis(exp_logits, grp[:, None, None], axis=1)[:, 0]
    top_logit, top_idx = lax.top_k(exp_logits, TOP_K)
    weights = (p_grp * jax.nn.softmax(top_logit, axis=-1)).astype(h.dtype)
    expert_id = (grp[:, None] * EXPERTS_PER_GROUP + top_idx).reshape(-1)
    n_assign = n_tok * TOP_K
    order = jnp.argsort(expert_id)
    sorted_e = expert_id[order]
    token_of = order // TOP_K
    counts = jnp.bincount(expert_id, length=N_EXPERTS)
    padded = ((counts + MOE_BLOCK - 1) // MOE_BLOCK) * MOE_BLOCK
    pad_end = jnp.cumsum(padded)
    pad_start = pad_end - padded
    raw_start = jnp.cumsum(counts) - counts
    dest = pad_start[sorted_e] + (jnp.arange(n_assign) - raw_start[sorted_e])
    n_blocks = (n_assign + MOE_BLOCK - 1) // MOE_BLOCK + N_EXPERTS
    cap = n_blocks * MOE_BLOCK
    buf = jnp.zeros((cap, d), h.dtype).at[dest].set(h[token_of])
    block_expert = jnp.minimum(jnp.searchsorted(pad_end, jnp.arange(n_blocks) * MOE_BLOCK, side='right'),
                               N_EXPERTS - 1)

    def expert_block(args):
        xb, e = args
        return (jax.nn.silu(xb @ w_gate[e]) * (xb @ w_up[e])) @ w_down[e]

    out = lax.map(expert_block, (buf.reshape(n_blocks, MOE_BLOCK, d), block_expert)).reshape(cap, d)
    y = jnp.zeros((n_assign, d), h.dtype).at[order].set(out[dest]).reshape(n_tok, TOP_K, d)
    return jnp.einsum('tk,tkd->td', weights, y)

def second_inputs(seed: int = 0) -> dict:
    key = jax.random.key(seed)
    keys = iter(jax.random.split(key, 48))
    f32 = jnp.float32

    def nrm(shape, scale):
        return scale * jax.random.normal(next(keys), shape, f32)

    def gain(shape):
        return 1.0 + nrm(shape, 0.1)

    def unif(shape, lo, hi):
        return jax.random.uniform(next(keys), shape, f32, lo, hi)

    D, W, F = D_MODEL, GMLP_WIDTH, EXPERT_HIDDEN
    NA, NB = N_LAYERS_A, N_LAYERS_B
    return {
        'x': nrm((BATCH, SEQ, D), 1.0),
        'c': nrm((BATCH, D), 1.0),
        'ctx': nrm((BATCH, CTX_LEN, D), 1.0),
        'c_ctx': nrm((D,), 1.0),
        'ada_w': nrm((DEPTH, D, N_MOD * D), 0.5 * D ** -0.5),
        'ada_b': nrm((DEPTH, N_MOD * D), 0.05),
        'norm1_g': gain((DEPTH, D)),
        'norm2_g': gain((DEPTH, D)),
        'final_g': gain((D,)),
        'ga_w_in': nrm((NA, D, 2 * W), D ** -0.5),
        'ga_b_in': nrm((NA, 2 * W), 0.02),
        'ga_ln_g': gain((NA, W)),
        'ga_ln_b': nrm((NA, W), 0.02),
        'ga_w_s': nrm((NA, GMLP_GROUPS, CHUNK, CHUNK), 0.5 * CHUNK ** -0.5),
        'ga_b_s': gain((NA, GMLP_GROUPS, CHUNK)),
        'ga_w_out': nrm((NA, W, D), W ** -0.5),
        'ga_b_out': nrm((NA, D), 0.02),
        'rw_mu': unif((NB, N_MOD, D), 0.0, 1.0),
        'rw_wr': nrm((NB, D, D), D ** -0.5),
        'rw_wk': nrm((NB, D, D), D ** -0.5),
        'rw_wv': nrm((NB, D, D), D ** -0.5),
        'rw_wo': nrm((NB, D, D), D ** -0.5),
        'rw_w0': unif((NB, N_DIR, D), -6.0, 0.0),
        'rw_w1': nrm((NB, N_DIR, D, DECAY_LORA), 0.5 * D ** -0.5),
        'rw_w2': nrm((NB, N_DIR, DECAY_LORA, D), 0.5 * DECAY_LORA ** -0.5),
        'rw_a0': nrm((NB, N_DIR, D), 0.5),
        'rw_a1': nrm((NB, N_DIR, D, AAA_LORA), 0.5 * D ** -0.5),
        'rw_a2': nrm((NB, N_DIR, AAA_LORA, D), 0.5 * AAA_LORA ** -0.5),
        'rw_g1': nrm((NB, D, GATE_LORA), D ** -0.5),
        'rw_g2': nrm((NB, GATE_LORA, D), GATE_LORA ** -0.5),
        'rw_k_k': 0.85 + nrm((NB, D), 0.05),
        'rw_k_a': gain((NB, D)),
        'rw_r_k': nrm((NB, RWKV_HEADS, RWKV_HEAD), 0.1),
        'rw_ln_g': gain((NB, D)),
        'rw_ln_b': nrm((NB, D), 0.02),
        'moe_w_grp': nrm((DEPTH, D, N_GROUPS), D ** -0.5),
        'moe_b_grp': nrm((DEPTH, N_GROUPS), 0.01),
        'moe_w_exp': nrm((DEPTH, D, N_EXPERTS), D ** -0.5),
        'moe_b_exp': nrm((DEPTH, N_EXPERTS), 0.01),
        'moe_w_gate': nrm((DEPTH, N_EXPERTS, D, F), D ** -0.5),
        'moe_w_up': nrm((DEPTH, N_EXPERTS, D, F), D ** -0.5),
        'moe_w_down': nrm((DEPTH, N_EXPERTS, F, D), F ** -0.5),
    }

def second_block(x, c, ctx, c_ctx, ada_w, ada_b, norm1_g, norm2_g, final_g,
              ga_w_in, ga_b_in, ga_ln_g, ga_ln_b, ga_w_s, ga_b_s, ga_w_out, ga_b_out,
              rw_mu, rw_wr, rw_wk, rw_wv, rw_wo, rw_w0, rw_w1, rw_w2, rw_a0, rw_a1, rw_a2,
              rw_g1, rw_g2, rw_k_k, rw_k_a, rw_r_k, rw_ln_g, rw_ln_b,
              moe_w_grp, moe_b_grp, moe_w_exp, moe_b_exp, moe_w_gate, moe_w_up, moe_w_down):
    bsz, n, d = x.shape
    rows = n // GRID_W
    xc = ctx
    silu_c = jax.nn.silu(c)
    silu_cc = jax.nn.silu(c_ctx)
    for i in range(DEPTH):
        last = i == DEPTH - 1
        j = i // N_MIXERS
        mod_l = silu_c @ ada_w[i] + ada_b[i]
        mod_c = silu_cc @ ada_w[i] + ada_b[i]
        sh1, sc1, gt1, sh2, sc2, gt2 = jnp.split(mod_l[:, None, :], N_MOD, axis=-1)
        csh1, csc1, cgt1, csh2, csc2, cgt2 = jnp.split(mod_c, N_MOD, axis=-1)
        hl = rmsnorm_2(x, norm1_g[i]) * (1 + sc1) + sh1
        hc = rmsnorm_2(xc, norm1_g[i]) * (1 + csc1) + csh1
        if i % N_MIXERS == 0:
            gp = (ga_w_in[j], ga_b_in[j], ga_ln_g[j], ga_ln_b[j], ga_w_s[j], ga_b_s[j], ga_w_out[j], ga_b_out[j])
            yl = gmlp_mixer(hl, *gp)
            yc = None if last else gmlp_mixer(hc, *gp)
        else:
            yc, yl = rwkv_mixer(hc, hl, rows, not last, rw_mu[j], rw_wr[j], rw_wk[j], rw_wv[j], rw_wo[j],
                                rw_w0[j], rw_w1[j], rw_w2[j], rw_a0[j], rw_a1[j], rw_a2[j], rw_g1[j], rw_g2[j],
                                rw_k_k[j], rw_k_a[j], rw_r_k[j], rw_ln_g[j], rw_ln_b[j])
        x = x + gt1 * yl
        hl2 = rmsnorm_2(x, norm2_g[i]) * (1 + sc2) + sh2
        mp = (moe_w_grp[i], moe_b_grp[i], moe_w_exp[i], moe_b_exp[i], moe_w_gate[i], moe_w_up[i], moe_w_down[i])
        if last:
            x = x + gt2 * hier_moe(hl2.reshape(-1, d), *mp).reshape(x.shape)
        else:
            xc = xc + cgt1 * yc
            hc2 = rmsnorm_2(xc, norm2_g[i]) * (1 + csc2) + csh2
            out = hier_moe(jnp.concatenate([hl2.reshape(-1, d), hc2.reshape(-1, d)], axis=0), *mp)
            x = x + gt2 * out[:bsz * n].reshape(x.shape)
            xc = xc + cgt2 * out[bsz * n:].reshape(xc.shape)
    return rmsnorm_2(x, final_g)


def setup_inputs(seed=0):
    out = dict(first_inputs(seed))
    for name, value in second_inputs(seed + 1).items():
        if name != "x":
            out[name + "_2"] = value
    return out


def reference(
    x, norm_mix_pre, norm_mix_post, norm_ffn_pre, norm_ffn_post, ffn_w_gate, ffn_w_up,
    ffn_w_down, ab_w_in, ab_w_out, gla_w_gate_up, gla_b_gate, gla_norm, cd_w_in, cd_w_out,
    swa_sinks, mla_q_norm, mla_w_uq, mla_kv_norm, mla_w_ukv, c_2, ctx_2, c_ctx_2, ada_w_2,
    ada_b_2, norm1_g_2, norm2_g_2, final_g_2, ga_w_in_2, ga_b_in_2, ga_ln_g_2, ga_ln_b_2,
    ga_w_s_2, ga_b_s_2, ga_w_out_2, ga_b_out_2, rw_mu_2, rw_wr_2, rw_wk_2, rw_wv_2, rw_wo_2,
    rw_w0_2, rw_w1_2, rw_w2_2, rw_a0_2, rw_a1_2, rw_a2_2, rw_g1_2, rw_g2_2, rw_k_k_2, rw_k_a_2,
    rw_r_k_2, rw_ln_g_2, rw_ln_b_2, moe_w_grp_2, moe_b_grp_2, moe_w_exp_2, moe_b_exp_2,
    moe_w_gate_2, moe_w_up_2, moe_w_down_2,
):
    x = first_block(
        x, norm_mix_pre, norm_mix_post, norm_ffn_pre, norm_ffn_post, ffn_w_gate, ffn_w_up,
        ffn_w_down, ab_w_in, ab_w_out, gla_w_gate_up, gla_b_gate, gla_norm, cd_w_in, cd_w_out,
        swa_sinks, mla_q_norm, mla_w_uq, mla_kv_norm, mla_w_ukv,
    )
    return second_block(
        x, c_2, ctx_2, c_ctx_2, ada_w_2, ada_b_2, norm1_g_2, norm2_g_2, final_g_2, ga_w_in_2,
        ga_b_in_2, ga_ln_g_2, ga_ln_b_2, ga_w_s_2, ga_b_s_2, ga_w_out_2, ga_b_out_2, rw_mu_2,
        rw_wr_2, rw_wk_2, rw_wv_2, rw_wo_2, rw_w0_2, rw_w1_2, rw_w2_2, rw_a0_2, rw_a1_2,
        rw_a2_2, rw_g1_2, rw_g2_2, rw_k_k_2, rw_k_a_2, rw_r_k_2, rw_ln_g_2, rw_ln_b_2,
        moe_w_grp_2, moe_b_grp_2, moe_w_exp_2, moe_b_exp_2, moe_w_gate_2, moe_w_up_2,
        moe_w_down_2,
    )


_drawn_inputs = setup_inputs


def setup_inputs(seed=0):
    import zlib

    import numpy as np

    out = dict(_drawn_inputs(seed))
    spreads = {}
    factors = {'norm_ffn_post': 3.097,
     'gla_norm': 3.304,
     'mla_q_norm': 8.0,
     'mla_kv_norm': 7.469,
     'ctx_2': 2.899,
     'c_ctx_2': 3.631,
     'norm1_g_2': 2.757,
     'norm2_g_2': 3.103,
     'ga_b_in_2': 8.0,
     'ga_ln_g_2': 8.0,
     'ga_ln_b_2': 8.0,
     'ga_b_s_2': 5.233,
     'ga_b_out_2': 8.0,
     'rw_w1_2': 8.0,
     'rw_w2_2': 8.0,
     'rw_a0_2': 3.274,
     'rw_a1_2': 6.447,
     'rw_a2_2': 6.36,
     'rw_k_k_2': 172.128,
     'rw_k_a_2': 2.945,
     'rw_ln_g_2': 6.78,
     'rw_ln_b_2': 62.059,
     'moe_b_grp_2': 8.0,
     'moe_b_exp_2': 8.0,
     'swa_sinks': 24.155}
    for name, (base, spread) in spreads.items():
        noise = np.random.default_rng([zlib.crc32(name.encode()), seed]).standard_normal(out[name].shape)
        drawn = base * np.exp(spread * noise) if base else spread * noise
        out[name] = jnp.asarray(drawn.astype(out[name].dtype))
    for name, factor in factors.items():
        out[name] = (out[name] * factor).astype(out[name].dtype)
    return out
```

```python
import math
from contextlib import ExitStack

import numpy as np
import concourse.bass as bass
from concourse import mybir

F32 = mybir.dt.float32
I32 = mybir.dt.int32
ACT = mybir.ActivationFunctionType
ALU = mybir.AluOpType
AX = mybir.AxisListType

P = 128
D = 1024
SEQ = 512
CTX = 256
ALL = SEQ + CTX
KD = D // P
NT = SEQ // P
NA = ALL // P
BANK = 512
EPS = 1e-6


class Stage:

    zeroed = []

    def __init__(self, nc, name):
        self.nc, self.name = nc, name

    def __enter__(self):
        self.stack = ExitStack()
        self.sems = []
        return self

    def sb(self, name, shape, dt=F32):
        return self.stack.enter_context(self.nc.sbuf_tensor(f"{self.name}_{name}", shape, dt))

    def ps(self, name, shape, dt=F32):
        return self.stack.enter_context(self.nc.psum_tensor(f"{self.name}_{name}", shape, dt))

    def sem(self, name):
        s = self.nc.alloc_semaphore(f"{self.name}_{name}")
        self.sems.append(s)
        return s

    def block(self):
        return self.nc.Block()

    def __exit__(self, *exc):
        self.stack.close()
        if exc[0] is None:
            for s in Stage.zeroed:
                self.nc.release_semaphore(s)
            for s in self.sems:
                self.nc.gpsimd.sem_clear(s)
            Stage.zeroed = self.sems


class Chain:

    def __init__(self, eng, sem, base=0):
        self.eng, self.sem, self.base, self.n = eng, sem, base, 0

    def mark(self, ins):
        ins.then_inc(self.sem, 1)
        self.n += 1

    def wait(self):
        self.eng.wait_ge(self.sem, self.base + self.n)

    def step(self, ins):
        self.mark(ins)
        self.wait()


def kslices(k):
    return [(a, min(P, k - a)) for a in range(0, k, P)]


def project(nc, name, hT, n_tok, jobs, stores=(), const=None, parts=None):
    with Stage(nc, name) as st:
        K = jobs[0]["w"].shape[0]
        ks = kslices(K)
        cw = max(j["w"].shape[1] for j in jobs)
        wbuf = [st.sb(f"w{b}", [P, len(ks), cw]) for b in range(2)]
        banks = [st.ps(f"bank{b}", [P, BANK]) for b in range(8)]
        w_loaded = [st.sem(f"w_loaded{b}") for b in range(2)]
        products_done = st.sem("products_done")
        act_done, dve_done = st.sem("act_done"), st.sem("dve_done")
        act_step, dve_step = st.sem("act_step"), st.sem("dve_step")
        stored = st.sem("stored")

        groups = []
        for c, job in enumerate(jobs):
            width = job["w"].shape[1]
            if job["mode"] == "F":
                for j, (f0, fw) in enumerate(kslices(width)):
                    for n0, nw in parts or [(n0, min(BANK, n_tok - n0)) for n0 in range(0, n_tok, BANK)]:
                        groups.append((c, j, f0, fw, n0, nw))
            else:
                for j, (n0, nw) in enumerate(kslices(n_tok)):
                    groups.append((c, j, n0, nw, 0, width))
        last_of = {}
        for g, grp in enumerate(groups):
            last_of[grp[0]] = g
        engine_of = []
        for g, grp in enumerate(groups):
            e = jobs[grp[0]].get("eng", "any")
            engine_of.append(("act", "dve")[g % 2] if e == "any" else e)
        nth = [engine_of[:g + 1].count(engine_of[g]) for g in range(len(groups))]

        def view(g):
            c, j, a, aw, b0, bw = groups[g]
            return banks[g % 8][0:aw, 0:bw]

        with st.block() as block:
            @block.sync
            def _(sp):
                for c, job in enumerate(jobs):
                    if c >= 2:
                        sp.wait_ge(products_done, last_of[c - 2] + 1)
                    full = K // P
                    width = job["w"].shape[1]
                    if full:
                        sp.dma_start(wbuf[c % 2][:, 0:full, 0:width],
                                     job["w"][0:full * P, :].rearrange("(k p) n -> p k n", p=P)
                                     ).then_inc(w_loaded[c % 2], 16)
                    if K % P:
                        sp.dma_start(wbuf[c % 2][0:K % P, full, 0:width],
                                     job["w"][full * P:K, :]).then_inc(w_loaded[c % 2], 16)
                sp.wait_ge(act_done, engine_of.count("act"))
                sp.wait_ge(dve_done, engine_of.count("dve"))
                for dst, src in stores:
                    sp.dma_start(dst, src).then_inc(stored, 16)
                if stores:
                    sp.wait_ge(stored, 16 * len(stores))

            @block.tensor
            def _(pe):
                seen = -1
                per = 16 * ((K // P > 0) + (K % P > 0))
                for g, (c, j, a, aw, b0, bw) in enumerate(groups):
                    job = jobs[c]
                    if c != seen:
                        pe.wait_ge(w_loaded[c % 2], per * (c // 2 + 1))
                        seen = c
                    if g >= 8:
                        pe.wait_ge(act_done if engine_of[g - 8] == "act" else dve_done, nth[g - 8])
                    w = wbuf[c % 2]
                    bias = job.get("bias")
                    for k, (_, kw) in enumerate(ks):
                        if job["mode"] == "F":
                            lhsT, rhs = w[0:kw, k, a:a + aw], hT[0:kw, k, b0:b0 + bw]
                        else:
                            lhsT, rhs = hT[0:kw, k, a:a + aw], w[0:kw, k, 0:bw]
                        mm = nc.tensor.matmul(view(g), lhsT, rhs, start=(k == 0),
                                              stop=(k == len(ks) - 1 and bias is None))
                    if bias is not None:
                        mm = nc.tensor.matmul(view(g), const["ones"][0:1, 0:aw], bias, start=False, stop=True)
                    mm.then_inc(products_done, 1)

            def ends(which, eng, engine, chain, done):
                for g, (c, j, a, aw, b0, bw) in enumerate(groups):
                    if engine_of[g] == which:
                        eng.wait_ge(products_done, g + 1)
                        jobs[c]["epi"](which, engine, chain, j, b0, view(g)).then_inc(done, 1)

            @block.scalar
            def _(act):
                ends("act", act, nc.scalar, Chain(act, act_step), act_done)

            @block.vector
            def _(dve):
                ends("dve", dve, nc.vector, Chain(dve, dve_step), dve_done)


def copy_to(dest):
    def epi(which, engine, chain, j, n0, ps):
        if which == "act":
            return engine.activation(dest(j, n0), ps, ACT.Copy)
        return engine.tensor_copy(dest(j, n0), ps)
    return epi


def norm_transpose(nc, name, S, tiles, hT, cols=None, rows=None, h_dram=None, scaled=True):
    T = len(tiles)
    width = tiles[0].shape[1]
    kd = width // P
    halves = -(-kd // 4)
    with Stage(nc, name) as st:
        junk = st.sb("squares", [P, width])
        ss = st.sb("sum_sq", [P, T])
        rms = st.sb("rms", [P, T])
        rstd = st.sb("rstd", [P, T])
        xn = [st.sb(f"xn{b}", [P, width]) for b in range(2)]
        tp = [st.ps(f"tp{b}", [P, 4, P]) for b in range(4)]
        rms_ready, xn_ready = st.sem("rms_ready"), st.sem("xn_ready")
        dve_step, act_step = st.sem("dve_step"), st.sem("act_step")
        turned = st.sem("turned")
        emptied = [st.sem("act_emptied"), st.sem("dve_emptied")]
        stored = [st.sem("stored0"), st.sem("stored1")]

        def empty(which, engine, g):
            t, h = g // halves, g % halves
            n = min(4, kd - 4 * h)
            src = tp[g % 4]
            if cols is None:
                dst = hT[:, 4 * h:4 * h + n, t * P:(t + 1) * P]
                if which == "act":
                    return engine.activation(dst, src[:, 0:n, :], ACT.Copy)
                return engine.tensor_copy(dst, src[:, 0:n, :])
            gain, bias = cols[t]
            for q in range(n):
                d = 4 * h + q
                dst = hT[:, d, t * P:(t + 1) * P]
                if which == "act":
                    ins = engine.activation(dst, src[:, q, :], ACT.Identity,
                                            scale=gain[:, d:d + 1],
                                            bias=bias[:, d:d + 1] if bias is not None else 0.0)
                elif bias is None:
                    ins = engine.tensor_scalar(dst, src[:, q, :], gain[:, d:d + 1], None, ALU.mult)
                else:
                    ins = engine.tensor_scalar(dst, src[:, q, :], gain[:, d:d + 1], bias[:, d:d + 1],
                                               ALU.mult, ALU.add)
            return ins

        G = T * halves
        with st.block() as block:
            @block.scalar
            def _(act):
                steps = Chain(act, act_step)
                if scaled:
                    for t in range(T):
                        steps.step(nc.scalar.activation(junk[:], tiles[t], ACT.Square, accum_out=ss[:, t:t + 1]))
                    steps.wait()
                    nc.scalar.activation(rms[:], ss[:], ACT.Sqrt, scale=1.0 / width, bias=S.eps6[:, 0:1]).then_inc(rms_ready, 1)
                for g in range(0, G, 2):
                    act.wait_ge(turned, g + 1)
                    empty("act", nc.scalar, g).then_inc(emptied[0], 1)

            @block.vector
            def _(dve):
                steps = Chain(dve, dve_step)
                if scaled:
                    dve.wait_ge(rms_ready, 1)
                    steps.step(nc.vector.reciprocal(rstd[:], rms[:]))

                def make(t):
                    if t >= 2:
                        dve.wait_ge(turned, (t - 1) * halves)
                        if h_dram is not None:
                            dve.wait_ge(stored[t % 2], 16 * (t // 2))
                    if rows is None:
                        nc.vector.tensor_scalar(xn[t % 2][:], tiles[t], rstd[:, t:t + 1], None, ALU.mult).then_inc(xn_ready, 1)
                    else:
                        steps.step(nc.vector.scalar_tensor_tensor(out=xn[t % 2][:], in0=tiles[t], scalar=rstd[:, t:t + 1],
                                                                  in1=rows[t][0], op0=ALU.mult, op1=ALU.mult))
                        nc.vector.tensor_tensor(xn[t % 2][:], xn[t % 2][:], rows[t][1], ALU.add).then_inc(xn_ready, 1)

                if scaled:
                    make(0)
                for t in range(T):
                    if scaled and t + 1 < T:
                        make(t + 1)
                    for g in range(t * halves, (t + 1) * halves):
                        if g % 2:
                            dve.wait_ge(turned, g + 1)
                            empty("dve", nc.vector, g).then_inc(emptied[1], 1)

            @block.tensor
            def _(pe):
                for g in range(G):
                    t, h = g // halves, g % halves
                    if scaled and h == 0:
                        pe.wait_ge(xn_ready, t + 1)
                    if g >= 4:
                        pe.wait_ge(emptied[g % 2], (g - 4) // 2 + 1)
                    src = xn[t % 2] if scaled else tiles[t]
                    for q in range(min(4, kd - 4 * h)):
                        d = 4 * h + q
                        mm = nc.tensor.transpose(tp[g % 4][:, q, :], src[:, d * P:(d + 1) * P], S.ident[:, :])
                    mm.then_inc(turned, 1)

            if h_dram is not None:
                @block.sync
                def _(sp):
                    for t in range(T):
                        sp.wait_ge(xn_ready, t + 1)
                        sp.dma_start(h_dram[t * P:(t + 1) * P, :], xn[t % 2][:]).then_inc(stored[t % 2], 16)
                    for u in range(min(2, T)):
                        sp.wait_ge(stored[u], 16 * ((T - u + 1) // 2))


def residual_norm(nc, name, S, y, x_tiles, gain_row):
    T = len(x_tiles)
    with Stage(nc, name) as st:
        row = st.sb("row", [P, D])
        junk = st.sb("squares", [P, D])
        ss = st.sb("sum_sq", [P, T])
        rms = st.sb("rms", [P, T])
        rstd = st.sb("rstd", [P, T])
        row_loaded, rms_ready = st.sem("row_loaded"), st.sem("rms_ready")
        act_step, dve_step = st.sem("act_step"), st.sem("dve_step")
        with st.block() as block:
            @block.sync
            def _(sp):
                sp.dma_start(row[:], gain_row.partition_broadcast(P)).then_inc(row_loaded, 16)

            @block.scalar
            def _(act):
                steps = Chain(act, act_step)
                for t in range(T):
                    steps.step(nc.scalar.activation(junk[:], y[:, t, :], ACT.Square, accum_out=ss[:, t:t + 1]))
                steps.wait()
                nc.scalar.activation(rms[:], ss[:], ACT.Sqrt, scale=1.0 / D, bias=S.eps6[:, 0:1]).then_inc(rms_ready, 1)

            @block.vector
            def _(dve):
                steps = Chain(dve, dve_step)
                dve.wait_ge(rms_ready, 1)
                steps.step(nc.vector.reciprocal(rstd[:], rms[:]))
                dve.wait_ge(row_loaded, 16)
                for t in range(T):
                    steps.mark(nc.vector.scalar_tensor_tensor(out=y[:, t, :], in0=y[:, t, :], scalar=rstd[:, t:t + 1],
                                                              in1=row[:], op0=ALU.mult, op1=ALU.mult))
                steps.wait()
                for t in range(T):
                    steps.mark(nc.vector.tensor_tensor(x_tiles[t], x_tiles[t], y[:, t, :], ALU.add))
                steps.wait()


class Shared:
    pass


def constants():
    i = np.arange(P)
    f = np.float32
    out = {"ident": np.eye(P, dtype=f), "ones": np.ones((P, P), f)}
    out["eps"] = np.tile(np.array([[1e-6, 1e-5, 64e-5, 1e-12]], f), (P, 1))
    return out


HD = 64


def attention(nc, name, S, qT, kT, v, out, heads, dh, scale, back, group=1, slope0=None, rel=None, extra=None,
              causal=None, sinks=None):
    W = 4 * P
    with Stage(nc, name) as st:
        q = [st.sb(f"q{u}", [dh, SEQ]) for u in range(2)]
        k = [st.sb(f"k{u}", [dh, SEQ]) for u in range(2)]
        vv = [st.sb(f"v{u}", [P, NT, HD]) for u in range(2)]
        o = [st.sb(f"o{u}", [P, NT, HD]) for u in range(2)]
        sink = [st.sb(f"sink{u}", [P, 1]) for u in range(2)]
        relt, extrat, bias = st.sb("rel", [P, W]), st.sb("extra", [P, W]), st.sb("bias", [P, W])
        slope = st.sb("slope", [P, 1])
        logits = [st.sb(f"logits{b}", [P, W]) for b in range(2)]
        probs = [st.sb(f"probs{b}", [P, W]) for b in range(2)]
        probsT = [st.sb(f"probsT{b}", [P, W]) for b in range(2)]
        top = [st.sb(f"top{b}", [P, 1]) for b in range(2)]
        negtop = [st.sb(f"negtop{b}", [P, 1]) for b in range(2)]
        den = [st.sb(f"den{b}", [P, 1]) for b in range(2)]
        sinkexp = [st.sb(f"sinkexp{b}", [P, 1]) for b in range(2)]
        rden = [st.sb(f"rden{b}", [P, 1]) for b in range(2)]
        ps_s = [st.ps(f"ps_s{b}", [P, W]) for b in range(2)]
        ps_t = [st.ps(f"ps_t{b}", [P, W]) for b in range(2)]
        ps_o = [st.ps(f"ps_o{b}", [P, W]) for b in range(2)]
        const_loaded = st.sem("const_loaded")
        head_loaded = [st.sem(f"head_loaded{u}") for u in range(2)]
        scores_ready, max_ready, probs_ready = st.sem("scores_ready"), st.sem("max_ready"), st.sem("probs_ready")
        turned, turned_copied = st.sem("turned"), st.sem("turned_copied")
        out_ready, out_scaled = st.sem("out_ready"), st.sem("out_scaled")
        stored = [st.sem(f"stored{u}") for u in range(2)]
        dve_step, unit_begun = st.sem("dve_step"), st.sem("unit_begun")
        loads = 4 if sinks is not None else 3
        AHEAD = 2

        def k0(b):
            return max(0, b - back)

        with st.block() as block:
            @block.sync
            def _(sp):
                if causal is not None:
                    sp.dma_start(bias[:], causal).then_inc(const_loaded, 16)
                else:
                    sp.dma_start(relt[:], rel).then_inc(const_loaded, 16)
                    sp.dma_start(extrat[:], extra).then_inc(const_loaded, 16)
                def load(h, u):
                    hk = h // group if group > 1 else h
                    sp.dma_start(q[u][:], qT[bass.ds(h, 1), :, :].rearrange("a d t -> (a d) t")).then_inc(head_loaded[u], 16)
                    sp.dma_start(k[u][:], kT[bass.ds(hk, 1), :, :].rearrange("a d t -> (a d) t")).then_inc(head_loaded[u], 16)
                    sp.dma_start(vv[u][:], v.rearrange("(t p) c -> p t c", p=P)[:, :, bass.ds(hk * HD, HD)]).then_inc(head_loaded[u], 16)
                    if sinks is not None:
                        sp.dma_start(sink[u][:], sinks[bass.ds(h, 1)].partition_broadcast(P)).then_inc(head_loaded[u], 16)

                def store(h, u):
                    sp.wait_ge(out_scaled, h * NT + NT + AHEAD)
                    sp.dma_start(out.rearrange("(t p) c -> p t c", p=P)[:, :, bass.ds(h * HD, HD)], o[u][:]).then_inc(stored[u], 16)

                load(0, 0)
                load(1, 1)
                with sp.Fori(0, heads // 2 - 1) as i:
                    for u in range(2):
                        store(2 * i + u, u)
                        sp.wait_ge(stored[u], 16 * i + 16)
                        load(2 * i + 2 + u, u)
                for u in range(2):
                    store(heads - 2 + u, u)
                    sp.wait_ge(stored[u], 16 * (heads // 2))

            @block.tensor
            def _(pe):
                pe.sem_inc(scores_ready, AHEAD)
                pe.sem_inc(turned, AHEAD)
                pe.sem_inc(out_ready, AHEAD)

                def scores(n, u, b):
                    pe.wait_ge(max_ready, n - 1 + AHEAD)
                    w = (b + 1 - k0(b)) * P
                    nc.tensor.matmul(ps_s[b % 2][:, 0:w], q[u][:, b * P:(b + 1) * P], k[u][:, k0(b) * P:(b + 1) * P],
                                     start=True, stop=True).then_inc(scores_ready, 1)

                def turn(n, u, b):
                    pe.wait_ge(probs_ready, n + 1 + AHEAD)
                    pe.wait_ge(turned_copied, n - 1 + AHEAD)
                    for j in range(b + 1 - k0(b)):
                        mm = nc.tensor.transpose(ps_t[b % 2][:, j * P:(j + 1) * P], probs[b % 2][:, j * P:(j + 1) * P], S.ident[:, :])
                    mm.then_inc(turned, 1)

                def weigh(n, u, b):
                    pe.wait_ge(turned_copied, n + 1 + AHEAD)
                    pe.wait_ge(out_scaled, n - 1 + AHEAD)
                    m = b + 1 - k0(b)
                    for j in range(m):
                        mm = nc.tensor.matmul(ps_o[b % 2][:, 0:HD], probsT[b % 2][:, j * P:(j + 1) * P], vv[u][:, k0(b) + j, :],
                                              start=(j == 0), stop=(j == m - 1))
                    mm.then_inc(out_ready, 1)

                with pe.Fori(0, heads // 2) as i:
                    for u in range(2):
                        n = (2 * i + u) * NT
                        pe.wait_ge(head_loaded[u], 16 * loads * i + 16 * loads)
                        scores(n, u, 0)
                        for b in range(NT):
                            if b + 1 < NT:
                                scores(n + b + 1, u, b + 1)
                            turn(n + b, u, b)
                            weigh(n + b, u, b)

            @block.scalar
            def _(act):
                act.sem_inc(probs_ready, AHEAD)
                with act.Fori(0, heads // 2) as i:
                    for u in range(2):
                        for b in range(NT):
                            n = (2 * i + u) * NT + b
                            w = (b + 1 - k0(b)) * P
                            act.wait_ge(max_ready, n + 1 + AHEAD)
                            act.wait_ge(turned, n - 1 + AHEAD)
                            if sinks is not None:
                                act.activation(sinkexp[b % 2][:], sink[u][:], ACT.Exp, bias=negtop[b % 2][:])
                            act.activation(probs[b % 2][:, 0:w], logits[b % 2][:, 0:w], ACT.Exp, bias=negtop[b % 2][:],
                                           accum_out=den[b % 2][:]).then_inc(probs_ready, 1)

            @block.vector
            def _(dve):
                dve.sem_inc(max_ready, AHEAD)
                dve.sem_inc(turned_copied, AHEAD)
                dve.sem_inc(out_scaled, AHEAD)
                dve.wait_ge(const_loaded, 16 if causal is not None else 32)
                per = NT * (4 if sinks is not None else 2) + (2 if causal is None else 0)
                if causal is None:
                    nc.vector.memset(slope[:], slope0).then_inc(dve_step, 1)
                start = 1 if causal is None else 0
                if start:
                    dve.wait_ge(dve_step, 1)

                def biggest(n, u, b, steps):
                    w = (b + 1 - k0(b)) * P
                    dve.wait_ge(scores_ready, n + 1 + AHEAD)
                    dve.wait_ge(probs_ready, n - 1 + AHEAD)
                    dve.sem_inc(unit_begun, 1)
                    steps.step(nc.vector.tensor_tensor_reduce(out=logits[b % 2][:, 0:w], in0=ps_s[b % 2][:, 0:w], in1=bias[:, W - w:W],
                                                              scale=scale, scalar=-3e38, op0=ALU.add, op1=ALU.max,
                                                              accum_out=top[b % 2][:]))
                    if sinks is not None:
                        steps.step(nc.vector.tensor_tensor(top[b % 2][:], top[b % 2][:], sink[u][:], ALU.max))
                    nc.vector.tensor_scalar(negtop[b % 2][:], top[b % 2][:], -1.0, None, ALU.mult).then_inc(max_ready, 1)

                def finish(n, u, b, steps):
                    w = (b + 1 - k0(b)) * P
                    dve.wait_ge(turned, n + 1 + AHEAD)
                    dve.wait_ge(out_ready, n - 1 + AHEAD)
                    nc.vector.tensor_copy(probsT[b % 2][:, 0:w], ps_t[b % 2][:, 0:w]).then_inc(turned_copied, 1)
                    if sinks is not None:
                        steps.step(nc.vector.tensor_tensor(den[b % 2][:], den[b % 2][:], sinkexp[b % 2][:], ALU.add))
                    steps.step(nc.vector.reciprocal(rden[b % 2][:], den[b % 2][:]))
                    dve.wait_ge(out_ready, n + 1 + AHEAD)
                    nc.vector.tensor_scalar(o[u][:, b, :], ps_o[b % 2][:, 0:HD], rden[b % 2][:, 0:1], None, ALU.mult).then_inc(out_scaled, 1)

                with dve.Fori(0, heads // 2) as i:
                    for u in range(2):
                        n = (2 * i + u) * NT
                        steps = Chain(dve, dve_step, (2 * i + u) * per + start)
                        dve.wait_ge(head_loaded[u], 16 * loads * i + 16 * loads)
                        if causal is None:
                            steps.step(nc.vector.scalar_tensor_tensor(out=bias[:], in0=relt[:], scalar=slope[:, 0:1], in1=extrat[:],
                                                                      op0=ALU.mult, op1=ALU.add))
                            steps.step(nc.vector.tensor_scalar(slope[:], slope[:], 0.5, None, ALU.mult))
                        biggest(n, u, 0, steps)
                        for b in range(NT):
                            if b + 1 < NT:
                                biggest(n + b + 1, u, b + 1, steps)
                            finish(n + b, u, b, steps)
                        assert steps.n == per


A_PATTERNS = ((128, 1), (512, 4), (2048, 16))
BIG = 1e30


def attention_tables():
    delta = (np.arange(P)[:, None] + 3 * P - np.arange(4 * P)[None, :]).astype(np.int64)
    count = sum(((delta >= 0) & (delta <= w) & (delta % d == 0)).astype(np.int64) for w, d in A_PATTERNS)
    seen = count > 0
    swa = (delta >= 0) & (delta <= 127)
    f = np.float32
    return {
        "dil_rel": np.where(seen, delta, BIG).astype(f),
        "dil_extra": np.where(seen, np.log(np.maximum(count, 1)) * 8.0, 0.0).astype(f),
        "swa_rel": np.where(swa, delta, BIG).astype(f),
        "zero_extra": np.zeros((P, 4 * P), f),
        "causal": np.where(delta >= 0, 0.0, -BIG).astype(f),
    }

B_HEADS, B_DK, B_DV, B_CHUNK = 4, 64, 128, 64


def gla_decay(nc, name, S, z, log_a):
    width = z.shape[1] * z.shape[2]
    with Stage(nc, name) as st:
        t1, t2 = st.sb("t1", [P, width]), st.sb("t2", [P, width])
        act_step, dve_step, stored = st.sem("act_step"), st.sem("dve_step"), st.sem("stored")
        zf = z[:].rearrange("p t c -> p (t c)")
        with st.block() as block:
            @block.scalar
            def _(act):
                steps = Chain(act, act_step)
                steps.step(nc.scalar.activation(t1[:], zf, ACT.Abs))
                steps.step(nc.scalar.activation(t1[:], t1[:], ACT.Exp, scale=-1.0))
                steps.step(nc.scalar.activation(t1[:], t1[:], ACT.Ln, bias=S.ones[:, 0:1]))

            @block.vector
            def _(dve):
                steps = Chain(dve, dve_step)
                steps.step(nc.vector.tensor_scalar(t2[:], zf, 0.0, 1.0 / 16, ALU.min, ALU.mult))
                dve.wait_ge(act_step, 3)
                steps.step(nc.vector.scalar_tensor_tensor(out=t1[:], in0=t1[:], scalar=-1.0 / 16, in1=t2[:], op0=ALU.mult, op1=ALU.add))

            @block.sync
            def _(sp):
                sp.wait_ge(dve_step, 2)
                sp.dma_start(log_a.rearrange("(t p) c -> p t c", p=P), t1[:].rearrange("p (t c) -> p t c", t=NT)).then_inc(stored, 16)
                sp.wait_ge(stored, 16)


def gla(nc, name, S, qT, kT, v, r, log_a, tri, norm_row, out, col0):
    NC = SEQ // B_CHUNK
    with Stage(nc, name) as st:
        trit, normt = st.sb("tri", [P, P]), st.sb("norm", [P, B_DV])
        q, k = st.sb("q", [B_DK, SEQ]), st.sb("k", [B_DK, SEQ])
        vt, rt = st.sb("v", [P, NT, B_DV]), st.sb("r", [P, NT, B_DV])
        la = st.sb("log_a", [P, NT, B_DK])
        cum, mid, last = st.sb("cum", [B_DK, SEQ]), st.sb("mid", [B_DK, SEQ]), st.sb("last", [B_DK, SEQ])
        e_q, e_k, e_b, e_l = (st.sb(f"e_{x}", [B_DK, SEQ]) for x in "qkbl")
        decay = st.sb("decay", [B_DK, NC])
        att, klT = st.sb("att", [P, NT, P]), st.sb("klT", [P, NT, B_DK])
        state = st.sb("state", [B_DK, NC, B_DV])
        o, gate = st.sb("o", [P, NT, B_DV]), st.sb("gate", [P, NT, B_DV])
        junk, ss, rms, rstd = st.sb("squares", [P, B_DV]), st.sb("sum_sq", [P, NT]), st.sb("rms", [P, NT]), st.sb("rstd", [P, NT])
        p_cum = st.ps("p_cum", [B_DK, SEQ])
        p_att = st.ps("p_att", [P, NT, P])
        p_kl = st.ps("p_kl", [P, NT, B_DK])
        p_ds = [st.ps(f"p_ds{b}", [B_DK, 4, B_DV]) for b in range(2)]
        p_o = st.ps("p_o", [P, NT, B_DV])
        const_loaded, loaded, stored = st.sem("const_loaded"), st.sem("loaded"), st.sem("stored")
        cum_ready, turned_ready, states_fed, out_ready = st.sem("cum_ready"), st.sem("turned_ready"), st.sem("states_fed"), st.sem("out_ready")
        act_step, dve_step, pe_passed = st.sem("act_step"), st.sem("dve_step"), st.sem("pe_passed")
        A, V = 12, 20

        def chunks(x):
            return x[:].rearrange("d (n c) -> d n c", c=B_CHUNK)

        with st.block() as block:
            @block.sync
            def _(sp):
                sp.dma_start(trit[:], tri).then_inc(const_loaded, 16)
                sp.dma_start(normt[:], norm_row.partition_broadcast(P)).then_inc(const_loaded, 16)

                def load(h):
                    sp.dma_start(q[:], qT[bass.ds(h, 1), :, :].rearrange("a d t -> (a d) t")).then_inc(loaded, 16)
                    sp.dma_start(k[:], kT[bass.ds(h, 1), :, :].rearrange("a d t -> (a d) t")).then_inc(loaded, 16)
                    sp.dma_start(vt[:], v.rearrange("(t p) c -> p t c", p=P)[:, :, bass.ds(h * B_DV, B_DV)]).then_inc(loaded, 16)
                    sp.dma_start(rt[:], r.rearrange("(t p) c -> p t c", p=P)[:, :, bass.ds(h * B_DV, B_DV)]).then_inc(loaded, 16)
                    sp.dma_start(la[:], log_a.rearrange("(t p) c -> p t c", p=P)[:, :, bass.ds(h * B_DK, B_DK)]).then_inc(loaded, 16)

                load(0)
                with sp.Fori(0, B_HEADS) as h:
                    sp.wait_ge(dve_step, h * V + V)
                    sp.dma_start(out.rearrange("(t p) c -> p t c", p=P)[:, :, bass.ds(h * B_DV + col0, B_DV)], o[:]).then_inc(stored, 16)
                    sp.wait_ge(stored, 16 * h + 16)
                    load((h + 1) % B_HEADS)
                sp.wait_ge(loaded, 16 * 5 * (B_HEADS + 1))

            @block.tensor
            def _(pe):
                pe.wait_ge(const_loaded, 32)
                with pe.Fori(0, B_HEADS) as h:
                    pe.wait_ge(loaded, h * 80 + 80)
                    for t in range(NT):
                        mm = nc.tensor.matmul(p_cum[:, t * P:(t + 1) * P], la[:, t, :], trit[:], start=True, stop=True)
                    mm.then_inc(cum_ready, 1)
                    pe.wait_ge(dve_step, h * V + 7)
                    for t in range(NT):
                        c = slice(t * P, (t + 1) * P)
                        nc.tensor.matmul(p_att[:, t, :], e_k[:, c], e_q[:, c], start=True, stop=True)
                        mm = nc.tensor.transpose(p_kl[:, t, :], e_l[:, c], S.ident[0:B_DK, 0:B_DK])
                    mm.then_inc(turned_ready, 1)
                    pe.wait_ge(act_step, h * A + 6)
                    pe.sem_inc(pe_passed, 1)
                    for n in range(NC):
                        s = slice(B_CHUNK * (n % 2), B_CHUNK * (n % 2) + B_CHUNK)
                        mm = nc.tensor.matmul(p_ds[n % 2][:, n // 2, :], klT[s, n // 2, :], vt[s, n // 2, :], start=True, stop=True)
                    mm.then_inc(states_fed, 1)
                    pe.wait_ge(dve_step, h * V + 16)
                    for t in range(NT):
                        nc.tensor.matmul(p_o[:, t, :], att[:, t, :], vt[:, t, :], start=True, stop=False, skip_group_check=True)
                        for n in (2 * t, 2 * t + 1):
                            s = slice(B_CHUNK * (n % 2), B_CHUNK * (n % 2) + B_CHUNK)
                            mm = nc.tensor.matmul(p_o[s, t, :], e_b[:, n * B_CHUNK:(n + 1) * B_CHUNK], state[:, n, :],
                                                  start=False, stop=(n % 2 == 1), skip_group_check=True)
                    mm.then_inc(out_ready, 1)

            @block.scalar
            def _(act):
                with act.Fori(0, B_HEADS) as h:
                    steps = Chain(act, act_step, h * A)
                    act.wait_ge(dve_step, h * V + 3)
                    steps.mark(nc.scalar.activation(e_q[:], mid[:], ACT.Exp))
                    steps.mark(nc.scalar.activation(e_k[:], mid[:], ACT.Exp, scale=-1.0))
                    steps.mark(nc.scalar.activation(e_b[:], cum[:], ACT.Exp))
                    steps.mark(nc.scalar.activation(e_l[:], last[:], ACT.Exp))
                    steps.mark(nc.scalar.activation(decay[:], chunks(cum)[:, :, B_CHUNK - 1], ACT.Exp))
                    act.wait_ge(turned_ready, h + 1)
                    steps.step(nc.scalar.activation(klT[:], p_kl[:], ACT.Copy))
                    act.wait_ge(loaded, h * 80 + 80)
                    steps.mark(nc.scalar.activation(gate[:], rt[:], ACT.Silu))
                    act.wait_ge(out_ready, h + 1)
                    for t in range(NT):
                        steps.step(nc.scalar.activation(junk[:], p_o[:, t, :], ACT.Square, accum_out=ss[:, t:t + 1]))
                    steps.step(nc.scalar.activation(rms[:], ss[:], ACT.Sqrt, scale=1.0 / B_DV, bias=S.eps6[:, 0:1]))
                    assert steps.n == A

            @block.vector
            def _(dve):
                dve.wait_ge(const_loaded, 32)
                with dve.Fori(0, B_HEADS) as h:
                    steps = Chain(dve, dve_step, h * V)
                    dve.wait_ge(cum_ready, h + 1)
                    steps.step(nc.vector.tensor_copy(cum[:], p_cum[:]))
                    c3 = chunks(cum)
                    steps.mark(nc.vector.tensor_tensor(chunks(mid), c3, c3[:, :, B_CHUNK // 2 - 1:B_CHUNK // 2].broadcast_to([B_DK, NC, B_CHUNK]), ALU.subtract))
                    steps.step(nc.vector.tensor_tensor(chunks(last), c3[:, :, B_CHUNK - 1:B_CHUNK].broadcast_to([B_DK, NC, B_CHUNK]), c3, ALU.subtract))
                    dve.wait_ge(act_step, h * A + 5)
                    for e, x, scale in ((e_q, q, B_DK ** -0.5), (e_k, k, 1.0), (e_l, k, 1.0), (e_b, q, B_DK ** -0.5)):
                        steps.mark(nc.vector.scalar_tensor_tensor(out=e[:], in0=e[:], scalar=scale, in1=x[:], op0=ALU.mult, op1=ALU.mult))
                    steps.wait()
                    dve.wait_ge(turned_ready, h + 1)
                    steps.mark(nc.vector.tensor_tensor(att[:], p_att[:], trit[:].rearrange("s (a c) -> s a c", a=1).broadcast_to([P, NT, P]), ALU.mult))
                    steps.step(nc.vector.memset(state[:, 0, :], 0.0))
                    dve.wait_ge(states_fed, h + 1)
                    for n in range(NC - 1):
                        steps.step(nc.vector.scalar_tensor_tensor(out=state[:, n + 1, :], in0=state[:, n, :], scalar=decay[:, n:n + 1],
                                                                  in1=p_ds[n % 2][:, n // 2, :], op0=ALU.mult, op1=ALU.add))
                    dve.wait_ge(act_step, h * A + 12)
                    steps.step(nc.vector.reciprocal(rstd[:], rms[:]))
                    for t in range(NT - 1):
                        nc.vector.scalar_tensor_tensor(out=o[:, t, :], in0=p_o[:, t, :], scalar=rstd[:, t:t + 1], in1=normt[:], op0=ALU.mult, op1=ALU.mult)
                    t = NT - 1
                    steps.step(nc.vector.scalar_tensor_tensor(out=o[:, t, :], in0=p_o[:, t, :], scalar=rstd[:, t:t + 1], in1=normt[:], op0=ALU.mult, op1=ALU.mult))
                    steps.mark(nc.vector.tensor_tensor(o[:], o[:], gate[:], ALU.mult))
                    while steps.n < V:
                        steps.mark(nc.vector.nop())
                    assert steps.n == V, steps.n


def gla_tables():
    i = np.arange(P)
    tri = (i[:, None] <= i[None, :]) & (i[:, None] // B_CHUNK == i[None, :] // B_CHUNK)
    return {"gla_tri": tri.astype(np.float32)}


D_FF = 2816
FT = D_FF // P


def swiglu_up(nc, name, hT, w_gate_up, guT):
    with Stage(nc, name) as st:
        w = [st.sb(f"w{u}", [P, 2, KD, P]) for u in range(2)]
        sg = [st.sb(f"gate{u}", [P, SEQ]) for u in range(2)]
        p_g = [st.ps(f"p_g{u}", [P, SEQ]) for u in range(2)]
        p_u = [st.ps(f"p_u{u}", [P, SEQ]) for u in range(2)]
        loaded = [st.sem(f"loaded{u}") for u in range(2)]
        gate_ready, up_ready, gated, multiplied = st.sem("gate_ready"), st.sem("up_ready"), st.sem("gated"), st.sem("multiplied")
        AHEAD = 2
        with st.block() as block:
            @block.sync
            def _(sp):
                for u in range(2):
                    sp.dma_start(w[u][:], w_gate_up[u]).then_inc(loaded[u], 16)
                with sp.Fori(0, FT // 2 - 1) as i:
                    for u in range(2):
                        sp.wait_ge(up_ready, 2 * i + u + 1 + AHEAD)
                        sp.dma_start(w[u][:], w_gate_up[bass.ds(2 * i + 2 + u, 1)].rearrange("a p g k f -> (a p) g k f")).then_inc(loaded[u], 16)

            @block.tensor
            def _(pe):
                pe.sem_inc(up_ready, AHEAD)
                with pe.Fori(0, FT // 2) as i:
                    for u in range(2):
                        s = 2 * i + u
                        pe.wait_ge(loaded[u], 16 * i + 16)
                        pe.wait_ge(multiplied, s - 1 + AHEAD)
                        for g, (p, ready) in enumerate(((p_g[u], gate_ready), (p_u[u], up_ready))):
                            for k in range(KD):
                                mm = nc.tensor.matmul(p[:], w[u][:, g, k, :], hT[:, k, 0:SEQ], start=(k == 0), stop=(k == KD - 1))
                            mm.then_inc(ready, 1)

            @block.scalar
            def _(act):
                with act.Fori(0, FT // 2) as i:
                    for u in range(2):
                        s = 2 * i + u
                        act.wait_ge(gate_ready, s + 1)
                        act.wait_ge(multiplied, s - 1 + AHEAD)
                        nc.scalar.activation(sg[u][:], p_g[u][:], ACT.Silu).then_inc(gated, 1)

            @block.vector
            def _(dve):
                dve.sem_inc(multiplied, AHEAD)
                with dve.Fori(0, FT // 2) as i:
                    for u in range(2):
                        s = 2 * i + u
                        dve.wait_ge(gated, s + 1)
                        dve.wait_ge(up_ready, s + 1 + AHEAD)
                        nc.vector.tensor_tensor(guT[:, bass.ds(s, 1), :].rearrange("p a t -> p (a t)"), sg[u][:], p_u[u][:], ALU.mult).then_inc(multiplied, 1)


D_HEADS, D_NOPE, D_ROPE = 8, 64, 32


def rope_tables():
    half = D_ROPE // 2
    freqs = (np.float32(10000.0) ** (-np.arange(half, dtype=np.float32) / np.float32(half))).astype(np.float32)
    ang = np.arange(SEQ, dtype=np.float32)[:, None] * freqs[None, :]
    def lay(x):
        return np.ascontiguousarray(x.astype(np.float32).reshape(NT, P, half).transpose(1, 0, 2))
    return {"cos": lay(np.cos(ang)), "sin": lay(np.sin(ang))}


def mla_heads(nc, name, S, q, kv, k_rope, cos, sin, qT_d, kT_d, v_d):
    half = D_ROPE // 2
    HQ = D_NOPE + D_ROPE
    with Stage(nc, name) as st:
        ct, sn = st.sb("cos", [P, NT, half]), st.sb("sin", [P, NT, half])
        tmp = [st.sb(f"tmp{n}", [P, NT, D_HEADS, half]) for n in range(4)]
        kp = st.sb("k_pe", [P, NT, D_ROPE])
        kk = st.sb("keys", [P, NT, D_HEADS, HQ])
        outT = [st.sb(f"outT{b}", [HQ, SEQ]) for b in range(4)]
        tp = [st.ps(f"tp{b}", [HQ, SEQ]) for b in range(4)]
        loaded, dve_step, act_step, pool_step = st.sem("loaded"), st.sem("dve_step"), st.sem("act_step"), st.sem("pool_step")
        turned = st.sem("turned")
        emptied = [st.sem("act_emptied"), st.sem("dve_emptied")]
        stored, v_stored = [st.sem(f"stored{b}") for b in range(4)], st.sem("v_stored")
        q4 = q[:].rearrange("p t (h c) -> p t h c", h=D_HEADS)
        kv4 = kv[:].rearrange("p t (h c) -> p t h c", h=D_HEADS)
        QS = 4 * 6
        G = 2 * D_HEADS
        ROTATED = QS + 6 + NT

        with st.block() as block:
            @block.sync
            def _(sp):
                sp.dma_start(ct[:], cos).then_inc(loaded, 16)
                sp.dma_start(sn[:], sin).then_inc(loaded, 16)
                for t in range(NT):
                    sp.dma_start(v_d[t * P:(t + 1) * P, :].rearrange("p (h c) -> p h c", h=D_HEADS), kv4[:, t, :, D_NOPE:2 * D_NOPE]).then_inc(v_stored, 16)
                for g in range(G):
                    sp.wait_ge(emptied[g % 2], g // 2 + 1)
                    dst = qT_d if g < D_HEADS else kT_d
                    sp.dma_start(dst[g % D_HEADS], outT[g % 4][:]).then_inc(stored[g % 4], 16)
                for b in range(4):
                    sp.wait_ge(stored[b], 16 * (G // 4))
                sp.wait_ge(v_stored, 16 * NT)

            @block.gpsimd
            def _(pool):
                for t in range(NT):
                    nc.gpsimd.tensor_copy(kk[:, t, :, 0:D_NOPE], kv4[:, t, :, 0:D_NOPE]).then_inc(pool_step, 1)

            def empty(which, engine, eng, g):
                eng.wait_ge(turned, g + 1)
                if g >= 4:
                    eng.wait_ge(stored[g % 4], 16 * (g // 4))
                if which == "act":
                    engine.activation(outT[g % 4][:], tp[g % 4][:], ACT.Copy).then_inc(emptied[0], 1)
                else:
                    engine.tensor_copy(outT[g % 4][:], tp[g % 4][:]).then_inc(emptied[1], 1)

            @block.vector
            def _(dve):
                steps = Chain(dve, dve_step)
                dve.wait_ge(loaded, 32)

                for t in range(NT):
                    x1, x2 = q4[:, t, :, D_NOPE:D_NOPE + half], q4[:, t, :, D_NOPE + half:HQ]
                    c = ct[:, t:t + 1, :].broadcast_to([P, D_HEADS, half])
                    s = sn[:, t:t + 1, :].broadcast_to([P, D_HEADS, half])
                    for n, (x, y) in enumerate(((x1, c), (x2, s), (x2, c), (x1, s))):
                        steps.mark(nc.vector.tensor_tensor(tmp[n][:, t], x, y, ALU.mult))
                    steps.wait()
                    steps.mark(nc.vector.tensor_tensor(x1, tmp[0][:, t], tmp[1][:, t], ALU.subtract))
                    steps.mark(nc.vector.tensor_tensor(x2, tmp[2][:, t], tmp[3][:, t], ALU.add))
                steps.wait()
                x1, x2 = k_rope[:, :, 0:half], k_rope[:, :, half:D_ROPE]
                for n, (x, y) in enumerate(((x1, ct), (x2, sn), (x2, ct), (x1, sn))):
                    steps.mark(nc.vector.tensor_tensor(tmp[n][:, :, 0, :], x, y[:], ALU.mult))
                steps.wait()
                steps.mark(nc.vector.tensor_tensor(kp[:, :, 0:half], tmp[0][:, :, 0, :], tmp[1][:, :, 0, :], ALU.subtract))
                steps.step(nc.vector.tensor_tensor(kp[:, :, half:D_ROPE], tmp[2][:, :, 0, :], tmp[3][:, :, 0, :], ALU.add))
                for t in range(NT):
                    steps.mark(nc.vector.tensor_copy(kk[:, t, :, D_NOPE:HQ], kp[:, t:t + 1, :].broadcast_to([P, D_HEADS, D_ROPE])))
                assert steps.n == ROTATED
                for g in range(1, G, 2):
                    empty("dve", nc.vector, dve, g)

            @block.scalar
            def _(act):
                for g in range(0, G, 2):
                    empty("act", nc.scalar, act, g)

            @block.tensor
            def _(pe):
                pe.wait_ge(dve_step, ROTATED)
                pe.wait_ge(pool_step, NT)
                for g in range(G):
                    if g >= 4:
                        pe.wait_ge(emptied[g % 2], (g - 4) // 2 + 1)
                    src = q4 if g < D_HEADS else kk
                    for t in range(NT):
                        mm = nc.tensor.transpose(tp[g % 4][:, t * P:(t + 1) * P], src[:, t, g % D_HEADS, :], S.ident[:, :])
                    mm.then_inc(turned, 1)


def load_all(nc, name, pairs):
    with Stage(nc, name) as st:
        loaded = st.sem("loaded")
        with st.block() as block:
            @block.sync
            def _(sp):
                for dst, src in pairs:
                    sp.dma_start(dst, src).then_inc(loaded, 16)
                sp.wait_ge(loaded, 16 * len(pairs))


def gated_ffn(nc, name, S, x_tiles, hT, gcol, post_row, w_gate_up, w_down):
    norm_transpose(nc, name + "n", S, x_tiles, hT, cols=[(gcol, None)] * NT)
    with ExitStack() as mem:
        guT = mem.enter_context(nc.sbuf_tensor(name + "_guT", [P, FT, SEQ], F32))
        y = mem.enter_context(nc.sbuf_tensor(name + "_y", [P, NT, D], F32))
        swiglu_up(nc, name + "u", hT, w_gate_up, guT)
        W = 256
        project(nc, name + "d", guT, SEQ,
                [dict(w=w_down[:, c * W:(c + 1) * W], mode="T", epi=copy_to(lambda j, n0, c=c: y[:, j, c * W:(c + 1) * W]))
                 for c in range(D // W)])
        residual_norm(nc, name + "r", S, y, x_tiles, post_row)


def mix_out(nc, name, S, x_tiles, hT, mixed, w_out, post_row):
    with ExitStack() as mem:
        m = mem.enter_context(nc.sbuf_tensor(name + "_m", [P, NT, D], F32))
        y = mem.enter_context(nc.sbuf_tensor(name + "_y", [P, NT, D], F32))
        load_all(nc, name + "l", [(m[:], mixed.rearrange("(t p) d -> p t d", p=P))])
        norm_transpose(nc, name + "t", S, [m[:, t, :] for t in range(NT)], hT, scaled=False)
        project(nc, name + "p", hT, SEQ,
                [dict(w=w_out[:, c * BANK:(c + 1) * BANK], mode="T", epi=copy_to(lambda j, n0, c=c: y[:, j, c * BANK:(c + 1) * BANK]))
                 for c in range(D // BANK)])
        residual_norm(nc, name + "r", S, y, x_tiles, post_row)


def dram(nc, name, shape, dt=F32):
    return nc.dram_tensor(name, shape, dt, kind="Internal").ap()


FIRST_COLS = (("norm_mix_pre", 2 * KD), ("norm_ffn_pre", 2 * KD), ("mla_q_norm", 3), ("mla_kv_norm", 2))


def first_block(nc, S, a, x_tiles, hT):
    c = {}
    at = 0
    for n, w in FIRST_COLS:
        c[n] = S.first_cols[:, at:at + w]
        at += w
    mixed = dram(nc, "mixed0", [SEQ, D])
    norm_transpose(nc, "n0", S, x_tiles, hT, cols=[(c["norm_mix_pre"][:, 0:KD], None)] * NT)
    qk_a, v_a = dram(nc, "qk_a", [2 * 8, HD, SEQ]), dram(nc, "v_a", [SEQ, 512])
    qk_b = dram(nc, "qk_b", [2 * B_HEADS, B_DK, SEQ])
    v_b, r_b, log_a = dram(nc, "v_b", [SEQ, 512]), dram(nc, "r_b", [SEQ, 512]), dram(nc, "log_a", [SEQ, 256])
    w = a["ab_w_in"]
    with ExitStack() as mem:
        def sb(n, shape):
            return mem.enter_context(nc.sbuf_tensor(n, shape, F32))
        qka, qkb = sb("qka", [P, 8, SEQ]), sb("qkb", [P, 4, SEQ])
        vrt = sb("vrt", [P, 3, NT, 512])
        gT = sb("gT", [P, 1, SEQ])
        jobs = [dict(w=w[:, 512 * n:512 * n + 512], mode="F", epi=copy_to(lambda j, n0, n=n: qka[:, 4 * n + j, :])) for n in range(2)]
        jobs += [dict(w=w[:, 1536:2048], mode="F", epi=copy_to(lambda j, n0: qkb[:, j, :]))]
        jobs += [dict(w=w[:, o:o + 512], mode="T", epi=copy_to(lambda j, n0, n=n: vrt[:, n, j, :])) for n, o in enumerate((1024, 2048, 2560))]
        jobs += [dict(w=w[:, 3072:3088], mode="F", epi=copy_to(lambda j, n0: gT[0:16, 0, :]))]
        tok = "(t p) c -> p t c"
        project(nc, "p0", hT, SEQ, jobs, stores=[
            (qk_a.rearrange("(j u) d t -> (u d) j t", u=2), qka[:]),
            (qk_b.rearrange("(j u) d t -> (u d) j t", u=2), qkb[:]),
            (v_a.rearrange(tok, p=P), vrt[:, 0]), (v_b.rearrange(tok, p=P), vrt[:, 1]), (r_b.rearrange(tok, p=P), vrt[:, 2])])
        z = sb("z", [P, NT, 256])
        brow = sb("b_gate_row", [1, 256])
        load_all(nc, "gl", [(brow[:], a["gla_b_gate"].rearrange("(o c) -> o c", o=1))])
        project(nc, "gz", gT, SEQ, [dict(w=a["gla_w_gate_up"], mode="T", bias=brow[:], epi=copy_to(lambda j, n0: z[:, j, :]))], const={"ones": S.ones})
        gla_decay(nc, "gd", S, z, log_a)
    attention(nc, "at0", S, qk_a[0:8], qk_a[8:16], v_a, mixed[:, 0:512], 8, HD, HD ** -0.5, 3,
              slope0=-4.0, rel=a["dil_rel"], extra=a["dil_extra"])
    gla(nc, "gla", S, qk_b[0:4], qk_b[4:8], v_b, r_b, log_a, a["gla_tri"], a["gla_norm"], mixed, 512)
    mix_out(nc, "mo0", S, x_tiles, hT, mixed, a["ab_w_out"], a["norm_mix_post"][0])
    gated_ffn(nc, "f0", S, x_tiles, hT, c["norm_ffn_pre"][:, 0:KD], a["norm_ffn_post"][0], a["ffn_w_gate_up"][0], a["ffn_w_down"][0])
    norm_transpose(nc, "n1", S, x_tiles, hT, cols=[(c["norm_mix_pre"][:, KD:2 * KD], None)] * NT)
    qk_c, v_c = dram(nc, "qk_c", [10, HD, SEQ]), dram(nc, "v_c", [SEQ, 128])
    qT_d, kT_d, v_d = dram(nc, "qT_d", [8, 96, SEQ]), dram(nc, "kT_d", [8, 96, SEQ]), dram(nc, "v_d", [SEQ, 512])
    w = a["cd_w_in"]
    with ExitStack() as mem:
        def sb(n, shape):
            return mem.enter_context(nc.sbuf_tensor(n, shape, F32))
        qkc = sb("qkc", [P, 5, SEQ])
        vq, kvr = sb("vq", [P, NT, 512]), sb("kvr", [P, NT, 288])
        jobs = [dict(w=w[:, 0:512], mode="F", epi=copy_to(lambda j, n0: qkc[:, j, :])),
                dict(w=w[:, 512:640], mode="F", epi=copy_to(lambda j, n0: qkc[:, 4, :])),
                dict(w=w[:, 640:1152], mode="T", epi=copy_to(lambda j, n0: vq[:, j, :])),
                dict(w=w[:, 1152:1440], mode="T", epi=copy_to(lambda j, n0: kvr[:, j, :]))]
        project(nc, "p1", hT, SEQ, jobs, stores=[
            (qk_c.rearrange("(j u) d t -> (u d) j t", u=2), qkc[:]), (v_c.rearrange("(t p) c -> p t c", p=P), vq[:, :, 0:128])])
        cqT, ckvT = sb("cqT", [P, 3, SEQ]), sb("ckvT", [P, 2, SEQ])
        norm_transpose(nc, "nq", S, [vq[:, t, 128:512] for t in range(NT)], cqT, cols=[(c["mla_q_norm"], None)] * NT)
        norm_transpose(nc, "nkv", S, [kvr[:, t, 0:256] for t in range(NT)], ckvT, cols=[(c["mla_kv_norm"], None)] * NT)
        q, kv = sb("q_d", [P, NT, 768]), sb("kv_d", [P, NT, 1024])
        project(nc, "uq", cqT, SEQ, [dict(w=a["mla_w_uq"][:, 384 * n:384 * n + 384], mode="T",
                                          epi=copy_to(lambda j, n0, n=n: q[:, j, 384 * n:384 * n + 384])) for n in range(2)])
        project(nc, "ukv", ckvT, SEQ, [dict(w=a["mla_w_ukv"][:, 512 * n:512 * n + 512], mode="T",
                                            epi=copy_to(lambda j, n0, n=n: kv[:, j, 512 * n:512 * n + 512])) for n in range(2)])
        mla_heads(nc, "mh", S, q, kv, kvr[:, :, 256:288], a["cos"], a["sin"], qT_d, kT_d, v_d)
    attention(nc, "at1", S, qk_c[0:8], qk_c[8:10], v_c, mixed[:, 0:512], 8, HD, HD ** -0.5, 1, group=4,
              slope0=-4.0, rel=a["swa_rel"], extra=a["zero_extra"], sinks=a["swa_sinks"])
    attention(nc, "at2", S, qT_d, kT_d, v_d, mixed[:, 512:1024], 8, 96, 96 ** -0.5, 3, causal=a["causal"])
    mix_out(nc, "mo1", S, x_tiles, hT, mixed, a["cd_w_out"], a["norm_mix_post"][1])
    gated_ffn(nc, "f1", S, x_tiles, hT, c["norm_ffn_pre"][:, KD:2 * KD], a["norm_ffn_post"][1], a["ffn_w_gate_up"][1], a["ffn_w_down"][1])


def columns(v):
    return np.ascontiguousarray(np.asarray(v).reshape(-1, P).T)


def first_layout(inp):
    out = {n: np.ascontiguousarray(inp[n][0]) for n in ("ab_w_in", "ab_w_out", "gla_w_gate_up", "gla_b_gate", "gla_norm", "cd_w_in", "cd_w_out",
                                                        "swa_sinks", "mla_w_uq", "mla_w_ukv")}
    for n in ("norm_mix_post", "norm_ffn_post", "ffn_w_down"):
        out[n] = np.ascontiguousarray(inp[n])
    gu = np.stack([inp["ffn_w_gate"], inp["ffn_w_up"]], 1)
    out["ffn_w_gate_up"] = np.ascontiguousarray(gu.reshape(2, 2, KD, P, FT, P).transpose(0, 4, 3, 1, 2, 5))
    out["x"] = np.ascontiguousarray(inp["x"][0])
    out["first_cols"] = np.concatenate([columns(inp[n]) for n, _ in FIRST_COLS], 1)
    return out


N_MOD = 6
W_GMLP = 2048
GROUPS = 16
E_GROUPS, E_PER, N_EXP, HID = 4, 8, 32, 512


def modulation(nc, name, S, cT, ada_w, bias, mods):
    with ExitStack() as mem:
        sc = mem.enter_context(nc.sbuf_tensor(name + "_silu", [P, KD, 2], F32))
        brow = mem.enter_context(nc.sbuf_tensor(name + "_bias", [1, N_MOD * D], F32))
        out = mem.enter_context(nc.sbuf_tensor(name + "_out", [2, N_MOD * D], F32))
        with Stage(nc, name + "s") as st:
            loaded, done = st.sem("loaded"), st.sem("done")
            with st.block() as block:
                @block.sync
                def _(sp):
                    sp.dma_start(sc[:], cT).then_inc(loaded, 16)
                    sp.dma_start(brow[:], bias.rearrange("(o c) -> o c", o=1)).then_inc(loaded, 16)
                    sp.wait_ge(loaded, 32)

                @block.scalar
                def _(act):
                    act.wait_ge(loaded, 32)
                    nc.scalar.activation(sc[:], sc[:], ACT.Silu).then_inc(done, 1)
                    act.wait_ge(done, 1)
        project(nc, name + "p", sc, 2,
                [dict(w=ada_w[:, c * BANK:(c + 1) * BANK], mode="T", bias=brow[0:1, c * BANK:(c + 1) * BANK],
                      epi=copy_to(lambda j, n0, c=c: out[:, c * BANK:(c + 1) * BANK])) for c in range(N_MOD * D // BANK)],
                const={"ones": S.ones}, stores=[(mods, out[:])])


def modulation_columns(nc, name, S, mods, gcol, out):
    with Stage(nc, name) as st:
        rows = [st.sb(f"rows{w}", [N_MOD * KD, P]) for w in range(2)]
        tp = [st.ps(f"tp{w}", [P, N_MOD * KD]) for w in range(2)]
        loaded, turned, dve_step = st.sem("loaded"), st.sem("turned"), st.sem("dve_step")
        with st.block() as block:
            @block.sync
            def _(sp):
                for w in range(2):
                    sp.dma_start(rows[w][:], mods[w].rearrange("(k p) -> k p", p=P)).then_inc(loaded, 16)

            @block.tensor
            def _(pe):
                pe.wait_ge(loaded, 32)
                for w in range(2):
                    nc.tensor.transpose(tp[w][:], rows[w][:], S.ident[0:N_MOD * KD, 0:N_MOD * KD]).then_inc(turned, 1)

            @block.vector
            def _(dve):
                steps = Chain(dve, dve_step)
                for w in range(2):
                    dve.wait_ge(turned, w + 1)
                    gain, bias = out[w]
                    steps.mark(nc.vector.scalar_tensor_tensor(out=gain, in0=tp[w][:, KD:2 * KD], scalar=1.0, in1=gcol, op0=ALU.add, op1=ALU.mult))
                    steps.mark(nc.vector.tensor_copy(bias, tp[w][:, 0:KD]))
                steps.wait()


def modulation_rows(nc, name, mods, g_row, out):
    with Stage(nc, name) as st:
        g = st.sb("g", [P, D])
        loaded, dve_step = st.sem("loaded"), st.sem("dve_step")
        with st.block() as block:
            @block.sync
            def _(sp):
                sp.dma_start(g[:], g_row.partition_broadcast(P)).then_inc(loaded, 16)
                for w in range(len(out)):
                    sp.dma_start(out[w][0], mods[w, 4 * D:5 * D].partition_broadcast(P)).then_inc(loaded, 16)
                    sp.dma_start(out[w][1], mods[w, 3 * D:4 * D].partition_broadcast(P)).then_inc(loaded, 16)
                sp.wait_ge(loaded, 16 * (1 + 2 * len(out)))

            @block.vector
            def _(dve):
                steps = Chain(dve, dve_step)
                dve.wait_ge(loaded, 16 * (1 + 2 * len(out)))
                for w in range(len(out)):
                    steps.mark(nc.vector.scalar_tensor_tensor(out=out[w][0], in0=out[w][0], scalar=1.0, in1=g[:], op0=ALU.add, op1=ALU.mult))
                steps.wait()


def gated_residual(x_tile, gate_row, tmp):
    def epi(which, engine, chain, j, n0, ps):
        chain.step(engine.tensor_tensor(tmp[:, j % 2], ps, gate_row(j), ALU.mult))
        return engine.tensor_tensor(x_tile(j), x_tile(j), tmp[:, j % 2], ALU.add)
    return epi


def spatial_gate(nc, name, S, uT, v, ln_rows, w_sT, b_s):
    with Stage(nc, name) as st:
        gain, shift = st.sb("gain", [P, W_GMLP]), st.sb("shift", [P, W_GMLP])
        ws = st.sb("w_s", [P, GROUPS, P])
        bs = st.sb("b_s", [1, GROUPS, P])
        stats = st.sb("stats", [P, W_GMLP // BANK, 6])
        mv = st.sb("mean_var", [P, 2])
        rms, rstd, variance = st.sb("rms", [P, 1]), st.sb("rstd", [P, 1]), st.sb("variance", [P, 1])
        banks = [st.ps(f"bank{b}", [P, 4, P]) for b in range(8)]
        loaded, normed, mixed, emptied = st.sem("loaded"), st.sem("normed"), st.sem("mixed"), st.sem("emptied")
        dve_step, var_ready, rms_ready = st.sem("dve_step"), st.sem("var_ready"), st.sem("rms_ready")
        nb = W_GMLP // BANK
        with st.block() as block:
            @block.sync
            def _(sp):
                sp.dma_start(gain[:], ln_rows[0].partition_broadcast(P)).then_inc(loaded, 16)
                sp.dma_start(shift[:], ln_rows[1].partition_broadcast(P)).then_inc(loaded, 16)
                sp.dma_start(ws[:], w_sT).then_inc(loaded, 16)
                sp.dma_start(bs[:], b_s).then_inc(loaded, 16)

            @block.vector
            def _(dve):
                steps = Chain(dve, dve_step)
                dve.wait_ge(loaded, 64)

                def gate(t):
                    for q in range(4):
                        dve.wait_ge(mixed, 4 * t + q + 1)
                        u = uT[:, 4 * q:4 * q + 4, t * P:(t + 1) * P]
                        nc.vector.tensor_tensor(u, u, banks[(4 * t + q) % 8][:], ALU.mult).then_inc(emptied, 1)

                for t in range(NA):
                    for b in range(nb):
                        steps.mark(nc.vector.bn_stats(stats[:, b, :], v[:, t, b * BANK:(b + 1) * BANK]))
                    steps.wait()
                    steps.mark(nc.vector.bn_aggr(mv[:], stats[:].rearrange("p b s -> p (b s)")))
                    steps.wait()
                    nc.vector.tensor_scalar(variance[:], mv[:, 1:2], 1.0, None, ALU.mult).then_inc(var_ready, 1)
                    dve.wait_ge(rms_ready, t + 1)
                    steps.step(nc.vector.reciprocal(rstd[:], rms[:]))
                    steps.step(nc.vector.tensor_scalar(v[:, t, :], v[:, t, :], mv[:, 0:1], rstd[:, 0:1], ALU.subtract, ALU.mult))
                    steps.step(nc.vector.tensor_tensor(v[:, t, :], v[:, t, :], gain[:], ALU.mult))
                    nc.vector.tensor_tensor(v[:, t, :], v[:, t, :], shift[:], ALU.add).then_inc(normed, 1)
                    if t:
                        gate(t - 1)
                gate(NA - 1)

            @block.scalar
            def _(act):
                for t in range(NA):
                    act.wait_ge(var_ready, t + 1)
                    nc.scalar.activation(rms[:], variance[:], ACT.Sqrt, bias=S.eps[:, 1:2]).then_inc(rms_ready, 1)

            @block.tensor
            def _(pe):
                pe.wait_ge(loaded, 64)
                for t in range(NA):
                    pe.wait_ge(normed, t + 1)
                    for q in range(4):
                        n = 4 * t + q
                        if n >= 8:
                            pe.wait_ge(emptied, n - 7)
                        for g in range(4):
                            gg = 4 * q + g
                            nc.tensor.matmul(banks[n % 8][:, g, :], v[:, t, gg * P:(gg + 1) * P], ws[:, gg, :], start=True, stop=False)
                            mm = nc.tensor.matmul(banks[n % 8][:, g, :], S.ones[0:1, :], bs[0:1, gg, :], start=False, stop=True)
                        mm.then_inc(mixed, 1)


def route(nc, name, S, logits, T, n_blocks, a, dest, weight, table, experts):
    cap = (n_blocks + 1) * P
    with Stage(nc, name) as st:
        def sb(n, shape, dt=F32):
            return st.sb(n, shape, dt)
        rank4, rank8 = sb("rank4", [P, 4]), sb("rank8", [P, 8])
        before, column = sb("before", [P, P]), sb("column", [P, 1])
        tokens, zeros = sb("tokens", [P, T], I32), sb("zeros", [P, n_blocks + 1], I32)
        gm, gsum, gtop = sb("gm", [P, T]), sb("gsum", [P, T]), sb("gtop", [P, T])
        gd, ge, gs, goh = (sb(n, [P, T, 4]) for n in ("gd", "ge", "gs", "goh"))
        part = sb("part", [P, T, 4, 8])
        el, el2, sc1 = sb("el", [P, T, 8]), sb("el2", [P, T, 8]), sb("sc1", [P, T, 8])
        oh = [sb(f"oh{n}", [P, T, 8]) for n in range(2)]
        top = [sb(f"top{n}", [P, T]) for n in range(2)]
        first = sb("first", [P, T])
        diff, ediff, den, share = sb("diff", [P, T]), sb("ediff", [P, T]), sb("den", [P, T]), sb("share", [P, T])
        E = [sb(f"E{n}", [P, T, 4, 8]) for n in range(2)]
        both = sb("both", [P, T, N_EXP])
        counts, blocks, ends, starts = sb("counts", [P, N_EXP]), sb("blocks", [P, N_EXP]), sb("ends", [P, N_EXP]), sb("starts", [P, N_EXP])
        place, picked = sb("place", [P, T, N_EXP]), sb("picked", [P, T, N_EXP])
        destf = sb("destf", [P, 2, T])
        past, owner, owner_i = sb("past", [P, N_EXP]), sb("owner", [P, 1]), sb("owner_i", [P, 1], I32)
        p_pos, p_cnt = st.ps("p_pos", [P, T, N_EXP]), st.ps("p_cnt", [P, N_EXP])
        loaded, dve_step, exp_ready, counted = st.sem("loaded"), st.sem("dve_step"), st.sem("exp_ready"), st.sem("counted")
        stored, cleared, table_cleared = st.sem("stored"), st.sem("cleared"), st.sem("table_cleared")
        rank_ready, shifted, differed, placed, owned = (st.sem(n) for n in ("both_ready", "shifted", "differed", "placed", "owned"))
        scattered = S.scattered

        def bc(x, n):
            return x.rearrange("p (t o) -> p t o", o=1).broadcast_to([P, T, n])

        def table_row(x, n):
            return x.rearrange("p (o n) -> p o n", o=1).broadcast_to([P, T, n])

        with st.block() as block:
            @block.sync
            def _(sp):
                for dst, src in ((rank4, a["rank8"][:, 4:8]), (rank8, a["rank8"]), (before, a["before"]), (column, a["column"]),
                                 (tokens, a["token_ids"][:, 0:T])):
                    sp.dma_start(dst[:], src).then_inc(loaded, 16)
                sp.wait_ge(cleared, 1)
                sp.dma_start(table.rearrange("(p b) o -> p (b o)", p=P), zeros[:]).then_inc(table_cleared, 16)
                sp.wait_ge(owned, 1)
                sp.dma_start(experts.rearrange("(p o) -> p o", o=1), owner_i[:]).then_inc(stored, 16)
                sp.wait_ge(stored, 16)

            @block.gpsimd
            def _(pool):
                nc.gpsimd.memset(zeros[:], 0).then_inc(cleared, 1)
                pool.wait_ge(placed, 1)
                pool.wait_ge(table_cleared, 16)
                pool.wait_ge(loaded, 80)
                for n in range(2):
                    for t in range(T):
                        pool.indirect_dma_start(table, bass.IndirectOffsetOnAxis(dest[:, n, t:t + 1], 0), tokens[:, t:t + 1], None).then_inc(scattered, 16)
                pool.wait_ge(scattered, 16 * 2 * T)

            @block.scalar
            def _(act):
                act.wait_ge(shifted, 1)
                nc.scalar.activation(ge[:], gd[:], ACT.Exp).then_inc(exp_ready, 1)
                act.wait_ge(differed, 1)
                nc.scalar.activation(ediff[:], diff[:], ACT.Exp).then_inc(exp_ready, 1)

            @block.tensor
            def _(pe):
                pe.wait_ge(loaded, 80)
                pe.wait_ge(rank_ready, 1)
                for t in range(T):
                    for t2 in range(t + 1):
                        nc.tensor.matmul(p_pos[:, t, :], before[:] if t2 == t else S.ones[:], both[:, t2, :], start=(t2 == 0), stop=(t2 == t))
                for t in range(T):
                    mm = nc.tensor.matmul(p_cnt[:], S.ones[:], both[:, t, :], start=(t == 0), stop=(t == T - 1))
                mm.then_inc(counted, 1)

            @block.vector
            def _(dve):
                c = Chain(dve, dve_step)
                V = nc.vector
                dve.wait_ge(loaded, 80)
                gl = logits[:, :, 0:4]
                c.step(V.tensor_reduce(gm[:], gl, AX.X, ALU.max))
                V.tensor_tensor(gd[:], gl, bc(gm[:], 4), ALU.subtract).then_inc(shifted, 1)
                dve.wait_ge(exp_ready, 1)
                c.mark(V.tensor_reduce(gsum[:], ge[:], AX.X, ALU.add))
                c.step(V.tensor_scalar(gs[:], gd[:], 0.0, None, ALU.is_ge))
                c.step(V.tensor_tensor(gs[:], gs[:], table_row(rank4[:], 4), ALU.mult))
                c.step(V.tensor_reduce(gtop[:], gs[:], AX.X, ALU.max))
                c.step(V.tensor_tensor(goh[:], gs[:], bc(gtop[:], 4), ALU.is_equal))
                goh8 = goh[:].rearrange("p t (g o) -> p t g o", o=1).broadcast_to([P, T, 4, 8])
                c.step(V.tensor_tensor(part[:], logits[:, :, 4:36].rearrange("p t (g e) -> p t g e", g=4), goh8, ALU.mult))
                c.step(V.tensor_tensor(el[:], part[:, :, 0, :], part[:, :, 1, :], ALU.add))
                c.step(V.tensor_tensor(el[:], el[:], part[:, :, 2, :], ALU.add))
                c.step(V.tensor_tensor(el[:], el[:], part[:, :, 3, :], ALU.add))
                for n, src in enumerate((el, el2)):
                    if n:
                        c.step(V.scalar_tensor_tensor(out=el2[:], in0=oh[0][:], scalar=-BIG, in1=el[:], op0=ALU.mult, op1=ALU.add))
                    c.step(V.tensor_reduce(top[n][:], src[:], AX.X, ALU.max))
                    c.step(V.tensor_tensor(sc1[:], src[:], bc(top[n][:], 8), ALU.is_equal))
                    c.step(V.tensor_tensor(sc1[:], sc1[:], table_row(rank8[:], 8), ALU.mult))
                    c.step(V.tensor_reduce(first[:], sc1[:], AX.X, ALU.max))
                    c.step(V.tensor_tensor(oh[n][:], sc1[:], bc(first[:], 8), ALU.is_equal))
                    for t in range(T):
                        c.mark(V.tensor_tensor(E[n][:, t], goh[:, t, :].rearrange("p (g o) -> p g o", o=1).broadcast_to([P, 4, 8]),
                                               oh[n][:, t:t + 1, :].broadcast_to([P, 4, 8]), ALU.mult))
                    c.wait()
                V.tensor_tensor(both[:], E[0][:].rearrange("p t g e -> p t (g e)"), E[1][:].rearrange("p t g e -> p t (g e)"), ALU.add).then_inc(rank_ready, 1)
                V.tensor_tensor(diff[:], top[1][:], top[0][:], ALU.subtract).then_inc(differed, 1)
                dve.wait_ge(exp_ready, 2)
                c.step(V.tensor_scalar(den[:], ediff[:], 1.0, None, ALU.add))
                c.step(V.tensor_tensor(den[:], den[:], gsum[:], ALU.mult))
                c.step(V.reciprocal(weight[:, 0, :], den[:]))
                c.mark(V.tensor_tensor(weight[:, 1, :], weight[:, 0, :], ediff[:], ALU.mult))
                dve.wait_ge(counted, 1)
                c.mark(V.tensor_copy(counts[:], p_cnt[:]))
                c.step(V.memset(blocks[:], 0.0))
                for m in range(T):
                    c.step(V.scalar_tensor_tensor(out=blocks[:], in0=counts[:], scalar=float(P * m), in1=blocks[:], op0=ALU.is_gt, op1=ALU.add))
                c.step(V.tensor_tensor_scan(ends[:], S.ones[:, 0:N_EXP], blocks[:], 0.0, ALU.mult, ALU.add))
                c.step(V.tensor_tensor(starts[:], ends[:], blocks[:], ALU.subtract))
                c.step(V.tensor_scalar(starts[:], starts[:], float(P), None, ALU.mult))
                c.step(V.tensor_tensor(place[:], p_pos[:], table_row(starts[:], N_EXP), ALU.add))
                for n in range(2):
                    c.step(V.tensor_tensor(picked[:], place[:], E[n][:].rearrange("p t g e -> p t (g e)"), ALU.mult))
                    c.step(V.tensor_reduce(destf[:, n, :], picked[:], AX.X, ALU.add))
                V.tensor_copy(dest[:], destf[:]).then_inc(placed, 1)
                c.step(V.tensor_scalar(past[:], ends[:], column[:, 0:1], None, ALU.is_le))
                c.step(V.tensor_reduce(owner[:], past[:], AX.X, ALU.add))
                c.step(V.tensor_scalar(owner[:], owner[:], float(N_EXP - 1), None, ALU.min))
                V.tensor_copy(owner_i[:], owner[:]).then_inc(owned, 1)
                dve.wait_ge(placed, 1)


def experts_run(nc, name, S, n_blocks, table, experts, h, w_gu, w_d, y):
    KH = HID // P
    with Stage(nc, name) as st:
        erow = st.sb("experts", [1, n_blocks], I32)
        rows = [st.sb(f"rows{u}", [P, 1], I32) for u in range(2)]
        xg = [st.sb(f"xg{u}", [P, D]) for u in range(2)]
        xT = [st.sb(f"xT{u}", [P, KD, P]) for u in range(2)]
        wgu = [st.sb(f"wgu{u}", [P, 2, KD, HID]) for u in range(2)]
        wd = [st.sb(f"wd{u}", [P, KH, D]) for u in range(2)]
        sg, act_in = st.sb("gate", [P, HID]), st.sb("gated", [P, HID])
        aT = st.sb("gatedT", [P, KH, P])
        yo = [st.sb(f"y{u}", [P, D]) for u in range(2)]
        p_x = [st.ps(f"p_x{n}", [P, 4, P]) for n in range(2)]
        p_g, p_u, p_a = st.ps("p_g", [P, HID]), st.ps("p_u", [P, HID]), st.ps("p_a", [P, KH, P])
        p_y = [st.ps(f"p_y{n}", [P, BANK]) for n in range(2)]
        experts_loaded = st.sem("experts_loaded")
        rows_loaded = [st.sem(f"rows_loaded{u}") for u in range(2)]
        gathered = S.gathered
        gu_loaded, d_loaded = [st.sem(f"gu_loaded{u}") for u in range(2)], [st.sem(f"d_loaded{u}") for u in range(2)]
        x_turned, x_copied = st.sem("x_turned"), [st.sem("x_copied0"), st.sem("x_copied1")]
        gate_ready, up_ready, silu_ready, gated = st.sem("gate_ready"), st.sem("up_ready"), st.sem("silu_ready"), st.sem("gated")
        a_turned, a_copied, y_ready = st.sem("a_turned"), st.sem("a_copied"), st.sem("y_ready")
        y_copied = [st.sem("y_copied0"), st.sem("y_copied1")]
        stored = [st.sem(f"stored{u}") for u in range(2)]
        gather_free = st.sem("gather_free")
        H = n_blocks // 2
        with st.block() as block:
            @block.sync
            def _(sp):
                sp.dma_start(erow[:], experts[0:n_blocks].rearrange("(o b) -> o b", o=1)).then_inc(experts_loaded, 16)
                sp.wait_ge(experts_loaded, 16)

                def load_rows(b, u):
                    sp.dma_start(rows[u][:], table[bass.ds(b * P, P), :]).then_inc(rows_loaded[u], 16)

                def expert(b):
                    return sp.value_load(erow[0:1, bass.ds(b, 1)], min_val=0, max_val=N_EXP - 1)

                def load_gu(e, u):
                    sp.dma_start(wgu[u][:], w_gu[bass.ds(e, 1)].rearrange("a p g k f -> (a p) g k f")).then_inc(gu_loaded[u], 16)

                def load_d(e, u):
                    sp.dma_start(wd[u][:], w_d[bass.ds(e, 1)].rearrange("a p k f -> (a p) k f")).then_inc(d_loaded[u], 16)

                def store(b, u):
                    sp.wait_ge(y_copied[0], b + 2)
                    sp.wait_ge(y_copied[1], b + 2)
                    sp.dma_start(y[bass.ds(b * P, P), :], yo[u][:]).then_inc(stored[u], 16)

                load_rows(0, 0)
                load_rows(1, 1)
                for u in range(2):
                    e = expert(u)
                    load_gu(e, u)
                    load_d(e, u)
                with sp.Fori(0, H - 1) as i:
                    for u in range(2):
                        b = 2 * i + u
                        sp.wait_ge(gathered[u], 16 * i + 16)
                        load_rows(b + 2, u)
                        e = expert(b + 2)
                        sp.wait_ge(gated, b + 2)
                        load_gu(e, u)
                        store(b, u)
                        sp.wait_ge(stored[u], 16 * i + 16)
                        load_d(e, u)
                sp.wait_ge(gathered[0], 16 * H)
                load_rows(n_blocks, 0)
                for u in range(2):
                    store(n_blocks - 2 + u, u)
                for u in range(2):
                    sp.wait_ge(stored[u], 16 * H)
                sp.wait_ge(rows_loaded[0], 16 * (H + 1))

            @block.gpsimd
            def _(pool):
                def gather(u):
                    pool.indirect_dma_start(xg[u][:], None, h, bass.IndirectOffsetOnAxis(rows[u][:, 0:1], 0)).then_inc(gathered[u], 16)

                for u in range(2):
                    pool.wait_ge(rows_loaded[u], 16)
                    gather(u)
                with pool.Fori(0, H - 1) as i:
                    for u in range(2):
                        pool.wait_ge(rows_loaded[u], 16 * i + 32)
                        pool.wait_ge(x_turned, 4 * i + 2 * u + 2)
                        pool.sem_inc(gather_free, 1)
                        gather(u)
                pool.wait_ge(rows_loaded[0], 16 * (H + 1))
                pool.wait_ge(x_turned, 2 * (n_blocks - 1))
                gather(0)
                pool.wait_ge(gathered[0], 16 * (H + 1))

            @block.tensor
            def _(pe):
                def turn(b, u, i, first=False):
                    pe.wait_ge(gathered[u], 16 * i + 16)
                    for n in range(2):
                        if not first:
                            pe.wait_ge(x_copied[n], b)
                        for q in range(4):
                            d = 4 * n + q
                            mm = nc.tensor.transpose(p_x[n][:, q, :], xg[u][:, d * P:(d + 1) * P], S.ident[:, :])
                        mm.then_inc(x_turned, 1)

                turn(0, 0, 0, True)
                pe.sem_inc(a_turned, 1)
                with pe.Fori(0, H) as i:
                    for u in range(2):
                        b = 2 * i + u
                        pe.wait_ge(x_copied[0], b + 1)
                        pe.wait_ge(x_copied[1], b + 1)
                        pe.wait_ge(gu_loaded[u], 16 * i + 16)
                        pe.wait_ge(gated, b + 1)
                        for g, (p, ready) in enumerate(((p_g, gate_ready), (p_u, up_ready))):
                            for k in range(KD):
                                mm = nc.tensor.matmul(p[:], xT[u][:, k, :], wgu[u][:, g, k, :], start=(k == 0), stop=(k == KD - 1))
                            mm.then_inc(ready, 1)
                        turn(b + 1, 1 - u, i + u)
                        pe.wait_ge(gated, b + 2)
                        pe.wait_ge(a_copied, b + 1)
                        for k in range(KH):
                            mm = nc.tensor.transpose(p_a[:, k, :], act_in[:, k * P:(k + 1) * P], S.ident[:, :])
                        mm.then_inc(a_turned, 1)
                        pe.wait_ge(a_copied, b + 2)
                        pe.wait_ge(d_loaded[u], 16 * i + 16)
                        for n in range(2):
                            pe.wait_ge(y_copied[n], b + 1)
                            for k in range(KH):
                                mm = nc.tensor.matmul(p_y[n][:], aT[:, k, :], wd[u][:, k, n * BANK:(n + 1) * BANK], start=(k == 0), stop=(k == KH - 1))
                            mm.then_inc(y_ready, 1)

            @block.scalar
            def _(act):
                act.sem_inc(a_copied, 1)
                act.sem_inc(y_copied[0], 1)

                def copy_x(b, u):
                    act.wait_ge(x_turned, 2 * b + 1)
                    nc.scalar.activation(xT[u][:, 0:4, :], p_x[0][:], ACT.Copy).then_inc(x_copied[0], 1)

                copy_x(0, 0)
                with act.Fori(0, H) as i:
                    for u in range(2):
                        b = 2 * i + u
                        act.wait_ge(gate_ready, b + 1)
                        act.wait_ge(gated, b + 1)
                        nc.scalar.activation(sg[:], p_g[:], ACT.Silu).then_inc(silu_ready, 1)
                        copy_x(b + 1, 1 - u)
                        act.wait_ge(a_turned, b + 2)
                        nc.scalar.activation(aT[:], p_a[:], ACT.Copy).then_inc(a_copied, 1)
                        act.wait_ge(y_ready, 2 * b + 1)
                        nc.scalar.activation(yo[u][:, 0:BANK], p_y[0][:], ACT.Copy).then_inc(y_copied[0], 1)

            @block.vector
            def _(dve):
                dve.sem_inc(gated, 1)
                dve.sem_inc(y_copied[1], 1)

                def copy_x(b, u):
                    dve.wait_ge(x_turned, 2 * b + 2)
                    nc.vector.tensor_copy(xT[u][:, 4:8, :], p_x[1][:]).then_inc(x_copied[1], 1)

                copy_x(0, 0)
                with dve.Fori(0, H) as i:
                    for u in range(2):
                        b = 2 * i + u
                        dve.wait_ge(silu_ready, b + 1)
                        dve.wait_ge(up_ready, b + 1)
                        dve.wait_ge(a_turned, b + 1)
                        nc.vector.tensor_tensor(act_in[:], sg[:], p_u[:], ALU.mult).then_inc(gated, 1)
                        copy_x(b + 1, 1 - u)
                        dve.wait_ge(y_ready, 2 * b + 2)
                        nc.vector.tensor_copy(yo[u][:, BANK:D], p_y[1][:]).then_inc(y_copied[1], 1)


def combine(nc, name, S, x_tiles, T0, dest, weight, y, gate_row):
    T = len(x_tiles)
    with Stage(nc, name) as st:
        row = st.sb("gate", [P, D])
        ya = [[st.sb(f"y{n}{u}", [P, D]) for u in range(2)] for n in range(2)]
        loaded, dve_step = st.sem("loaded"), st.sem("dve_step")
        fetched = S.fetched
        with st.block() as block:
            @block.sync
            def _(sp):
                sp.dma_start(row[:], gate_row.partition_broadcast(P)).then_inc(loaded, 16)

            @block.gpsimd
            def _(pool):
                for t in range(T):
                    if t >= 2:
                        pool.wait_ge(dve_step, 4 * (t - 1))
                    for n in range(2):
                        pool.indirect_dma_start(ya[n][t % 2][:], None, y, bass.IndirectOffsetOnAxis(dest[:, n, T0 + t:T0 + t + 1], 0)).then_inc(fetched[t % 2], 16)
                for u in range(min(2, T)):
                    pool.wait_ge(fetched[u], 32 * ((T - u + 1) // 2))

            @block.vector
            def _(dve):
                steps = Chain(dve, dve_step)
                dve.wait_ge(loaded, 16)
                for t in range(T):
                    dve.wait_ge(fetched[t % 2], 32 * (t // 2 + 1))
                    y0, y1 = ya[0][t % 2][:], ya[1][t % 2][:]
                    steps.step(nc.vector.tensor_scalar(y0, y0, weight[:, 0, T0 + t:T0 + t + 1], None, ALU.mult))
                    steps.step(nc.vector.scalar_tensor_tensor(out=y0, in0=y1, scalar=weight[:, 1, T0 + t:T0 + t + 1], in1=y0, op0=ALU.mult, op1=ALU.add))
                    steps.step(nc.vector.tensor_tensor(y0, y0, row[:], ALU.mult))
                    steps.step(nc.vector.tensor_tensor(x_tiles[t], x_tiles[t], y0, ALU.add))


def route_tables():
    i = np.arange(P)
    return {"rank8": np.tile(np.arange(8, 0, -1, dtype=np.float32), (P, 1)),
            "before": (i[:, None] < i[None, :]).astype(np.float32),
            "column": i[:, None].astype(np.float32),
            "token_ids": (np.arange(NA)[None, :] * P + i[:, None]).astype(np.int32)}


SECOND_COLS = (("norm1_g_2", 2 * KD), ("ga_b_in_2_u", W_GMLP // P))
N_BLOCKS = (44, 40)


def moe(nc, name, S, a, layer, streams, hT, mods):
    tiles = [(t, w) for ts, w in streams for t in ts]
    T = len(tiles)
    nb = N_BLOCKS[layer]
    assert nb % 2 == 0 and nb >= (2 * T * P + N_EXP * (P - 1)) // P
    h = dram(nc, name + "_h", [T * P, D])
    table, experts = dram(nc, name + "_table", [(nb + 1) * P, 1], I32), dram(nc, name + "_experts", [P], I32)
    y = dram(nc, name + "_y", [nb * P, D])
    with ExitStack() as mem:
        def sb(n, shape, dt=F32):
            return mem.enter_context(nc.sbuf_tensor(f"{name}_{n}", shape, dt))
        dest, weight = sb("dest", [P, 2, T], I32), sb("weight", [P, 2, T])
        with ExitStack() as mem2:
            rows = [[mem2.enter_context(nc.sbuf_tensor(f"{name}_row{w}{n}", [P, D], F32)) for n in range(2)] for w in range(len(streams))]
            modulation_rows(nc, name + "m", mods, a["norm2_g_2"][layer], [(r[0][:], r[1][:]) for r in rows])
            norm_transpose(nc, name + "n", S, [t for t, _ in tiles], hT, rows=[(rows[w][0][:], rows[w][1][:]) for _, w in tiles], h_dram=h)
            logits = mem2.enter_context(nc.sbuf_tensor(f"{name}_logits", [P, T, 36], F32))
            brow = mem2.enter_context(nc.sbuf_tensor(f"{name}_brow", [1, 36], F32))
            load_all(nc, name + "b", [(brow[:], a["moe_b_2"][layer].rearrange("(o c) -> o c", o=1))])
            project(nc, name + "g", hT, T * P, [dict(w=a["moe_w_route_2"][layer], mode="T", bias=brow[:], epi=copy_to(lambda j, n0: logits[:, j, :]))],
                    const={"ones": S.ones})
            S.scattered = S.pool_sems[layer][0]
            route(nc, name + "r", S, logits, T, nb, a, dest, weight, table, experts)
        S.gathered = S.pool_sems[layer][1:3]
        experts_run(nc, name + "e", S, nb, table, experts, h, a["moe_w_gu_2"][layer], a["moe_w_down_2"][layer], y)
        at = 0
        for n, (ts, w) in enumerate(streams):
            S.fetched = S.pool_sems[layer][3 + 2 * n:5 + 2 * n]
            combine(nc, f"{name}c{n}", S, ts, at, dest, weight, y, mods[w, 5 * D:6 * D])
            at += len(ts)


def gmlp(nc, S, a, x_tiles, c_tiles, hT, mods):
    with ExitStack() as mem:
        def sb(n, shape):
            return mem.enter_context(nc.sbuf_tensor("gm_" + n, shape, F32))
        uT = sb("uT", [P, GROUPS, ALL])
        bias_u = S.second_cols[:, 2 * KD:2 * KD + W_GMLP // P]
        with ExitStack() as mem2:
            v = mem2.enter_context(nc.sbuf_tensor("gm_v", [P, NA, W_GMLP], F32))
            brow = mem2.enter_context(nc.sbuf_tensor("gm_brow", [1, W_GMLP], F32))
            load_all(nc, "gmb", [(brow[:], a["ga_b_in_2_v"].rearrange("(o c) -> o c", o=1))])

            def epi_u(c):
                def epi(which, engine, chain, j, n0, ps):
                    f = 4 * c + j
                    return engine.activation(uT[:, f, n0:n0 + ps.shape[1]], ps, ACT.Gelu, bias=bias_u[:, f:f + 1])
                return epi

            def epi_v(c):
                def epi(which, engine, chain, j, n0, ps):
                    return engine.activation(v[:, j, c * BANK:(c + 1) * BANK], ps, ACT.Gelu)
                return epi

            w = a["ga_w_in_2"]
            jobs = [dict(w=w[:, c * BANK:(c + 1) * BANK], mode="F", eng="act", epi=epi_u(c)) for c in range(4)]
            jobs += [dict(w=w[:, W_GMLP + c * BANK:W_GMLP + (c + 1) * BANK], mode="T", eng="act", bias=brow[0:1, c * BANK:(c + 1) * BANK], epi=epi_v(c)) for c in range(4)]
            project(nc, "gmi", hT, ALL, jobs, const={"ones": S.ones})
            spatial_gate(nc, "gms", S, uT, v, (a["ga_ln_g_2"], a["ga_ln_b_2"]), a["ga_w_sT_2"], a["ga_b_s_2"])
        brow = sb("brow_out", [1, D])
        gates = [sb(f"gate{w}", [P, D]) for w in range(2)]
        W = 256
        tmp = sb("tmp", [P, 2, W])
        load_all(nc, "gmc", [(brow[:], a["ga_b_out_2"].rearrange("(o c) -> o c", o=1))] +
                 [(gates[w][:], mods[w, 2 * D:3 * D].partition_broadcast(P)) for w in range(2)])
        tiles = x_tiles + c_tiles
        jobs = []
        for c in range(D // W):
            s = slice(c * W, (c + 1) * W)
            jobs.append(dict(w=a["ga_w_out_2"][:, s], mode="T", eng="dve", bias=brow[0:1, s],
                             epi=gated_residual(lambda j, s=s: tiles[j][:, s], lambda j, s=s: gates[j >= NT][:, s], tmp)))
        project(nc, "gmo", uT, ALL, jobs, const={"ones": S.ones})


def second_block_a(nc, S, a, x_tiles, c_tiles, hT, mods):
    for layer in range(2):
        modulation(nc, f"ad{layer}", S, a["cT_2"], a["ada_w_2"][layer], a["ada_b_2"][layer], mods[layer])
    cols = S.mod_cols
    modulation_columns(nc, "mc0", S, mods[0], S.second_cols[:, 0:KD], cols)
    norm_transpose(nc, "sn0", S, x_tiles + c_tiles, hT, cols=[cols[0]] * NT + [cols[1]] * (NA - NT))
    gmlp(nc, S, a, x_tiles, c_tiles, hT, mods[0])
    moe(nc, "moe0", S, a, 0, ((x_tiles, 0), (c_tiles, 1)), hT, mods[0])


def second_layout(inp):
    g = lambda n: np.asarray(inp[n])
    out = {n: np.ascontiguousarray(g(n)[0]) for n in ("ga_w_in_2", "ga_ln_g_2", "ga_ln_b_2", "ga_w_out_2", "ga_b_out_2")}
    for n in ("ada_w_2", "ada_b_2", "norm2_g_2"):
        out[n] = np.ascontiguousarray(g(n))
    out["ctx_2"] = np.ascontiguousarray(g("ctx_2")[0])
    out["cT_2"] = np.ascontiguousarray(np.stack([columns(g("c_2")[0]), columns(g("c_ctx_2"))], 2))
    out["ga_w_sT_2"] = np.ascontiguousarray(g("ga_w_s_2")[0].transpose(2, 0, 1))
    out["ga_b_s_2"] = np.ascontiguousarray(g("ga_b_s_2")[0][None])
    out["ga_b_in_2_v"] = np.ascontiguousarray(g("ga_b_in_2")[0, W_GMLP:])
    out["moe_w_route_2"] = np.ascontiguousarray(np.concatenate([g("moe_w_grp_2"), g("moe_w_exp_2")], 2))
    out["moe_b_2"] = np.ascontiguousarray(np.concatenate([g("moe_b_grp_2"), g("moe_b_exp_2")], 1))
    gu = np.stack([g("moe_w_gate_2"), g("moe_w_up_2")], 2)
    out["moe_w_gu_2"] = np.ascontiguousarray(gu.reshape(2, N_EXP, 2, KD, P, HID).transpose(0, 1, 4, 2, 3, 5))
    out["moe_w_down_2"] = np.ascontiguousarray(g("moe_w_down_2").reshape(2, N_EXP, HID // P, P, D).transpose(0, 1, 3, 2, 4))
    out["second_cols"] = np.concatenate([columns(g("norm1_g_2")), columns(g("ga_b_in_2")[0, :W_GMLP])], 1)
    return out


HEADS, HK = 16, 64
CH = 64
STEPS = ALL // CH
CSTEPS = CTX // CH
GRID = 64
LEVELS = 5
LOG_DECAY = -math.exp(-0.5)


def token_shift(nc, name, hT, xx):
    rows = SEQ // GRID
    with Stage(nc, name) as st:
        dve_step = st.sem("dve_step")
        with st.block() as block:
            @block.vector
            def _(dve):
                steps = Chain(dve, dve_step)

                def sub(dst, shifted, here):
                    steps.mark(nc.vector.tensor_tensor(dst, shifted, here, ALU.subtract))

                def edge(dst, here):
                    steps.mark(nc.vector.tensor_scalar(dst, here, -1.0, None, ALU.mult))

                C = CTX
                b, f = slice(0, 4), slice(4, 8)
                sub(xx[:, b, 1:C], hT[:, b, 0:C - 1], hT[:, b, 1:C])
                edge(xx[:, b, 0:1], hT[:, b, 0:1])
                sub(xx[:, f, 0:C - 1], hT[:, f, 1:C], hT[:, f, 0:C - 1])
                edge(xx[:, f, C - 1:C], hT[:, f, C - 1:C])
                for k in range(0, 2):
                    g, o = (t[:, k, C:].rearrange("p (r c) -> p r c", c=GRID) for t in (hT, xx))
                    sub(o[:, :, 1:], g[:, :, :GRID - 1], g[:, :, 1:])
                    edge(o[:, :, 0:1], g[:, :, 0:1])
                for k in range(2, 4):
                    g, o = (t[:, k, C:].rearrange("p (r c) -> p r c", c=GRID) for t in (hT, xx))
                    sub(o[:, :, :GRID - 1], g[:, :, 1:], g[:, :, :GRID - 1])
                    edge(o[:, :, GRID - 1:], g[:, :, GRID - 1:])
                u, d = slice(4, 6), slice(6, 8)
                sub(xx[:, u, C + GRID:], hT[:, u, C:ALL - GRID], hT[:, u, C + GRID:])
                edge(xx[:, u, C:C + GRID], hT[:, u, C:C + GRID])
                sub(xx[:, d, C:ALL - GRID], hT[:, d, C + GRID:], hT[:, d, C:ALL - GRID])
                edge(xx[:, d, ALL - GRID:], hT[:, d, ALL - GRID:])
                steps.wait()


def token_mix(nc, name, hT, xx, mu, out):
    with Stage(nc, name) as st:
        dve_step = st.sem("dve_step")
        with st.block() as block:
            @block.vector
            def _(dve):
                steps = Chain(dve, dve_step)
                for d in range(KD):
                    steps.mark(nc.vector.scalar_tensor_tensor(out=out[:, d, :], in0=xx[:, d, :], scalar=mu[:, d:d + 1], in1=hT[:, d, :], op0=ALU.mult, op1=ALU.add))
                steps.wait()


def backward(x):
    return x.rearrange("p (c t) -> p c t", t=CH)[:, ::-1, :]


def chunked(x):
    return x.rearrange("p (c t) -> p c t", t=CH)


def rwkv_scan(nc, name, S, a, kF, rF, sgF, aF, vS, yS, bS):
    with Stage(nc, name) as st:
        sb = st.sb
        masks = sb("masks", [P, 4, P])
        lower = sb("lower", [P, P])
        join = sb("join", [P, LEVELS + 1, P])
        join0 = sb("join0", [P, P])
        keep = sb("keep", [P, ALL])
        halves = sb("halves", [P, P])
        cols = [sb(f"cols{u}", [P, 4]) for u in range(2)]
        k2, sg, aa = ([sb(f"{n}{u}", [P, ALL]) for u in range(2)] for n in ("k", "sg", "a"))
        r2 = [sb(f"r{u}", [P, SEQ]) for u in range(2)]
        vs = [sb(f"v{u}", [P, STEPS, HK]) for u in range(2)]
        lw, L, G, G2, sq, nrm, kk, km, t1 = (sb(n, [P, ALL]) for n in ("lw", "L", "G", "G2", "sq", "nrm", "kk", "km", "t1"))
        e_inc, e_exc, e_neg = (sb(n, [P, ALL]) for n in ("e_inc", "e_exc", "e_neg"))
        em, ee = sb("em", [P, STEPS]), sb("ee", [P, STEPS])
        oneminus = sb("oneminus", [P, 1])
        ar = sb("ar", [P, STEPS, 2, P])
        bh, kh = sb("bh", [P, STEPS, P]), sb("kh", [P, STEPS, P])
        AM = sb("AM", [P, STEPS, 4, P])
        bT, kT = sb("bT", [P, STEPS, P]), sb("kT", [P, STEPS, P])
        T, R = sb("T", [P, STEPS, P]), sb("R", [P, STEPS, P])
        off = [sb(f"off{n}", [P, 4, P]) for n in range(2)]
        Z = [sb(f"Z{n}", [P, 4, P]) for n in range(2)]
        Sm, X, SA = sb("Sm", [P, HK]), sb("X", [P, HK]), sb("SA", [P, HK])
        yo, yb = sb("y", [P, SEQ // CH, HK]), sb("yb", [P, SEQ // CH, HK])
        bon = sb("bonus", [P, SEQ // CH])
        rk = sb("rk", [P, SEQ // CH, P])
        bank = [st.ps(f"bank{n}", [P, BANK]) for n in range(8)]
        names = ("lw_ready sq_ready g_ready ss_ready nrm_ready exp_ready cleared bd_ready pb_ready pb_masked pn_ready pn_masked tr_ready tr_copied "
                 "off_ready z_ready z_copied tz_ready tz_added zr_ready zr_added x_ready x_copied sa_ready sa_copied ds_ready sm_ready "
                 "y_ready y_copied bon_ready yb_ready head_done dve_step act_step const_loaded y_free").split()
        s = {n: st.sem(n) for n in names}
        loaded = [st.sem(f"loaded{u}") for u in range(2)]
        stored = st.sem("stored")
        LOADS = 5 + 4
        NG = STEPS // 4
        NZ = LEVELS * NG
        lat = SEQ // CH
        lo, hi = slice(0, HK), slice(HK, P)

        def cs(x):
            return x[:].rearrange("p (c t) -> p c t", t=CH)

        def quad(x):
            return x.rearrange("p (c t) -> p c t", c=4)

        def over4(m):
            return m.rearrange("p (o t) -> p o t", o=1).broadcast_to([P, 4, P])

        with st.block() as block:
            @block.sync
            def _(sp):
                for dst, src in ((masks, "rw_masks"), (lower, "rw_lower"), (join, "rw_join"), (join0, "rw_join0"), (keep, "rw_keep"), (halves, "rw_halves")):
                    sp.dma_start(dst[:], a[src]).then_inc(s["const_loaded"], 16)

                def load(h, u):
                    hs = bass.ds(h * HK, HK)
                    for z, rows in ((0, lo), (1, hi)):
                        sp.dma_start(k2[u][rows, :], kF[z][hs, :]).then_inc(loaded[u], 16)
                        sp.dma_start(r2[u][rows, :], rF[z][hs, :]).then_inc(loaded[u], 16)
                        sp.dma_start(sg[u][rows, :], sgF[z][hs, :]).then_inc(loaded[u], 16)
                        sp.dma_start(aa[u][rows, :], aF[z][hs, :]).then_inc(loaded[u], 16)
                    sp.dma_start(cols[u][:], a["rw_cols"][bass.ds(h, 1)].rearrange("a p c -> (a p) c")).then_inc(loaded[u], 16)
                    for z, rows in ((0, lo), (1, hi)):
                        sp.dma_start(vs[u][rows, :, :], vS[z].rearrange("s t c -> t s c")[:, :, hs]).then_inc(loaded[u], 16)

                def store(h):
                    sp.wait_ge(s["head_done"], h + 1)
                    hs = bass.ds(h * HK, HK)
                    for z, rows in ((0, lo), (1, hi)):
                        for d, src in ((yS, yo), (bS, yb)):
                            sp.dma_start(d[z].rearrange("(c t) n -> t c n", t=CH)[:, :, hs], src[rows, :, :]).then_inc(stored, 16)

                load(0, 0)
                load(1, 1)
                sp.sem_inc(s["y_free"], 1)
                with sp.Fori(0, HEADS // 2 - 1) as i:
                    for u in range(2):
                        h = 2 * i + u
                        store(h)
                        sp.wait_ge(stored, h * 64 + 64)
                        sp.sem_inc(s["y_free"], 1)
                        load(h + 2, u)
                for u in range(2):
                    h = HEADS - 2 + u
                    store(h)
                    sp.wait_ge(stored, h * 64 + 64)
                    sp.sem_inc(s["y_free"], 1)

            NL = 11

            @block.gpsimd
            def _(pool):
                for x in (ar, bh, kh, rk):
                    nc.gpsimd.memset(x[:], 0.0).then_inc(s["cleared"], 1)
                pool.wait_ge(s["const_loaded"], 96)
                with pool.Fori(0, HEADS) as h:
                    for n in range(NZ):
                        l, g = n // NG, n % NG
                        pool.wait_ge(s["pb_masked"], h * STEPS + 4 * g + 4)
                        if n >= 2:
                            pool.wait_ge(s["z_ready"], h * NZ + n - 1)
                        nc.gpsimd.tensor_tensor(off[n % 2][:], AM[:, 4 * g:4 * g + 4, 0, :], over4(join[:, l + 1, :]), ALU.mult).then_inc(s["off_ready"], 1)

            @block.scalar
            def _(act):
                with act.Fori(0, HEADS // 2) as i:
                    for u in range(2):
                        h = 2 * i + u
                        act.wait_ge(loaded[u], i * 16 * NL + 16 * NL)
                        A = nc.scalar.activation
                        A(lw[:], sg[u][:], ACT.Copy, scale=LOG_DECAY).then_inc(s["lw_ready"], 1)
                        A(sq[:], k2[u][:], ACT.Square, scale=cols[u][:, 0:1]).then_inc(s["sq_ready"], 1)
                        act.wait_ge(s["ss_ready"], h + 1)
                        for n, (c0, c1) in enumerate(((0, 512), (512, ALL))):
                            A(nrm[:, c0:c1], bank[n][:, 0:c1 - c0], ACT.Sqrt, bias=S.eps[:, 3:4]).then_inc(s["nrm_ready"], 1)
                        act.wait_ge(s["g_ready"], h + 1)
                        for dst, rows, src, sign in ((e_inc, lo, G, 1.0), (e_inc, hi, G2, -1.0), (e_exc, lo, G2, 1.0), (e_exc, hi, G, -1.0),
                                                     (e_neg, lo, G, -1.0), (e_neg, hi, G2, 1.0)):
                            A(dst[rows, :], src[rows, :], ACT.Exp, scale=sign).then_inc(s["exp_ready"], 1)
                        A(em[:], cs(L)[:, :, CH - 1], ACT.Exp, scale=0.5).then_inc(s["exp_ready"], 1)
                        for g in range(NG):
                            for n, dst in enumerate((bT, kT)):
                                act.wait_ge(s["tr_ready"], h * 2 * NG + 2 * g + n + 1)
                                A(dst[:, 4 * g:4 * g + 4, :], quad(bank[3 + n][:]), ACT.Copy).then_inc(s["tr_copied"], 1)
                        for n in range(NZ):
                            act.wait_ge(s["z_ready"], h * NZ + n + 1)
                            if n >= 2:
                                act.wait_ge(s["zr_ready"], h * NZ + n - 1)
                            A(Z[n % 2][:], quad(bank[4 + n % 2][:]), ACT.Copy).then_inc(s["z_copied"], 1)
                        for j in range(STEPS):
                            act.wait_ge(s["x_ready"], h * STEPS + j + 1)
                            A(X[:], bank[0][:, 0:HK], ACT.Copy).then_inc(s["x_copied"], 1)
                            act.wait_ge(s["sa_ready"], h * STEPS + j + 1)
                            A(SA[:], bank[1][:, 0:HK], ACT.Copy).then_inc(s["sa_copied"], 1)

            VS = 9 + 4

            @block.vector
            def _(dve):
                dve.wait_ge(s["const_loaded"], 96)
                dve.wait_ge(s["cleared"], 4)
                V = nc.vector
                with dve.Fori(0, HEADS // 2) as i:
                    for u in range(2):
                        h = 2 * i + u
                        c = Chain(dve, s["dve_step"], h * 24)
                        dve.wait_ge(loaded[u], i * 16 * NL + 16 * NL)
                        dve.wait_ge(s["lw_ready"], h + 1)
                        c.step(V.tensor_tensor_scan(L[:], keep[:], lw[:], 0.0, ALU.mult, ALU.add))
                        c.step(V.scalar_tensor_tensor(out=cs(G), in0=cs(L)[:, :, CH - 1:CH].broadcast_to([P, STEPS, CH]), scalar=-0.5, in1=cs(L), op0=ALU.mult, op1=ALU.add))
                        V.tensor_tensor(G2[:], G[:], lw[:], ALU.subtract).then_inc(s["g_ready"], 1)
                        c.step(V.tensor_scalar(oneminus[:], cols[u][:, 1:2], -1.0, 1.0, ALU.mult, ALU.add))
                        c.step(V.tensor_scalar(t1[:], aa[u][:], cols[u][:, 1:2], oneminus[:, 0:1], ALU.mult, ALU.add))
                        c.mark(V.tensor_tensor(km[:], k2[u][:], t1[:], ALU.mult))
                        dve.wait_ge(s["nrm_ready"], 2 * h + 2)
                        c.step(V.reciprocal(nrm[:], nrm[:]))
                        c.step(V.scalar_tensor_tensor(out=kk[:], in0=k2[u][:], scalar=cols[u][:, 0:1], in1=nrm[:], op0=ALU.mult, op1=ALU.mult))
                        c.step(V.tensor_tensor(t1[:], kk[:], aa[u][:], ALU.mult))
                        dve.wait_ge(s["exp_ready"], 7 * h + 7)
                        for z, rows in ((0, lo), (1, hi)):
                            q = slice(z * CH, z * CH + CH)
                            V.scalar_tensor_tensor(out=ar[rows, :, 0, q], in0=cs(kk)[rows], scalar=-1.0, in1=cs(e_exc)[rows], op0=ALU.mult, op1=ALU.mult)
                            V.tensor_tensor(ar[rows, CSTEPS:, 1, q], cs(r2[u])[rows], cs(e_inc)[rows, CSTEPS:], ALU.mult)
                            V.tensor_tensor(bh[rows, :, q], cs(t1)[rows], cs(e_neg)[rows], ALU.mult)
                            V.tensor_tensor(kh[rows, :, q], cs(km)[rows], cs(e_neg)[rows], ALU.mult)
                            c.step(V.scalar_tensor_tensor(out=rk[rows, :, q], in0=cs(r2[u])[rows], scalar=cols[u][rows, 2:3], in1=cs(km)[rows, CSTEPS:], op0=ALU.mult, op1=ALU.mult))
                        V.tensor_tensor(ee[:, 0:STEPS - 1], em[:, 0:STEPS - 1], em[:, 1:STEPS], ALU.mult).then_inc(s["bd_ready"], 1)
                        for g in range(NG):
                            g4 = slice(4 * g, 4 * g + 4)
                            for j in range(4 * g, 4 * g + 4):
                                dve.wait_ge(s["pb_ready"], h * STEPS + j + 1)
                                if j < CSTEPS:
                                    V.tensor_tensor(AM[:, j, 0::2, :], quad(bank[j % 2][:])[:, 0::2, :], masks[:, 0::2, :], ALU.mult).then_inc(s["pb_masked"], 1)
                                else:
                                    V.tensor_tensor(AM[:, j], quad(bank[j % 2][:]), masks[:], ALU.mult).then_inc(s["pb_masked"], 1)
                            dve.wait_ge(s["pn_ready"], h * NG + g + 1)
                            c.mark(V.tensor_tensor(T[:, g4, :], quad(bank[2][:]), over4(join0[:]), ALU.mult))
                            dve.wait_ge(s["pb_masked"], h * STEPS + 4 * g + 4)
                            c.step(V.tensor_tensor(R[:, g4, :], AM[:, g4, 0, :], over4(join[:, 0, :]), ALU.mult))
                            V.tensor_tensor(T[:, g4, :], T[:, g4, :], over4(S.ident[:]), ALU.add)
                            V.tensor_tensor(R[:, g4, :], R[:, g4, :], over4(S.ident[:]), ALU.add).then_inc(s["pn_masked"], 1)
                        for n in range(NZ):
                            l, g = n // NG, n % NG
                            g4 = slice(4 * g, 4 * g + 4)
                            if l < LEVELS - 1:
                                dve.wait_ge(s["tz_ready"], h * (NZ - NG) + n + 1)
                                V.tensor_tensor(T[:, g4, :], T[:, g4, :], quad(bank[6][:]), ALU.add).then_inc(s["tz_added"], 1)
                            dve.wait_ge(s["zr_ready"], h * NZ + n + 1)
                            V.tensor_tensor(R[:, g4, :], R[:, g4, :], quad(bank[7][:]), ALU.add).then_inc(s["zr_added"], 1)
                        dve.wait_ge(s["y_free"], h + 1)
                        V.memset(Sm[:], 0.0).then_inc(s["sm_ready"], 1)
                        for j in range(STEPS):
                            if j >= CSTEPS:
                                dve.wait_ge(s["y_ready"], h * lat + j - CSTEPS + 1)
                                n = j - CSTEPS
                                V.tensor_copy(yo[lo, n, :], bank[4 + j % 2][lo, 0:HK])
                                V.tensor_copy(yo[hi, lat - 1 - n, :], bank[4 + j % 2][hi, 0:HK]).then_inc(s["y_copied"], 1)
                            if j < STEPS - 1:
                                dve.wait_ge(s["ds_ready"], h * (STEPS - 1) + j + 1)
                                V.tensor_scalar(Sm[:], bank[2 + j % 2][:, 0:HK], ee[:, j:j + 1], None, ALU.mult).then_inc(s["sm_ready"], 1)
                        dve.wait_ge(s["bon_ready"], h + 1)
                        c.step(V.tensor_copy(bon[:], bank[6][:, 0:lat]))
                        V.tensor_tensor(yb[lo, :, :], vs[u][lo, CSTEPS:, :], bon[lo, :].rearrange("p (c o) -> p c o", o=1).broadcast_to([HK, lat, HK]), ALU.mult)
                        V.tensor_tensor(yb[hi, ::-1, :], vs[u][hi, CSTEPS:, :], bon[hi, :].rearrange("p (c o) -> p c o", o=1).broadcast_to([HK, lat, HK]), ALU.mult).then_inc(s["head_done"], 1)
                        while c.n < 24:
                            c.mark(V.nop())
                        assert c.n == 24, c.n

            @block.tensor
            def _(pe):
                pe.wait_ge(s["const_loaded"], 96)
                mmul = nc.tensor.matmul
                with pe.Fori(0, HEADS // 2) as i:
                    for u in range(2):
                        h = 2 * i + u
                        pe.wait_ge(s["sq_ready"], h + 1)
                        for n, (c0, c1) in enumerate(((0, 512), (512, ALL))):
                            mm = mmul(bank[n][:, 0:c1 - c0], halves[:], sq[:, c0:c1], start=True, stop=True)
                        mm.then_inc(s["ss_ready"], 1)
                        pe.wait_ge(s["bd_ready"], h + 1)
                        for g in range(NG):
                            for j in range(4 * g, 4 * g + 4):
                                if j >= 2:
                                    pe.wait_ge(s["pb_masked"], h * STEPS + j - 1)
                                b = bank[j % 2]
                                w = P if j < CSTEPS else 2 * P
                                rhs = ar[:, j].rearrange("p a t -> p (a t)")[:, 0:w]
                                mmul(b[:, 0:w], bh[:, j, :], rhs, start=True, stop=True)
                                mmul(b[:, 2 * P:2 * P + w], kh[:, j, :], rhs, start=True, stop=True).then_inc(s["pb_ready"], 1)
                            if g >= 1:
                                pe.wait_ge(s["pn_masked"], h * NG + g)
                            for j in range(4 * g, 4 * g + 4):
                                mm = mmul(bank[2][:, (j % 4) * P:(j % 4 + 1) * P], ar[:, j, 0, :], bh[:, j, :], start=True, stop=True)
                            mm.then_inc(s["pn_ready"], 1)
                            for n, src in enumerate((bh, kh)):
                                if g >= 1:
                                    pe.wait_ge(s["tr_copied"], h * 2 * NG + 2 * g - 1 + n)
                                for j in range(4 * g, 4 * g + 4):
                                    mm = nc.tensor.transpose(bank[3 + n][:, (j % 4) * P:(j % 4 + 1) * P], src[:, j, :], S.ident[:])
                                mm.then_inc(s["tr_ready"], 1)
                        pe.wait_ge(s["tr_copied"], h * 2 * NG + 2 * NG)

                        def grow_z(n):
                            l, g = n // NG, n % NG
                            pe.wait_ge(s["off_ready"], h * NZ + n + 1)
                            if l == 0:
                                pe.wait_ge(s["pn_masked"], h * NG + g + 1)
                            else:
                                pe.wait_ge(s["tz_added"], h * (NZ - NG) + (l - 1) * NG + g + 1)
                            if n >= 2:
                                pe.wait_ge(s["z_copied"], h * NZ + n - 1)
                            for q in range(4):
                                mm = mmul(bank[4 + n % 2][:, q * P:(q + 1) * P], off[n % 2][:, q, :], T[:, 4 * g + q, :], start=True, stop=True)
                            mm.then_inc(s["z_ready"], 1)

                        grow_z(0)
                        for n in range(NZ):
                            l, g = n // NG, n % NG
                            if n + 1 < NZ:
                                grow_z(n + 1)
                            pe.wait_ge(s["z_copied"], h * NZ + n + 1)
                            if l < LEVELS - 1:
                                if l > 0:
                                    pe.wait_ge(s["zr_added"], h * NZ + n - NG + 1)
                                if n >= 1:
                                    pe.wait_ge(s["tz_added"], h * (NZ - NG) + n)
                                for q in range(4):
                                    mm = mmul(bank[6][:, q * P:(q + 1) * P], R[:, 4 * g + q, :], Z[n % 2][:, q, :], start=True, stop=True)
                                mm.then_inc(s["tz_ready"], 1)
                            if n >= 1:
                                pe.wait_ge(s["zr_added"], h * NZ + n)
                            for q in range(4):
                                mm = mmul(bank[7][:, q * P:(q + 1) * P], Z[n % 2][:, q, :], R[:, 4 * g + q, :], start=True, stop=True)
                            mm.then_inc(s["zr_ready"], 1)
                        pe.wait_ge(s["zr_added"], h * NZ + NZ)
                        for n in range(lat):
                            mm = mmul(bank[6][:, n:n + 1], rk[:, n, :], S.ones[:, 0:1], start=True, stop=True)
                        mm.then_inc(s["bon_ready"], 1)
                        for j in range(STEPS):
                            v = vs[u][:, j, :]
                            pe.wait_ge(s["sm_ready"], h * STEPS + j + 1)
                            mmul(bank[0][:, 0:HK], ar[:, j, 0, :], Sm[:], start=True, stop=False)
                            mmul(bank[0][:, 0:HK], AM[:, j, 2, :], v, start=False, stop=True).then_inc(s["x_ready"], 1)
                            pe.wait_ge(s["x_copied"], h * STEPS + j + 1)
                            mmul(bank[1][:, 0:HK], R[:, j, :], X[:], start=True, stop=True).then_inc(s["sa_ready"], 1)
                            pe.wait_ge(s["sa_copied"], h * STEPS + j + 1)
                            if j < STEPS - 1:
                                d = bank[2 + j % 2][:, 0:HK]
                                mmul(d, S.ident[:], Sm[:], start=True, stop=False)
                                mmul(d, kT[:, j, :], v, start=False, stop=False)
                                mmul(d, bT[:, j, :], SA[:], start=False, stop=True).then_inc(s["ds_ready"], 1)
                            if j >= CSTEPS:
                                n = j - CSTEPS
                                if n >= 2:
                                    pe.wait_ge(s["y_copied"], h * lat + n - 1)
                                yp = bank[4 + j % 2][:, 0:HK]
                                mmul(yp, ar[:, j, 1, :], Sm[:], start=True, stop=False)
                                mmul(yp, AM[:, j, 3, :], v, start=False, stop=False)
                                mmul(yp, AM[:, j, 1, :], SA[:], start=False, stop=True).then_inc(s["y_ready"], 1)


def rwkv_tables():
    i = np.arange(CH)
    z1 = np.zeros((CH, CH))
    f = np.float32

    def bd(fwd, bwd):
        return np.block([[fwd, z1], [z1, bwd]]).astype(f)

    early, same = i[:, None] < i[None, :], i[:, None] == i[None, :]
    strict = bd(early, early.T)
    incl = bd(early | same, early.T | same)
    joins = []
    for l in range(LEVELS + 1):
        m = 1 << l
        b = (i[:, None] // (2 * m) == i[None, :] // (2 * m)) & (i[:, None] % (2 * m) < m) & (i[None, :] % (2 * m) >= m)
        joins.append(bd(b, b.T))
    keep = np.ones((P, ALL), f)
    keep[:, ::CH] = 0.0
    return {"rw_masks": np.ascontiguousarray(np.stack([strict, incl, strict, incl], 1)), "rw_lower": np.ascontiguousarray(strict.T),
            "rw_join": np.ascontiguousarray(np.stack(joins, 1)), "rw_join0": np.ascontiguousarray(joins[0].T),
            "rw_keep": keep, "rw_halves": bd(np.ones((CH, CH)), np.ones((CH, CH)))}


def rwkv_join(nc, name, S, a, yS, bS, gate, out):
    with Stage(nc, name) as st:
        y = [[st.sb(f"y{n}{u}", [P, D]) for n in range(4)] for u in range(2)]
        gain, shift = st.sb("gain", [P, D]), st.sb("shift", [P, D])
        g = [st.sb(f"gate{u}", [P, D]) for u in range(2)]
        mean, var, rms = st.sb("mean", [P, HEADS]), st.sb("var", [P, HEADS]), st.sb("rms", [P, HEADS])
        sq = st.sb("sq", [P, D])
        const_loaded, loaded = st.sem("const_loaded"), [st.sem(f"loaded{u}") for u in range(2)]
        dve_step, squared, var_ready, rms_ready, centred = (st.sem(n) for n in ("dve_step", "squared", "var_ready", "rms_ready", "centred"))

        def hv(x):
            return x[:].rearrange("p (h c) -> p h c", c=HK)

        def per_head(x):
            return x[:].rearrange("p (h o) -> p h o", o=1).broadcast_to([P, HEADS, HK])

        SV = 12
        with st.block() as block:
            @block.sync
            def _(sp):
                sp.dma_start(gain[:], a["rw_ln_g_2"].partition_broadcast(P)).then_inc(const_loaded, 16)
                sp.dma_start(shift[:], a["rw_ln_b_2"].partition_broadcast(P)).then_inc(const_loaded, 16)
                for t in range(NT):
                    if t >= 2:
                        sp.wait_ge(dve_step, SV * (t - 1))
                    rows = slice(t * P, (t + 1) * P)
                    for n, src in enumerate((yS[0], yS[1], bS[0], bS[1])):
                        sp.dma_start(y[t % 2][n][:], src[rows, :]).then_inc(loaded[t % 2], 16)
                    sp.dma_start(g[t % 2][:], gate[rows, :]).then_inc(loaded[t % 2], 16)

            @block.scalar
            def _(act):
                for t in range(NT):
                    act.wait_ge(centred, t + 1)
                    nc.scalar.activation(sq[:], y[t % 2][0][:], ACT.Square).then_inc(squared, 1)
                    act.wait_ge(var_ready, t + 1)
                    nc.scalar.activation(rms[:], var[:], ACT.Sqrt, scale=1.0 / HK, bias=S.eps[:, 2:3]).then_inc(rms_ready, 1)

            @block.vector
            def _(dve):
                V = nc.vector
                dve.wait_ge(const_loaded, 32)
                for t in range(NT):
                    c = Chain(dve, dve_step, t * SV)
                    y0, y1, b0, b1 = y[t % 2]
                    dve.wait_ge(loaded[t % 2], 80 * (t // 2 + 1))
                    c.step(V.tensor_tensor(y0[:], y0[:], y1[:], ALU.add))
                    c.step(V.tensor_reduce(mean[:], hv(y0), AX.X, ALU.add))
                    c.step(V.tensor_scalar(mean[:], mean[:], 1.0 / HK, None, ALU.mult))
                    V.tensor_tensor(hv(y0), hv(y0), per_head(mean), ALU.subtract).then_inc(centred, 1)
                    c.mark(V.tensor_tensor(b0[:], b0[:], b1[:], ALU.add))
                    dve.wait_ge(squared, t + 1)
                    V.tensor_reduce(var[:], hv(sq), AX.X, ALU.add).then_inc(var_ready, 1)
                    dve.wait_ge(rms_ready, t + 1)
                    c.step(V.reciprocal(rms[:], rms[:]))
                    c.step(V.tensor_tensor(hv(y0), hv(y0), per_head(rms), ALU.mult))
                    c.step(V.tensor_tensor(y0[:], y0[:], gain[:], ALU.mult))
                    c.step(V.tensor_tensor(y0[:], y0[:], shift[:], ALU.add))
                    c.step(V.tensor_tensor(y0[:], y0[:], b0[:], ALU.add))
                    c.step(V.tensor_tensor(out[:, t, :], y0[:], g[t % 2][:], ALU.mult))
                    while c.n < SV:
                        c.mark(V.nop())
                    c.wait()
                    assert c.n == SV, c.n


RW_COLS = (("mu", 6 * KD), ("w0", 2 * KD), ("a0", 2 * KD), ("norm1", KD))


def rwkv(nc, S, a, x_tiles, c_tiles, hT, mods):
    c = {}
    at = 0
    for n, w in RW_COLS:
        c[n] = S.rw_cols[:, at:at + w]
        at += w
    cols = S.mod_cols
    modulation_columns(nc, "mc1", S, mods, c["norm1"], cols)
    norm_transpose(nc, "sn1", S, c_tiles + x_tiles, hT, cols=[cols[1]] * (NA - NT) + [cols[0]] * NT)
    kF, sgF, aF = ([dram(nc, f"rw_{n}{z}", [D, ALL]) for z in range(2)] for n in ("k", "sg", "a"))
    rF = [dram(nc, f"rw_r{z}", [D, SEQ]) for z in range(2)]
    vS = [dram(nc, f"rw_v{z}", [STEPS, CH, D]) for z in range(2)]
    yS, bS = ([dram(nc, f"rw_{n}{z}", [SEQ, D]) for z in range(2)] for n in ("y", "bon"))
    gate = dram(nc, "rw_gate", [SEQ, D])
    parts = ((0, CTX), (CTX, SEQ))
    fdram = "(k p) t -> p k t"
    with ExitStack() as mem:
        xx = mem.enter_context(nc.sbuf_tensor("rw_xx", [P, KD, ALL], F32))
        mix = mem.enter_context(nc.sbuf_tensor("rw_mix", [P, KD, ALL], F32))
        token_shift(nc, "rws", hT, xx)

        def mixed(j, n):
            token_mix(nc, n, hT, xx, c["mu"][:, j * KD:(j + 1) * KD], mix)

        def both_orders(fwd, bwd, lead):
            def epi(which, engine, chain, j, n0, ps):
                w = ps.shape[1]
                o = slice(n0 - lead, n0 - lead + w)
                copy = (lambda d, s_: engine.activation(d, s_, ACT.Copy)) if which == "act" else engine.tensor_copy
                copy(fwd(j)[:, o], ps)
                return copy(backward(bwd(j)[:, o]), chunked(ps))
            return epi

        with ExitStack() as m2:
            f, b = (m2.enter_context(nc.sbuf_tensor(f"rw_rf{z}", [P, KD, SEQ], F32)) for z in range(2))
            mixed(0, "rm0")
            project(nc, "rp0", mix, SEQ, [dict(w=a["rw_wr_2"][:, q * BANK:(q + 1) * BANK], mode="F",
                                              epi=both_orders(lambda j, q=q: f[:, 4 * q + j, :], lambda j, q=q: b[:, 4 * q + j, :], CTX)) for q in range(2)],
                    parts=parts[1:], stores=[(rF[0].rearrange(fdram, p=P), f[:]), (rF[1].rearrange(fdram, p=P), b[:])])
        with ExitStack() as m2:
            f, b = (m2.enter_context(nc.sbuf_tensor(f"rw_kf{z}", [P, KD, ALL], F32)) for z in range(2))
            mixed(2, "rm2")
            project(nc, "rp2", mix, ALL, [dict(w=a["rw_wk_2"][:, q * BANK:(q + 1) * BANK], mode="F",
                                              epi=both_orders(lambda j, q=q: f[:, 4 * q + j, :], lambda j, q=q: b[:, 4 * q + j, :], 0)) for q in range(2)],
                    parts=parts, stores=[(kF[0].rearrange(fdram, p=P), f[:]), (kF[1].rearrange(fdram, p=P), b[:])])
        with ExitStack() as m2:
            v = m2.enter_context(nc.sbuf_tensor("rw_vt", [P, NA, D], F32))
            mixed(3, "rm3")
            stores = [(vS[0].rearrange("(q s) t c -> (s t) q c", s=2), v[:])]
            for j in range(STEPS):
                step = CSTEPS - 1 - j if j < CSTEPS else STEPS - 1 - (j - CSTEPS)
                stores.append((vS[1][step], v[CH * (j % 2):CH * (j % 2) + CH, j // 2, :]))
            project(nc, "rp3", mix, ALL, [dict(w=a["rw_wv_2"][:, q * BANK:(q + 1) * BANK], mode="T",
                                              epi=copy_to(lambda j, n0, q=q: v[:, j, q * BANK:(q + 1) * BANK])) for q in range(2)], stores=stores)
        for j, n, func, w1, w2, base, outF in ((1, "w", ACT.Tanh, "rw_w1_2", "rw_w2_2", c["w0"], sgF), (4, "a", ACT.Copy, "rw_a1_2", "rw_a2_2", c["a0"], aF)):
            with ExitStack() as m2:
                low = [m2.enter_context(nc.sbuf_tensor(f"rw_low{n}{z}", [HK, 1, ALL], F32)) for z in range(2)]
                f = [m2.enter_context(nc.sbuf_tensor(f"rw_out{n}{z}", [P, KD, ALL], F32)) for z in range(2)]
                mixed(j, f"rm{n}")

                def squash(z, func=func):
                    def epi(which, engine, chain, j, n0, ps):
                        return engine.activation(low[z][:, 0, n0:n0 + ps.shape[1]], ps, func)
                    return epi

                def sigmoid(z, q, base=base):
                    def epi(which, engine, chain, j, n0, ps):
                        d = 4 * q + j
                        o = slice(n0, n0 + ps.shape[1])
                        bias = base[:, z * KD + d:z * KD + d + 1]
                        if z == 0:
                            return engine.activation(f[0][:, d, o], ps, ACT.Sigmoid, bias=bias)
                        return engine.activation(backward(f[1][:, d, o]), chunked(ps), ACT.Sigmoid, bias=bias)
                    return epi

                project(nc, f"rl{n}", mix, ALL, [dict(w=a[w1][z], mode="F", eng="act", epi=squash(z)) for z in range(2)], parts=parts)
                for z in range(2):
                    project(nc, f"ro{n}{z}", low[z], ALL, [dict(w=a[w2][z][:, q * BANK:(q + 1) * BANK], mode="F", eng="act", epi=sigmoid(z, q)) for q in range(2)],
                            parts=parts, stores=[(outF[z].rearrange(fdram, p=P), f[z][:])])
        with ExitStack() as m2:
            low = m2.enter_context(nc.sbuf_tensor("rw_glow", [P, 2, SEQ], F32))
            g = m2.enter_context(nc.sbuf_tensor("rw_gt", [P, NT, D], F32))
            mixed(5, "rm5")

            def squash_g(which, engine, chain, j, n0, ps):
                return engine.activation(low[0:ps.shape[0], j, 0:SEQ], ps, ACT.Sigmoid)

            project(nc, "rg1", mix, SEQ, [dict(w=a["rw_g1_2"], mode="F", eng="act", epi=squash_g)], parts=parts[1:])
            project(nc, "rg2", low, SEQ, [dict(w=a["rw_g2_2"][:, q * BANK:(q + 1) * BANK], mode="T",
                                              epi=copy_to(lambda j, n0, q=q: g[:, j, q * BANK:(q + 1) * BANK])) for q in range(2)],
                    stores=[(gate.rearrange("(t p) c -> p t c", p=P), g[:])])
    S.free_hT()
    rwkv_scan(nc, "scan", S, a, kF, rF, sgF, aF, vS, yS, bS)
    hT = S.take_hT()
    with ExitStack() as mem:
        o = mem.enter_context(nc.sbuf_tensor("rw_o", [P, NT, D], F32))
        row = mem.enter_context(nc.sbuf_tensor("rw_gaterow", [P, D], F32))
        tmp = mem.enter_context(nc.sbuf_tensor("rw_tmp", [P, 2, BANK], F32))
        rwkv_join(nc, "rwj", S, a, yS, bS, gate, o)
        load_all(nc, "rwl", [(row[:], mods[0, 2 * D:3 * D].partition_broadcast(P))])
        norm_transpose(nc, "rwt", S, [o[:, t, :] for t in range(NT)], hT, scaled=False)
        project(nc, "rwo", hT, SEQ, [dict(w=a["rw_wo_2"][:, q * BANK:(q + 1) * BANK], mode="T", eng="dve",
                                         epi=gated_residual(lambda j, q=q: x_tiles[j][:, q * BANK:(q + 1) * BANK], lambda j, q=q: row[:, q * BANK:(q + 1) * BANK], tmp)) for q in range(2)])
    return hT


def final_norm(nc, S, x_tiles, gain, out):
    T = len(x_tiles)
    with Stage(nc, "fin") as st:
        row, junk = st.sb("row", [P, D]), st.sb("squares", [P, D])
        ss, rms, rstd = st.sb("sum_sq", [P, T]), st.sb("rms", [P, T]), st.sb("rstd", [P, T])
        y = st.sb("y", [P, T, D])
        row_loaded, rms_ready, scaled, act_step, dve_step = (st.sem(n) for n in ("row_loaded", "rms_ready", "scaled", "act_step", "dve_step"))
        stored = st.sem("stored")
        with st.block() as block:
            @block.sync
            def _(sp):
                sp.dma_start(row[:], gain.partition_broadcast(P)).then_inc(row_loaded, 16)
                for t in range(T):
                    sp.wait_ge(scaled, t + 1)
                    sp.dma_start(out[t * P:(t + 1) * P, :], y[:, t, :]).then_inc(stored, 16)
                sp.wait_ge(stored, 16 * T)

            @block.scalar
            def _(act):
                steps = Chain(act, act_step)
                for t in range(T):
                    steps.step(nc.scalar.activation(junk[:], x_tiles[t], ACT.Square, accum_out=ss[:, t:t + 1]))
                nc.scalar.activation(rms[:], ss[:], ACT.Sqrt, scale=1.0 / D, bias=S.eps6[:, 0:1]).then_inc(rms_ready, 1)

            @block.vector
            def _(dve):
                steps = Chain(dve, dve_step)
                dve.wait_ge(rms_ready, 1)
                steps.step(nc.vector.reciprocal(rstd[:], rms[:]))
                dve.wait_ge(row_loaded, 16)
                for t in range(T):
                    nc.vector.scalar_tensor_tensor(out=y[:, t, :], in0=x_tiles[t], scalar=rstd[:, t:t + 1], in1=row[:], op0=ALU.mult, op1=ALU.mult).then_inc(scaled, 1)


def second_block_b(nc, S, a, x_tiles, c_tiles, hT, mods, out):
    hT = rwkv(nc, S, a, x_tiles, c_tiles, hT, mods[1])
    moe(nc, "moe1", S, a, 1, ((x_tiles, 0),), hT, mods[1])
    final_norm(nc, S, x_tiles, a["final_g_2"], out)


def rwkv_layout(inp):
    g = lambda n: np.asarray(inp[n])
    out = {n: np.ascontiguousarray(g(n)[0]) for n in ("rw_wr_2", "rw_wk_2", "rw_wv_2", "rw_wo_2", "rw_w1_2", "rw_w2_2", "rw_a1_2", "rw_a2_2", "rw_g1_2", "rw_g2_2", "rw_ln_g_2", "rw_ln_b_2")}
    out["final_g_2"] = np.ascontiguousarray(g("final_g_2"))
    out["rwkv_cols"] = np.concatenate([columns(g("rw_mu_2")), columns(g("rw_w0_2")), columns(g("rw_a0_2")), columns(g("norm1_g_2")[1])], 1)
    per = np.stack([g("rw_k_k_2")[0].reshape(HEADS, HK), g("rw_k_a_2")[0].reshape(HEADS, HK), g("rw_r_k_2")[0], g("rw_r_k_2")[0]], 2)
    out["rw_cols"] = np.ascontiguousarray(np.concatenate([per, per], 1))
    return out



def network(nc, a, out):
    Stage.zeroed = []
    S = Shared()
    with ExitStack() as mem:
        def sb(n, shape):
            return mem.enter_context(nc.sbuf_tensor(n, shape, F32))
        S.pool_sems = [[nc.alloc_semaphore(f"pool_dma{l}{n}") for n in range(7)] for l in range(2)]
        S.ident, S.ones, S.eps = sb("identity", [P, P]), sb("ones", [P, P]), sb("epsilons", [P, 4])
        S.eps6 = S.eps[:, 0:1]
        S.first_cols, S.second_cols, S.rw_cols = sb("first_columns", [P, 37]), sb("second_columns", [P, 32]), sb("rwkv_columns", [P, 88])
        mod_cols = sb("mod_columns", [P, 4, KD])
        S.mod_cols = [(mod_cols[:, 0], mod_cols[:, 1]), (mod_cols[:, 2], mod_cols[:, 3])]
        x = sb("x", [P, NT, D])
        hT_mem = ExitStack()
        taken = []

        def take_hT():
            taken.append(1)
            return hT_mem.enter_context(nc.sbuf_tensor(f"hT{len(taken)}", [P, KD, ALL], F32))

        S.take_hT, S.free_hT = take_hT, hT_mem.close
        mods = dram(nc, "mods", [2, 2, N_MOD * D])
        tok = "(t p) d -> p t d"
        load_all(nc, "consts", [(S.ident[:], a["ident"]), (S.ones[:], a["ones"]), (S.eps[:], a["eps"]), (S.first_cols[:], a["first_cols"]),
                                (S.second_cols[:], a["second_cols"]), (S.rw_cols[:], a["rwkv_cols"]), (x[:], a["x"].rearrange(tok, p=P))])
        x_tiles = [x[:, t, :] for t in range(NT)]
        with ExitStack() as first:
            first_block(nc, S, a, x_tiles, first.enter_context(nc.sbuf_tensor("first_hT", [P, KD, ALL], F32)))
        xc = sb("xc", [P, NA - NT, D])
        c_tiles = [xc[:, t, :] for t in range(NA - NT)]
        hT = take_hT()
        load_all(nc, "context", [(xc[:], a["ctx_2"].rearrange(tok, p=P))])
        second_block_a(nc, S, a, x_tiles, c_tiles, hT, mods)
        second_block_b(nc, S, a, x_tiles, c_tiles, hT, mods, out)
        hT_mem.close()


def kernel(**inputs):
    import concourse.bacc as bacc
    from concourse.bass_utils import run_bass_kernel_spmd

    inp = {n: np.asarray(v) for n, v in inputs.items()}
    arrays = {}
    for part in (first_layout(inp), second_layout(inp), rwkv_layout(inp), constants(), attention_tables(), gla_tables(),
                 rope_tables(), route_tables(), rwkv_tables()):
        arrays.update(part)
    nc = bacc.Bacc("TRN2", target_bir_lowering=False, num_devices=1)
    a = {n: nc.dram_tensor(f"in_{n}_dram", v.shape, mybir.dt.from_np(v.dtype), kind="ExternalInput").ap() for n, v in arrays.items()}
    out = nc.dram_tensor("out_0_dram", (1, SEQ, D), F32, kind="ExternalOutput").ap()
    network(nc, a, out[0])
    r = run_bass_kernel_spmd(nc, [{f"in_{n}_dram": v for n, v in arrays.items()}], core_ids=[0])
    return r.results[0]["out_0_dram"]
```

```python
import math
from contextlib import ExitStack

import numpy as np
import concourse.bass as bass
from concourse import mybir

F32 = mybir.dt.float32
I32 = mybir.dt.int32
ACT = mybir.ActivationFunctionType
ALU = mybir.AluOpType
AX = mybir.AxisListType

P = 128
D = 1024
SEQ = 512
CTX = 256
ALL = SEQ + CTX
KD = D // P
NT = SEQ // P
NA = ALL // P
BANK = 512
EPS = 1e-6


class Stage:

    zeroed = []

    def __init__(self, nc, name):
        self.nc, self.name = nc, name

    def __enter__(self):
        self.stack = ExitStack()
        self.sems = []
        return self

    def sb(self, name, shape, dt=F32):
        return self.stack.enter_context(self.nc.sbuf_tensor(f"{self.name}_{name}", shape, dt))

    def ps(self, name, shape, dt=F32):
        return self.stack.enter_context(self.nc.psum_tensor(f"{self.name}_{name}", shape, dt))

    def sem(self, name):
        s = self.nc.alloc_semaphore(f"{self.name}_{name}")
        self.sems.append(s)
        return s

    def block(self):
        return self.nc.Block()

    def __exit__(self, *exc):
        self.stack.close()
        if exc[0] is None:
            for s in Stage.zeroed:
                self.nc.release_semaphore(s)
            for s in self.sems:
                self.nc.gpsimd.sem_clear(s)
            Stage.zeroed = self.sems


class Chain:

    def __init__(self, eng, sem, base=0):
        self.eng, self.sem, self.base, self.n = eng, sem, base, 0

    def mark(self, ins):
        ins.then_inc(self.sem, 1)
        self.n += 1

    def wait(self):
        self.eng.wait_ge(self.sem, self.base + self.n)

    def step(self, ins):
        self.mark(ins)
        self.wait()


def kslices(k):
    return [(a, min(P, k - a)) for a in range(0, k, P)]


def project(nc, name, hT, n_tok, jobs, const=None, parts=None, mix=None):
    with Stage(nc, name) as st:
        K = jobs[0]["w"].shape[0]
        ks = kslices(K)
        cw = max(j["w"].shape[1] for j in jobs)
        wbuf = [st.sb(f"w{b}", [P, len(ks), cw]) for b in range(2)]
        banks = [st.ps(f"bank{b}", [P, BANK]) for b in range(8)]
        w_loaded = [st.sem(f"w_loaded{b}") for b in range(2)]
        products_done = st.sem("products_done")
        act_done, dve_done = st.sem("act_done"), st.sem("dve_done")
        act_step, dve_step = st.sem("act_step"), st.sem("dve_step")
        stored, mixed = st.sem("stored"), st.sem("mixed")

        groups = []
        for c, job in enumerate(jobs):
            width = job["w"].shape[1]
            if job["mode"] == "F":
                for j, (f0, fw) in enumerate(kslices(width)):
                    for n0, nw in parts or [(n0, min(BANK, n_tok - n0)) for n0 in range(0, n_tok, BANK)]:
                        groups.append((c, j, f0, fw, n0, nw))
            else:
                for j, (n0, nw) in enumerate(kslices(n_tok)):
                    groups.append((c, j, n0, nw, 0, width))
        last_of = {}
        for g, grp in enumerate(groups):
            last_of[grp[0]] = g
        engine_of = []
        for g, grp in enumerate(groups):
            e = jobs[grp[0]].get("eng", "any")
            engine_of.append(("act", "dve")[g % 2] if e == "any" else e)
        nth = [engine_of[:g + 1].count(engine_of[g]) for g in range(len(groups))]

        def view(g):
            c, j, a, aw, b0, bw = groups[g]
            return banks[g % 8][0:aw, 0:bw]

        n_stores = sum(len(job.get("stores", ())) for job in jobs)

        with st.block() as block:
            @block.sync
            def _(sp):
                def store(c):
                    ended = engine_of[:last_of[c] + 1]
                    for which, done in (("act", act_done), ("dve", dve_done)):
                        if which in ended:
                            sp.wait_ge(done, ended.count(which))
                    for dst, src in jobs[c].get("stores", ()):
                        sp.dma_start(dst, src).then_inc(stored, 16)

                for c, job in enumerate(jobs):
                    if c >= 2:
                        sp.wait_ge(products_done, last_of[c - 2] + 1)
                    full = K // P
                    width = job["w"].shape[1]
                    if full:
                        sp.dma_start(wbuf[c % 2][:, 0:full, 0:width],
                                     job["w"][0:full * P, :].rearrange("(k p) n -> p k n", p=P)
                                     ).then_inc(w_loaded[c % 2], 16)
                    if K % P:
                        sp.dma_start(wbuf[c % 2][0:K % P, full, 0:width],
                                     job["w"][full * P:K, :]).then_inc(w_loaded[c % 2], 16)
                    if c >= 2 and jobs[c - 2].get("stores"):
                        store(c - 2)
                for c in range(max(0, len(jobs) - 2), len(jobs)):
                    store(c)
                if n_stores:
                    sp.wait_ge(stored, 16 * n_stores)

            @block.tensor
            def _(pe):
                seen = -1
                per = 16 * ((K // P > 0) + (K % P > 0))
                for g, (c, j, a, aw, b0, bw) in enumerate(groups):
                    job = jobs[c]
                    if c != seen:
                        pe.wait_ge(w_loaded[c % 2], per * (c // 2 + 1))
                        seen = c
                    if g >= 8:
                        pe.wait_ge(act_done if engine_of[g - 8] == "act" else dve_done, nth[g - 8])
                    w = wbuf[c % 2]
                    bias = job.get("bias")
                    x = job.get("x", hT)
                    for k, (_, kw) in enumerate(ks):
                        if mix and g == 0:
                            pe.wait_ge(mixed, k + 1)
                        if job["mode"] == "F":
                            lhsT, rhs = w[0:kw, k, a:a + aw], x[0:kw, k, b0:b0 + bw]
                        else:
                            lhsT, rhs = x[0:kw, k, a:a + aw], w[0:kw, k, 0:bw]
                        mm = nc.tensor.matmul(view(g), lhsT, rhs, start=(k == 0),
                                              stop=(k == len(ks) - 1 and bias is None))
                    if bias is not None:
                        mm = nc.tensor.matmul(view(g), const["ones"][0:1, 0:aw], bias, start=False, stop=True)
                    mm.then_inc(products_done, 1)

            def ends(which, eng, engine, chain, done):
                for g, (c, j, a, aw, b0, bw) in enumerate(groups):
                    if engine_of[g] == which:
                        eng.wait_ge(products_done, g + 1)
                        jobs[c]["epi"](which, engine, chain, j, b0, view(g)).then_inc(done, 1)

            @block.scalar
            def _(act):
                ends("act", act, nc.scalar, Chain(act, act_step), act_done)

            @block.vector
            def _(dve):
                if mix:
                    h, xx, mu = mix
                    for k in range(len(ks)):
                        nc.vector.scalar_tensor_tensor(out=hT[:, k, :], in0=xx[:, k, :], scalar=mu[:, k:k + 1], in1=h[:, k, :],
                                                       op0=ALU.mult, op1=ALU.add).then_inc(mixed, 1)
                ends("dve", dve, nc.vector, Chain(dve, dve_step), dve_done)


def copy_to(dest):
    def epi(which, engine, chain, j, n0, ps):
        if which == "act":
            return engine.activation(dest(j, n0), ps, ACT.Copy)
        return engine.tensor_copy(dest(j, n0), ps)
    return epi


def norm_transpose(nc, name, S, tiles, hT, cols=None, rows=None, h_dram=None, scaled=True):
    T = len(tiles)
    width = tiles[0].shape[1]
    kd = width // P
    halves = -(-kd // 4)
    with Stage(nc, name) as st:
        junk = st.sb("squares", [P, width])
        ss = st.sb("sum_sq", [P, T])
        rms = st.sb("rms", [P, T])
        rstd = st.sb("rstd", [P, T])
        xn = [st.sb(f"xn{b}", [P, width]) for b in range(2)]
        tp = [st.ps(f"tp{b}", [P, 4, P]) for b in range(4)]
        rms_ready, xn_ready = st.sem("rms_ready"), st.sem("xn_ready")
        dve_step, act_step = st.sem("dve_step"), st.sem("act_step")
        turned = st.sem("turned")
        emptied = [st.sem("act_emptied"), st.sem("dve_emptied")]
        stored = [st.sem("stored0"), st.sem("stored1")]

        def empty(which, engine, g):
            t, h = g // halves, g % halves
            n = min(4, kd - 4 * h)
            src = tp[g % 4]
            if cols is None:
                dst = hT[:, 4 * h:4 * h + n, t * P:(t + 1) * P]
                if which == "act":
                    return engine.activation(dst, src[:, 0:n, :], ACT.Copy)
                return engine.tensor_copy(dst, src[:, 0:n, :])
            gain, bias = cols[t]
            for q in range(n):
                d = 4 * h + q
                dst = hT[:, d, t * P:(t + 1) * P]
                if which == "act":
                    ins = engine.activation(dst, src[:, q, :], ACT.Identity,
                                            scale=gain[:, d:d + 1],
                                            bias=bias[:, d:d + 1] if bias is not None else 0.0)
                elif bias is None:
                    ins = engine.tensor_scalar(dst, src[:, q, :], gain[:, d:d + 1], None, ALU.mult)
                else:
                    ins = engine.tensor_scalar(dst, src[:, q, :], gain[:, d:d + 1], bias[:, d:d + 1],
                                               ALU.mult, ALU.add)
            return ins

        G = T * halves
        with st.block() as block:
            @block.scalar
            def _(act):
                steps = Chain(act, act_step)
                if scaled:
                    for t in range(T):
                        steps.step(nc.scalar.activation(junk[:], tiles[t], ACT.Square, accum_out=ss[:, t:t + 1]))
                    steps.wait()
                    nc.scalar.activation(rms[:], ss[:], ACT.Sqrt, scale=1.0 / width, bias=S.eps6[:, 0:1]).then_inc(rms_ready, 1)
                for g in range(0, G, 2):
                    act.wait_ge(turned, g + 1)
                    empty("act", nc.scalar, g).then_inc(emptied[0], 1)

            @block.vector
            def _(dve):
                steps = Chain(dve, dve_step)
                if scaled:
                    dve.wait_ge(rms_ready, 1)
                    steps.step(nc.vector.reciprocal(rstd[:], rms[:]))

                def make(t):
                    if t >= 2:
                        dve.wait_ge(turned, (t - 1) * halves)
                        if h_dram is not None:
                            dve.wait_ge(stored[t % 2], 16 * (t // 2))
                    if rows is None:
                        nc.vector.tensor_scalar(xn[t % 2][:], tiles[t], rstd[:, t:t + 1], None, ALU.mult).then_inc(xn_ready, 1)
                    else:
                        steps.step(nc.vector.scalar_tensor_tensor(out=xn[t % 2][:], in0=tiles[t], scalar=rstd[:, t:t + 1],
                                                                  in1=rows[t][0], op0=ALU.mult, op1=ALU.mult))
                        nc.vector.tensor_tensor(xn[t % 2][:], xn[t % 2][:], rows[t][1], ALU.add).then_inc(xn_ready, 1)

                if scaled:
                    make(0)
                for t in range(T):
                    if scaled and t + 1 < T:
                        make(t + 1)
                    for g in range(t * halves, (t + 1) * halves):
                        if g % 2:
                            dve.wait_ge(turned, g + 1)
                            empty("dve", nc.vector, g).then_inc(emptied[1], 1)

            @block.tensor
            def _(pe):
                for g in range(G):
                    t, h = g // halves, g % halves
                    if scaled and h == 0:
                        pe.wait_ge(xn_ready, t + 1)
                    if g >= 4:
                        pe.wait_ge(emptied[g % 2], (g - 4) // 2 + 1)
                    src = xn[t % 2] if scaled else tiles[t]
                    for q in range(min(4, kd - 4 * h)):
                        d = 4 * h + q
                        mm = nc.tensor.transpose(tp[g % 4][:, q, :], src[:, d * P:(d + 1) * P], S.ident[:, :])
                    mm.then_inc(turned, 1)

            if h_dram is not None:
                @block.sync
                def _(sp):
                    for t in range(T):
                        sp.wait_ge(xn_ready, t + 1)
                        sp.dma_start(h_dram[t * P:(t + 1) * P, :], xn[t % 2][:]).then_inc(stored[t % 2], 16)
                    for u in range(min(2, T)):
                        sp.wait_ge(stored[u], 16 * ((T - u + 1) // 2))


def residual_norm(nc, name, S, y, x_tiles, gain_row):
    T = len(x_tiles)
    with Stage(nc, name) as st:
        row = st.sb("row", [P, D])
        junk = st.sb("squares", [P, D])
        ss = st.sb("sum_sq", [P, T])
        rms = st.sb("rms", [P, T])
        rstd = st.sb("rstd", [P, T])
        row_loaded, rms_ready = st.sem("row_loaded"), st.sem("rms_ready")
        act_step, dve_step = st.sem("act_step"), st.sem("dve_step")
        with st.block() as block:
            @block.sync
            def _(sp):
                sp.dma_start(row[:], gain_row.partition_broadcast(P)).then_inc(row_loaded, 16)

            @block.scalar
            def _(act):
                steps = Chain(act, act_step)
                for t in range(T):
                    steps.step(nc.scalar.activation(junk[:], y[:, t, :], ACT.Square, accum_out=ss[:, t:t + 1]))
                steps.wait()
                nc.scalar.activation(rms[:], ss[:], ACT.Sqrt, scale=1.0 / D, bias=S.eps6[:, 0:1]).then_inc(rms_ready, 1)

            @block.vector
            def _(dve):
                steps = Chain(dve, dve_step)
                dve.wait_ge(rms_ready, 1)
                steps.step(nc.vector.reciprocal(rstd[:], rms[:]))
                dve.wait_ge(row_loaded, 16)
                for t in range(T):
                    steps.mark(nc.vector.scalar_tensor_tensor(out=y[:, t, :], in0=y[:, t, :], scalar=rstd[:, t:t + 1],
                                                              in1=row[:], op0=ALU.mult, op1=ALU.mult))
                steps.wait()
                for t in range(T):
                    steps.mark(nc.vector.tensor_tensor(x_tiles[t], x_tiles[t], y[:, t, :], ALU.add))
                steps.wait()


class Shared:
    pass


def constants():
    i = np.arange(P)
    f = np.float32
    out = {"ident": np.eye(P, dtype=f), "ones": np.ones((P, P), f)}
    out["eps"] = np.tile(np.array([[1e-6, 1e-5, 64e-5, 1e-12]], f), (P, 1))
    return out


HD = 64


def attention(nc, name, S, qT, kT, v, out, heads, dh, scale, back, group=1, slope0=None, rel=None, extra=None,
              causal=None, sinks=None):
    W = 4 * P
    with Stage(nc, name) as st:
        q = [st.sb(f"q{u}", [dh, SEQ]) for u in range(2)]
        k = [st.sb(f"k{u}", [dh, SEQ]) for u in range(2)]
        vv = [st.sb(f"v{u}", [P, NT, HD]) for u in range(2)]
        o = [st.sb(f"o{u}", [P, NT, HD]) for u in range(2)]
        sink = [st.sb(f"sink{u}", [P, 1]) for u in range(2)]
        relt, extrat = st.sb("rel", [P, W]), st.sb("extra", [P, W])
        bias = [st.sb(f"bias{u}", [P, W]) for u in range(2 if causal is None else 1)] * (1 if causal is None else 2)
        slope = st.sb("slope", [P, 1])
        logits = [st.sb(f"logits{b}", [P, W]) for b in range(2)]
        probs = [st.sb(f"probs{b}", [P, W]) for b in range(2)]
        probsT = [st.sb(f"probsT{b}", [P, W]) for b in range(2)]
        top = [st.sb(f"top{b}", [P, 1]) for b in range(2)]
        negtop = [st.sb(f"negtop{b}", [P, 1]) for b in range(2)]
        den = [st.sb(f"den{b}", [P, 1]) for b in range(2)]
        sinkexp = [st.sb(f"sinkexp{b}", [P, 1]) for b in range(2)]
        rden = [st.sb(f"rden{b}", [P, 1]) for b in range(2)]
        ps_s = [st.ps(f"ps_s{b}", [P, W]) for b in range(2)]
        ps_t = [st.ps(f"ps_t{b}", [P, W]) for b in range(2)]
        ps_o = [st.ps(f"ps_o{b}", [P, W]) for b in range(2)]
        const_loaded = st.sem("const_loaded")
        head_loaded = [st.sem(f"head_loaded{u}") for u in range(2)]
        scores_ready, max_ready, probs_ready = st.sem("scores_ready"), st.sem("max_ready"), st.sem("probs_ready")
        turned, turned_copied = st.sem("turned"), st.sem("turned_copied")
        out_ready, out_scaled = st.sem("out_ready"), st.sem("out_scaled")
        stored = [st.sem(f"stored{u}") for u in range(2)]
        dve_step, unit_begun = st.sem("dve_step"), st.sem("unit_begun")
        loads = 4 if sinks is not None else 3
        AHEAD = 2

        units = [(u, b) for u in range(2) for b in range(NT)]

        def k0(b):
            return max(0, b - back)

        with st.block() as block:
            @block.sync
            def _(sp):
                if causal is not None:
                    sp.dma_start(bias[0][:], causal).then_inc(const_loaded, 16)
                else:
                    sp.dma_start(relt[:], rel).then_inc(const_loaded, 16)
                    sp.dma_start(extrat[:], extra).then_inc(const_loaded, 16)
                def load(h, u):
                    hk = h // group if group > 1 else h
                    sp.dma_start(q[u][:], qT[bass.ds(h, 1), :, :].rearrange("a d t -> (a d) t")).then_inc(head_loaded[u], 16)
                    sp.dma_start(k[u][:], kT[bass.ds(hk, 1), :, :].rearrange("a d t -> (a d) t")).then_inc(head_loaded[u], 16)
                    sp.dma_start(vv[u][:], v.rearrange("(t p) c -> p t c", p=P)[:, :, bass.ds(hk * HD, HD)]).then_inc(head_loaded[u], 16)
                    if sinks is not None:
                        sp.dma_start(sink[u][:], sinks[bass.ds(h, 1)].partition_broadcast(P)).then_inc(head_loaded[u], 16)

                def store(h, u):
                    sp.wait_ge(out_scaled, h * NT + NT + AHEAD)
                    sp.dma_start(out.rearrange("(t p) c -> p t c", p=P)[:, :, bass.ds(h * HD, HD)], o[u][:]).then_inc(stored[u], 16)

                load(0, 0)
                load(1, 1)
                with sp.Fori(0, heads // 2 - 1) as i:
                    for u in range(2):
                        store(2 * i + u, u)
                        sp.wait_ge(stored[u], 16 * i + 16)
                        load(2 * i + 2 + u, u)
                for u in range(2):
                    store(heads - 2 + u, u)
                    sp.wait_ge(stored[u], 16 * (heads // 2))

            @block.tensor
            def _(pe):
                pe.sem_inc(scores_ready, AHEAD)
                pe.sem_inc(turned, AHEAD)
                pe.sem_inc(out_ready, AHEAD)

                def scores(n, u, b):
                    pe.wait_ge(max_ready, n - 1 + AHEAD)
                    w = (b + 1 - k0(b)) * P
                    nc.tensor.matmul(ps_s[b % 2][:, 0:w], q[u][:, b * P:(b + 1) * P], k[u][:, k0(b) * P:(b + 1) * P],
                                     start=True, stop=True).then_inc(scores_ready, 1)

                def turn(n, u, b):
                    pe.wait_ge(probs_ready, n + 1 + AHEAD)
                    pe.wait_ge(turned_copied, n - 1 + AHEAD)
                    for j in range(b + 1 - k0(b)):
                        mm = nc.tensor.transpose(ps_t[b % 2][:, j * P:(j + 1) * P], probs[b % 2][:, j * P:(j + 1) * P], S.ident[:, :])
                    mm.then_inc(turned, 1)

                def weigh(n, u, b):
                    pe.wait_ge(turned_copied, n + 1 + AHEAD)
                    pe.wait_ge(out_scaled, n - 1 + AHEAD)
                    m = b + 1 - k0(b)
                    for j in range(m):
                        mm = nc.tensor.matmul(ps_o[b % 2][:, 0:HD], probsT[b % 2][:, j * P:(j + 1) * P], vv[u][:, k0(b) + j, :],
                                              start=(j == 0), stop=(j == m - 1))
                    mm.then_inc(out_ready, 1)

                with pe.Fori(0, heads // 2) as i:
                    def ahead(x):
                        if x < len(units):
                            u, b = units[x]
                            if b == 0:
                                pe.wait_ge(head_loaded[u], 16 * loads * i + 16 * loads)
                            scores(i * len(units) + x, u, b)

                    ahead(0)
                    ahead(1)
                    for x, (u, b) in enumerate(units):
                        turn(i * len(units) + x, u, b)
                        ahead(x + 2)
                        weigh(i * len(units) + x, u, b)

            @block.scalar
            def _(act):
                act.sem_inc(probs_ready, AHEAD)
                with act.Fori(0, heads // 2) as i:
                    for u in range(2):
                        for b in range(NT):
                            n = (2 * i + u) * NT + b
                            w = (b + 1 - k0(b)) * P
                            act.wait_ge(max_ready, n + 1 + AHEAD)
                            act.wait_ge(turned, n - 1 + AHEAD)
                            if sinks is not None:
                                act.activation(sinkexp[b % 2][:], sink[u][:], ACT.Exp, bias=negtop[b % 2][:])
                            act.activation(probs[b % 2][:, 0:w], logits[b % 2][:, 0:w], ACT.Exp, bias=negtop[b % 2][:],
                                           accum_out=den[b % 2][:]).then_inc(probs_ready, 1)

            @block.vector
            def _(dve):
                dve.sem_inc(max_ready, AHEAD)
                dve.sem_inc(turned_copied, AHEAD)
                dve.sem_inc(out_scaled, AHEAD)
                dve.wait_ge(const_loaded, 16 if causal is not None else 32)
                per = len(units) * (4 if sinks is not None else 2) + (4 if causal is None else 0)
                if causal is None:
                    nc.vector.memset(slope[:], slope0).then_inc(dve_step, 1)
                start = 1 if causal is None else 0
                if start:
                    dve.wait_ge(dve_step, 1)

                def biggest(n, u, b, steps):
                    w = (b + 1 - k0(b)) * P
                    dve.wait_ge(scores_ready, n + 1 + AHEAD)
                    dve.wait_ge(probs_ready, n - 1 + AHEAD)
                    dve.sem_inc(unit_begun, 1)
                    steps.step(nc.vector.tensor_tensor_reduce(out=logits[b % 2][:, 0:w], in0=ps_s[b % 2][:, 0:w], in1=bias[u][:, W - w:W],
                                                              scale=scale, scalar=-3e38, op0=ALU.add, op1=ALU.max,
                                                              accum_out=top[b % 2][:]))
                    if sinks is not None:
                        steps.step(nc.vector.tensor_tensor(top[b % 2][:], top[b % 2][:], sink[u][:], ALU.max))
                    nc.vector.tensor_scalar(negtop[b % 2][:], top[b % 2][:], -1.0, None, ALU.mult).then_inc(max_ready, 1)

                def copy_turned(n, b, steps):
                    w = (b + 1 - k0(b)) * P
                    dve.wait_ge(turned, n + 1 + AHEAD)
                    dve.wait_ge(out_ready, n - 1 + AHEAD)
                    nc.vector.tensor_copy(probsT[b % 2][:, 0:w], ps_t[b % 2][:, 0:w]).then_inc(turned_copied, 1)
                    if sinks is not None:
                        steps.step(nc.vector.tensor_tensor(den[b % 2][:], den[b % 2][:], sinkexp[b % 2][:], ALU.add))
                    dve.wait_ge(out_scaled, n - 1 + AHEAD)
                    steps.step(nc.vector.reciprocal(rden[b % 2][:], den[b % 2][:]))

                def finish(n, u, b):
                    dve.wait_ge(out_ready, n + 1 + AHEAD)
                    nc.vector.tensor_scalar(o[u][:, b, :], ps_o[b % 2][:, 0:HD], rden[b % 2][:, 0:1], None, ALU.mult).then_inc(out_scaled, 1)

                with dve.Fori(0, heads // 2) as i:
                    steps = Chain(dve, dve_step, i * per + start)
                    if causal is None:
                        for u in range(2):
                            steps.step(nc.vector.scalar_tensor_tensor(out=bias[u][:], in0=relt[:], scalar=slope[:, 0:1], in1=extrat[:],
                                                                      op0=ALU.mult, op1=ALU.add))
                            steps.step(nc.vector.tensor_scalar(slope[:], slope[:], 0.5, None, ALU.mult))
                    for x, (u, b) in enumerate(units):
                        n = i * len(units) + x
                        for y in ((0, 1) if x == 0 else (x + 1,)):
                            if y < len(units):
                                if units[y][1] == 0:
                                    dve.wait_ge(head_loaded[units[y][0]], 16 * loads * i + 16 * loads)
                                biggest(i * len(units) + y, *units[y], steps)
                        copy_turned(n, b, steps)
                        if x >= 1:
                            finish(n - 1, *units[x - 1])
                    finish(i * len(units) + len(units) - 1, *units[-1])
                    assert steps.n == per


A_PATTERNS = ((128, 1), (512, 4), (2048, 16))
BIG = 1e30


def attention_tables():
    delta = (np.arange(P)[:, None] + 3 * P - np.arange(4 * P)[None, :]).astype(np.int64)
    count = sum(((delta >= 0) & (delta <= w) & (delta % d == 0)).astype(np.int64) for w, d in A_PATTERNS)
    seen = count > 0
    swa = (delta >= 0) & (delta <= 127)
    f = np.float32
    return {
        "dil_rel": np.where(seen, delta, BIG).astype(f),
        "dil_extra": np.where(seen, np.log(np.maximum(count, 1)) * 8.0, 0.0).astype(f),
        "swa_rel": np.where(swa, delta, BIG).astype(f),
        "zero_extra": np.zeros((P, 4 * P), f),
        "causal": np.where(delta >= 0, 0.0, -BIG).astype(f),
    }

B_HEADS, B_DK, B_DV, B_CHUNK = 4, 64, 128, 64


def gla_decay(nc, name, S, z, log_a):
    width = z.shape[1] * z.shape[2]
    with Stage(nc, name) as st:
        t1, t2 = st.sb("t1", [P, width]), st.sb("t2", [P, width])
        act_step, dve_step, stored = st.sem("act_step"), st.sem("dve_step"), st.sem("stored")
        zf = z[:].rearrange("p t c -> p (t c)")
        with st.block() as block:
            @block.scalar
            def _(act):
                steps = Chain(act, act_step)
                steps.step(nc.scalar.activation(t1[:], zf, ACT.Abs))
                steps.step(nc.scalar.activation(t1[:], t1[:], ACT.Exp, scale=-1.0))
                steps.step(nc.scalar.activation(t1[:], t1[:], ACT.Ln, bias=S.ones[:, 0:1]))

            @block.vector
            def _(dve):
                steps = Chain(dve, dve_step)
                steps.step(nc.vector.tensor_scalar(t2[:], zf, 0.0, 1.0 / 16, ALU.min, ALU.mult))
                dve.wait_ge(act_step, 3)
                steps.step(nc.vector.scalar_tensor_tensor(out=t1[:], in0=t1[:], scalar=-1.0 / 16, in1=t2[:], op0=ALU.mult, op1=ALU.add))

            @block.sync
            def _(sp):
                sp.wait_ge(dve_step, 2)
                sp.dma_start(log_a.rearrange("(t p) c -> p t c", p=P), t1[:].rearrange("p (t c) -> p t c", t=NT)).then_inc(stored, 16)
                sp.wait_ge(stored, 16)


def gla(nc, name, S, qT, kT, v, r, log_a, tri, norm_row, out, col0):
    NC = SEQ // B_CHUNK
    with Stage(nc, name) as st:
        trit, normt = st.sb("tri", [P, P]), st.sb("norm", [P, B_DV])
        q, k = st.sb("q", [B_DK, SEQ]), st.sb("k", [B_DK, SEQ])
        vt, rt = st.sb("v", [P, NT, B_DV]), st.sb("r", [P, NT, B_DV])
        la = st.sb("log_a", [P, NT, B_DK])
        cum, mid, last = st.sb("cum", [B_DK, SEQ]), st.sb("mid", [B_DK, SEQ]), st.sb("last", [B_DK, SEQ])
        e_q, e_k, e_b, e_l = (st.sb(f"e_{x}", [B_DK, SEQ]) for x in "qkbl")
        decay = st.sb("decay", [B_DK, NC])
        att, klT = st.sb("att", [P, NT, P]), st.sb("klT", [P, NT, B_DK])
        state = st.sb("state", [B_DK, NC, B_DV])
        o, gate = st.sb("o", [P, NT, B_DV]), st.sb("gate", [P, NT, B_DV])
        junk, ss, rms, rstd = st.sb("squares", [P, B_DV]), st.sb("sum_sq", [P, NT]), st.sb("rms", [P, NT]), st.sb("rstd", [P, NT])
        p_cum = st.ps("p_cum", [B_DK, SEQ])
        p_att = st.ps("p_att", [P, NT, P])
        p_kl = st.ps("p_kl", [P, NT, B_DK])
        p_ds = [st.ps(f"p_ds{b}", [B_DK, 4, B_DV]) for b in range(2)]
        p_o = st.ps("p_o", [P, NT, B_DV])
        const_loaded, loaded, stored = st.sem("const_loaded"), st.sem("loaded"), st.sem("stored")
        cum_ready, turned_ready, states_fed, out_ready = st.sem("cum_ready"), st.sem("turned_ready"), st.sem("states_fed"), st.sem("out_ready")
        act_step, dve_step, pe_passed = st.sem("act_step"), st.sem("dve_step"), st.sem("pe_passed")
        A, V = 12, 20

        def chunks(x):
            return x[:].rearrange("d (n c) -> d n c", c=B_CHUNK)

        with st.block() as block:
            @block.sync
            def _(sp):
                sp.dma_start(trit[:], tri).then_inc(const_loaded, 16)
                sp.dma_start(normt[:], norm_row.partition_broadcast(P)).then_inc(const_loaded, 16)

                def load(h):
                    sp.dma_start(q[:], qT[bass.ds(h, 1), :, :].rearrange("a d t -> (a d) t")).then_inc(loaded, 16)
                    sp.dma_start(k[:], kT[bass.ds(h, 1), :, :].rearrange("a d t -> (a d) t")).then_inc(loaded, 16)
                    sp.dma_start(vt[:], v.rearrange("(t p) c -> p t c", p=P)[:, :, bass.ds(h * B_DV, B_DV)]).then_inc(loaded, 16)
                    sp.dma_start(rt[:], r.rearrange("(t p) c -> p t c", p=P)[:, :, bass.ds(h * B_DV, B_DV)]).then_inc(loaded, 16)
                    sp.dma_start(la[:], log_a.rearrange("(t p) c -> p t c", p=P)[:, :, bass.ds(h * B_DK, B_DK)]).then_inc(loaded, 16)

                load(0)
                with sp.Fori(0, B_HEADS) as h:
                    sp.wait_ge(dve_step, h * V + V)
                    sp.dma_start(out.rearrange("(t p) c -> p t c", p=P)[:, :, bass.ds(h * B_DV + col0, B_DV)], o[:]).then_inc(stored, 16)
                    sp.wait_ge(stored, 16 * h + 16)
                    load((h + 1) % B_HEADS)
                sp.wait_ge(loaded, 16 * 5 * (B_HEADS + 1))

            @block.tensor
            def _(pe):
                pe.wait_ge(const_loaded, 32)
                with pe.Fori(0, B_HEADS) as h:
                    pe.wait_ge(loaded, h * 80 + 80)
                    for t in range(NT):
                        mm = nc.tensor.matmul(p_cum[:, t * P:(t + 1) * P], la[:, t, :], trit[:], start=True, stop=True)
                    mm.then_inc(cum_ready, 1)
                    pe.wait_ge(dve_step, h * V + 7)
                    for t in range(NT):
                        c = slice(t * P, (t + 1) * P)
                        nc.tensor.matmul(p_att[:, t, :], e_k[:, c], e_q[:, c], start=True, stop=True)
                        mm = nc.tensor.transpose(p_kl[:, t, :], e_l[:, c], S.ident[0:B_DK, 0:B_DK])
                    mm.then_inc(turned_ready, 1)
                    pe.wait_ge(act_step, h * A + 6)
                    pe.sem_inc(pe_passed, 1)
                    for n in range(NC):
                        s = slice(B_CHUNK * (n % 2), B_CHUNK * (n % 2) + B_CHUNK)
                        mm = nc.tensor.matmul(p_ds[n % 2][:, n // 2, :], klT[s, n // 2, :], vt[s, n // 2, :], start=True, stop=True)
                    mm.then_inc(states_fed, 1)
                    pe.wait_ge(dve_step, h * V + 16)
                    for t in range(NT):
                        nc.tensor.matmul(p_o[:, t, :], att[:, t, :], vt[:, t, :], start=True, stop=False, skip_group_check=True)
                        for n in (2 * t, 2 * t + 1):
                            s = slice(B_CHUNK * (n % 2), B_CHUNK * (n % 2) + B_CHUNK)
                            mm = nc.tensor.matmul(p_o[s, t, :], e_b[:, n * B_CHUNK:(n + 1) * B_CHUNK], state[:, n, :],
                                                  start=False, stop=(n % 2 == 1), skip_group_check=True)
                    mm.then_inc(out_ready, 1)

            @block.scalar
            def _(act):
                with act.Fori(0, B_HEADS) as h:
                    steps = Chain(act, act_step, h * A)
                    act.wait_ge(dve_step, h * V + 3)
                    steps.mark(nc.scalar.activation(e_q[:], mid[:], ACT.Exp))
                    steps.mark(nc.scalar.activation(e_k[:], mid[:], ACT.Exp, scale=-1.0))
                    steps.mark(nc.scalar.activation(e_b[:], cum[:], ACT.Exp))
                    steps.mark(nc.scalar.activation(e_l[:], last[:], ACT.Exp))
                    steps.mark(nc.scalar.activation(decay[:], chunks(cum)[:, :, B_CHUNK - 1], ACT.Exp))
                    act.wait_ge(turned_ready, h + 1)
                    steps.step(nc.scalar.activation(klT[:], p_kl[:], ACT.Copy))
                    act.wait_ge(loaded, h * 80 + 80)
                    steps.mark(nc.scalar.activation(gate[:], rt[:], ACT.Silu))
                    act.wait_ge(out_ready, h + 1)
                    for t in range(NT):
                        steps.step(nc.scalar.activation(junk[:], p_o[:, t, :], ACT.Square, accum_out=ss[:, t:t + 1]))
                    steps.step(nc.scalar.activation(rms[:], ss[:], ACT.Sqrt, scale=1.0 / B_DV, bias=S.eps6[:, 0:1]))
                    assert steps.n == A

            @block.vector
            def _(dve):
                dve.wait_ge(const_loaded, 32)
                with dve.Fori(0, B_HEADS) as h:
                    steps = Chain(dve, dve_step, h * V)
                    dve.wait_ge(cum_ready, h + 1)
                    steps.step(nc.vector.tensor_copy(cum[:], p_cum[:]))
                    c3 = chunks(cum)
                    steps.mark(nc.vector.tensor_tensor(chunks(mid), c3, c3[:, :, B_CHUNK // 2 - 1:B_CHUNK // 2].broadcast_to([B_DK, NC, B_CHUNK]), ALU.subtract))
                    steps.step(nc.vector.tensor_tensor(chunks(last), c3[:, :, B_CHUNK - 1:B_CHUNK].broadcast_to([B_DK, NC, B_CHUNK]), c3, ALU.subtract))
                    dve.wait_ge(act_step, h * A + 5)
                    for e, x, scale in ((e_q, q, B_DK ** -0.5), (e_k, k, 1.0), (e_l, k, 1.0), (e_b, q, B_DK ** -0.5)):
                        steps.mark(nc.vector.scalar_tensor_tensor(out=e[:], in0=e[:], scalar=scale, in1=x[:], op0=ALU.mult, op1=ALU.mult))
                    steps.wait()
                    dve.wait_ge(turned_ready, h + 1)
                    steps.mark(nc.vector.tensor_tensor(att[:], p_att[:], trit[:].rearrange("s (a c) -> s a c", a=1).broadcast_to([P, NT, P]), ALU.mult))
                    steps.step(nc.vector.memset(state[:, 0, :], 0.0))
                    dve.wait_ge(states_fed, h + 1)
                    for n in range(NC - 1):
                        steps.step(nc.vector.scalar_tensor_tensor(out=state[:, n + 1, :], in0=state[:, n, :], scalar=decay[:, n:n + 1],
                                                                  in1=p_ds[n % 2][:, n // 2, :], op0=ALU.mult, op1=ALU.add))
                    dve.wait_ge(act_step, h * A + 12)
                    steps.step(nc.vector.reciprocal(rstd[:], rms[:]))
                    for t in range(NT - 1):
                        nc.vector.scalar_tensor_tensor(out=o[:, t, :], in0=p_o[:, t, :], scalar=rstd[:, t:t + 1], in1=normt[:], op0=ALU.mult, op1=ALU.mult)
                    t = NT - 1
                    steps.step(nc.vector.scalar_tensor_tensor(out=o[:, t, :], in0=p_o[:, t, :], scalar=rstd[:, t:t + 1], in1=normt[:], op0=ALU.mult, op1=ALU.mult))
                    steps.mark(nc.vector.tensor_tensor(o[:], o[:], gate[:], ALU.mult))
                    while steps.n < V:
                        steps.mark(nc.vector.nop())
                    assert steps.n == V, steps.n


def gla_tables():
    i = np.arange(P)
    tri = (i[:, None] <= i[None, :]) & (i[:, None] // B_CHUNK == i[None, :] // B_CHUNK)
    return {"gla_tri": tri.astype(np.float32)}


D_FF = 2816
FT = D_FF // P


def swiglu_up(nc, name, hT, w_gate_up, guT):
    with Stage(nc, name) as st:
        w = [st.sb(f"w{u}", [P, 2, KD, P]) for u in range(2)]
        sg = [st.sb(f"gate{u}", [P, SEQ]) for u in range(2)]
        p_g = [st.ps(f"p_g{u}", [P, SEQ]) for u in range(2)]
        p_u = [st.ps(f"p_u{u}", [P, SEQ]) for u in range(2)]
        loaded = [st.sem(f"loaded{u}") for u in range(2)]
        gate_ready, up_ready, gated, multiplied = st.sem("gate_ready"), st.sem("up_ready"), st.sem("gated"), st.sem("multiplied")
        AHEAD = 2
        with st.block() as block:
            @block.sync
            def _(sp):
                for u in range(2):
                    sp.dma_start(w[u][:], w_gate_up[u]).then_inc(loaded[u], 16)
                with sp.Fori(0, FT // 2 - 1) as i:
                    for u in range(2):
                        sp.wait_ge(up_ready, 2 * i + u + 1 + AHEAD)
                        sp.dma_start(w[u][:], w_gate_up[bass.ds(2 * i + 2 + u, 1)].rearrange("a p g k f -> (a p) g k f")).then_inc(loaded[u], 16)

            @block.tensor
            def _(pe):
                pe.sem_inc(up_ready, AHEAD)
                with pe.Fori(0, FT // 2) as i:
                    for u in range(2):
                        s = 2 * i + u
                        pe.wait_ge(loaded[u], 16 * i + 16)
                        pe.wait_ge(multiplied, s - 1 + AHEAD)
                        for g, (p, ready) in enumerate(((p_g[u], gate_ready), (p_u[u], up_ready))):
                            for k in range(KD):
                                mm = nc.tensor.matmul(p[:], w[u][:, g, k, :], hT[:, k, 0:SEQ], start=(k == 0), stop=(k == KD - 1))
                            mm.then_inc(ready, 1)

            @block.scalar
            def _(act):
                with act.Fori(0, FT // 2) as i:
                    for u in range(2):
                        s = 2 * i + u
                        act.wait_ge(gate_ready, s + 1)
                        act.wait_ge(multiplied, s - 1 + AHEAD)
                        nc.scalar.activation(sg[u][:], p_g[u][:], ACT.Silu).then_inc(gated, 1)

            @block.vector
            def _(dve):
                dve.sem_inc(multiplied, AHEAD)
                with dve.Fori(0, FT // 2) as i:
                    for u in range(2):
                        s = 2 * i + u
                        dve.wait_ge(gated, s + 1)
                        dve.wait_ge(up_ready, s + 1 + AHEAD)
                        nc.vector.tensor_tensor(guT[:, bass.ds(s, 1), :].rearrange("p a t -> p (a t)"), sg[u][:], p_u[u][:], ALU.mult).then_inc(multiplied, 1)


D_HEADS, D_NOPE, D_ROPE = 8, 64, 32


def rope_tables():
    half = D_ROPE // 2
    freqs = (np.float32(10000.0) ** (-np.arange(half, dtype=np.float32) / np.float32(half))).astype(np.float32)
    ang = np.arange(SEQ, dtype=np.float32)[:, None] * freqs[None, :]
    def lay(x):
        return np.ascontiguousarray(x.astype(np.float32).reshape(NT, P, half).transpose(1, 0, 2))
    return {"cos": lay(np.cos(ang)), "sin": lay(np.sin(ang))}


def mla_heads(nc, name, S, q, kv, k_rope, cos, sin, qT_d, kT_d, v_d):
    half = D_ROPE // 2
    HQ = D_NOPE + D_ROPE
    with Stage(nc, name) as st:
        ct, sn = st.sb("cos", [P, NT, half]), st.sb("sin", [P, NT, half])
        tmp = [st.sb(f"tmp{n}", [P, NT, D_HEADS, half]) for n in range(4)]
        kp = st.sb("k_pe", [P, NT, D_ROPE])
        kk = st.sb("keys", [P, NT, D_HEADS, HQ])
        outT = [st.sb(f"outT{b}", [HQ, SEQ]) for b in range(4)]
        tp = [st.ps(f"tp{b}", [HQ, SEQ]) for b in range(4)]
        loaded, dve_step, act_step, pool_step = st.sem("loaded"), st.sem("dve_step"), st.sem("act_step"), st.sem("pool_step")
        turned = st.sem("turned")
        emptied = [st.sem("act_emptied"), st.sem("dve_emptied")]
        stored, v_stored = [st.sem(f"stored{b}") for b in range(4)], st.sem("v_stored")
        q4 = q[:].rearrange("p t (h c) -> p t h c", h=D_HEADS)
        kv4 = kv[:].rearrange("p t (h c) -> p t h c", h=D_HEADS)
        QS = 4 * 6
        G = 2 * D_HEADS
        ROTATED = QS + 6 + NT

        with st.block() as block:
            @block.sync
            def _(sp):
                sp.dma_start(ct[:], cos).then_inc(loaded, 16)
                sp.dma_start(sn[:], sin).then_inc(loaded, 16)
                for t in range(NT):
                    sp.dma_start(v_d[t * P:(t + 1) * P, :].rearrange("p (h c) -> p h c", h=D_HEADS), kv4[:, t, :, D_NOPE:2 * D_NOPE]).then_inc(v_stored, 16)
                for g in range(G):
                    sp.wait_ge(emptied[g % 2], g // 2 + 1)
                    dst = qT_d if g < D_HEADS else kT_d
                    sp.dma_start(dst[g % D_HEADS], outT[g % 4][:]).then_inc(stored[g % 4], 16)
                for b in range(4):
                    sp.wait_ge(stored[b], 16 * (G // 4))
                sp.wait_ge(v_stored, 16 * NT)

            @block.gpsimd
            def _(pool):
                for t in range(NT):
                    nc.gpsimd.tensor_copy(kk[:, t, :, 0:D_NOPE], kv4[:, t, :, 0:D_NOPE]).then_inc(pool_step, 1)

            def empty(which, engine, eng, g):
                eng.wait_ge(turned, g + 1)
                if g >= 4:
                    eng.wait_ge(stored[g % 4], 16 * (g // 4))
                if which == "act":
                    engine.activation(outT[g % 4][:], tp[g % 4][:], ACT.Copy).then_inc(emptied[0], 1)
                else:
                    engine.tensor_copy(outT[g % 4][:], tp[g % 4][:]).then_inc(emptied[1], 1)

            @block.vector
            def _(dve):
                steps = Chain(dve, dve_step)
                dve.wait_ge(loaded, 32)

                for t in range(NT):
                    x1, x2 = q4[:, t, :, D_NOPE:D_NOPE + half], q4[:, t, :, D_NOPE + half:HQ]
                    c = ct[:, t:t + 1, :].broadcast_to([P, D_HEADS, half])
                    s = sn[:, t:t + 1, :].broadcast_to([P, D_HEADS, half])
                    for n, (x, y) in enumerate(((x1, c), (x2, s), (x2, c), (x1, s))):
                        steps.mark(nc.vector.tensor_tensor(tmp[n][:, t], x, y, ALU.mult))
                    steps.wait()
                    steps.mark(nc.vector.tensor_tensor(x1, tmp[0][:, t], tmp[1][:, t], ALU.subtract))
                    steps.mark(nc.vector.tensor_tensor(x2, tmp[2][:, t], tmp[3][:, t], ALU.add))
                steps.wait()
                x1, x2 = k_rope[:, :, 0:half], k_rope[:, :, half:D_ROPE]
                for n, (x, y) in enumerate(((x1, ct), (x2, sn), (x2, ct), (x1, sn))):
                    steps.mark(nc.vector.tensor_tensor(tmp[n][:, :, 0, :], x, y[:], ALU.mult))
                steps.wait()
                steps.mark(nc.vector.tensor_tensor(kp[:, :, 0:half], tmp[0][:, :, 0, :], tmp[1][:, :, 0, :], ALU.subtract))
                steps.step(nc.vector.tensor_tensor(kp[:, :, half:D_ROPE], tmp[2][:, :, 0, :], tmp[3][:, :, 0, :], ALU.add))
                for t in range(NT):
                    steps.mark(nc.vector.tensor_copy(kk[:, t, :, D_NOPE:HQ], kp[:, t:t + 1, :].broadcast_to([P, D_HEADS, D_ROPE])))
                assert steps.n == ROTATED
                for g in range(1, G, 2):
                    empty("dve", nc.vector, dve, g)

            @block.scalar
            def _(act):
                for g in range(0, G, 2):
                    empty("act", nc.scalar, act, g)

            @block.tensor
            def _(pe):
                pe.wait_ge(dve_step, ROTATED)
                pe.wait_ge(pool_step, NT)
                for g in range(G):
                    if g >= 4:
                        pe.wait_ge(emptied[g % 2], (g - 4) // 2 + 1)
                    src = q4 if g < D_HEADS else kk
                    for t in range(NT):
                        mm = nc.tensor.transpose(tp[g % 4][:, t * P:(t + 1) * P], src[:, t, g % D_HEADS, :], S.ident[:, :])
                    mm.then_inc(turned, 1)


def load_all(nc, name, pairs):
    with Stage(nc, name) as st:
        loaded = st.sem("loaded")
        with st.block() as block:
            @block.sync
            def _(sp):
                for dst, src in pairs:
                    sp.dma_start(dst, src).then_inc(loaded, 16)
                sp.wait_ge(loaded, 16 * len(pairs))


def gated_ffn(nc, name, S, x_tiles, hT, gcol, post_row, w_gate_up, w_down):
    norm_transpose(nc, name + "n", S, x_tiles, hT, cols=[(gcol, None)] * NT)
    with ExitStack() as mem:
        guT = mem.enter_context(nc.sbuf_tensor(name + "_guT", [P, FT, SEQ], F32))
        y = mem.enter_context(nc.sbuf_tensor(name + "_y", [P, NT, D], F32))
        swiglu_up(nc, name + "u", hT, w_gate_up, guT)
        W = 256
        project(nc, name + "d", guT, SEQ,
                [dict(w=w_down[:, c * W:(c + 1) * W], mode="T", epi=copy_to(lambda j, n0, c=c: y[:, j, c * W:(c + 1) * W]))
                 for c in range(D // W)])
        residual_norm(nc, name + "r", S, y, x_tiles, post_row)


def mix_out(nc, name, S, x_tiles, hT, mixed, w_out, post_row):
    with ExitStack() as mem:
        m = mem.enter_context(nc.sbuf_tensor(name + "_m", [P, NT, D], F32))
        y = mem.enter_context(nc.sbuf_tensor(name + "_y", [P, NT, D], F32))
        load_all(nc, name + "l", [(m[:], mixed.rearrange("(t p) d -> p t d", p=P))])
        norm_transpose(nc, name + "t", S, [m[:, t, :] for t in range(NT)], hT, scaled=False)
        project(nc, name + "p", hT, SEQ,
                [dict(w=w_out[:, c * BANK:(c + 1) * BANK], mode="T", epi=copy_to(lambda j, n0, c=c: y[:, j, c * BANK:(c + 1) * BANK]))
                 for c in range(D // BANK)])
        residual_norm(nc, name + "r", S, y, x_tiles, post_row)


def dram(nc, name, shape, dt=F32):
    return nc.dram_tensor(name, shape, dt, kind="Internal").ap()


FIRST_COLS = (("norm_mix_pre", 2 * KD), ("norm_ffn_pre", 2 * KD), ("mla_q_norm", 3), ("mla_kv_norm", 2))


def first_block(nc, S, a, x_tiles, hT):
    c = {}
    at = 0
    for n, w in FIRST_COLS:
        c[n] = S.first_cols[:, at:at + w]
        at += w
    mixed = dram(nc, "mixed0", [SEQ, D])
    norm_transpose(nc, "n0", S, x_tiles, hT, cols=[(c["norm_mix_pre"][:, 0:KD], None)] * NT)
    qk_a, v_a = dram(nc, "qk_a", [2 * 8, HD, SEQ]), dram(nc, "v_a", [SEQ, 512])
    qk_b = dram(nc, "qk_b", [2 * B_HEADS, B_DK, SEQ])
    v_b, r_b, log_a = dram(nc, "v_b", [SEQ, 512]), dram(nc, "r_b", [SEQ, 512]), dram(nc, "log_a", [SEQ, 256])
    w = a["ab_w_in"]
    with ExitStack() as mem:
        def sb(n, shape):
            return mem.enter_context(nc.sbuf_tensor(n, shape, F32))
        qka, qkb = sb("qka", [P, 8, SEQ]), sb("qkb", [P, 4, SEQ])
        vrt = sb("vrt", [P, 3, NT, 512])
        gT = sb("gT", [P, 1, SEQ])
        tok, two = "(t p) c -> p t c", "(j u) d t -> (u d) j t"
        jobs = [dict(w=w[:, 512 * n:512 * n + 512], mode="F", epi=copy_to(lambda j, n0, n=n: qka[:, 4 * n + j, :]),
                     stores=[(qk_a[8 * n:8 * n + 8].rearrange(two, u=2), qka[:, 4 * n:4 * n + 4])]) for n in range(2)]
        jobs += [dict(w=w[:, 1536:2048], mode="F", epi=copy_to(lambda j, n0: qkb[:, j, :]), stores=[(qk_b.rearrange(two, u=2), qkb[:])])]
        jobs += [dict(w=w[:, o:o + 512], mode="T", epi=copy_to(lambda j, n0, n=n: vrt[:, n, j, :]), stores=[(d.rearrange(tok, p=P), vrt[:, n])])
                 for n, (o, d) in enumerate(((1024, v_a), (2048, v_b), (2560, r_b)))]
        jobs += [dict(w=w[:, 3072:3088], mode="F", epi=copy_to(lambda j, n0: gT[0:16, 0, :]))]
        project(nc, "p0", hT, SEQ, jobs)
        z = sb("z", [P, NT, 256])
        brow = sb("b_gate_row", [1, 256])
        load_all(nc, "gl", [(brow[:], a["gla_b_gate"].rearrange("(o c) -> o c", o=1))])
        project(nc, "gz", gT, SEQ, [dict(w=a["gla_w_gate_up"], mode="T", bias=brow[:], epi=copy_to(lambda j, n0: z[:, j, :]))], const={"ones": S.ones})
        gla_decay(nc, "gd", S, z, log_a)
    attention(nc, "at0", S, qk_a[0:8], qk_a[8:16], v_a, mixed[:, 0:512], 8, HD, HD ** -0.5, 3,
              slope0=-4.0, rel=a["dil_rel"], extra=a["dil_extra"])
    gla(nc, "gla", S, qk_b[0:4], qk_b[4:8], v_b, r_b, log_a, a["gla_tri"], a["gla_norm"], mixed, 512)
    mix_out(nc, "mo0", S, x_tiles, hT, mixed, a["ab_w_out"], a["norm_mix_post"][0])
    gated_ffn(nc, "f0", S, x_tiles, hT, c["norm_ffn_pre"][:, 0:KD], a["norm_ffn_post"][0], a["ffn_w_gate_up"][0], a["ffn_w_down"][0])
    norm_transpose(nc, "n1", S, x_tiles, hT, cols=[(c["norm_mix_pre"][:, KD:2 * KD], None)] * NT)
    qk_c, v_c = dram(nc, "qk_c", [10, HD, SEQ]), dram(nc, "v_c", [SEQ, 128])
    qT_d, kT_d, v_d = dram(nc, "qT_d", [8, 96, SEQ]), dram(nc, "kT_d", [8, 96, SEQ]), dram(nc, "v_d", [SEQ, 512])
    w = a["cd_w_in"]
    with ExitStack() as mem:
        def sb(n, shape):
            return mem.enter_context(nc.sbuf_tensor(n, shape, F32))
        qkc = sb("qkc", [P, 5, SEQ])
        vq, kvr = sb("vq", [P, NT, 512]), sb("kvr", [P, NT, 288])
        two = "(j u) d t -> (u d) j t"
        jobs = [dict(w=w[:, 0:512], mode="F", epi=copy_to(lambda j, n0: qkc[:, j, :]), stores=[(qk_c[0:8].rearrange(two, u=2), qkc[:, 0:4])]),
                dict(w=w[:, 512:640], mode="F", epi=copy_to(lambda j, n0: qkc[:, 4, :]), stores=[(qk_c[8:10].rearrange(two, u=2), qkc[:, 4:5])]),
                dict(w=w[:, 640:1152], mode="T", epi=copy_to(lambda j, n0: vq[:, j, :]), stores=[(v_c.rearrange("(t p) c -> p t c", p=P), vq[:, :, 0:128])]),
                dict(w=w[:, 1152:1440], mode="T", epi=copy_to(lambda j, n0: kvr[:, j, :]))]
        project(nc, "p1", hT, SEQ, jobs)
        cqT, ckvT = sb("cqT", [P, 3, SEQ]), sb("ckvT", [P, 2, SEQ])
        norm_transpose(nc, "nq", S, [vq[:, t, 128:512] for t in range(NT)], cqT, cols=[(c["mla_q_norm"], None)] * NT)
        norm_transpose(nc, "nkv", S, [kvr[:, t, 0:256] for t in range(NT)], ckvT, cols=[(c["mla_kv_norm"], None)] * NT)
        q, kv = sb("q_d", [P, NT, 768]), sb("kv_d", [P, NT, 1024])
        project(nc, "uq", cqT, SEQ, [dict(w=a["mla_w_uq"][:, 384 * n:384 * n + 384], mode="T",
                                          epi=copy_to(lambda j, n0, n=n: q[:, j, 384 * n:384 * n + 384])) for n in range(2)])
        project(nc, "ukv", ckvT, SEQ, [dict(w=a["mla_w_ukv"][:, 512 * n:512 * n + 512], mode="T",
                                            epi=copy_to(lambda j, n0, n=n: kv[:, j, 512 * n:512 * n + 512])) for n in range(2)])
        mla_heads(nc, "mh", S, q, kv, kvr[:, :, 256:288], a["cos"], a["sin"], qT_d, kT_d, v_d)
    attention(nc, "at1", S, qk_c[0:8], qk_c[8:10], v_c, mixed[:, 0:512], 8, HD, HD ** -0.5, 1, group=4,
              slope0=-4.0, rel=a["swa_rel"], extra=a["zero_extra"], sinks=a["swa_sinks"])
    attention(nc, "at2", S, qT_d, kT_d, v_d, mixed[:, 512:1024], 8, 96, 96 ** -0.5, 3, causal=a["causal"])
    mix_out(nc, "mo1", S, x_tiles, hT, mixed, a["cd_w_out"], a["norm_mix_post"][1])
    gated_ffn(nc, "f1", S, x_tiles, hT, c["norm_ffn_pre"][:, KD:2 * KD], a["norm_ffn_post"][1], a["ffn_w_gate_up"][1], a["ffn_w_down"][1])


def columns(v):
    return np.ascontiguousarray(np.asarray(v).reshape(-1, P).T)


def first_layout(inp):
    out = {n: np.ascontiguousarray(inp[n][0]) for n in ("ab_w_in", "ab_w_out", "gla_w_gate_up", "gla_b_gate", "gla_norm", "cd_w_in", "cd_w_out",
                                                        "swa_sinks", "mla_w_uq", "mla_w_ukv")}
    for n in ("norm_mix_post", "norm_ffn_post", "ffn_w_down"):
        out[n] = np.ascontiguousarray(inp[n])
    gu = np.stack([inp["ffn_w_gate"], inp["ffn_w_up"]], 1)
    out["ffn_w_gate_up"] = np.ascontiguousarray(gu.reshape(2, 2, KD, P, FT, P).transpose(0, 4, 3, 1, 2, 5))
    out["x"] = np.ascontiguousarray(inp["x"][0])
    out["first_cols"] = np.concatenate([columns(inp[n]) for n, _ in FIRST_COLS], 1)
    return out


N_MOD = 6
W_GMLP = 2048
GROUPS = 16
E_GROUPS, E_PER, N_EXP, HID = 4, 8, 32, 512


def modulation(nc, name, S, cT, ada_w, bias, mods):
    with ExitStack() as mem:
        sc = mem.enter_context(nc.sbuf_tensor(name + "_silu", [P, KD, 2], F32))
        brow = mem.enter_context(nc.sbuf_tensor(name + "_bias", [1, N_MOD * D], F32))
        out = mem.enter_context(nc.sbuf_tensor(name + "_out", [2, N_MOD * D], F32))
        with Stage(nc, name + "s") as st:
            loaded, done = st.sem("loaded"), st.sem("done")
            with st.block() as block:
                @block.sync
                def _(sp):
                    sp.dma_start(sc[:], cT).then_inc(loaded, 16)
                    sp.dma_start(brow[:], bias.rearrange("(o c) -> o c", o=1)).then_inc(loaded, 16)
                    sp.wait_ge(loaded, 32)

                @block.scalar
                def _(act):
                    act.wait_ge(loaded, 32)
                    nc.scalar.activation(sc[:], sc[:], ACT.Silu).then_inc(done, 1)
                    act.wait_ge(done, 1)
        project(nc, name + "p", sc, 2,
                [dict(w=ada_w[:, c * BANK:(c + 1) * BANK], mode="T", bias=brow[0:1, c * BANK:(c + 1) * BANK],
                      epi=copy_to(lambda j, n0, c=c: out[:, c * BANK:(c + 1) * BANK]),
                      stores=[(mods[:, c * BANK:(c + 1) * BANK], out[:, c * BANK:(c + 1) * BANK])]) for c in range(N_MOD * D // BANK)],
                const={"ones": S.ones})


def modulation_columns(nc, name, S, mods, gcol, out):
    with Stage(nc, name) as st:
        rows = [st.sb(f"rows{w}", [N_MOD * KD, P]) for w in range(2)]
        tp = [st.ps(f"tp{w}", [P, N_MOD * KD]) for w in range(2)]
        loaded, turned, dve_step = st.sem("loaded"), st.sem("turned"), st.sem("dve_step")
        with st.block() as block:
            @block.sync
            def _(sp):
                for w in range(2):
                    sp.dma_start(rows[w][:], mods[w].rearrange("(k p) -> k p", p=P)).then_inc(loaded, 16)

            @block.tensor
            def _(pe):
                pe.wait_ge(loaded, 32)
                for w in range(2):
                    nc.tensor.transpose(tp[w][:], rows[w][:], S.ident[0:N_MOD * KD, 0:N_MOD * KD]).then_inc(turned, 1)

            @block.vector
            def _(dve):
                steps = Chain(dve, dve_step)
                for w in range(2):
                    dve.wait_ge(turned, w + 1)
                    gain, bias = out[w]
                    steps.mark(nc.vector.scalar_tensor_tensor(out=gain, in0=tp[w][:, KD:2 * KD], scalar=1.0, in1=gcol, op0=ALU.add, op1=ALU.mult))
                    steps.mark(nc.vector.tensor_copy(bias, tp[w][:, 0:KD]))
                steps.wait()


def modulation_rows(nc, name, mods, g_row, out):
    with Stage(nc, name) as st:
        g = st.sb("g", [P, D])
        loaded, dve_step = st.sem("loaded"), st.sem("dve_step")
        with st.block() as block:
            @block.sync
            def _(sp):
                sp.dma_start(g[:], g_row.partition_broadcast(P)).then_inc(loaded, 16)
                for w in range(len(out)):
                    sp.dma_start(out[w][0], mods[w, 4 * D:5 * D].partition_broadcast(P)).then_inc(loaded, 16)
                    sp.dma_start(out[w][1], mods[w, 3 * D:4 * D].partition_broadcast(P)).then_inc(loaded, 16)
                sp.wait_ge(loaded, 16 * (1 + 2 * len(out)))

            @block.vector
            def _(dve):
                steps = Chain(dve, dve_step)
                dve.wait_ge(loaded, 16 * (1 + 2 * len(out)))
                for w in range(len(out)):
                    steps.mark(nc.vector.scalar_tensor_tensor(out=out[w][0], in0=out[w][0], scalar=1.0, in1=g[:], op0=ALU.add, op1=ALU.mult))
                steps.wait()


def gated_residual(x_tile, gate_row, tmp):
    def epi(which, engine, chain, j, n0, ps):
        chain.step(engine.tensor_tensor(tmp[:, j % 2], ps, gate_row(j), ALU.mult))
        return engine.tensor_tensor(x_tile(j), x_tile(j), tmp[:, j % 2], ALU.add)
    return epi


def spatial_gate(nc, name, S, uT, v, ln_rows, w_sT, b_s):
    with Stage(nc, name) as st:
        gain, shift = st.sb("gain", [P, W_GMLP]), st.sb("shift", [P, W_GMLP])
        ws = st.sb("w_s", [P, GROUPS, P])
        bs = st.sb("b_s", [1, GROUPS, P])
        stats = st.sb("stats", [P, W_GMLP // BANK, 6])
        mv = st.sb("mean_var", [P, 2])
        rms, rstd, variance = st.sb("rms", [P, 1]), st.sb("rstd", [P, 1]), st.sb("variance", [P, 1])
        banks = [st.ps(f"bank{b}", [P, 4, P]) for b in range(8)]
        loaded, normed, mixed, emptied = st.sem("loaded"), st.sem("normed"), st.sem("mixed"), st.sem("emptied")
        dve_step, var_ready, rms_ready = st.sem("dve_step"), st.sem("var_ready"), st.sem("rms_ready")
        nb = W_GMLP // BANK
        with st.block() as block:
            @block.sync
            def _(sp):
                sp.dma_start(gain[:], ln_rows[0].partition_broadcast(P)).then_inc(loaded, 16)
                sp.dma_start(shift[:], ln_rows[1].partition_broadcast(P)).then_inc(loaded, 16)
                sp.dma_start(ws[:], w_sT).then_inc(loaded, 16)
                sp.dma_start(bs[:], b_s).then_inc(loaded, 16)

            @block.vector
            def _(dve):
                steps = Chain(dve, dve_step)
                dve.wait_ge(loaded, 64)

                def gate(t):
                    for q in range(4):
                        dve.wait_ge(mixed, 4 * t + q + 1)
                        u = uT[:, 4 * q:4 * q + 4, t * P:(t + 1) * P]
                        nc.vector.tensor_tensor(u, u, banks[(4 * t + q) % 8][:], ALU.mult).then_inc(emptied, 1)

                for t in range(NA):
                    for b in range(nb):
                        steps.mark(nc.vector.bn_stats(stats[:, b, :], v[:, t, b * BANK:(b + 1) * BANK]))
                    steps.wait()
                    steps.mark(nc.vector.bn_aggr(mv[:], stats[:].rearrange("p b s -> p (b s)")))
                    steps.wait()
                    nc.vector.tensor_scalar(variance[:], mv[:, 1:2], 1.0, None, ALU.mult).then_inc(var_ready, 1)
                    dve.wait_ge(rms_ready, t + 1)
                    steps.step(nc.vector.reciprocal(rstd[:], rms[:]))
                    steps.step(nc.vector.tensor_scalar(v[:, t, :], v[:, t, :], mv[:, 0:1], rstd[:, 0:1], ALU.subtract, ALU.mult))
                    steps.step(nc.vector.tensor_tensor(v[:, t, :], v[:, t, :], gain[:], ALU.mult))
                    nc.vector.tensor_tensor(v[:, t, :], v[:, t, :], shift[:], ALU.add).then_inc(normed, 1)
                    if t:
                        gate(t - 1)
                gate(NA - 1)

            @block.scalar
            def _(act):
                for t in range(NA):
                    act.wait_ge(var_ready, t + 1)
                    nc.scalar.activation(rms[:], variance[:], ACT.Sqrt, bias=S.eps[:, 1:2]).then_inc(rms_ready, 1)

            @block.tensor
            def _(pe):
                pe.wait_ge(loaded, 64)
                for t in range(NA):
                    pe.wait_ge(normed, t + 1)
                    for q in range(4):
                        n = 4 * t + q
                        if n >= 8:
                            pe.wait_ge(emptied, n - 7)
                        for g in range(4):
                            gg = 4 * q + g
                            nc.tensor.matmul(banks[n % 8][:, g, :], v[:, t, gg * P:(gg + 1) * P], ws[:, gg, :], start=True, stop=False)
                            mm = nc.tensor.matmul(banks[n % 8][:, g, :], S.ones[0:1, :], bs[0:1, gg, :], start=False, stop=True)
                        mm.then_inc(mixed, 1)


def route(nc, name, S, logits, T, n_blocks, a, dest, weight, table, experts):
    cap = (n_blocks + 1) * P
    with Stage(nc, name) as st:
        def sb(n, shape, dt=F32):
            return st.sb(n, shape, dt)
        rank4, rank8 = sb("rank4", [P, 4]), sb("rank8", [P, 8])
        before, column = sb("before", [P, P]), sb("column", [P, 1])
        tokens, zeros = sb("tokens", [P, T], I32), sb("zeros", [P, n_blocks + 1], I32)
        gm, gsum, gtop = sb("gm", [P, T]), sb("gsum", [P, T]), sb("gtop", [P, T])
        gd, ge, gs, goh = (sb(n, [P, T, 4]) for n in ("gd", "ge", "gs", "goh"))
        part = sb("part", [P, T, 4, 8])
        el, el2, sc1 = sb("el", [P, T, 8]), sb("el2", [P, T, 8]), sb("sc1", [P, T, 8])
        oh = [sb(f"oh{n}", [P, T, 8]) for n in range(2)]
        top = [sb(f"top{n}", [P, T]) for n in range(2)]
        first = sb("first", [P, T])
        diff, ediff, den, share = sb("diff", [P, T]), sb("ediff", [P, T]), sb("den", [P, T]), sb("share", [P, T])
        E = [sb(f"E{n}", [P, T, 4, 8]) for n in range(2)]
        both = sb("both", [P, T, N_EXP])
        counts, blocks, ends, starts = sb("counts", [P, N_EXP]), sb("blocks", [P, N_EXP]), sb("ends", [P, N_EXP]), sb("starts", [P, N_EXP])
        place, picked = sb("place", [P, T, N_EXP]), sb("picked", [P, T, N_EXP])
        destf = sb("destf", [P, 2, T])
        past, owner, owner_i = sb("past", [P, N_EXP]), sb("owner", [P, 1]), sb("owner_i", [P, 1], I32)
        H = n_blocks // 2
        evens, begun = sb("evens", [P, H]), sb("begun", [P, H])
        pairs, pairs_i = sb("pairs", [P, 1]), sb("pairs_i", [P, 1], I32)
        p_pos, p_cnt = st.ps("p_pos", [P, T, N_EXP]), st.ps("p_cnt", [P, N_EXP])
        loaded, dve_step, exp_ready, counted = st.sem("loaded"), st.sem("dve_step"), st.sem("exp_ready"), st.sem("counted")
        stored, cleared, table_cleared = st.sem("stored"), st.sem("cleared"), st.sem("table_cleared")
        rank_ready, shifted, differed, placed, owned = (st.sem(n) for n in ("both_ready", "shifted", "differed", "placed", "owned"))
        scattered = S.scattered

        def bc(x, n):
            return x.rearrange("p (t o) -> p t o", o=1).broadcast_to([P, T, n])

        def table_row(x, n):
            return x.rearrange("p (o n) -> p o n", o=1).broadcast_to([P, T, n])

        with st.block() as block:
            @block.sync
            def _(sp):
                for dst, src in ((rank4, a["rank8"][:, 4:8]), (rank8, a["rank8"]), (before, a["before"]), (column, a["column"]),
                                 (tokens, a["token_ids"][:, 0:T]), (evens, a["evens"][:, 0:H])):
                    sp.dma_start(dst[:], src).then_inc(loaded, 16)
                sp.wait_ge(cleared, 1)
                sp.dma_start(table.rearrange("(p b) o -> p (b o)", p=P), zeros[:]).then_inc(table_cleared, 16)
                sp.wait_ge(owned, 1)
                sp.dma_start(experts[0:n_blocks].rearrange("(p o) -> p o", o=1), owner_i[0:n_blocks, :]).then_inc(stored, 16)
                sp.dma_start(experts[n_blocks:n_blocks + 1].rearrange("(p o) -> p o", o=1), pairs_i[0:1, :]).then_inc(stored, 16)
                sp.wait_ge(stored, 32)

            @block.gpsimd
            def _(pool):
                nc.gpsimd.memset(zeros[:], 0).then_inc(cleared, 1)
                pool.wait_ge(placed, 1)
                pool.wait_ge(table_cleared, 16)
                pool.wait_ge(loaded, 96)
                for n in range(2):
                    for t in range(T):
                        pool.indirect_dma_start(table, bass.IndirectOffsetOnAxis(dest[:, n, t:t + 1], 0), tokens[:, t:t + 1], None).then_inc(scattered, 16)
                pool.wait_ge(scattered, 16 * 2 * T)

            @block.scalar
            def _(act):
                act.wait_ge(shifted, 1)
                nc.scalar.activation(ge[:], gd[:], ACT.Exp).then_inc(exp_ready, 1)
                act.wait_ge(differed, 1)
                nc.scalar.activation(ediff[:], diff[:], ACT.Exp).then_inc(exp_ready, 1)

            @block.tensor
            def _(pe):
                pe.wait_ge(loaded, 96)
                pe.wait_ge(rank_ready, 1)
                for t in range(T):
                    for t2 in range(t + 1):
                        nc.tensor.matmul(p_pos[:, t, :], before[:] if t2 == t else S.ones[:], both[:, t2, :], start=(t2 == 0), stop=(t2 == t))
                for t in range(T):
                    mm = nc.tensor.matmul(p_cnt[:], S.ones[:], both[:, t, :], start=(t == 0), stop=(t == T - 1))
                mm.then_inc(counted, 1)

            @block.vector
            def _(dve):
                c = Chain(dve, dve_step)
                V = nc.vector
                dve.wait_ge(loaded, 96)
                gl = logits[:, :, 0:4]
                c.step(V.tensor_reduce(gm[:], gl, AX.X, ALU.max))
                V.tensor_tensor(gd[:], gl, bc(gm[:], 4), ALU.subtract).then_inc(shifted, 1)
                dve.wait_ge(exp_ready, 1)
                c.mark(V.tensor_reduce(gsum[:], ge[:], AX.X, ALU.add))
                c.step(V.tensor_scalar(gs[:], gd[:], 0.0, None, ALU.is_ge))
                c.step(V.tensor_tensor(gs[:], gs[:], table_row(rank4[:], 4), ALU.mult))
                c.step(V.tensor_reduce(gtop[:], gs[:], AX.X, ALU.max))
                c.step(V.tensor_tensor(goh[:], gs[:], bc(gtop[:], 4), ALU.is_equal))
                goh8 = goh[:].rearrange("p t (g o) -> p t g o", o=1).broadcast_to([P, T, 4, 8])
                c.step(V.tensor_tensor(part[:], logits[:, :, 4:36].rearrange("p t (g e) -> p t g e", g=4), goh8, ALU.mult))
                c.step(V.tensor_tensor(el[:], part[:, :, 0, :], part[:, :, 1, :], ALU.add))
                c.step(V.tensor_tensor(el[:], el[:], part[:, :, 2, :], ALU.add))
                c.step(V.tensor_tensor(el[:], el[:], part[:, :, 3, :], ALU.add))
                for n, src in enumerate((el, el2)):
                    if n:
                        c.step(V.scalar_tensor_tensor(out=el2[:], in0=oh[0][:], scalar=-BIG, in1=el[:], op0=ALU.mult, op1=ALU.add))
                    c.step(V.tensor_reduce(top[n][:], src[:], AX.X, ALU.max))
                    c.step(V.tensor_tensor(sc1[:], src[:], bc(top[n][:], 8), ALU.is_equal))
                    c.step(V.tensor_tensor(sc1[:], sc1[:], table_row(rank8[:], 8), ALU.mult))
                    c.step(V.tensor_reduce(first[:], sc1[:], AX.X, ALU.max))
                    c.step(V.tensor_tensor(oh[n][:], sc1[:], bc(first[:], 8), ALU.is_equal))
                    for t in range(T):
                        c.mark(V.tensor_tensor(E[n][:, t], goh[:, t, :].rearrange("p (g o) -> p g o", o=1).broadcast_to([P, 4, 8]),
                                               oh[n][:, t:t + 1, :].broadcast_to([P, 4, 8]), ALU.mult))
                    c.wait()
                V.tensor_tensor(both[:], E[0][:].rearrange("p t g e -> p t (g e)"), E[1][:].rearrange("p t g e -> p t (g e)"), ALU.add).then_inc(rank_ready, 1)
                V.tensor_tensor(diff[:], top[1][:], top[0][:], ALU.subtract).then_inc(differed, 1)
                dve.wait_ge(exp_ready, 2)
                c.step(V.tensor_scalar(den[:], ediff[:], 1.0, None, ALU.add))
                c.step(V.tensor_tensor(den[:], den[:], gsum[:], ALU.mult))
                c.step(V.reciprocal(weight[:, 0, :], den[:]))
                c.mark(V.tensor_tensor(weight[:, 1, :], weight[:, 0, :], ediff[:], ALU.mult))
                dve.wait_ge(counted, 1)
                c.mark(V.tensor_copy(counts[:], p_cnt[:]))
                c.step(V.memset(blocks[:], 0.0))
                for m in range(T):
                    c.step(V.scalar_tensor_tensor(out=blocks[:], in0=counts[:], scalar=float(P * m), in1=blocks[:], op0=ALU.is_gt, op1=ALU.add))
                c.step(V.tensor_tensor_scan(ends[:], S.ones[:, 0:N_EXP], blocks[:], 0.0, ALU.mult, ALU.add))
                c.step(V.tensor_tensor(starts[:], ends[:], blocks[:], ALU.subtract))
                c.step(V.tensor_scalar(starts[:], starts[:], float(P), None, ALU.mult))
                c.step(V.tensor_tensor(place[:], p_pos[:], table_row(starts[:], N_EXP), ALU.add))
                for n in range(2):
                    c.step(V.tensor_tensor(picked[:], place[:], E[n][:].rearrange("p t g e -> p t (g e)"), ALU.mult))
                    c.step(V.tensor_reduce(destf[:, n, :], picked[:], AX.X, ALU.add))
                V.tensor_copy(dest[:], destf[:]).then_inc(placed, 1)
                c.step(V.tensor_scalar(begun[:], evens[:], ends[:, N_EXP - 1:N_EXP], None, ALU.is_lt))
                c.step(V.tensor_reduce(pairs[:], begun[:], AX.X, ALU.add))
                c.step(V.tensor_copy(pairs_i[:], pairs[:]))
                c.step(V.tensor_scalar(past[:], ends[:], column[:, 0:1], None, ALU.is_le))
                c.step(V.tensor_reduce(owner[:], past[:], AX.X, ALU.add))
                c.step(V.tensor_scalar(owner[:], owner[:], float(N_EXP - 1), None, ALU.min))
                V.tensor_copy(owner_i[:], owner[:]).then_inc(owned, 1)
                dve.wait_ge(placed, 1)


def experts_run(nc, name, S, n_blocks, table, experts, h, w_gu, w_d, y):
    KH = HID // P
    with Stage(nc, name) as st:
        erow = st.sb("experts", [1, n_blocks + 1], I32)
        rows = [st.sb(f"rows{u}", [P, 1], I32) for u in range(2)]
        xg = [st.sb(f"xg{u}", [P, D]) for u in range(2)]
        xT = [st.sb(f"xT{u}", [P, KD, P]) for u in range(2)]
        wgu = [st.sb(f"wgu{u}", [P, 2, KD, HID]) for u in range(2)]
        wd = [st.sb(f"wd{u}", [P, KH, D]) for u in range(2)]
        sg, act_in = st.sb("gate", [P, HID]), st.sb("gated", [P, HID])
        aT = st.sb("gatedT", [P, KH, P])
        yo = [st.sb(f"y{u}", [P, D]) for u in range(2)]
        p_x = [st.ps(f"p_x{n}", [P, 4, P]) for n in range(2)]
        p_g, p_u, p_a = st.ps("p_g", [P, HID]), st.ps("p_u", [P, HID]), st.ps("p_a", [P, KH, P])
        p_y = [st.ps(f"p_y{n}", [P, BANK]) for n in range(2)]
        experts_loaded = st.sem("experts_loaded")
        rows_loaded = [st.sem(f"rows_loaded{u}") for u in range(2)]
        gathered = S.gathered
        gu_loaded, d_loaded = [st.sem(f"gu_loaded{u}") for u in range(2)], [st.sem(f"d_loaded{u}") for u in range(2)]
        x_turned, x_copied = st.sem("x_turned"), [st.sem("x_copied0"), st.sem("x_copied1")]
        gate_ready, up_ready, silu_ready, gated = st.sem("gate_ready"), st.sem("up_ready"), st.sem("silu_ready"), st.sem("gated")
        a_turned, a_copied, y_ready = st.sem("a_turned"), st.sem("a_copied"), st.sem("y_ready")
        y_copied = [st.sem("y_copied0"), st.sem("y_copied1")]
        stored = [st.sem(f"stored{u}") for u in range(2)]
        gather_free, tail_free, zeroed = st.sem("gather_free"), st.sem("tail_free"), st.sem("zeroed")
        zeros = st.sb("zeros", [P, D])
        H = n_blocks // 2

        def pairs_in_use(eng):
            eng.wait_ge(experts_loaded, 16)
            return eng.value_load(erow[0:1, n_blocks:n_blocks + 1], min_val=1, max_val=H)

        with st.block() as block:
            @block.sync
            def _(sp):
                sp.dma_start(erow[:], experts[0:n_blocks + 1].rearrange("(o b) -> o b", o=1)).then_inc(experts_loaded, 16)
                pairs = pairs_in_use(sp)

                def load_rows(b, u):
                    sp.dma_start(rows[u][:], table[bass.ds(b * P, P), :]).then_inc(rows_loaded[u], 16)

                def expert(b):
                    return sp.value_load(erow[0:1, bass.ds(b, 1)], min_val=0, max_val=N_EXP - 1)

                def load_gu(e, u):
                    sp.dma_start(wgu[u][:], w_gu[bass.ds(e, 1)].rearrange("a p g k f -> (a p) g k f")).then_inc(gu_loaded[u], 16)

                def load_d(e, u):
                    sp.dma_start(wd[u][:], w_d[bass.ds(e, 1)].rearrange("a p k f -> (a p) k f")).then_inc(d_loaded[u], 16)

                def store(b, u, done):
                    sp.wait_ge(y_copied[0], done)
                    sp.wait_ge(y_copied[1], done)
                    sp.dma_start(y[bass.ds(b * P, P), :], yo[u][:]).then_inc(stored[u], 16)

                load_rows(0, 0)
                load_rows(1, 1)
                for u in range(2):
                    e = expert(u)
                    load_gu(e, u)
                    load_d(e, u)
                sp.wait_ge(zeroed, 1)
                with sp.Fori(0, H - 1) as i:
                    with sp.If(i + 1 < pairs):
                        for u in range(2):
                            b = 2 * i + u
                            sp.wait_ge(gathered[u], 16 * i + 16)
                            load_rows(b + 2, u)
                            e = expert(b + 2)
                            sp.wait_ge(gated, b + 2)
                            load_gu(e, u)
                            store(b, u, b + 2)
                            sp.wait_ge(stored[u], 16 * i + 16)
                            load_d(e, u)
                    with sp.Else():
                        for u in range(2):
                            sp.dma_start(y[bass.ds((2 * i + 2 + u) * P, P), :], zeros[:]).then_inc(stored[u], 16)
                sp.wait_ge(gathered[0], 16 * pairs)
                sp.sem_inc(tail_free, 1)
                load_rows(2 * pairs, 0)
                for u in range(2):
                    store(2 * pairs - 2 + u, u, 2 * pairs + u)
                sp.wait_ge(rows_loaded[0], 16 * pairs + 16)
                sp.sem_inc(tail_free, 1)
                for u in range(2):
                    sp.wait_ge(stored[u], 16 * H)

            @block.gpsimd
            def _(pool):
                def gather(u):
                    pool.indirect_dma_start(xg[u][:], None, h, bass.IndirectOffsetOnAxis(rows[u][:, 0:1], 0)).then_inc(gathered[u], 16)

                nc.gpsimd.memset(zeros[:], 0.0).then_inc(zeroed, 1)
                for u in range(2):
                    pool.wait_ge(rows_loaded[u], 16)
                    gather(u)
                pairs = pairs_in_use(pool)
                with pool.Fori(0, H - 1) as i:
                    with pool.If(i + 1 < pairs):
                        for u in range(2):
                            pool.wait_ge(rows_loaded[u], 16 * i + 32)
                            pool.wait_ge(x_turned, 4 * i + 2 * u + 2)
                            pool.sem_inc(gather_free, 1)
                            gather(u)
                pool.wait_ge(rows_loaded[0], 16 * pairs + 16)
                pool.wait_ge(x_turned, 4 * pairs)
                pool.sem_inc(gather_free, 1)
                gather(0)
                pool.wait_ge(gathered[0], 16 * pairs + 16)

            @block.tensor
            def _(pe):
                def turn(b, u, i, first=False):
                    pe.wait_ge(gathered[u], 16 * i + 16)
                    for n in range(2):
                        if not first:
                            pe.wait_ge(x_copied[n], b)
                        for q in range(4):
                            d = 4 * n + q
                            mm = nc.tensor.transpose(p_x[n][:, q, :], xg[u][:, d * P:(d + 1) * P], S.ident[:, :])
                        mm.then_inc(x_turned, 1)

                pairs = pairs_in_use(pe)
                turn(0, 0, 0, True)
                pe.sem_inc(a_turned, 1)
                with pe.Fori(0, H) as i:
                    with pe.If(i < pairs):
                        for u in range(2):
                            b = 2 * i + u
                            pe.wait_ge(x_copied[0], b + 1)
                            pe.wait_ge(x_copied[1], b + 1)
                            pe.wait_ge(gu_loaded[u], 16 * i + 16)
                            pe.wait_ge(gated, b + 1)
                            for g, (p, ready) in enumerate(((p_g, gate_ready), (p_u, up_ready))):
                                for k in range(KD):
                                    mm = nc.tensor.matmul(p[:], xT[u][:, k, :], wgu[u][:, g, k, :], start=(k == 0), stop=(k == KD - 1))
                                mm.then_inc(ready, 1)
                            turn(b + 1, 1 - u, i + u)
                            pe.wait_ge(gated, b + 2)
                            pe.wait_ge(a_copied, b + 1)
                            for k in range(KH):
                                mm = nc.tensor.transpose(p_a[:, k, :], act_in[:, k * P:(k + 1) * P], S.ident[:, :])
                            mm.then_inc(a_turned, 1)
                            pe.wait_ge(a_copied, b + 2)
                            pe.wait_ge(d_loaded[u], 16 * i + 16)
                            for n in range(2):
                                pe.wait_ge(y_copied[n], b + 1)
                                for k in range(KH):
                                    mm = nc.tensor.matmul(p_y[n][:], aT[:, k, :], wd[u][:, k, n * BANK:(n + 1) * BANK], start=(k == 0), stop=(k == KH - 1))
                                mm.then_inc(y_ready, 1)

            @block.scalar
            def _(act):
                pairs = pairs_in_use(act)
                act.sem_inc(a_copied, 1)
                act.sem_inc(y_copied[0], 1)

                def copy_x(b, u):
                    act.wait_ge(x_turned, 2 * b + 1)
                    nc.scalar.activation(xT[u][:, 0:4, :], p_x[0][:], ACT.Copy).then_inc(x_copied[0], 1)

                copy_x(0, 0)
                with act.Fori(0, H) as i:
                    with act.If(i < pairs):
                        for u in range(2):
                            b = 2 * i + u
                            act.wait_ge(gate_ready, b + 1)
                            act.wait_ge(gated, b + 1)
                            nc.scalar.activation(sg[:], p_g[:], ACT.Silu).then_inc(silu_ready, 1)
                            copy_x(b + 1, 1 - u)
                            act.wait_ge(a_turned, b + 2)
                            nc.scalar.activation(aT[:], p_a[:], ACT.Copy).then_inc(a_copied, 1)
                            act.wait_ge(y_ready, 2 * b + 1)
                            nc.scalar.activation(yo[u][:, 0:BANK], p_y[0][:], ACT.Copy).then_inc(y_copied[0], 1)

            @block.vector
            def _(dve):
                pairs = pairs_in_use(dve)
                dve.sem_inc(gated, 1)
                dve.sem_inc(y_copied[1], 1)

                def copy_x(b, u):
                    dve.wait_ge(x_turned, 2 * b + 2)
                    nc.vector.tensor_copy(xT[u][:, 4:8, :], p_x[1][:]).then_inc(x_copied[1], 1)

                copy_x(0, 0)
                with dve.Fori(0, H) as i:
                    with dve.If(i < pairs):
                        for u in range(2):
                            b = 2 * i + u
                            dve.wait_ge(silu_ready, b + 1)
                            dve.wait_ge(up_ready, b + 1)
                            dve.wait_ge(a_turned, b + 1)
                            nc.vector.tensor_tensor(act_in[:], sg[:], p_u[:], ALU.mult).then_inc(gated, 1)
                            copy_x(b + 1, 1 - u)
                            dve.wait_ge(y_ready, 2 * b + 2)
                            nc.vector.tensor_copy(yo[u][:, BANK:D], p_y[1][:]).then_inc(y_copied[1], 1)


def combine(nc, name, S, x_tiles, T0, dest, weight, y, gate_row):
    T = len(x_tiles)
    with Stage(nc, name) as st:
        row = st.sb("gate", [P, D])
        ya = [[st.sb(f"y{n}{u}", [P, D]) for u in range(2)] for n in range(2)]
        loaded, dve_step = st.sem("loaded"), st.sem("dve_step")
        fetched = S.fetched
        with st.block() as block:
            @block.sync
            def _(sp):
                sp.dma_start(row[:], gate_row.partition_broadcast(P)).then_inc(loaded, 16)

            @block.gpsimd
            def _(pool):
                for t in range(T):
                    if t >= 2:
                        pool.wait_ge(dve_step, 4 * (t - 1))
                    for n in range(2):
                        pool.indirect_dma_start(ya[n][t % 2][:], None, y, bass.IndirectOffsetOnAxis(dest[:, n, T0 + t:T0 + t + 1], 0)).then_inc(fetched[t % 2], 16)
                for u in range(min(2, T)):
                    pool.wait_ge(fetched[u], 32 * ((T - u + 1) // 2))

            @block.vector
            def _(dve):
                steps = Chain(dve, dve_step)
                dve.wait_ge(loaded, 16)
                for t in range(T):
                    dve.wait_ge(fetched[t % 2], 32 * (t // 2 + 1))
                    y0, y1 = ya[0][t % 2][:], ya[1][t % 2][:]
                    steps.step(nc.vector.tensor_scalar(y0, y0, weight[:, 0, T0 + t:T0 + t + 1], None, ALU.mult))
                    steps.step(nc.vector.scalar_tensor_tensor(out=y0, in0=y1, scalar=weight[:, 1, T0 + t:T0 + t + 1], in1=y0, op0=ALU.mult, op1=ALU.add))
                    steps.step(nc.vector.tensor_tensor(y0, y0, row[:], ALU.mult))
                    steps.step(nc.vector.tensor_tensor(x_tiles[t], x_tiles[t], y0, ALU.add))


def route_tables():
    i = np.arange(P)
    return {"rank8": np.tile(np.arange(8, 0, -1, dtype=np.float32), (P, 1)),
            "before": (i[:, None] < i[None, :]).astype(np.float32),
            "column": i[:, None].astype(np.float32), "evens": np.tile(np.arange(0, max(N_BLOCKS), 2, dtype=np.float32), (P, 1)),
            "token_ids": (np.arange(NA)[None, :] * P + i[:, None]).astype(np.int32)}


SECOND_COLS = (("norm1_g_2", 2 * KD), ("ga_b_in_2_u", W_GMLP // P))
N_BLOCKS = (44, 40)


def moe(nc, name, S, a, layer, streams, hT, mods):
    tiles = [(t, w) for ts, w in streams for t in ts]
    T = len(tiles)
    nb = N_BLOCKS[layer]
    assert nb % 2 == 0 and nb >= (2 * T * P + N_EXP * (P - 1)) // P
    h = dram(nc, name + "_h", [T * P, D])
    table, experts = dram(nc, name + "_table", [(nb + 1) * P, 1], I32), dram(nc, name + "_experts", [P], I32)
    y = dram(nc, name + "_y", [nb * P, D])
    with ExitStack() as mem:
        def sb(n, shape, dt=F32):
            return mem.enter_context(nc.sbuf_tensor(f"{name}_{n}", shape, dt))
        dest, weight = sb("dest", [P, 2, T], I32), sb("weight", [P, 2, T])
        with ExitStack() as mem2:
            rows = [[mem2.enter_context(nc.sbuf_tensor(f"{name}_row{w}{n}", [P, D], F32)) for n in range(2)] for w in range(len(streams))]
            modulation_rows(nc, name + "m", mods, a["norm2_g_2"][layer], [(r[0][:], r[1][:]) for r in rows])
            norm_transpose(nc, name + "n", S, [t for t, _ in tiles], hT, rows=[(rows[w][0][:], rows[w][1][:]) for _, w in tiles], h_dram=h)
            logits = mem2.enter_context(nc.sbuf_tensor(f"{name}_logits", [P, T, 36], F32))
            brow = mem2.enter_context(nc.sbuf_tensor(f"{name}_brow", [1, 36], F32))
            load_all(nc, name + "b", [(brow[:], a["moe_b_2"][layer].rearrange("(o c) -> o c", o=1))])
            project(nc, name + "g", hT, T * P, [dict(w=a["moe_w_route_2"][layer], mode="T", bias=brow[:], epi=copy_to(lambda j, n0: logits[:, j, :]))],
                    const={"ones": S.ones})
            S.scattered = S.pool_sems[layer][0]
            route(nc, name + "r", S, logits, T, nb, a, dest, weight, table, experts)
        S.gathered = S.pool_sems[layer][1:3]
        experts_run(nc, name + "e", S, nb, table, experts, h, a["moe_w_gu_2"][layer], a["moe_w_down_2"][layer], y)
        at = 0
        for n, (ts, w) in enumerate(streams):
            S.fetched = S.pool_sems[layer][3 + 2 * n:5 + 2 * n]
            combine(nc, f"{name}c{n}", S, ts, at, dest, weight, y, mods[w, 5 * D:6 * D])
            at += len(ts)


def gmlp(nc, S, a, x_tiles, c_tiles, hT, mods):
    with ExitStack() as mem:
        def sb(n, shape):
            return mem.enter_context(nc.sbuf_tensor("gm_" + n, shape, F32))
        uT = sb("uT", [P, GROUPS, ALL])
        bias_u = S.second_cols[:, 2 * KD:2 * KD + W_GMLP // P]
        with ExitStack() as mem2:
            v = mem2.enter_context(nc.sbuf_tensor("gm_v", [P, NA, W_GMLP], F32))
            brow = mem2.enter_context(nc.sbuf_tensor("gm_brow", [1, W_GMLP], F32))
            load_all(nc, "gmb", [(brow[:], a["ga_b_in_2_v"].rearrange("(o c) -> o c", o=1))])

            def epi_u(c):
                def epi(which, engine, chain, j, n0, ps):
                    f = 4 * c + j
                    return engine.activation(uT[:, f, n0:n0 + ps.shape[1]], ps, ACT.Gelu, bias=bias_u[:, f:f + 1])
                return epi

            def epi_v(c):
                def epi(which, engine, chain, j, n0, ps):
                    return engine.activation(v[:, j, c * BANK:(c + 1) * BANK], ps, ACT.Gelu)
                return epi

            w = a["ga_w_in_2"]
            jobs = [dict(w=w[:, c * BANK:(c + 1) * BANK], mode="F", eng="act", epi=epi_u(c)) for c in range(4)]
            jobs += [dict(w=w[:, W_GMLP + c * BANK:W_GMLP + (c + 1) * BANK], mode="T", eng="act", bias=brow[0:1, c * BANK:(c + 1) * BANK], epi=epi_v(c)) for c in range(4)]
            project(nc, "gmi", hT, ALL, jobs, const={"ones": S.ones})
            spatial_gate(nc, "gms", S, uT, v, (a["ga_ln_g_2"], a["ga_ln_b_2"]), a["ga_w_sT_2"], a["ga_b_s_2"])
        brow = sb("brow_out", [1, D])
        gates = [sb(f"gate{w}", [P, D]) for w in range(2)]
        W = 256
        tmp = sb("tmp", [P, 2, W])
        load_all(nc, "gmc", [(brow[:], a["ga_b_out_2"].rearrange("(o c) -> o c", o=1))] +
                 [(gates[w][:], mods[w, 2 * D:3 * D].partition_broadcast(P)) for w in range(2)])
        tiles = x_tiles + c_tiles
        jobs = []
        for c in range(D // W):
            s = slice(c * W, (c + 1) * W)
            jobs.append(dict(w=a["ga_w_out_2"][:, s], mode="T", eng="dve", bias=brow[0:1, s],
                             epi=gated_residual(lambda j, s=s: tiles[j][:, s], lambda j, s=s: gates[j >= NT][:, s], tmp)))
        project(nc, "gmo", uT, ALL, jobs, const={"ones": S.ones})


def second_block_a(nc, S, a, x_tiles, c_tiles, hT, mods):
    for layer in range(2):
        modulation(nc, f"ad{layer}", S, a["cT_2"], a["ada_w_2"][layer], a["ada_b_2"][layer], mods[layer])
    cols = S.mod_cols
    modulation_columns(nc, "mc0", S, mods[0], S.second_cols[:, 0:KD], cols)
    norm_transpose(nc, "sn0", S, x_tiles + c_tiles, hT, cols=[cols[0]] * NT + [cols[1]] * (NA - NT))
    gmlp(nc, S, a, x_tiles, c_tiles, hT, mods[0])
    moe(nc, "moe0", S, a, 0, ((x_tiles, 0), (c_tiles, 1)), hT, mods[0])


def second_layout(inp):
    g = lambda n: np.asarray(inp[n])
    out = {n: np.ascontiguousarray(g(n)[0]) for n in ("ga_w_in_2", "ga_ln_g_2", "ga_ln_b_2", "ga_w_out_2", "ga_b_out_2")}
    for n in ("ada_w_2", "ada_b_2", "norm2_g_2"):
        out[n] = np.ascontiguousarray(g(n))
    out["ctx_2"] = np.ascontiguousarray(g("ctx_2")[0])
    out["cT_2"] = np.ascontiguousarray(np.stack([columns(g("c_2")[0]), columns(g("c_ctx_2"))], 2))
    out["ga_w_sT_2"] = np.ascontiguousarray(g("ga_w_s_2")[0].transpose(2, 0, 1))
    out["ga_b_s_2"] = np.ascontiguousarray(g("ga_b_s_2")[0][None])
    out["ga_b_in_2_v"] = np.ascontiguousarray(g("ga_b_in_2")[0, W_GMLP:])
    out["moe_w_route_2"] = np.ascontiguousarray(np.concatenate([g("moe_w_grp_2"), g("moe_w_exp_2")], 2))
    out["moe_b_2"] = np.ascontiguousarray(np.concatenate([g("moe_b_grp_2"), g("moe_b_exp_2")], 1))
    gu = np.stack([g("moe_w_gate_2"), g("moe_w_up_2")], 2)
    out["moe_w_gu_2"] = np.ascontiguousarray(gu.reshape(2, N_EXP, 2, KD, P, HID).transpose(0, 1, 4, 2, 3, 5))
    out["moe_w_down_2"] = np.ascontiguousarray(g("moe_w_down_2").reshape(2, N_EXP, HID // P, P, D).transpose(0, 1, 3, 2, 4))
    out["second_cols"] = np.concatenate([columns(g("norm1_g_2")), columns(g("ga_b_in_2")[0, :W_GMLP])], 1)
    return out


HEADS, HK = 16, 64
CH = 64
STEPS = ALL // CH
CSTEPS = CTX // CH
GRID = 64
LEVELS = 5
LOG_DECAY = -math.exp(-0.5)


def token_shift(nc, name, hT, xx):
    rows = SEQ // GRID
    with Stage(nc, name) as st:
        dve_step = st.sem("dve_step")
        with st.block() as block:
            @block.vector
            def _(dve):
                steps = Chain(dve, dve_step)

                def sub(dst, shifted, here):
                    steps.mark(nc.vector.tensor_tensor(dst, shifted, here, ALU.subtract))

                def edge(dst, here):
                    steps.mark(nc.vector.tensor_scalar(dst, here, -1.0, None, ALU.mult))

                C = CTX
                b, f = slice(0, 4), slice(4, 8)
                sub(xx[:, b, 1:C], hT[:, b, 0:C - 1], hT[:, b, 1:C])
                edge(xx[:, b, 0:1], hT[:, b, 0:1])
                sub(xx[:, f, 0:C - 1], hT[:, f, 1:C], hT[:, f, 0:C - 1])
                edge(xx[:, f, C - 1:C], hT[:, f, C - 1:C])
                for k in range(0, 2):
                    g, o = (t[:, k, C:].rearrange("p (r c) -> p r c", c=GRID) for t in (hT, xx))
                    sub(o[:, :, 1:], g[:, :, :GRID - 1], g[:, :, 1:])
                    edge(o[:, :, 0:1], g[:, :, 0:1])
                for k in range(2, 4):
                    g, o = (t[:, k, C:].rearrange("p (r c) -> p r c", c=GRID) for t in (hT, xx))
                    sub(o[:, :, :GRID - 1], g[:, :, 1:], g[:, :, :GRID - 1])
                    edge(o[:, :, GRID - 1:], g[:, :, GRID - 1:])
                u, d = slice(4, 6), slice(6, 8)
                sub(xx[:, u, C + GRID:], hT[:, u, C:ALL - GRID], hT[:, u, C + GRID:])
                edge(xx[:, u, C:C + GRID], hT[:, u, C:C + GRID])
                sub(xx[:, d, C:ALL - GRID], hT[:, d, C + GRID:], hT[:, d, C:ALL - GRID])
                edge(xx[:, d, ALL - GRID:], hT[:, d, ALL - GRID:])
                steps.wait()


def backward(x):
    return x.rearrange("p (c t) -> p c t", t=CH)[:, ::-1, :]


def chunked(x):
    return x.rearrange("p (c t) -> p c t", t=CH)


def rwkv_scan(nc, name, S, a, kF, rF, sgF, aF, vS, yS, bS):
    NG = STEPS // 4
    NZ = LEVELS * NG
    lat = SEQ // CH
    assert CSTEPS == 4 and HEADS % 2 == 0
    WALK_PAIRS = [(2 * g, 2 * g + 1) for g in range(NG)]
    WALK_GROWTH = {n: 2 * NG + n for n in range(STEPS - 2 * NG)}
    SLOTS = 14
    assert len(WALK_GROWTH) <= 8 and SLOTS < NZ
    with Stage(nc, name) as st:
        sb = st.sb
        masks = sb("masks", [P, 4, P])
        join = sb("join", [P, LEVELS + 1, P])
        join0 = sb("join0", [P, P])
        keep = sb("keep", [P, ALL])
        halves = sb("halves", [P, P])
        cols = sb("cols", [P, 4])
        k2, sg, aa = (sb(n, [P, ALL]) for n in ("k", "sg", "a"))
        r2 = sb("r", [P, SEQ])
        vs = [sb(f"v{u}", [P, STEPS, HK]) for u in range(2)]
        lw, L, G, G2, sq, kk, km, t1, e_neg = (sb(n, [P, ALL]) for n in ("lw", "L", "G", "G2", "sq", "kk", "km", "t1", "e_neg"))
        e_exc, e_inc, nrm = lw, L, sq
        em = sb("em", [P, STEPS])
        ee = [sb(f"ee{u}", [P, STEPS]) for u in range(2)]
        oneminus = sb("oneminus", [P, 1])
        at_ctx = [sb(f"at_ctx{u}", [P, CSTEPS, P]) for u in range(2)]
        at_rt = [sb(f"at_rt{u}", [P, lat, 2, P]) for u in range(2)]
        bh, kh = sb("bh", [P, STEPS, P]), sb("kh", [P, STEPS, P])
        pairs_ctx = [sb(f"pairs_ctx{u}", [P, CSTEPS, 2, P]) for u in range(2)]
        pairs_lat = [sb(f"pairs_lat{u}", [P, lat, 4, P]) for u in range(2)]
        bT, kT = ([sb(f"{n}{u}", [P, STEPS, P]) for u in range(2)] for n in ("bT", "kT"))
        T = sb("T", [P, STEPS, P])
        R = [sb(f"R{u}", [P, STEPS, P]) for u in range(2)]
        off = [sb(f"off{n}", [P, 4, P]) for n in range(2)]
        Z = [sb(f"Z{n}", [P, 4, P]) for n in range(2)]
        Sm, X, SA = sb("Sm", [P, HK]), sb("X", [P, HK]), sb("SA", [P, HK])
        yo, yb = sb("y", [P, lat, HK]), sb("yb", [P, lat, HK])
        bon = sb("bonus", [P, lat])
        rk = sb("rk", [P, lat, P])
        bank = [st.ps(f"bank{n}", [P, BANK]) for n in range(8)]
        pair_bank, pn_bank, tr_bank, bon_bank = bank[0:2], bank[2], bank[3:5], bank[4]
        z_bank, tz_bank, zr_bank, ss_bank = bank[0:2], bank[2], bank[3], bank[4]
        x_psum, sa_psum, ds_psum, y_psum = bank[5][:, 0:HK], bank[5][:, HK:2 * HK], bank[6][:, 0:HK], bank[7][:, 0:HK]
        names = ("lw_ready sq_ready g_ready ss_ready nrm_ready exp_ready cleared bd_ready pb_ready pb_masked pn_ready pn_masked tr_ready tr_copied "
                 "off_ready z_ready z_copied tz_ready tz_added zr_ready zr_added x_ready x_copied sa_ready sa_copied ds_ready sm_ready "
                 "y_ready y_copied bon_ready bon_read bonus_done dve_step factor_step const_loaded y_free bonus_free loaded stored_y stored_bonus").split()
        s = {n: st.sem(n) for n in names}
        v_loaded = [st.sem(f"v_loaded{u}") for u in range(2)]
        LOADS = 9
        lo, hi = slice(0, HK), slice(HK, P)

        def at(u, j):
            return at_ctx[u][:, j, :] if j < CSTEPS else at_rt[u][:, j - CSTEPS, 0, :]

        def pair(u, j, kind):
            return pairs_ctx[u][:, j, kind // 2, :] if j < CSTEPS else pairs_lat[u][:, j - CSTEPS, kind, :]

        def pairs_of_group(u, g):
            return pairs_ctx[u][:, :, 0, :] if g == 0 else pairs_lat[u][:, 4 * g - 4:4 * g, 0, :]

        def cs(x):
            return x[:].rearrange("p (c t) -> p c t", t=CH)

        def quad(x):
            return x.rearrange("p (c t) -> p c t", c=4)

        def over4(m):
            return m.rearrange("p (o t) -> p o t", o=1).broadcast_to([P, 4, P])

        def every_head(eng, factors, body):
            last = HEADS - 1
            factors(0)
            body(0, 0, 0, None, 1)
            with eng.Fori(0, HEADS // 2 - 1) as i:
                body(2 * i + 1, 1, i, (2 * i, 0, i), 2 * i + 2)
                body(2 * i + 2, 0, i + 1, (2 * i + 1, 1, i), 2 * i + 3)
            body(last, 1, last // 2, (last - 1, 0, last // 2), None)

        LAST = (HEADS - 1, 1, (HEADS - 1) // 2)

        with st.block() as block:
            @block.sync
            def _(sp):
                for dst, src in ((masks, "rw_masks"), (join, "rw_join"), (join0, "rw_join0"), (keep, "rw_keep"), (halves, "rw_halves")):
                    sp.dma_start(dst[:], a[src]).then_inc(s["const_loaded"], 16)

                def load(h):
                    hs = bass.ds(h * HK, HK)
                    for z, rows in ((0, lo), (1, hi)):
                        for dst, src in ((k2, kF), (r2, rF), (sg, sgF), (aa, aF)):
                            sp.dma_start(dst[rows, :], src[z][hs, :]).then_inc(s["loaded"], 16)
                    sp.dma_start(cols[:], a["rw_cols"][bass.ds(h, 1)].rearrange("a p c -> (a p) c")).then_inc(s["loaded"], 16)

                def load_v(h, u):
                    for z, rows in ((0, lo), (1, hi)):
                        sp.dma_start(vs[u][rows, :, :], vS[z].rearrange("s t c -> t s c")[:, :, bass.ds(h * HK, HK)]).then_inc(v_loaded[u], 16)

                def store(d, src, h, sem):
                    for z, rows in ((0, lo), (1, hi)):
                        sp.dma_start(d[z].rearrange("(c t) n -> t c n", t=CH)[:, :, bass.ds(h * HK, HK)], src[rows, :, :]).then_inc(sem, 16)

                def store_walk(walk):
                    sp.wait_ge(s["y_copied"], walk[0] * lat + lat)
                    store(yS, yo, walk[0], s["stored_y"])

                def factors(h):
                    load(h)
                    load_v(h, 0)
                    load_v(h + 1, 1)
                    sp.sem_inc(s["y_free"], 1)
                    sp.sem_inc(s["bonus_free"], 1)

                def body(h, u, k, walk, ahead):
                    if ahead is not None:
                        sp.wait_ge(s["bd_ready"], h + 1)
                        load(ahead)
                    sp.wait_ge(s["bonus_done"], h + 1)
                    store(bS, yb, h, s["stored_bonus"])
                    if walk:
                        store_walk(walk)
                        if ahead is not None:
                            load_v(ahead, walk[1])
                    sp.wait_ge(s["stored_bonus"], h * 32 + 32)
                    sp.sem_inc(s["bonus_free"], 1)
                    if walk:
                        sp.wait_ge(s["stored_y"], walk[0] * 32 + 32)
                        sp.sem_inc(s["y_free"], 1)

                every_head(sp, factors, body)
                store_walk(LAST)
                sp.wait_ge(s["stored_y"], HEADS * 32)

            @block.gpsimd
            def _(pool):
                for x in (*at_ctx, *at_rt, bh, kh, rk):
                    nc.gpsimd.memset(x[:], 0.0).then_inc(s["cleared"], 1)
                pool.wait_ge(s["const_loaded"], 80)
                with pool.Fori(0, HEADS // 2) as i:
                    for u in range(2):
                        h = 2 * i + u
                        for n in range(NZ):
                            l, g = n // NG, n % NG
                            pool.wait_ge(s["pb_masked"], h * STEPS + 4 * g + 4)
                            if n >= 2:
                                pool.wait_ge(s["z_ready"], h * NZ + n - 1)
                            nc.gpsimd.tensor_tensor(off[n % 2][:], pairs_of_group(u, g), over4(join[:, l + 1, :]), ALU.mult).then_inc(s["off_ready"], 1)

            @block.scalar
            def _(act):
                A = nc.scalar.activation

                def walk_x(walk, j):
                    act.wait_ge(s["x_ready"], walk[0] * STEPS + j + 1)
                    A(X[:], x_psum, ACT.Copy).then_inc(s["x_copied"], 1)

                def walk_sa(walk, j):
                    act.wait_ge(s["sa_ready"], walk[0] * STEPS + j + 1)
                    A(SA[:], sa_psum, ACT.Copy).then_inc(s["sa_copied"], 1)

                def norm(h, n, c0, c1):
                    act.wait_ge(s["ss_ready"], 2 * h + n + 1)
                    A(nrm[:, c0:c1], ss_bank[:, 0:c1 - c0], ACT.Sqrt, bias=S.eps[:, 3:4]).then_inc(s["nrm_ready"], 1)

                def exps(*of):
                    for dst, rows, src, sign in of:
                        A(dst[rows, :], src[rows, :], ACT.Exp, scale=sign).then_inc(s["exp_ready"], 1)

                def factor_part(h, slot):
                    if slot == 0:
                        act.wait_ge(s["loaded"], h * 16 * LOADS + 16 * LOADS)
                        A(lw[:], sg[:], ACT.Copy, scale=LOG_DECAY).then_inc(s["lw_ready"], 1)
                        A(sq[:], k2[:], ACT.Square, scale=cols[:, 0:1]).then_inc(s["sq_ready"], 1)
                    if slot == 2:
                        norm(h, 0, 0, BANK)
                    if slot == 3:
                        act.wait_ge(s["g_ready"], h + 1)
                        A(em[:], cs(L)[:, :, CH - 1], ACT.Exp, scale=0.5).then_inc(s["exp_ready"], 1)
                        exps((e_exc, lo, G2, 1.0), (e_exc, hi, G, -1.0))
                    if slot == 4:
                        norm(h, 1, BANK, ALL)
                        exps((e_neg, lo, G, -1.0), (e_neg, hi, G2, 1.0))
                    if slot == 5:
                        act.wait_ge(s["exp_ready"], 7 * h + 1)
                        exps((e_inc, lo, G, 1.0), (e_inc, hi, G2, -1.0))

                def factors(h):
                    for slot in range(SLOTS):
                        factor_part(h, slot)

                def body(h, u, k, walk, ahead):
                    for g in range(NG):
                        if walk:
                            j0, j1 = WALK_PAIRS[g]
                            walk_x(walk, j0)
                            walk_sa(walk, j0)
                        for n, dst in enumerate((bT[u], kT[u])):
                            if walk:
                                (walk_x, walk_sa)[n](walk, j1)
                            act.wait_ge(s["tr_ready"], h * 2 * NG + 2 * g + n + 1)
                            A(dst[:, 4 * g:4 * g + 4, :], quad(tr_bank[n][:]), ACT.Copy).then_inc(s["tr_copied"], 1)

                    def copy_z(n):
                        act.wait_ge(s["z_ready"], h * NZ + n + 1)
                        if n >= 2:
                            act.wait_ge(s["zr_ready"], h * NZ + n - 1)
                        A(Z[n % 2][:], quad(z_bank[n % 2][:]), ACT.Copy).then_inc(s["z_copied"], 1)

                    copy_z(0)
                    for n in range(NZ):
                        if walk and n in WALK_GROWTH:
                            walk_x(walk, WALK_GROWTH[n])
                            walk_sa(walk, WALK_GROWTH[n])
                        if n + 1 < NZ:
                            copy_z(n + 1)
                        if ahead is not None and n < SLOTS:
                            factor_part(ahead, n)

                every_head(act, factors, body)
                for j in range(STEPS):
                    walk_x(LAST, j)
                    walk_sa(LAST, j)

            @block.vector
            def _(dve):
                dve.wait_ge(s["const_loaded"], 80)
                dve.wait_ge(s["cleared"], 7)
                V = nc.vector

                def walk_begin(walk):
                    dve.wait_ge(s["y_free"], walk[0] + 1)
                    V.memset(Sm[:], 0.0).then_inc(s["sm_ready"], 1)

                def walk_step(walk, j):
                    w, wu, _ = walk
                    if j < STEPS - 1:
                        dve.wait_ge(s["ds_ready"], w * (STEPS - 1) + j + 1)
                        V.tensor_scalar(Sm[:], ds_psum, ee[wu][:, j:j + 1], None, ALU.mult).then_inc(s["sm_ready"], 1)
                    if j >= CSTEPS:
                        n = j - CSTEPS
                        dve.wait_ge(s["y_ready"], w * lat + n + 1)
                        V.tensor_copy(yo[lo, n, :], y_psum[lo])
                        V.tensor_copy(yo[hi, lat - 1 - n, :], y_psum[hi]).then_inc(s["y_copied"], 1)

                def factor_part(c, h, u, slot):
                    if slot == 0:
                        dve.wait_ge(s["loaded"], h * 16 * LOADS + 16 * LOADS)
                    if slot == 1:
                        dve.wait_ge(s["lw_ready"], h + 1)
                        c.step(V.tensor_tensor_scan(L[:], keep[:], lw[:], 0.0, ALU.mult, ALU.add))
                    if slot == 2:
                        c.step(V.scalar_tensor_tensor(out=cs(G), in0=cs(L)[:, :, CH - 1:CH].broadcast_to([P, STEPS, CH]), scalar=-0.5, in1=cs(L), op0=ALU.mult, op1=ALU.add))
                        V.tensor_tensor(G2[:], G[:], lw[:], ALU.subtract).then_inc(s["g_ready"], 1)
                    if slot == 3:
                        c.step(V.tensor_scalar(oneminus[:], cols[:, 1:2], -1.0, 1.0, ALU.mult, ALU.add))
                        c.step(V.tensor_scalar(t1[:], aa[:], cols[:, 1:2], oneminus[:, 0:1], ALU.mult, ALU.add))
                    if slot == 4:
                        c.mark(V.tensor_tensor(km[:], k2[:], t1[:], ALU.mult))
                    if slot in (5, 6):
                        dve.wait_ge(s["nrm_ready"], 2 * h + 2)
                        part = slice((slot - 5) * (ALL // 2), (slot - 4) * (ALL // 2))
                        c.step(V.reciprocal(nrm[:, part], nrm[:, part]))
                    if slot == 7:
                        c.step(V.scalar_tensor_tensor(out=kk[:], in0=k2[:], scalar=cols[:, 0:1], in1=nrm[:], op0=ALU.mult, op1=ALU.mult))
                        c.step(V.tensor_tensor(t1[:], kk[:], aa[:], ALU.mult))
                    if slot >= 8:
                        z = (slot - 8) // 3
                        rows, q = (lo, hi)[z], slice(z * CH, z * CH + CH)
                    if slot in (8, 11):
                        dve.wait_ge(s["exp_ready"], 7 * h + 7)
                        V.scalar_tensor_tensor(out=at_ctx[u][rows, :, q], in0=cs(kk)[rows, 0:CSTEPS], scalar=-1.0, in1=cs(e_exc)[rows, 0:CSTEPS], op0=ALU.mult, op1=ALU.mult)
                        V.scalar_tensor_tensor(out=at_rt[u][rows, :, 0, q], in0=cs(kk)[rows, CSTEPS:], scalar=-1.0, in1=cs(e_exc)[rows, CSTEPS:], op0=ALU.mult, op1=ALU.mult)
                    if slot in (9, 12):
                        V.tensor_tensor(at_rt[u][rows, :, 1, q], cs(r2)[rows], cs(e_inc)[rows, CSTEPS:], ALU.mult)
                        V.tensor_tensor(bh[rows, :, q], cs(t1)[rows], cs(e_neg)[rows], ALU.mult)
                    if slot in (10, 13):
                        V.tensor_tensor(kh[rows, :, q], cs(km)[rows], cs(e_neg)[rows], ALU.mult)
                        c.step(V.scalar_tensor_tensor(out=rk[rows, :, q], in0=cs(r2)[rows], scalar=cols[rows, 2:3], in1=cs(km)[rows, CSTEPS:], op0=ALU.mult, op1=ALU.mult))
                    if slot == 13:
                        V.tensor_tensor(ee[u][:, 0:STEPS - 1], em[:, 0:STEPS - 1], em[:, 1:STEPS], ALU.mult).then_inc(s["bd_ready"], 1)
                        assert c.n == FACTOR_STEPS, c.n

                def factors(h):
                    c = Chain(dve, s["factor_step"], 0)
                    for slot in range(SLOTS):
                        factor_part(c, h, 0, slot)

                def body(h, u, k, walk, ahead):
                    if walk:
                        walk_begin(walk)
                    c = Chain(dve, s["dve_step"], h * 2 * NG)
                    dve.wait_ge(s["bon_ready"], h + 1)
                    V.tensor_copy(bon[:], bon_bank[:, 0:lat]).then_inc(s["bon_read"], 1)
                    for g in range(NG):
                        g4 = slice(4 * g, 4 * g + 4)
                        for j in range(4 * g, 4 * g + 4):
                            dve.wait_ge(s["pb_ready"], h * STEPS + j + 1)
                            if j < CSTEPS:
                                V.tensor_tensor(pairs_ctx[u][:, j], quad(pair_bank[j % 2][:])[:, 0::2, :], masks[:, 0::2, :], ALU.mult).then_inc(s["pb_masked"], 1)
                            else:
                                V.tensor_tensor(pairs_lat[u][:, j - CSTEPS], quad(pair_bank[j % 2][:]), masks[:], ALU.mult).then_inc(s["pb_masked"], 1)
                        if walk:
                            walk_step(walk, WALK_PAIRS[g][0])
                        dve.wait_ge(s["pn_ready"], h * NG + g + 1)
                        c.mark(V.tensor_tensor(T[:, g4, :], quad(pn_bank[:]), over4(join0[:]), ALU.mult))
                        dve.wait_ge(s["pb_masked"], h * STEPS + 4 * g + 4)
                        c.step(V.tensor_tensor(R[u][:, g4, :], pairs_of_group(u, g), over4(join[:, 0, :]), ALU.mult))
                        V.tensor_tensor(T[:, g4, :], T[:, g4, :], over4(S.ident[:]), ALU.add)
                        V.tensor_tensor(R[u][:, g4, :], R[u][:, g4, :], over4(S.ident[:]), ALU.add).then_inc(s["pn_masked"], 1)
                        if walk:
                            walk_step(walk, WALK_PAIRS[g][1])
                    dve.wait_ge(v_loaded[u], k * 32 + 32)
                    dve.wait_ge(s["bonus_free"], h + 1)
                    dve.wait_ge(s["bon_read"], h + 1)
                    V.tensor_tensor(yb[lo, :, :], vs[u][lo, CSTEPS:, :], bon[lo, :].rearrange("p (c o) -> p c o", o=1).broadcast_to([HK, lat, HK]), ALU.mult)
                    V.tensor_tensor(yb[hi, ::-1, :], vs[u][hi, CSTEPS:, :], bon[hi, :].rearrange("p (c o) -> p c o", o=1).broadcast_to([HK, lat, HK]), ALU.mult).then_inc(s["bonus_done"], 1)
                    if ahead is not None:
                        fc = Chain(dve, s["factor_step"], ahead * FACTOR_STEPS)
                    for n in range(NZ):
                        l, g = n // NG, n % NG
                        g4 = slice(4 * g, 4 * g + 4)
                        if l < LEVELS - 1:
                            dve.wait_ge(s["tz_ready"], h * (NZ - NG) + n + 1)
                            V.tensor_tensor(T[:, g4, :], T[:, g4, :], quad(tz_bank[:]), ALU.add).then_inc(s["tz_added"], 1)
                        dve.wait_ge(s["zr_ready"], h * NZ + n + 1)
                        V.tensor_tensor(R[u][:, g4, :], R[u][:, g4, :], quad(zr_bank[:]), ALU.add).then_inc(s["zr_added"], 1)
                        if walk and n in WALK_GROWTH:
                            walk_step(walk, WALK_GROWTH[n])
                        if ahead is not None and n < SLOTS:
                            factor_part(fc, ahead, 1 - u, n)
                    assert c.n == 2 * NG

                every_head(dve, factors, body)
                walk_begin(LAST)
                for j in range(STEPS):
                    walk_step(LAST, j)

            @block.tensor
            def _(pe):
                pe.wait_ge(s["const_loaded"], 80)
                mmul = nc.tensor.matmul

                def walk_state(walk, j):
                    w, wu, wk = walk
                    v = vs[wu][:, j, :]
                    if j == 0:
                        pe.wait_ge(v_loaded[wu], wk * 32 + 32)
                    mmul(x_psum, pair(wu, j, 2), v, start=True, stop=False)
                    pe.wait_ge(s["sm_ready"], w * STEPS + j + 1)
                    mmul(x_psum, at(wu, j), Sm[:], start=False, stop=True).then_inc(s["x_ready"], 1)
                    if j < STEPS - 1:
                        mmul(ds_psum, S.ident[:], Sm[:], start=True, stop=False)
                        mmul(ds_psum, kT[wu][:, j, :], v, start=False, stop=False)
                    if j >= CSTEPS:
                        if j > CSTEPS:
                            pe.wait_ge(s["y_copied"], w * lat + j - CSTEPS)
                        mmul(y_psum, at_rt[wu][:, j - CSTEPS, 1, :], Sm[:], start=True, stop=False)
                        mmul(y_psum, pair(wu, j, 3), v, start=False, stop=False)

                def walk_solve(walk, j):
                    w, wu, _ = walk
                    pe.wait_ge(s["x_copied"], w * STEPS + j + 1)
                    mmul(sa_psum, R[wu][:, j, :], X[:], start=True, stop=True).then_inc(s["sa_ready"], 1)

                def walk_share(walk, j):
                    w, wu, _ = walk
                    pe.wait_ge(s["sa_copied"], w * STEPS + j + 1)
                    if j < STEPS - 1:
                        mmul(ds_psum, bT[wu][:, j, :], SA[:], start=False, stop=True).then_inc(s["ds_ready"], 1)
                    if j >= CSTEPS:
                        mmul(y_psum, pair(wu, j, 1), SA[:], start=False, stop=True).then_inc(s["y_ready"], 1)

                def factor_part(h, slot):
                    if slot == 1:
                        pe.wait_ge(s["sq_ready"], h + 1)
                        mmul(ss_bank[:], halves[:], sq[:, 0:BANK], start=True, stop=True).then_inc(s["ss_ready"], 1)
                    if slot == 3:
                        pe.wait_ge(s["nrm_ready"], 2 * h + 1)
                        mmul(ss_bank[:, 0:ALL - BANK], halves[:], sq[:, BANK:ALL], start=True, stop=True).then_inc(s["ss_ready"], 1)

                def factors(h):
                    for slot in range(SLOTS):
                        factor_part(h, slot)

                def body(h, u, k, walk, ahead):
                    def part(what, j):
                        if walk and j is not None:
                            what(walk, j)

                    pe.wait_ge(s["bd_ready"], h + 1)
                    for n in range(lat):
                        mm = mmul(bon_bank[:, n:n + 1], rk[:, n, :], S.ones[:, 0:1], start=True, stop=True)
                    mm.then_inc(s["bon_ready"], 1)
                    for g in range(NG):
                        j0, j1 = WALK_PAIRS[g]
                        for j in range(4 * g, 4 * g + 4):
                            if j == 4 * g + 2:
                                part(walk_state, j0)
                            if j >= 2:
                                pe.wait_ge(s["pb_masked"], h * STEPS + j - 1)
                            b = pair_bank[j % 2]
                            if j < CSTEPS:
                                w, rhs = P, at_ctx[u][:, j, :]
                            else:
                                w, rhs = 2 * P, at_rt[u][:, j - CSTEPS].rearrange("p a t -> p (a t)")
                            mmul(b[:, 0:w], bh[:, j, :], rhs, start=True, stop=True)
                            mmul(b[:, 2 * P:2 * P + w], kh[:, j, :], rhs, start=True, stop=True).then_inc(s["pb_ready"], 1)
                        part(walk_solve, j0)
                        if g >= 1:
                            pe.wait_ge(s["pn_masked"], h * NG + g)
                        for j in range(4 * g, 4 * g + 4):
                            mm = mmul(pn_bank[:, (j % 4) * P:(j % 4 + 1) * P], at(u, j), bh[:, j, :], start=True, stop=True)
                        mm.then_inc(s["pn_ready"], 1)
                        part(walk_share, j0)
                        for n, src in enumerate((bh, kh)):
                            if g >= 1:
                                pe.wait_ge(s["tr_copied"], h * 2 * NG + 2 * g - 1 + n)
                            elif n == 1:
                                pe.wait_ge(s["bon_read"], h + 1)
                            for j in range(4 * g, 4 * g + 4):
                                mm = nc.tensor.transpose(tr_bank[n][:, (j % 4) * P:(j % 4 + 1) * P], src[:, j, :], S.ident[:])
                            mm.then_inc(s["tr_ready"], 1)
                            part((walk_state, walk_solve)[n], j1)
                        part(walk_share, j1)
                    pe.wait_ge(s["tr_copied"], h * 2 * NG + 2 * NG)

                    def grow_z(n):
                        l, g = n // NG, n % NG
                        pe.wait_ge(s["off_ready"], h * NZ + n + 1)
                        if l == 0:
                            pe.wait_ge(s["pn_masked"], h * NG + NG)
                        else:
                            pe.wait_ge(s["tz_added"], h * (NZ - NG) + (l - 1) * NG + g + 1)
                        if n >= 2:
                            pe.wait_ge(s["z_copied"], h * NZ + n - 1)
                        for q in range(4):
                            mm = mmul(z_bank[n % 2][:, q * P:(q + 1) * P], off[n % 2][:, q, :], T[:, 4 * g + q, :], start=True, stop=True)
                        mm.then_inc(s["z_ready"], 1)

                    grow_z(0)
                    for n in range(NZ):
                        l, g = n // NG, n % NG
                        j = WALK_GROWTH[n] if n in WALK_GROWTH else None
                        part(walk_state, j)
                        if n + 1 < NZ:
                            grow_z(n + 1)
                        part(walk_solve, j)
                        pe.wait_ge(s["z_copied"], h * NZ + n + 1)
                        if l < LEVELS - 1:
                            if l > 0:
                                pe.wait_ge(s["zr_added"], h * NZ + n - NG + 1)
                            if n >= 1:
                                pe.wait_ge(s["tz_added"], h * (NZ - NG) + n)
                            for q in range(4):
                                mm = mmul(tz_bank[:, q * P:(q + 1) * P], R[u][:, 4 * g + q, :], Z[n % 2][:, q, :], start=True, stop=True)
                            mm.then_inc(s["tz_ready"], 1)
                        if n >= 1:
                            pe.wait_ge(s["zr_added"], h * NZ + n)
                        for q in range(4):
                            mm = mmul(zr_bank[:, q * P:(q + 1) * P], Z[n % 2][:, q, :], R[u][:, 4 * g + q, :], start=True, stop=True)
                        mm.then_inc(s["zr_ready"], 1)
                        part(walk_share, j)
                        if ahead is not None and n < SLOTS:
                            factor_part(ahead, n)
                    pe.wait_ge(s["zr_added"], h * NZ + NZ)

                every_head(pe, factors, body)
                for j in range(STEPS):
                    for what in (walk_state, walk_solve, walk_share):
                        what(LAST, j)


FACTOR_STEPS = 11


def rwkv_tables():
    i = np.arange(CH)
    z1 = np.zeros((CH, CH))
    f = np.float32

    def bd(fwd, bwd):
        return np.block([[fwd, z1], [z1, bwd]]).astype(f)

    early, same = i[:, None] < i[None, :], i[:, None] == i[None, :]
    strict = bd(early, early.T)
    incl = bd(early | same, early.T | same)
    joins = []
    for l in range(LEVELS + 1):
        m = 1 << l
        b = (i[:, None] // (2 * m) == i[None, :] // (2 * m)) & (i[:, None] % (2 * m) < m) & (i[None, :] % (2 * m) >= m)
        joins.append(bd(b, b.T))
    keep = np.ones((P, ALL), f)
    keep[:, ::CH] = 0.0
    return {"rw_masks": np.ascontiguousarray(np.stack([strict, incl, strict, incl], 1)),
            "rw_join": np.ascontiguousarray(np.stack(joins, 1)), "rw_join0": np.ascontiguousarray(joins[0].T),
            "rw_keep": keep, "rw_halves": bd(np.ones((CH, CH)), np.ones((CH, CH)))}


def rwkv_join(nc, name, S, a, yS, bS, gate, out):
    with Stage(nc, name) as st:
        y = [[st.sb(f"y{n}{u}", [P, D]) for n in range(4)] for u in range(2)]
        gain, shift = st.sb("gain", [P, D]), st.sb("shift", [P, D])
        g = [st.sb(f"gate{u}", [P, D]) for u in range(2)]
        mean, var, rms = st.sb("mean", [P, HEADS]), st.sb("var", [P, HEADS]), st.sb("rms", [P, HEADS])
        sq = st.sb("sq", [P, D])
        const_loaded, loaded = st.sem("const_loaded"), [st.sem(f"loaded{u}") for u in range(2)]
        dve_step, squared, var_ready, rms_ready, centred = (st.sem(n) for n in ("dve_step", "squared", "var_ready", "rms_ready", "centred"))

        def hv(x):
            return x[:].rearrange("p (h c) -> p h c", c=HK)

        def per_head(x):
            return x[:].rearrange("p (h o) -> p h o", o=1).broadcast_to([P, HEADS, HK])

        SV = 12
        with st.block() as block:
            @block.sync
            def _(sp):
                sp.dma_start(gain[:], a["rw_ln_g_2"].partition_broadcast(P)).then_inc(const_loaded, 16)
                sp.dma_start(shift[:], a["rw_ln_b_2"].partition_broadcast(P)).then_inc(const_loaded, 16)
                for t in range(NT):
                    if t >= 2:
                        sp.wait_ge(dve_step, SV * (t - 1))
                    rows = slice(t * P, (t + 1) * P)
                    for n, src in enumerate((yS[0], yS[1], bS[0], bS[1])):
                        sp.dma_start(y[t % 2][n][:], src[rows, :]).then_inc(loaded[t % 2], 16)
                    sp.dma_start(g[t % 2][:], gate[rows, :]).then_inc(loaded[t % 2], 16)

            @block.scalar
            def _(act):
                for t in range(NT):
                    act.wait_ge(centred, t + 1)
                    nc.scalar.activation(sq[:], y[t % 2][0][:], ACT.Square).then_inc(squared, 1)
                    act.wait_ge(var_ready, t + 1)
                    nc.scalar.activation(rms[:], var[:], ACT.Sqrt, scale=1.0 / HK, bias=S.eps[:, 2:3]).then_inc(rms_ready, 1)

            @block.vector
            def _(dve):
                V = nc.vector
                dve.wait_ge(const_loaded, 32)
                for t in range(NT):
                    c = Chain(dve, dve_step, t * SV)
                    y0, y1, b0, b1 = y[t % 2]
                    dve.wait_ge(loaded[t % 2], 80 * (t // 2 + 1))
                    c.step(V.tensor_tensor(y0[:], y0[:], y1[:], ALU.add))
                    c.step(V.tensor_reduce(mean[:], hv(y0), AX.X, ALU.add))
                    c.step(V.tensor_scalar(mean[:], mean[:], 1.0 / HK, None, ALU.mult))
                    V.tensor_tensor(hv(y0), hv(y0), per_head(mean), ALU.subtract).then_inc(centred, 1)
                    c.mark(V.tensor_tensor(b0[:], b0[:], b1[:], ALU.add))
                    dve.wait_ge(squared, t + 1)
                    V.tensor_reduce(var[:], hv(sq), AX.X, ALU.add).then_inc(var_ready, 1)
                    dve.wait_ge(rms_ready, t + 1)
                    c.step(V.reciprocal(rms[:], rms[:]))
                    c.step(V.tensor_tensor(hv(y0), hv(y0), per_head(rms), ALU.mult))
                    c.step(V.tensor_tensor(y0[:], y0[:], gain[:], ALU.mult))
                    c.step(V.tensor_tensor(y0[:], y0[:], shift[:], ALU.add))
                    c.step(V.tensor_tensor(y0[:], y0[:], b0[:], ALU.add))
                    c.step(V.tensor_tensor(out[:, t, :], y0[:], g[t % 2][:], ALU.mult))
                    while c.n < SV:
                        c.mark(V.nop())
                    c.wait()
                    assert c.n == SV, c.n


RW_COLS = (("mu", 6 * KD), ("w0", 2 * KD), ("a0", 2 * KD), ("norm1", KD))


def rwkv(nc, S, a, x_tiles, c_tiles, hT, mods):
    c = {}
    at = 0
    for n, w in RW_COLS:
        c[n] = S.rw_cols[:, at:at + w]
        at += w
    cols = S.mod_cols
    modulation_columns(nc, "mc1", S, mods, c["norm1"], cols)
    norm_transpose(nc, "sn1", S, c_tiles + x_tiles, hT, cols=[cols[1]] * (NA - NT) + [cols[0]] * NT)
    kF, sgF, aF = ([dram(nc, f"rw_{n}{z}", [D, ALL]) for z in range(2)] for n in ("k", "sg", "a"))
    rF = [dram(nc, f"rw_r{z}", [D, SEQ]) for z in range(2)]
    vS = [dram(nc, f"rw_v{z}", [STEPS, CH, D]) for z in range(2)]
    yS, bS = ([dram(nc, f"rw_{n}{z}", [SEQ, D]) for z in range(2)] for n in ("y", "bon"))
    gate = dram(nc, "rw_gate", [SEQ, D])
    parts = ((0, CTX), (CTX, SEQ))
    fdram = "(k p) t -> p k t"
    with ExitStack() as mem:
        xx = mem.enter_context(nc.sbuf_tensor("rw_xx", [P, KD, ALL], F32))
        mix = mem.enter_context(nc.sbuf_tensor("rw_mix", [P, KD, ALL], F32))
        token_shift(nc, "rws", hT, xx)

        def mixed(j):
            return hT, xx, c["mu"][:, j * KD:(j + 1) * KD]

        def both_orders(fwd, bwd, lead):
            def epi(which, engine, chain, j, n0, ps):
                w = ps.shape[1]
                o = slice(n0 - lead, n0 - lead + w)
                copy = (lambda d, s_: engine.activation(d, s_, ACT.Copy)) if which == "act" else engine.tensor_copy
                copy(fwd(j)[:, o], ps)
                return copy(backward(bwd(j)[:, o]), chunked(ps))
            return epi

        def rows(t, q):
            return t.rearrange(fdram, p=P)[:, 4 * q:4 * q + 4, :]

        with ExitStack() as m2:
            f, b = (m2.enter_context(nc.sbuf_tensor(f"rw_rf{z}", [P, KD, SEQ], F32)) for z in range(2))
            project(nc, "rp0", mix, SEQ, [dict(w=a["rw_wr_2"][:, q * BANK:(q + 1) * BANK], mode="F",
                                              epi=both_orders(lambda j, q=q: f[:, 4 * q + j, :], lambda j, q=q: b[:, 4 * q + j, :], CTX),
                                              stores=[(rows(d, q), x[:, 4 * q:4 * q + 4]) for d, x in zip(rF, (f, b))]) for q in range(2)],
                    parts=parts[1:], mix=mixed(0))
        with ExitStack() as m2:
            f, b = (m2.enter_context(nc.sbuf_tensor(f"rw_kf{z}", [P, KD, ALL], F32)) for z in range(2))
            project(nc, "rp2", mix, ALL, [dict(w=a["rw_wk_2"][:, q * BANK:(q + 1) * BANK], mode="F",
                                              epi=both_orders(lambda j, q=q: f[:, 4 * q + j, :], lambda j, q=q: b[:, 4 * q + j, :], 0),
                                              stores=[(rows(d, q), x[:, 4 * q:4 * q + 4]) for d, x in zip(kF, (f, b))]) for q in range(2)],
                    parts=parts, mix=mixed(2))
        with ExitStack() as m2:
            v = m2.enter_context(nc.sbuf_tensor("rw_vt", [P, NA, D], F32))

            def v_stores(o):
                out = [(vS[0].rearrange("(q s) t c -> (s t) q c", s=2)[:, :, o], v[:, :, o])]
                for j in range(STEPS):
                    step = CSTEPS - 1 - j if j < CSTEPS else STEPS - 1 - (j - CSTEPS)
                    out.append((vS[1][step][:, o], v[CH * (j % 2):CH * (j % 2) + CH, j // 2, o]))
                return out

            project(nc, "rp3", mix, ALL, [dict(w=a["rw_wv_2"][:, q * BANK:(q + 1) * BANK], mode="T",
                                              epi=copy_to(lambda j, n0, q=q: v[:, j, q * BANK:(q + 1) * BANK]),
                                              stores=v_stores(slice(q * BANK, (q + 1) * BANK))) for q in range(2)], mix=mixed(3))
        for j, n, func, w1, w2, base, outF in ((1, "w", ACT.Tanh, "rw_w1_2", "rw_w2_2", c["w0"], sgF), (4, "a", ACT.Copy, "rw_a1_2", "rw_a2_2", c["a0"], aF)):
            with ExitStack() as m2:
                low = [m2.enter_context(nc.sbuf_tensor(f"rw_low{n}{z}", [HK, 1, ALL], F32)) for z in range(2)]
                f = [m2.enter_context(nc.sbuf_tensor(f"rw_out{n}{z}", [P, KD, ALL], F32)) for z in range(2)]

                def squash(z, func=func):
                    def epi(which, engine, chain, j, n0, ps):
                        return engine.activation(low[z][:, 0, n0:n0 + ps.shape[1]], ps, func)
                    return epi

                def sigmoid(z, q, base=base):
                    def epi(which, engine, chain, j, n0, ps):
                        d = 4 * q + j
                        o = slice(n0, n0 + ps.shape[1])
                        bias = base[:, z * KD + d:z * KD + d + 1]
                        if z == 0:
                            return engine.activation(f[0][:, d, o], ps, ACT.Sigmoid, bias=bias)
                        return engine.activation(backward(f[1][:, d, o]), chunked(ps), ACT.Sigmoid, bias=bias)
                    return epi

                project(nc, f"rl{n}", mix, ALL, [dict(w=a[w1][z], mode="F", eng="act", epi=squash(z)) for z in range(2)], parts=parts, mix=mixed(j))
                project(nc, f"ro{n}", low[0], ALL, [dict(w=a[w2][z][:, q * BANK:(q + 1) * BANK], x=low[z], mode="F", eng="act", epi=sigmoid(z, q),
                                                        stores=[(rows(outF[z], q), f[z][:, 4 * q:4 * q + 4])]) for z in range(2) for q in range(2)], parts=parts)
        with ExitStack() as m2:
            low = m2.enter_context(nc.sbuf_tensor("rw_glow", [P, 2, SEQ], F32))
            g = m2.enter_context(nc.sbuf_tensor("rw_gt", [P, NT, D], F32))

            def squash_g(which, engine, chain, j, n0, ps):
                return engine.activation(low[0:ps.shape[0], j, 0:SEQ], ps, ACT.Sigmoid)

            project(nc, "rg1", mix, SEQ, [dict(w=a["rw_g1_2"], mode="F", eng="act", epi=squash_g)], parts=parts[1:], mix=mixed(5))
            project(nc, "rg2", low, SEQ, [dict(w=a["rw_g2_2"][:, q * BANK:(q + 1) * BANK], mode="T",
                                              epi=copy_to(lambda j, n0, q=q: g[:, j, q * BANK:(q + 1) * BANK]),
                                              stores=[(gate.rearrange("(t p) c -> p t c", p=P)[:, :, q * BANK:(q + 1) * BANK], g[:, :, q * BANK:(q + 1) * BANK])])
                                         for q in range(2)])
    S.free_hT()
    rwkv_scan(nc, "scan", S, a, kF, rF, sgF, aF, vS, yS, bS)
    hT = S.take_hT()
    with ExitStack() as mem:
        o = mem.enter_context(nc.sbuf_tensor("rw_o", [P, NT, D], F32))
        row = mem.enter_context(nc.sbuf_tensor("rw_gaterow", [P, D], F32))
        tmp = mem.enter_context(nc.sbuf_tensor("rw_tmp", [P, 2, BANK], F32))
        rwkv_join(nc, "rwj", S, a, yS, bS, gate, o)
        load_all(nc, "rwl", [(row[:], mods[0, 2 * D:3 * D].partition_broadcast(P))])
        norm_transpose(nc, "rwt", S, [o[:, t, :] for t in range(NT)], hT, scaled=False)
        project(nc, "rwo", hT, SEQ, [dict(w=a["rw_wo_2"][:, q * BANK:(q + 1) * BANK], mode="T", eng="dve",
                                         epi=gated_residual(lambda j, q=q: x_tiles[j][:, q * BANK:(q + 1) * BANK], lambda j, q=q: row[:, q * BANK:(q + 1) * BANK], tmp)) for q in range(2)])
    return hT


def final_norm(nc, S, x_tiles, gain, out):
    T = len(x_tiles)
    with Stage(nc, "fin") as st:
        row, junk = st.sb("row", [P, D]), st.sb("squares", [P, D])
        ss, rms, rstd = st.sb("sum_sq", [P, T]), st.sb("rms", [P, T]), st.sb("rstd", [P, T])
        y = st.sb("y", [P, T, D])
        row_loaded, rms_ready, scaled, act_step, dve_step = (st.sem(n) for n in ("row_loaded", "rms_ready", "scaled", "act_step", "dve_step"))
        stored = st.sem("stored")
        with st.block() as block:
            @block.sync
            def _(sp):
                sp.dma_start(row[:], gain.partition_broadcast(P)).then_inc(row_loaded, 16)
                for t in range(T):
                    sp.wait_ge(scaled, t + 1)
                    sp.dma_start(out[t * P:(t + 1) * P, :], y[:, t, :]).then_inc(stored, 16)
                sp.wait_ge(stored, 16 * T)

            @block.scalar
            def _(act):
                steps = Chain(act, act_step)
                for t in range(T):
                    steps.step(nc.scalar.activation(junk[:], x_tiles[t], ACT.Square, accum_out=ss[:, t:t + 1]))
                nc.scalar.activation(rms[:], ss[:], ACT.Sqrt, scale=1.0 / D, bias=S.eps6[:, 0:1]).then_inc(rms_ready, 1)

            @block.vector
            def _(dve):
                steps = Chain(dve, dve_step)
                dve.wait_ge(rms_ready, 1)
                steps.step(nc.vector.reciprocal(rstd[:], rms[:]))
                dve.wait_ge(row_loaded, 16)
                for t in range(T):
                    nc.vector.scalar_tensor_tensor(out=y[:, t, :], in0=x_tiles[t], scalar=rstd[:, t:t + 1], in1=row[:], op0=ALU.mult, op1=ALU.mult).then_inc(scaled, 1)


def second_block_b(nc, S, a, x_tiles, c_tiles, hT, mods, out):
    hT = rwkv(nc, S, a, x_tiles, c_tiles, hT, mods[1])
    moe(nc, "moe1", S, a, 1, ((x_tiles, 0),), hT, mods[1])
    final_norm(nc, S, x_tiles, a["final_g_2"], out)


def rwkv_layout(inp):
    g = lambda n: np.asarray(inp[n])
    out = {n: np.ascontiguousarray(g(n)[0]) for n in ("rw_wr_2", "rw_wk_2", "rw_wv_2", "rw_wo_2", "rw_w1_2", "rw_w2_2", "rw_a1_2", "rw_a2_2", "rw_g1_2", "rw_g2_2", "rw_ln_g_2", "rw_ln_b_2")}
    out["final_g_2"] = np.ascontiguousarray(g("final_g_2"))
    out["rwkv_cols"] = np.concatenate([columns(g("rw_mu_2")), columns(g("rw_w0_2")), columns(g("rw_a0_2")), columns(g("norm1_g_2")[1])], 1)
    per = np.stack([g("rw_k_k_2")[0].reshape(HEADS, HK), g("rw_k_a_2")[0].reshape(HEADS, HK), g("rw_r_k_2")[0], g("rw_r_k_2")[0]], 2)
    out["rw_cols"] = np.ascontiguousarray(np.concatenate([per, per], 1))
    return out



def network(nc, a, out):
    Stage.zeroed = []
    S = Shared()
    with ExitStack() as mem:
        def sb(n, shape):
            return mem.enter_context(nc.sbuf_tensor(n, shape, F32))
        S.pool_sems = [[nc.alloc_semaphore(f"pool_dma{l}{n}") for n in range(7)] for l in range(2)]
        S.ident, S.ones, S.eps = sb("identity", [P, P]), sb("ones", [P, P]), sb("epsilons", [P, 4])
        S.eps6 = S.eps[:, 0:1]
        S.first_cols, S.second_cols, S.rw_cols = sb("first_columns", [P, 37]), sb("second_columns", [P, 32]), sb("rwkv_columns", [P, 88])
        mod_cols = sb("mod_columns", [P, 4, KD])
        S.mod_cols = [(mod_cols[:, 0], mod_cols[:, 1]), (mod_cols[:, 2], mod_cols[:, 3])]
        x = sb("x", [P, NT, D])
        hT_mem = ExitStack()
        taken = []

        def take_hT():
            taken.append(1)
            return hT_mem.enter_context(nc.sbuf_tensor(f"hT{len(taken)}", [P, KD, ALL], F32))

        S.take_hT, S.free_hT = take_hT, hT_mem.close
        mods = dram(nc, "mods", [2, 2, N_MOD * D])
        tok = "(t p) d -> p t d"
        load_all(nc, "consts", [(S.ident[:], a["ident"]), (S.ones[:], a["ones"]), (S.eps[:], a["eps"]), (S.first_cols[:], a["first_cols"]),
                                (S.second_cols[:], a["second_cols"]), (S.rw_cols[:], a["rwkv_cols"]), (x[:], a["x"].rearrange(tok, p=P))])
        x_tiles = [x[:, t, :] for t in range(NT)]
        with ExitStack() as first:
            first_block(nc, S, a, x_tiles, first.enter_context(nc.sbuf_tensor("first_hT", [P, KD, ALL], F32)))
        xc = hT_mem.enter_context(nc.sbuf_tensor("xc", [P, NA - NT, D], F32))
        c_tiles = [xc[:, t, :] for t in range(NA - NT)]
        hT = take_hT()
        load_all(nc, "context", [(xc[:], a["ctx_2"].rearrange(tok, p=P))])
        second_block_a(nc, S, a, x_tiles, c_tiles, hT, mods)
        second_block_b(nc, S, a, x_tiles, c_tiles, hT, mods, out)
        hT_mem.close()


def kernel(**inputs):
    import concourse.bacc as bacc
    from concourse.bass_utils import run_bass_kernel_spmd

    inp = {n: np.asarray(v) for n, v in inputs.items()}
    arrays = {}
    for part in (first_layout(inp), second_layout(inp), rwkv_layout(inp), constants(), attention_tables(), gla_tables(),
                 rope_tables(), route_tables(), rwkv_tables()):
        arrays.update(part)
    nc = bacc.Bacc("TRN2", target_bir_lowering=False, num_devices=1)
    a = {n: nc.dram_tensor(f"in_{n}_dram", v.shape, mybir.dt.from_np(v.dtype), kind="ExternalInput").ap() for n, v in arrays.items()}
    out = nc.dram_tensor("out_0_dram", (1, SEQ, D), F32, kind="ExternalOutput").ap()
    network(nc, a, out[0])
    r = run_bass_kernel_spmd(nc, [{f"in_{n}_dram": v for n, v in arrays.items()}], core_ids=[0])
    return r.results[0]["out_0_dram"]
```

```python
import math
from contextlib import ExitStack

import numpy as np
import concourse.bass as bass
from concourse import mybir

F32 = mybir.dt.float32
F32R = mybir.dt.float32r
I32 = mybir.dt.int32
ACT = mybir.ActivationFunctionType
ALU = mybir.AluOpType
AX = mybir.AxisListType

P = 128
D = 1024
SEQ = 512
CTX = 256
ALL = SEQ + CTX
KD = D // P
NT = SEQ // P
NA = ALL // P
BANK = 512
EPS = 1e-6


class Stage:

    zeroed = []

    def __init__(self, nc, name):
        self.nc, self.name = nc, name

    def __enter__(self):
        self.stack = ExitStack()
        self.sems = []
        return self

    def sb(self, name, shape, dt=F32):
        return self.stack.enter_context(self.nc.sbuf_tensor(f"{self.name}_{name}", shape, dt))

    def ps(self, name, shape, dt=F32):
        return self.stack.enter_context(self.nc.psum_tensor(f"{self.name}_{name}", shape, dt))

    def sem(self, name):
        s = self.nc.alloc_semaphore(f"{self.name}_{name}")
        self.sems.append(s)
        return s

    def block(self):
        return self.nc.Block()

    def __exit__(self, *exc):
        self.stack.close()
        if exc[0] is None:
            for s in Stage.zeroed:
                self.nc.release_semaphore(s)
            for s in self.sems:
                self.nc.gpsimd.sem_clear(s)
            Stage.zeroed = self.sems


def twice(x):
    return x.rearrange("p (o n) -> p o n", o=1).broadcast_to([x.shape[0], 2, x.shape[1]])


class Chain:

    def __init__(self, eng, sem, base=0):
        self.eng, self.sem, self.base, self.n = eng, sem, base, 0

    def mark(self, ins):
        ins.then_inc(self.sem, 1)
        self.n += 1

    def wait(self):
        self.eng.wait_ge(self.sem, self.base + self.n)

    def step(self, ins):
        self.mark(ins)
        self.wait()


def kslices(k):
    return [(a, min(P, k - a)) for a in range(0, k, P)]


def project(nc, name, hT, n_tok, jobs, const=None, parts=None, mix=None):
    with Stage(nc, name) as st:
        K = jobs[0]["w"].shape[0]
        ks = kslices(K)
        cw = max(j["w"].shape[1] for j in jobs)
        wbuf = [st.sb(f"w{b}", [P, len(ks), cw]) for b in range(2)]
        banks = [st.ps(f"bank{b}", [P, BANK]) for b in range(8)]
        w_loaded = [st.sem(f"w_loaded{b}") for b in range(2)]
        step = -(-len(ks) // 8)
        pieces = [(k0, min(k0 + step, K // P)) for k0 in range(0, K // P, step)]
        piece_loaded = [st.sem(f"piece_loaded{n}") for n in range(len(pieces))]
        products_done = st.sem("products_done")
        act_done, dve_done = st.sem("act_done"), st.sem("dve_done")
        act_step, dve_step = st.sem("act_step"), st.sem("dve_step")
        stored, mixed = st.sem("stored"), st.sem("mixed")

        groups = []
        for c, job in enumerate(jobs):
            width = job["w"].shape[1]
            if job["mode"] == "F":
                for j, (f0, fw) in enumerate(kslices(width)):
                    for n0, nw in parts or [(n0, min(BANK, n_tok - n0)) for n0 in range(0, n_tok, BANK)]:
                        groups.append((c, j, f0, fw, n0, nw))
            else:
                for j, (n0, nw) in enumerate(kslices(n_tok)):
                    groups.append((c, j, n0, nw, 0, width))
        last_of = {}
        for g, grp in enumerate(groups):
            last_of[grp[0]] = g
        engine_of = []
        for g, grp in enumerate(groups):
            e = jobs[grp[0]].get("eng", "any")
            engine_of.append(("act", "dve")[g % 2] if e == "any" else e)
        nth = [engine_of[:g + 1].count(engine_of[g]) for g in range(len(groups))]

        def view(g):
            c, j, a, aw, b0, bw = groups[g]
            return banks[g % 8][0:aw, 0:bw]

        n_stores = sum(len(job.get("stores", ())) for job in jobs)

        with st.block() as block:
            @block.sync
            def _(sp):
                def store(c):
                    ended = engine_of[:last_of[c] + 1]
                    for which, done in (("act", act_done), ("dve", dve_done)):
                        if which in ended:
                            sp.wait_ge(done, ended.count(which))
                    for dst, src in jobs[c].get("stores", ()):
                        sp.dma_start(dst, src).then_inc(stored, 16)

                for c, job in enumerate(jobs):
                    if c >= 2:
                        sp.wait_ge(products_done, last_of[c - 2] + 1)
                    full = K // P
                    width = job["w"].shape[1]
                    if c == 0:
                        for n, (k0, k1) in enumerate(pieces):
                            sp.dma_start(wbuf[0][:, k0:k1, 0:width],
                                         job["w"][k0 * P:k1 * P, :].rearrange("(k p) n -> p k n", p=P)).then_inc(piece_loaded[n], 16)
                    elif full:
                        sp.dma_start(wbuf[c % 2][:, 0:full, 0:width],
                                     job["w"][0:full * P, :].rearrange("(k p) n -> p k n", p=P)
                                     ).then_inc(w_loaded[c % 2], 16)
                    if K % P:
                        sp.dma_start(wbuf[c % 2][0:K % P, full, 0:width],
                                     job["w"][full * P:K, :]).then_inc(w_loaded[c % 2], 16)
                    if c >= 2 and jobs[c - 2].get("stores"):
                        store(c - 2)
                for c in range(max(0, len(jobs) - 2), len(jobs)):
                    store(c)
                if n_stores:
                    sp.wait_ge(stored, 16 * n_stores)

            @block.tensor
            def _(pe):
                seen = -1
                per = 16 * ((K // P > 0) + (K % P > 0))
                for g, (c, j, a, aw, b0, bw) in enumerate(groups):
                    job = jobs[c]
                    if c != seen:
                        before = 16 * (K // P > 0) if c % 2 == 0 else 0
                        if per * (c // 2 + 1) > before:
                            pe.wait_ge(w_loaded[c % 2], per * (c // 2 + 1) - before)
                        seen = c
                    if g >= 8:
                        pe.wait_ge(act_done if engine_of[g - 8] == "act" else dve_done, nth[g - 8])
                    w = wbuf[c % 2]
                    bias = job.get("bias")
                    x = job.get("x", hT)
                    for k, (_, kw) in enumerate(ks):
                        if g == 0:
                            for n, (k0, _) in enumerate(pieces):
                                if k == k0:
                                    pe.wait_ge(piece_loaded[n], 16)
                        if mix and g == 0:
                            pe.wait_ge(mixed, k + 1)
                        if job["mode"] == "F":
                            lhsT, rhs = w[0:kw, k, a:a + aw], x[0:kw, k, b0:b0 + bw]
                        else:
                            lhsT, rhs = x[0:kw, k, a:a + aw], w[0:kw, k, 0:bw]
                        mm = nc.tensor.matmul(view(g), lhsT, rhs, start=(k == 0),
                                              stop=(k == len(ks) - 1 and bias is None))
                    if bias is not None:
                        mm = nc.tensor.matmul(view(g), const["ones"][0:1, 0:aw], bias, start=False, stop=True)
                    mm.then_inc(products_done, 1)

            def ends(which, eng, engine, chain, done):
                for g, (c, j, a, aw, b0, bw) in enumerate(groups):
                    if engine_of[g] == which:
                        eng.wait_ge(products_done, g + 1)
                        jobs[c]["epi"](which, engine, chain, j, b0, view(g)).then_inc(done, 1)

            @block.scalar
            def _(act):
                ends("act", act, nc.scalar, Chain(act, act_step), act_done)

            @block.vector
            def _(dve):
                if mix:
                    h, xx, mu = mix
                    for k in range(len(ks)):
                        nc.vector.scalar_tensor_tensor(out=hT[:, k, :], in0=xx[:, k, :], scalar=mu[:, k:k + 1], in1=h[:, k, :],
                                                       op0=ALU.mult, op1=ALU.add).then_inc(mixed, 1)
                ends("dve", dve, nc.vector, Chain(dve, dve_step), dve_done)


def project_split(nc, name, hT, n_tok, jobs, const=None, parts=None, mix=None):
    RAW = 4
    with Stage(nc, name) as st:
        KT = jobs[0]["w"].shape[0] // P
        w = [st.sb(f"w{b}", [P, BANK]) for b in range(RAW)]
        w_hi, w_lo = ([st.sb(f"w_{n}{u}", [P, BANK], F32R) for u in range(2)] for n in ("hi", "lo"))
        x_hi, x_lo = ([st.sb(f"x_{n}{u}", [P, hT.shape[2]], F32R) for u in range(2)] for n in ("hi", "lo"))
        banks = [st.ps(f"bank{b}", [P, BANK]) for b in range(8)]
        loaded = [st.sem(f"loaded{b}") for b in range(RAW)]
        w_hi_made, w_lo_made, x_hi_made, x_lo_made = (st.sem(n) for n in ("w_hi_made", "w_lo_made", "x_hi_made", "x_lo_made"))
        step_done, group_done = st.sem("step_done"), st.sem("group_done")
        act_done, dve_done = st.sem("act_done"), st.sem("dve_done")
        act_step, dve_step = st.sem("act_step"), st.sem("dve_step")
        stored, mixed = st.sem("stored"), st.sem("mixed")

        groups, first_group = [], [0]
        for c, job in enumerate(jobs):
            width = job["w"].shape[1]
            if job["mode"] == "F":
                cuts = parts or [(n0, min(BANK, n_tok - n0)) for n0 in range(0, n_tok, BANK)]
                new = [(c, j, f0, fw, n0, nw) for j, (f0, fw) in enumerate(kslices(width)) for n0, nw in cuts]
            else:
                new = [(c, j, n0, nw, 0, width) for j, (n0, nw) in enumerate(kslices(n_tok))]
            groups += new
            first_group.append(len(groups))
        engine_of = [("act", "dve")[g % 2] if jobs[grp[0]].get("eng", "any") == "any" else jobs[grp[0]]["eng"]
                     for g, grp in enumerate(groups)]
        nth = [engine_of[:g + 1].count(engine_of[g]) for g in range(len(groups))]
        steps = [(c, k) for c in range(len(jobs)) for k in range(KT)]

        def view(g):
            c, j, a, aw, b0, bw = groups[g]
            return banks[g % 8][0:aw, 0:bw]

        def wait_used(eng, t):
            c, k = steps[t]
            if k == KT - 1:
                eng.wait_ge(group_done, first_group[c + 1])
            else:
                eng.wait_ge(step_done, c * (KT - 1) + k + 1)

        with st.block() as block:
            @block.sync
            def _(sp):
                def store(c):
                    ended = engine_of[:first_group[c + 1]]
                    for which, done in (("act", act_done), ("dve", dve_done)):
                        if which in ended:
                            sp.wait_ge(done, ended.count(which))
                    for dst, src in jobs[c].get("stores", ()):
                        sp.dma_start(dst, src).then_inc(stored, 16)

                for t, (c, k) in enumerate(steps):
                    if t >= RAW:
                        sp.wait_ge(w_lo_made, t - RAW + 1)
                    sp.dma_start(w[t % RAW][:, 0:jobs[c]["w"].shape[1]], jobs[c]["w"][k * P:(k + 1) * P, :]).then_inc(loaded[t % RAW], 16)
                    if c and k == KT - 1 and jobs[c - 1].get("stores"):
                        store(c - 1)
                store(len(jobs) - 1)
                n_stores = sum(len(job.get("stores", ())) for job in jobs)
                if n_stores:
                    sp.wait_ge(stored, 16 * n_stores)

            @block.tensor
            def _(pe):
                for t, (c, k) in enumerate(steps):
                    job, u = jobs[c], t % 2
                    pe.wait_ge(w_lo_made, t + 1)
                    pe.wait_ge(x_lo_made, t + 1)
                    bias = job.get("bias")
                    for g in range(first_group[c], first_group[c + 1]):
                        _, j, a, aw, b0, bw = groups[g]
                        if k == 0 and g >= 8:
                            pe.wait_ge(act_done if engine_of[g - 8] == "act" else dve_done, nth[g - 8])
                        if job["mode"] == "F":
                            l_hi, l_lo, r_hi, r_lo = w_hi[u], w_lo[u], x_hi[u], x_lo[u]
                        else:
                            l_hi, l_lo, r_hi, r_lo = x_hi[u], x_lo[u], w_hi[u], w_lo[u]
                        last = k == KT - 1
                        nc.tensor.matmul(view(g), l_hi[:, a:a + aw], r_hi[:, b0:b0 + bw], start=(k == 0), stop=False)
                        nc.tensor.matmul(view(g), l_hi[:, a:a + aw], r_lo[:, b0:b0 + bw], start=False, stop=False)
                        mm = nc.tensor.matmul(view(g), l_lo[:, a:a + aw], r_hi[:, b0:b0 + bw], start=False, stop=(last and bias is None))
                        if last and bias is not None:
                            mm = nc.tensor.matmul(view(g), const["ones"][0:1, 0:aw], bias, start=False, stop=True)
                        if last:
                            mm.then_inc(group_done, 1)
                    if not last:
                        mm.then_inc(step_done, 1)

            @block.gpsimd
            def _(pool):
                for t, (c, k) in enumerate(steps):
                    width = jobs[c]["w"].shape[1]
                    pool.wait_ge(w_hi_made, t + 1)
                    nc.gpsimd.tensor_tensor(w_lo[t % 2][:, 0:width], w[t % RAW][:, 0:width], w_hi[t % 2][:, 0:width], ALU.subtract).then_inc(w_lo_made, 1)

            def ends(which, eng, engine, chain, done, c, half):
                mid = (first_group[c] + first_group[c + 1]) // 2
                for g in range(first_group[c], mid) if half == 0 else range(mid, first_group[c + 1]):
                    if engine_of[g] == which:
                        eng.wait_ge(group_done, g + 1)
                        jobs[c]["epi"](which, engine, chain, groups[g][1], groups[g][4], view(g)).then_inc(done, 1)

            @block.scalar
            def _(act):
                chain = Chain(act, act_step)
                for t, (c, k) in enumerate(steps):
                    act.wait_ge(loaded[t % RAW], 16 * (t // RAW) + 16)
                    if t >= 2:
                        wait_used(act, t - 2)
                    width = jobs[c]["w"].shape[1]
                    nc.scalar.activation(w_hi[t % 2][:, 0:width], w[t % RAW][:, 0:width], ACT.Copy).then_inc(w_hi_made, 1)
                    if c and k < 2:
                        ends("act", act, nc.scalar, chain, act_done, c - 1, k)
                for half in range(2):
                    ends("act", act, nc.scalar, chain, act_done, len(jobs) - 1, half)

            @block.vector
            def _(dve):
                chain = Chain(dve, dve_step)
                for t, (c, k) in enumerate(steps):
                    if mix and c == 0:
                        h, xx, mu = mix
                        nc.vector.scalar_tensor_tensor(out=hT[:, k, :], in0=xx[:, k, :], scalar=mu[:, k:k + 1], in1=h[:, k, :],
                                                       op0=ALU.mult, op1=ALU.add).then_inc(mixed, 1)
                        dve.wait_ge(mixed, k + 1)
                    if t >= 2:
                        wait_used(dve, t - 2)
                    nc.vector.tensor_copy(x_hi[t % 2][:], hT[:, k, :]).then_inc(x_hi_made, 1)
                    dve.wait_ge(x_hi_made, t + 1)
                    nc.vector.tensor_tensor(x_lo[t % 2][:], hT[:, k, :], x_hi[t % 2][:], ALU.subtract).then_inc(x_lo_made, 1)
                    if c and k < 2:
                        ends("dve", dve, nc.vector, chain, dve_done, c - 1, k)
                for half in range(2):
                    ends("dve", dve, nc.vector, chain, dve_done, len(jobs) - 1, half)


def copy_to(dest, columns=None):
    def epi(which, engine, chain, j, n0, ps):
        ps = ps[:, 0:columns or ps.shape[1]]
        if which == "act":
            return engine.activation(dest(j, n0), ps, ACT.Copy)
        return engine.tensor_copy(dest(j, n0), ps)
    return epi


def norm_transpose(nc, name, S, tiles, hT, cols=None, rows=None, h_dram=None, scaled=True, lo=None):
    T = len(tiles)
    width = tiles[0].shape[1]
    kd = width // P
    halves = -(-kd // 4)
    with Stage(nc, name) as st:
        junk = st.sb("squares", [P, width])
        ss = st.sb("sum_sq", [P, T])
        rms = st.sb("rms", [P, T])
        rstd = st.sb("rstd", [P, T])
        xn = [st.sb(f"xn{b}", [P, width]) for b in range(2)]
        tp = [st.ps(f"tp{b}", [P, 4, P]) for b in range(4)]
        rms_ready, xn_ready = st.sem("rms_ready"), st.sem("xn_ready")
        dve_step, act_step = st.sem("dve_step"), st.sem("act_step")
        turned, hi_made = st.sem("turned"), st.sem("hi_made")
        emptied = [st.sem("act_emptied"), st.sem("dve_emptied")]
        stored = [st.sem("stored0"), st.sem("stored1")]

        def empty(which, engine, g):
            t, h = g // halves, g % halves
            n = min(4, kd - 4 * h)
            src = tp[g % 4]
            if cols is None:
                dst = hT[:, 4 * h:4 * h + n, t * P:(t + 1) * P]
                if which == "act":
                    return engine.activation(dst, src[:, 0:n, :], ACT.Copy)
                return engine.tensor_copy(dst, src[:, 0:n, :])
            gain, bias = cols[t]
            for q in range(n):
                d = 4 * h + q
                dst = hT[:, d, t * P:(t + 1) * P]
                if which == "act":
                    ins = engine.activation(dst, src[:, q, :], ACT.Identity,
                                            scale=gain[:, d:d + 1],
                                            bias=bias[:, d:d + 1] if bias is not None else 0.0)
                elif bias is None:
                    ins = engine.tensor_scalar(dst, src[:, q, :], gain[:, d:d + 1], None, ALU.mult)
                else:
                    ins = engine.tensor_scalar(dst, src[:, q, :], gain[:, d:d + 1], bias[:, d:d + 1],
                                               ALU.mult, ALU.add)
            return ins

        G = T * halves
        with st.block() as block:
            @block.scalar
            def _(act):
                steps = Chain(act, act_step)
                if scaled:
                    for t in range(T):
                        steps.step(nc.scalar.activation(junk[:], tiles[t], ACT.Square, accum_out=ss[:, t:t + 1]))
                    steps.wait()
                    nc.scalar.activation(rms[:], ss[:], ACT.Sqrt, scale=1.0 / width, bias=S.eps6[:, 0:1]).then_inc(rms_ready, 1)
                for g in range(G) if lo is not None else range(0, G, 2):
                    act.wait_ge(turned, g + 1)
                    empty("act", nc.scalar, g).then_inc(emptied[0] if lo is None else hi_made, 1)

            @block.vector
            def _(dve):
                steps = Chain(dve, dve_step)
                if scaled:
                    dve.wait_ge(rms_ready, 1)
                    steps.step(nc.vector.reciprocal(rstd[:], rms[:]))

                def make(t):
                    if t >= 2:
                        dve.wait_ge(turned, (t - 1) * halves)
                        if h_dram is not None:
                            dve.wait_ge(stored[t % 2], 16 * (t // 2))
                    if rows is None:
                        nc.vector.tensor_scalar(xn[t % 2][:], tiles[t], rstd[:, t:t + 1], None, ALU.mult).then_inc(xn_ready, 1)
                    else:
                        steps.step(nc.vector.scalar_tensor_tensor(out=xn[t % 2][:], in0=tiles[t], scalar=rstd[:, t:t + 1],
                                                                  in1=rows[t][0], op0=ALU.mult, op1=ALU.mult))
                        nc.vector.tensor_tensor(xn[t % 2][:], xn[t % 2][:], rows[t][1], ALU.add).then_inc(xn_ready, 1)

                if scaled:
                    make(0)
                for t in range(T):
                    if scaled and t + 1 < T:
                        make(t + 1)
                    for g in range(t * halves, (t + 1) * halves):
                        if lo is not None:
                            dve.wait_ge(hi_made, g + 1)
                            h = g % halves
                            for q in range(min(4, kd - 4 * h)):
                                d, at = 4 * h + q, slice(t * P, (t + 1) * P)
                                ins = nc.vector.scalar_tensor_tensor(out=lo[:, d, at], in0=tp[g % 4][:, q, :], scalar=cols[t][0][:, d:d + 1],
                                                                     in1=hT[:, d, at], op0=ALU.mult, op1=ALU.subtract)
                            ins.then_inc(emptied[g % 2], 1)
                        elif g % 2:
                            dve.wait_ge(turned, g + 1)
                            empty("dve", nc.vector, g).then_inc(emptied[1], 1)

            @block.tensor
            def _(pe):
                for g in range(G):
                    t, h = g // halves, g % halves
                    if scaled and h == 0:
                        pe.wait_ge(xn_ready, t + 1)
                    if g >= 4:
                        pe.wait_ge(emptied[g % 2], (g - 4) // 2 + 1)
                    src = xn[t % 2] if scaled else tiles[t]
                    for q in range(min(4, kd - 4 * h)):
                        d = 4 * h + q
                        mm = nc.tensor.transpose(tp[g % 4][:, q, :], src[:, d * P:(d + 1) * P], S.ident[:, :])
                    mm.then_inc(turned, 1)

            if h_dram is not None:
                @block.sync
                def _(sp):
                    for t in range(T):
                        sp.wait_ge(xn_ready, t + 1)
                        sp.dma_start(h_dram[t * P:(t + 1) * P, :], xn[t % 2][:]).then_inc(stored[t % 2], 16)
                    for u in range(min(2, T)):
                        sp.wait_ge(stored[u], 16 * ((T - u + 1) // 2))


def residual_norm(nc, name, S, y, x_tiles, gain_row):
    T = len(x_tiles)
    with Stage(nc, name) as st:
        row = st.sb("row", [P, D])
        junk = st.sb("squares", [P, D])
        ss = st.sb("sum_sq", [P, T])
        rms = st.sb("rms", [P, T])
        rstd = st.sb("rstd", [P, T])
        row_loaded, rms_ready = st.sem("row_loaded"), st.sem("rms_ready")
        act_step, dve_step = st.sem("act_step"), st.sem("dve_step")
        with st.block() as block:
            @block.sync
            def _(sp):
                sp.dma_start(row[:], gain_row.partition_broadcast(P)).then_inc(row_loaded, 16)

            @block.scalar
            def _(act):
                steps = Chain(act, act_step)
                for t in range(T):
                    steps.step(nc.scalar.activation(junk[:], y[:, t, :], ACT.Square, accum_out=ss[:, t:t + 1]))
                steps.wait()
                nc.scalar.activation(rms[:], ss[:], ACT.Sqrt, scale=1.0 / D, bias=S.eps6[:, 0:1]).then_inc(rms_ready, 1)

            @block.vector
            def _(dve):
                steps = Chain(dve, dve_step)
                dve.wait_ge(rms_ready, 1)
                steps.step(nc.vector.reciprocal(rstd[:], rms[:]))
                dve.wait_ge(row_loaded, 16)
                for t in range(T):
                    steps.mark(nc.vector.scalar_tensor_tensor(out=y[:, t, :], in0=y[:, t, :], scalar=rstd[:, t:t + 1],
                                                              in1=row[:], op0=ALU.mult, op1=ALU.mult))
                steps.wait()
                for t in range(T):
                    steps.mark(nc.vector.tensor_tensor(x_tiles[t], x_tiles[t], y[:, t, :], ALU.add))
                steps.wait()


class Shared:
    pass


def constants():
    i = np.arange(P)
    f = np.float32
    out = {"ident": np.eye(P, dtype=f), "ones": np.ones((P, P), f)}
    out["eps"] = np.tile(np.array([[1e-6, 1e-5, 64e-5, 1e-12]], f), (P, 1))
    return out


HD = 64


def attention(nc, name, S, qT, kT, v, out, heads, dh, scale, back, group=1, slope0=None, rel=None, extra=None,
              causal=None, sinks=None):
    W = 4 * P
    with Stage(nc, name) as st:
        q = [st.sb(f"q{u}", [dh, SEQ]) for u in range(2)]
        k = [st.sb(f"k{u}", [dh, SEQ]) for u in range(2)]
        vv = [st.sb(f"v{u}", [P, NT, HD]) for u in range(2)]
        o = [st.sb(f"o{u}", [P, NT, HD]) for u in range(2)]
        sink = [st.sb(f"sink{u}", [P, 1]) for u in range(2)]
        relt, extrat = st.sb("rel", [P, W]), st.sb("extra", [P, W])
        bias = [st.sb(f"bias{u}", [P, W]) for u in range(2 if causal is None else 1)] * (1 if causal is None else 2)
        slope = st.sb("slope", [P, 1])
        logits = [st.sb(f"logits{b}", [P, W]) for b in range(2)]
        probs = [st.sb(f"probs{b}", [P, W]) for b in range(2)]
        probsT = [st.sb(f"probsT{b}", [P, W]) for b in range(2)]
        top = [st.sb(f"top{b}", [P, 1]) for b in range(2)]
        negtop = [st.sb(f"negtop{b}", [P, 1]) for b in range(2)]
        den = [st.sb(f"den{b}", [P, 1]) for b in range(2)]
        sinkexp = [st.sb(f"sinkexp{b}", [P, 1]) for b in range(2)]
        rden = [st.sb(f"rden{b}", [P, 1]) for b in range(2)]
        ps_s = [st.ps(f"ps_s{b}", [P, W]) for b in range(2)]
        ps_t = [st.ps(f"ps_t{b}", [P, W]) for b in range(2)]
        ps_o = [st.ps(f"ps_o{b}", [P, W]) for b in range(2)]
        const_loaded = st.sem("const_loaded")
        head_loaded = [st.sem(f"head_loaded{u}") for u in range(2)]
        scores_ready, max_ready, probs_ready = st.sem("scores_ready"), st.sem("max_ready"), st.sem("probs_ready")
        turned, turned_copied = st.sem("turned"), st.sem("turned_copied")
        out_ready, out_scaled = st.sem("out_ready"), st.sem("out_scaled")
        stored = [st.sem(f"stored{u}") for u in range(2)]
        dve_step, unit_begun = st.sem("dve_step"), st.sem("unit_begun")
        loads = 4 if sinks is not None else 3
        AHEAD = 2

        units = [(u, b) for u in range(2) for b in range(NT)]

        def k0(b):
            return max(0, b - back)

        with st.block() as block:
            @block.sync
            def _(sp):
                if causal is not None:
                    sp.dma_start(bias[0][:], causal).then_inc(const_loaded, 16)
                else:
                    sp.dma_start(relt[:], rel).then_inc(const_loaded, 16)
                    sp.dma_start(extrat[:], extra).then_inc(const_loaded, 16)
                def load(h, u):
                    hk = h // group if group > 1 else h
                    sp.dma_start(q[u][:], qT[bass.ds(h, 1), :, :].rearrange("a d t -> (a d) t")).then_inc(head_loaded[u], 16)
                    sp.dma_start(k[u][:], kT[bass.ds(hk, 1), :, :].rearrange("a d t -> (a d) t")).then_inc(head_loaded[u], 16)
                    sp.dma_start(vv[u][:], v.rearrange("(t p) c -> p t c", p=P)[:, :, bass.ds(hk * HD, HD)]).then_inc(head_loaded[u], 16)
                    if sinks is not None:
                        sp.dma_start(sink[u][:], sinks[bass.ds(h, 1)].partition_broadcast(P)).then_inc(head_loaded[u], 16)

                def store(h, u):
                    sp.wait_ge(out_scaled, h * NT + NT + AHEAD)
                    sp.dma_start(out.rearrange("(t p) c -> p t c", p=P)[:, :, bass.ds(h * HD, HD)], o[u][:]).then_inc(stored[u], 16)

                load(0, 0)
                load(1, 1)
                with sp.Fori(0, heads // 2 - 1) as i:
                    for u in range(2):
                        store(2 * i + u, u)
                        sp.wait_ge(stored[u], 16 * i + 16)
                        load(2 * i + 2 + u, u)
                for u in range(2):
                    store(heads - 2 + u, u)
                    sp.wait_ge(stored[u], 16 * (heads // 2))

            @block.tensor
            def _(pe):
                pe.sem_inc(scores_ready, AHEAD)
                pe.sem_inc(turned, AHEAD)
                pe.sem_inc(out_ready, AHEAD)

                def scores(n, u, b):
                    pe.wait_ge(max_ready, n - 1 + AHEAD)
                    w = (b + 1 - k0(b)) * P
                    nc.tensor.matmul(ps_s[b % 2][:, 0:w], q[u][:, b * P:(b + 1) * P], k[u][:, k0(b) * P:(b + 1) * P],
                                     start=True, stop=True).then_inc(scores_ready, 1)

                def turn(n, u, b):
                    pe.wait_ge(probs_ready, n + 1 + AHEAD)
                    pe.wait_ge(turned_copied, n - 1 + AHEAD)
                    for j in range(b + 1 - k0(b)):
                        mm = nc.tensor.transpose(ps_t[b % 2][:, j * P:(j + 1) * P], probs[b % 2][:, j * P:(j + 1) * P], S.ident[:, :])
                    mm.then_inc(turned, 1)

                def weigh(n, u, b):
                    pe.wait_ge(turned_copied, n + 1 + AHEAD)
                    pe.wait_ge(out_scaled, n - 1 + AHEAD)
                    m = b + 1 - k0(b)
                    for j in range(m):
                        mm = nc.tensor.matmul(ps_o[b % 2][:, 0:2 * HD].rearrange("p (o n) -> p o n", o=2), probsT[b % 2][:, j * P:(j + 1) * P], twice(vv[u][:, k0(b) + j, :]),
                                              start=(j == 0), stop=(j == m - 1))
                    mm.then_inc(out_ready, 1)

                with pe.Fori(0, heads // 2) as i:
                    def ahead(x):
                        if x < len(units):
                            u, b = units[x]
                            if b == 0:
                                pe.wait_ge(head_loaded[u], 16 * loads * i + 16 * loads)
                            scores(i * len(units) + x, u, b)

                    ahead(0)
                    ahead(1)
                    for x, (u, b) in enumerate(units):
                        turn(i * len(units) + x, u, b)
                        ahead(x + 2)
                        weigh(i * len(units) + x, u, b)

            @block.scalar
            def _(act):
                act.sem_inc(probs_ready, AHEAD)
                with act.Fori(0, heads // 2) as i:
                    for u in range(2):
                        for b in range(NT):
                            n = (2 * i + u) * NT + b
                            w = (b + 1 - k0(b)) * P
                            act.wait_ge(max_ready, n + 1 + AHEAD)
                            act.wait_ge(turned, n - 1 + AHEAD)
                            if sinks is not None:
                                act.activation(sinkexp[b % 2][:], sink[u][:], ACT.Exp, bias=negtop[b % 2][:])
                            act.activation(probs[b % 2][:, 0:w], logits[b % 2][:, 0:w], ACT.Exp, bias=negtop[b % 2][:],
                                           accum_out=den[b % 2][:]).then_inc(probs_ready, 1)

            @block.vector
            def _(dve):
                dve.sem_inc(max_ready, AHEAD)
                dve.sem_inc(turned_copied, AHEAD)
                dve.sem_inc(out_scaled, AHEAD)
                dve.wait_ge(const_loaded, 16 if causal is not None else 32)
                per = len(units) * (4 if sinks is not None else 2) + (4 if causal is None else 0)
                if causal is None:
                    nc.vector.memset(slope[:], slope0).then_inc(dve_step, 1)
                start = 1 if causal is None else 0
                if start:
                    dve.wait_ge(dve_step, 1)

                def biggest(n, u, b, steps):
                    w = (b + 1 - k0(b)) * P
                    dve.wait_ge(scores_ready, n + 1 + AHEAD)
                    dve.wait_ge(probs_ready, n - 1 + AHEAD)
                    dve.sem_inc(unit_begun, 1)
                    steps.step(nc.vector.tensor_tensor_reduce(out=logits[b % 2][:, 0:w], in0=ps_s[b % 2][:, 0:w], in1=bias[u][:, W - w:W],
                                                              scale=scale, scalar=-3e38, op0=ALU.add, op1=ALU.max,
                                                              accum_out=top[b % 2][:]))
                    if sinks is not None:
                        steps.step(nc.vector.tensor_tensor(top[b % 2][:], top[b % 2][:], sink[u][:], ALU.max))
                    nc.vector.tensor_scalar(negtop[b % 2][:], top[b % 2][:], -1.0, None, ALU.mult).then_inc(max_ready, 1)

                def copy_turned(n, b, steps):
                    w = (b + 1 - k0(b)) * P
                    dve.wait_ge(turned, n + 1 + AHEAD)
                    dve.wait_ge(out_ready, n - 1 + AHEAD)
                    nc.vector.tensor_copy(probsT[b % 2][:, 0:w], ps_t[b % 2][:, 0:w]).then_inc(turned_copied, 1)
                    if sinks is not None:
                        steps.step(nc.vector.tensor_tensor(den[b % 2][:], den[b % 2][:], sinkexp[b % 2][:], ALU.add))
                    dve.wait_ge(out_scaled, n - 1 + AHEAD)
                    steps.step(nc.vector.reciprocal(rden[b % 2][:], den[b % 2][:]))

                def finish(n, u, b):
                    dve.wait_ge(out_ready, n + 1 + AHEAD)
                    nc.vector.tensor_scalar(o[u][:, b, :], ps_o[b % 2][:, 0:HD], rden[b % 2][:, 0:1], None, ALU.mult).then_inc(out_scaled, 1)

                with dve.Fori(0, heads // 2) as i:
                    steps = Chain(dve, dve_step, i * per + start)
                    if causal is None:
                        for u in range(2):
                            steps.step(nc.vector.scalar_tensor_tensor(out=bias[u][:], in0=relt[:], scalar=slope[:, 0:1], in1=extrat[:],
                                                                      op0=ALU.mult, op1=ALU.add))
                            steps.step(nc.vector.tensor_scalar(slope[:], slope[:], 0.5, None, ALU.mult))
                    for x, (u, b) in enumerate(units):
                        n = i * len(units) + x
                        for y in ((0, 1) if x == 0 else (x + 1,)):
                            if y < len(units):
                                if units[y][1] == 0:
                                    dve.wait_ge(head_loaded[units[y][0]], 16 * loads * i + 16 * loads)
                                biggest(i * len(units) + y, *units[y], steps)
                        copy_turned(n, b, steps)
                        if x >= 1:
                            finish(n - 1, *units[x - 1])
                    finish(i * len(units) + len(units) - 1, *units[-1])
                    assert steps.n == per


A_PATTERNS = ((128, 1), (512, 4), (2048, 16))
BIG = 1e30


def attention_tables():
    delta = (np.arange(P)[:, None] + 3 * P - np.arange(4 * P)[None, :]).astype(np.int64)
    count = sum(((delta >= 0) & (delta <= w) & (delta % d == 0)).astype(np.int64) for w, d in A_PATTERNS)
    seen = count > 0
    swa = (delta >= 0) & (delta <= 127)
    f = np.float32
    return {
        "dil_rel": np.where(seen, delta, BIG).astype(f),
        "dil_extra": np.where(seen, np.log(np.maximum(count, 1)) * 8.0, 0.0).astype(f),
        "swa_rel": np.where(swa, delta, BIG).astype(f),
        "zero_extra": np.zeros((P, 4 * P), f),
        "causal": np.where(delta >= 0, 0.0, -BIG).astype(f),
    }

B_HEADS, B_DK, B_DV, B_CHUNK = 4, 64, 128, 64


def gla_decay(nc, name, S, z, log_a):
    width = z.shape[1] * z.shape[2]
    with Stage(nc, name) as st:
        t1, t2 = st.sb("t1", [P, width]), st.sb("t2", [P, width])
        act_step, dve_step, stored = st.sem("act_step"), st.sem("dve_step"), st.sem("stored")
        zf = z[:].rearrange("p t c -> p (t c)")
        with st.block() as block:
            @block.scalar
            def _(act):
                steps = Chain(act, act_step)
                steps.step(nc.scalar.activation(t1[:], zf, ACT.Abs))
                steps.step(nc.scalar.activation(t1[:], t1[:], ACT.Exp, scale=-1.0))
                steps.step(nc.scalar.activation(t1[:], t1[:], ACT.Ln, bias=S.ones[:, 0:1]))

            @block.vector
            def _(dve):
                steps = Chain(dve, dve_step)
                steps.step(nc.vector.tensor_scalar(t2[:], zf, 0.0, 1.0 / 16, ALU.min, ALU.mult))
                dve.wait_ge(act_step, 3)
                steps.step(nc.vector.scalar_tensor_tensor(out=t1[:], in0=t1[:], scalar=-1.0 / 16, in1=t2[:], op0=ALU.mult, op1=ALU.add))

            @block.sync
            def _(sp):
                sp.wait_ge(dve_step, 2)
                sp.dma_start(log_a.rearrange("(t p) c -> p t c", p=P), t1[:].rearrange("p (t c) -> p t c", t=NT)).then_inc(stored, 16)
                sp.wait_ge(stored, 16)


def gla(nc, name, S, qT, kT, v, r, log_a, tri, norm_row, out, col0):
    NC = SEQ // B_CHUNK
    with Stage(nc, name) as st:
        trit, normt = st.sb("tri", [P, P]), st.sb("norm", [P, B_DV])
        qs, ks = ([st.sb(f"{n}{u}", [B_DK, SEQ]) for u in range(2)] for n in "qk")
        vts, rts = ([st.sb(f"{n}{u}", [P, NT, B_DV]) for u in range(2)] for n in "vr")
        las = [st.sb(f"log_a{u}", [P, NT, B_DK]) for u in range(2)]
        cum, mid, last = st.sb("cum", [B_DK, SEQ]), st.sb("mid", [B_DK, SEQ]), st.sb("last", [B_DK, SEQ])
        e_q, e_k, e_b, e_l = (st.sb(f"e_{x}", [B_DK, SEQ]) for x in "qkbl")
        decay = st.sb("decay", [B_DK, NC])
        att, klT = st.sb("att", [P, NT, P]), st.sb("klT", [P, NT, B_DK])
        state = st.sb("state", [B_DK, NC, B_DV])
        o, gate = st.sb("o", [P, NT, B_DV]), st.sb("gate", [P, NT, B_DV])
        junk, ss, rms, rstd = st.sb("squares", [P, B_DV]), st.sb("sum_sq", [P, NT]), st.sb("rms", [P, NT]), st.sb("rstd", [P, NT])
        p_cum = st.ps("p_cum", [B_DK, SEQ])
        p_att = st.ps("p_att", [P, NT, P])
        p_kl = st.ps("p_kl", [P, NT, B_DK])
        p_ds = [st.ps(f"p_ds{b}", [B_DK, 4, B_DV]) for b in range(2)]
        p_o = st.ps("p_o", [P, NT, B_DV])
        const_loaded, loaded, stored = st.sem("const_loaded"), [st.sem(f"loaded{u}") for u in range(2)], st.sem("stored")
        o_free, inputs_free = st.sem("o_free"), st.sem("inputs_free")
        cum_ready, turned_ready, states_fed, out_ready = st.sem("cum_ready"), st.sem("turned_ready"), st.sem("states_fed"), st.sem("out_ready")
        act_step, dve_step, pe_passed = st.sem("act_step"), st.sem("dve_step"), st.sem("pe_passed")
        A, V = 12, 20

        def chunks(x):
            return x[:].rearrange("d (n c) -> d n c", c=B_CHUNK)

        with st.block() as block:
            @block.sync
            def _(sp):
                sp.dma_start(trit[:], tri).then_inc(const_loaded, 16)
                sp.dma_start(normt[:], norm_row.partition_broadcast(P)).then_inc(const_loaded, 16)

                def load(h, u):
                    for dst, src in ((qs, qT), (ks, kT)):
                        sp.dma_start(dst[u][:], src[bass.ds(h, 1), :, :].rearrange("a d t -> (a d) t")).then_inc(loaded[u], 16)
                    for dst, src, w in ((vts, v, B_DV), (rts, r, B_DV), (las, log_a, B_DK)):
                        sp.dma_start(dst[u][:], src.rearrange("(t p) c -> p t c", p=P)[:, :, bass.ds(h * w, w)]).then_inc(loaded[u], 16)

                load(0, 0)
                load(1, 1)
                sp.sem_inc(o_free, 1)

                def finish(h, u):
                    sp.wait_ge(dve_step, h * V + V)
                    sp.sem_inc(inputs_free, 1)
                    sp.dma_start(out.rearrange("(t p) c -> p t c", p=P)[:, :, bass.ds(h * B_DV + col0, B_DV)], o[:]).then_inc(stored, 16)

                def release(h):
                    sp.wait_ge(stored, 16 * h + 16)
                    sp.sem_inc(o_free, 1)

                with sp.Fori(0, B_HEADS // 2 - 1) as i:
                    for u in range(2):
                        finish(2 * i + u, u)
                        load(2 * i + u + 2, u)
                        release(2 * i + u)
                for u in range(2):
                    finish(B_HEADS - 2 + u, u)
                    release(B_HEADS - 2 + u)

            @block.tensor
            def _(pe):
                pe.wait_ge(const_loaded, 32)
                with pe.Fori(0, B_HEADS // 2) as i:
                    for u in range(2):
                        h = 2 * i + u
                        q, k, vt, rt, la = qs[u], ks[u], vts[u], rts[u], las[u]
                        pe.wait_ge(loaded[u], i * 80 + 80)
                        for t in range(NT):
                            mm = nc.tensor.matmul(p_cum[:, t * P:(t + 1) * P], la[:, t, :], trit[:], start=True, stop=True)
                        mm.then_inc(cum_ready, 1)
                        pe.wait_ge(dve_step, h * V + 7)
                        for t in range(NT):
                            c = slice(t * P, (t + 1) * P)
                            nc.tensor.matmul(p_att[:, t, :], e_k[:, c], e_q[:, c], start=True, stop=True)
                            mm = nc.tensor.transpose(p_kl[:, t, :], e_l[:, c], S.ident[0:B_DK, 0:B_DK])
                        mm.then_inc(turned_ready, 1)
                        pe.wait_ge(act_step, h * A + 6)
                        pe.sem_inc(pe_passed, 1)
                        for n in range(NC):
                            s = slice(B_CHUNK * (n % 2), B_CHUNK * (n % 2) + B_CHUNK)
                            mm = nc.tensor.matmul(p_ds[n % 2][:, n // 2, :], klT[s, n // 2, :], vt[s, n // 2, :], start=True, stop=True)
                        mm.then_inc(states_fed, 1)
                        pe.wait_ge(dve_step, h * V + 16)
                        for t in range(NT):
                            nc.tensor.matmul(p_o[:, t, :], att[:, t, :], vt[:, t, :], start=True, stop=False, skip_group_check=True)
                            for n in (2 * t, 2 * t + 1):
                                s = slice(B_CHUNK * (n % 2), B_CHUNK * (n % 2) + B_CHUNK)
                                mm = nc.tensor.matmul(p_o[s, t, :], e_b[:, n * B_CHUNK:(n + 1) * B_CHUNK], state[:, n, :],
                                                      start=False, stop=(n % 2 == 1), skip_group_check=True)
                        mm.then_inc(out_ready, 1)

            @block.scalar
            def _(act):
                with act.Fori(0, B_HEADS // 2) as i:
                    for u in range(2):
                        h = 2 * i + u
                        q, k, vt, rt, la = qs[u], ks[u], vts[u], rts[u], las[u]
                        steps = Chain(act, act_step, h * A)
                        act.wait_ge(dve_step, h * V + 3)
                        steps.mark(nc.scalar.activation(e_q[:], mid[:], ACT.Exp))
                        steps.mark(nc.scalar.activation(e_k[:], mid[:], ACT.Exp, scale=-1.0))
                        steps.mark(nc.scalar.activation(e_b[:], cum[:], ACT.Exp))
                        steps.mark(nc.scalar.activation(e_l[:], last[:], ACT.Exp))
                        steps.mark(nc.scalar.activation(decay[:], chunks(cum)[:, :, B_CHUNK - 1], ACT.Exp))
                        act.wait_ge(turned_ready, h + 1)
                        steps.step(nc.scalar.activation(klT[:], p_kl[:], ACT.Copy))
                        act.wait_ge(loaded[u], i * 80 + 80)
                        steps.mark(nc.scalar.activation(gate[:], rt[:], ACT.Silu))
                        act.wait_ge(out_ready, h + 1)
                        for t in range(NT):
                            steps.step(nc.scalar.activation(junk[:], p_o[:, t, :], ACT.Square, accum_out=ss[:, t:t + 1]))
                        steps.step(nc.scalar.activation(rms[:], ss[:], ACT.Sqrt, scale=1.0 / B_DV, bias=S.eps6[:, 0:1]))
                        assert steps.n == A

            @block.vector
            def _(dve):
                dve.wait_ge(const_loaded, 32)
                with dve.Fori(0, B_HEADS // 2) as i:
                    for u in range(2):
                        h = 2 * i + u
                        q, k, vt, rt, la = qs[u], ks[u], vts[u], rts[u], las[u]
                        steps = Chain(dve, dve_step, h * V)
                        dve.wait_ge(cum_ready, h + 1)
                        steps.step(nc.vector.tensor_copy(cum[:], p_cum[:]))
                        c3 = chunks(cum)
                        steps.mark(nc.vector.tensor_tensor(chunks(mid), c3, c3[:, :, B_CHUNK // 2 - 1:B_CHUNK // 2].broadcast_to([B_DK, NC, B_CHUNK]), ALU.subtract))
                        steps.step(nc.vector.tensor_tensor(chunks(last), c3[:, :, B_CHUNK - 1:B_CHUNK].broadcast_to([B_DK, NC, B_CHUNK]), c3, ALU.subtract))
                        dve.wait_ge(act_step, h * A + 5)
                        for e, x, scale in ((e_q, q, B_DK ** -0.5), (e_k, k, 1.0), (e_l, k, 1.0), (e_b, q, B_DK ** -0.5)):
                            steps.mark(nc.vector.scalar_tensor_tensor(out=e[:], in0=e[:], scalar=scale, in1=x[:], op0=ALU.mult, op1=ALU.mult))
                        steps.wait()
                        dve.wait_ge(turned_ready, h + 1)
                        steps.mark(nc.vector.tensor_tensor(att[:], p_att[:], trit[:].rearrange("s (a c) -> s a c", a=1).broadcast_to([P, NT, P]), ALU.mult))
                        steps.step(nc.vector.memset(state[:, 0, :], 0.0))
                        dve.wait_ge(states_fed, h + 1)
                        for n in range(NC - 1):
                            steps.step(nc.vector.scalar_tensor_tensor(out=state[:, n + 1, :], in0=state[:, n, :], scalar=decay[:, n:n + 1],
                                                                      in1=p_ds[n % 2][:, n // 2, :], op0=ALU.mult, op1=ALU.add))
                        dve.wait_ge(act_step, h * A + 12)
                        dve.wait_ge(o_free, h + 1)
                        steps.step(nc.vector.reciprocal(rstd[:], rms[:]))
                        for t in range(NT - 1):
                            nc.vector.scalar_tensor_tensor(out=o[:, t, :], in0=p_o[:, t, :], scalar=rstd[:, t:t + 1], in1=normt[:], op0=ALU.mult, op1=ALU.mult)
                        t = NT - 1
                        steps.step(nc.vector.scalar_tensor_tensor(out=o[:, t, :], in0=p_o[:, t, :], scalar=rstd[:, t:t + 1], in1=normt[:], op0=ALU.mult, op1=ALU.mult))
                        steps.mark(nc.vector.tensor_tensor(o[:], o[:], gate[:], ALU.mult))
                        while steps.n < V:
                            steps.mark(nc.vector.nop())
                        assert steps.n == V, steps.n


def gla_tables():
    i = np.arange(P)
    tri = (i[:, None] <= i[None, :]) & (i[:, None] // B_CHUNK == i[None, :] // B_CHUNK)
    return {"gla_tri": tri.astype(np.float32)}


D_FF = 2816
FT = D_FF // P


def swiglu_up(nc, name, h_hi, h_lo, w_gate_up, guT, cond, ada_w, ada, spare):
    AC = ada_w.shape[1] // (FT + 2)
    assert AC * (FT + 2) == ada_w.shape[1]
    with Stage(nc, name) as st:
        w = st.sb("w", [P, 2, KD, P])
        w_hi, w_lo = ([st.sb(f"w_{n}{u}", [P, 2, KD, P], F32R) for u in range(2)] for n in ("hi", "lo"))
        sg = [st.sb(f"gate{u}", [P, SEQ]) for u in range(2)]
        p_g = [st.ps(f"p_g{u}", [P, SEQ]) for u in range(2)]
        p_u = [st.ps(f"p_u{u}", [P, SEQ]) for u in range(2)]
        loaded = st.sem("loaded")
        hi_made, lo_made = st.sem("hi_made"), st.sem("lo_made")
        gate_ready, up_ready, gated, multiplied = st.sem("gate_ready"), st.sem("up_ready"), st.sem("gated"), st.sem("multiplied")
        ada_buf = [spare[:, :, u * AC:(u + 1) * AC] for u in range(2)]
        ada_loaded = [st.sem(f"ada_loaded{u}") for u in range(2)]
        ada_step, ada_done = st.sem("ada_step"), st.sem("ada_done")
        AHEAD = 2
        TERMS = 2 * KD
        with st.block() as block:
            @block.sync
            def _(sp):
                def load(s):
                    sp.dma_start(w[:], w_gate_up[bass.ds(s, 1)].rearrange("a p g k f -> (a p) g k f")).then_inc(loaded, 16)

                def load_ada(c, u):
                    sp.dma_start(ada_buf[u], ada_w[:, bass.ds(c * AC, AC)].rearrange("(k p) n -> p k n", p=P)).then_inc(ada_loaded[u], 16)

                def next_loads(s, u, last=False):
                    sp.wait_ge(lo_made, 2 * s + 2)
                    if not last:
                        load(s + 1)
                    sp.wait_ge(ada_done, s + 1)
                    load_ada(s + 2, u)

                load(0)
                load_ada(0, 0)
                load_ada(1, 1)
                with sp.Fori(0, FT // 2 - 1) as i:
                    for u in range(2):
                        next_loads(2 * i + u, u)
                next_loads(FT - 2, 0)
                next_loads(FT - 1, 1, True)

            @block.tensor
            def _(pe):
                pe.sem_inc(up_ready, AHEAD)
                with pe.Fori(0, FT // 2) as i:
                    for u in range(2):
                        s = 2 * i + u
                        pe.wait_ge(multiplied, s - 1 + AHEAD)
                        for g, (p, ready) in enumerate(((p_g[u], gate_ready), (p_u[u], up_ready))):
                            pe.wait_ge(lo_made, 2 * s + g + 1)
                            for k in range(KD):
                                nc.tensor.matmul(p[:], w_hi[u][:, g, k, :], h_hi[:, k, :], start=(k == 0), stop=False)
                                nc.tensor.matmul(p[:], w_hi[u][:, g, k, :], h_lo[:, k, :], start=False, stop=False)
                                mm = nc.tensor.matmul(p[:], w_lo[u][:, g, k, :], h_hi[:, k, :], start=False, stop=(k == KD - 1))
                            mm.then_inc(ready, 1)

            @block.gpsimd
            def _(pool):
                with pool.Fori(0, FT // 2) as i:
                    for u in range(2):
                        for g in range(2):
                            pool.wait_ge(hi_made, 4 * i + 2 * u + g + 1)
                            nc.gpsimd.tensor_tensor(w_lo[u][:, g], w[:, g], w_hi[u][:, g], ALU.subtract).then_inc(lo_made, 1)

            @block.scalar
            def _(act):
                def split(s, u):
                    act.wait_ge(loaded, 16 * s + 16)
                    act.wait_ge(up_ready, s - 1 + AHEAD)
                    for g in range(2):
                        nc.scalar.activation(w_hi[u][:, g], w[:, g], ACT.Copy).then_inc(hi_made, 1)

                def gate(s, u):
                    act.wait_ge(gate_ready, s + 1)
                    act.wait_ge(multiplied, s - 1 + AHEAD)
                    nc.scalar.activation(sg[u][:], p_g[u][:], ACT.Silu).then_inc(gated, 1)

                split(0, 0)
                with act.Fori(0, FT // 2 - 1) as i:
                    for u in range(2):
                        split(2 * i + u + 1, 1 - u)
                        gate(2 * i + u, u)
                split(FT - 1, 1)
                gate(FT - 2, 0)
                gate(FT - 1, 1)

            @block.vector
            def _(dve):
                dve.sem_inc(multiplied, AHEAD)

                def ada_terms(c, u, k0):
                    dve.wait_ge(ada_loaded[u], 16 * k0 + 16)
                    for n in range(TERMS):
                        k, which = n // 2, n % 2
                        dst, src = ada[:, which, bass.ds(c * AC, AC)], ada_buf[u][:, k, :]
                        if k:
                            dve.wait_ge(ada_step, c * TERMS + n - 1)
                            ins = nc.vector.scalar_tensor_tensor(out=dst, in0=src, scalar=cond[:, k, which:which + 1], in1=dst, op0=ALU.mult, op1=ALU.add)
                        else:
                            ins = nc.vector.tensor_scalar(dst, src, cond[:, k, which:which + 1], None, ALU.mult)
                        ins.then_inc(ada_step, 1)
                    dve.wait_ge(ada_step, c * TERMS + TERMS)
                    dve.sem_inc(ada_done, 1)

                for u in range(2):
                    ada_terms(u, u, 0)
                with dve.Fori(0, FT // 2) as i:
                    for u in range(2):
                        s = 2 * i + u
                        dve.wait_ge(gated, s + 1)
                        dve.wait_ge(up_ready, s + 1 + AHEAD)
                        nc.vector.tensor_tensor(guT[:, bass.ds(s, 1), :].rearrange("p a t -> p (a t)"), sg[u][:], p_u[u][:], ALU.mult).then_inc(multiplied, 1)
                        ada_terms(s + 2, u, i + 1)


D_HEADS, D_NOPE, D_ROPE = 8, 64, 32


def rope_tables():
    half = D_ROPE // 2
    freqs = (np.float32(10000.0) ** (-np.arange(half, dtype=np.float32) / np.float32(half))).astype(np.float32)
    ang = np.arange(SEQ, dtype=np.float32)[:, None] * freqs[None, :]
    def lay(x):
        return np.ascontiguousarray(x.astype(np.float32).reshape(NT, P, half).transpose(1, 0, 2))
    return {"cos": lay(np.cos(ang)), "sin": lay(np.sin(ang))}


def mla_heads(nc, name, S, q, kv, k_rope, cos, sin, qT_d, kT_d, v_d):
    half = D_ROPE // 2
    HQ = D_NOPE + D_ROPE
    with Stage(nc, name) as st:
        ct, sn = st.sb("cos", [P, NT, half]), st.sb("sin", [P, NT, half])
        tmp = [st.sb(f"tmp{n}", [P, NT, D_HEADS, half]) for n in range(4)]
        kp = st.sb("k_pe", [P, NT, D_ROPE])
        kk = st.sb("keys", [P, NT, D_HEADS, HQ])
        outT = [st.sb(f"outT{b}", [HQ, SEQ]) for b in range(4)]
        tp = [st.ps(f"tp{b}", [HQ, SEQ]) for b in range(4)]
        loaded, dve_step, act_step, pool_step = st.sem("loaded"), st.sem("dve_step"), st.sem("act_step"), st.sem("pool_step")
        turned = st.sem("turned")
        emptied = [st.sem("act_emptied"), st.sem("dve_emptied")]
        stored, v_stored = [st.sem(f"stored{b}") for b in range(4)], st.sem("v_stored")
        q4 = q[:].rearrange("p t (h c) -> p t h c", h=D_HEADS)
        kv4 = kv[:].rearrange("p t (h c) -> p t h c", h=D_HEADS)
        QS = 4 * 6
        G = 2 * D_HEADS
        ROTATED = QS + 6 + NT

        with st.block() as block:
            @block.sync
            def _(sp):
                sp.dma_start(ct[:], cos).then_inc(loaded, 16)
                sp.dma_start(sn[:], sin).then_inc(loaded, 16)
                for t in range(NT):
                    sp.dma_start(v_d[t * P:(t + 1) * P, :].rearrange("p (h c) -> p h c", h=D_HEADS), kv4[:, t, :, D_NOPE:2 * D_NOPE]).then_inc(v_stored, 16)
                for g in range(G):
                    sp.wait_ge(emptied[g % 2], g // 2 + 1)
                    dst = qT_d if g < D_HEADS else kT_d
                    sp.dma_start(dst[g % D_HEADS], outT[g % 4][:]).then_inc(stored[g % 4], 16)
                for b in range(4):
                    sp.wait_ge(stored[b], 16 * (G // 4))
                sp.wait_ge(v_stored, 16 * NT)

            @block.gpsimd
            def _(pool):
                for t in range(NT):
                    nc.gpsimd.tensor_copy(kk[:, t, :, 0:D_NOPE], kv4[:, t, :, 0:D_NOPE]).then_inc(pool_step, 1)

            def empty(which, engine, eng, g):
                eng.wait_ge(turned, g + 1)
                if g >= 4:
                    eng.wait_ge(stored[g % 4], 16 * (g // 4))
                if which == "act":
                    engine.activation(outT[g % 4][:], tp[g % 4][:], ACT.Copy).then_inc(emptied[0], 1)
                else:
                    engine.tensor_copy(outT[g % 4][:], tp[g % 4][:]).then_inc(emptied[1], 1)

            @block.vector
            def _(dve):
                steps = Chain(dve, dve_step)
                dve.wait_ge(loaded, 32)

                for t in range(NT):
                    x1, x2 = q4[:, t, :, D_NOPE:D_NOPE + half], q4[:, t, :, D_NOPE + half:HQ]
                    c = ct[:, t:t + 1, :].broadcast_to([P, D_HEADS, half])
                    s = sn[:, t:t + 1, :].broadcast_to([P, D_HEADS, half])
                    for n, (x, y) in enumerate(((x1, c), (x2, s), (x2, c), (x1, s))):
                        steps.mark(nc.vector.tensor_tensor(tmp[n][:, t], x, y, ALU.mult))
                    steps.wait()
                    steps.mark(nc.vector.tensor_tensor(x1, tmp[0][:, t], tmp[1][:, t], ALU.subtract))
                    steps.mark(nc.vector.tensor_tensor(x2, tmp[2][:, t], tmp[3][:, t], ALU.add))
                steps.wait()
                x1, x2 = k_rope[:, :, 0:half], k_rope[:, :, half:D_ROPE]
                for n, (x, y) in enumerate(((x1, ct), (x2, sn), (x2, ct), (x1, sn))):
                    steps.mark(nc.vector.tensor_tensor(tmp[n][:, :, 0, :], x, y[:], ALU.mult))
                steps.wait()
                steps.mark(nc.vector.tensor_tensor(kp[:, :, 0:half], tmp[0][:, :, 0, :], tmp[1][:, :, 0, :], ALU.subtract))
                steps.step(nc.vector.tensor_tensor(kp[:, :, half:D_ROPE], tmp[2][:, :, 0, :], tmp[3][:, :, 0, :], ALU.add))
                for t in range(NT):
                    steps.mark(nc.vector.tensor_copy(kk[:, t, :, D_NOPE:HQ], kp[:, t:t + 1, :].broadcast_to([P, D_HEADS, D_ROPE])))
                assert steps.n == ROTATED
                for g in range(1, G, 2):
                    empty("dve", nc.vector, dve, g)

            @block.scalar
            def _(act):
                for g in range(0, G, 2):
                    empty("act", nc.scalar, act, g)

            @block.tensor
            def _(pe):
                pe.wait_ge(dve_step, ROTATED)
                pe.wait_ge(pool_step, NT)
                for g in range(G):
                    if g >= 4:
                        pe.wait_ge(emptied[g % 2], (g - 4) // 2 + 1)
                    src = q4 if g < D_HEADS else kk
                    for t in range(NT):
                        mm = nc.tensor.transpose(tp[g % 4][:, t * P:(t + 1) * P], src[:, t, g % D_HEADS, :], S.ident[:, :])
                    mm.then_inc(turned, 1)


def load_all(nc, name, pairs):
    with Stage(nc, name) as st:
        loaded = st.sem("loaded")
        with st.block() as block:
            @block.sync
            def _(sp):
                for dst, src in pairs:
                    sp.dma_start(dst, src).then_inc(loaded, 16)
                sp.wait_ge(loaded, 16 * len(pairs))


def gated_ffn(nc, name, S, x_tiles, hT, gcol, post_row, w_gate_up, w_down, ada_w, modulate):
    with ExitStack() as mem:
        guT = mem.enter_context(nc.sbuf_tensor(name + "_guT", [P, FT, SEQ], F32))
        with ExitStack() as mem2:
            h_hi, h_lo = (mem2.enter_context(nc.sbuf_tensor(f"{name}_h_{n}", [P, KD, SEQ], F32R)) for n in ("hi", "lo"))
            norm_transpose(nc, name + "n", S, x_tiles, h_hi, cols=[(gcol, None)] * NT, lo=h_lo)
            ada = mem2.enter_context(nc.sbuf_tensor(name + "_ada", [P, 2, N_MOD * D], F32))
            swiglu_up(nc, name + "u", h_hi, h_lo, w_gate_up, guT, S.cond, ada_w, ada, hT)
            modulate(ada)
        y = mem.enter_context(nc.sbuf_tensor(name + "_y", [P, NT, D], F32))
        project_split(nc, name + "d", guT, SEQ,
                      [dict(w=w_down[:, c * BANK:(c + 1) * BANK], mode="T", epi=copy_to(lambda j, n0, c=c: y[:, j, c * BANK:(c + 1) * BANK]))
                       for c in range(D // BANK)])
        residual_norm(nc, name + "r", S, y, x_tiles, post_row)


def mix_out(nc, name, S, x_tiles, hT, mixed, w_out, post_row):
    with ExitStack() as mem:
        m = mem.enter_context(nc.sbuf_tensor(name + "_m", [P, NT, D], F32))
        y = mem.enter_context(nc.sbuf_tensor(name + "_y", [P, NT, D], F32))
        load_all(nc, name + "l", [(m[:], mixed.rearrange("(t p) d -> p t d", p=P))])
        norm_transpose(nc, name + "t", S, [m[:, t, :] for t in range(NT)], hT, scaled=False)
        project_split(nc, name + "p", hT[:, :, 0:SEQ], SEQ,
                [dict(w=w_out[:, c * BANK:(c + 1) * BANK], mode="T", epi=copy_to(lambda j, n0, c=c: y[:, j, c * BANK:(c + 1) * BANK]))
                 for c in range(D // BANK)])
        residual_norm(nc, name + "r", S, y, x_tiles, post_row)


def dram(nc, name, shape, dt=F32):
    return nc.dram_tensor(name, shape, dt, kind="Internal").ap()


FIRST_COLS = (("norm_mix_pre", 2 * KD), ("norm_ffn_pre", 2 * KD), ("mla_q_norm", 3), ("mla_kv_norm", 2))


def first_block(nc, S, a, x_tiles, hT, mods):
    c = {}
    at = 0
    for n, w in FIRST_COLS:
        c[n] = S.first_cols[:, at:at + w]
        at += w
    mixed = dram(nc, "mixed0", [SEQ, D])
    norm_transpose(nc, "n0", S, x_tiles, hT, cols=[(c["norm_mix_pre"][:, 0:KD], None)] * NT)
    qk_a, v_a = dram(nc, "qk_a", [2 * 8, HD, SEQ]), dram(nc, "v_a", [SEQ, 512])
    qk_b = dram(nc, "qk_b", [2 * B_HEADS, B_DK, SEQ])
    v_b, r_b, log_a = dram(nc, "v_b", [SEQ, 512]), dram(nc, "r_b", [SEQ, 512]), dram(nc, "log_a", [SEQ, 256])
    w = a["ab_w_in"]
    with ExitStack() as mem:
        def sb(n, shape):
            return mem.enter_context(nc.sbuf_tensor(n, shape, F32))
        qka, qkb = sb("qka", [P, 8, SEQ]), sb("qkb", [P, 4, SEQ])
        vrt = sb("vrt", [P, 3, NT, 512])
        gT = sb("gT", [P, 1, SEQ])
        tok, two = "(t p) c -> p t c", "(j u) d t -> (u d) j t"
        jobs = [dict(w=w[:, 512 * n:512 * n + 512], mode="F", epi=copy_to(lambda j, n0, n=n: qka[:, 4 * n + j, :]),
                     stores=[(qk_a[8 * n:8 * n + 8].rearrange(two, u=2), qka[:, 4 * n:4 * n + 4])]) for n in range(2)]
        jobs += [dict(w=w[:, 1536:2048], mode="F", epi=copy_to(lambda j, n0: qkb[:, j, :]), stores=[(qk_b.rearrange(two, u=2), qkb[:])])]
        jobs += [dict(w=w[:, o:o + 512], mode="T", epi=copy_to(lambda j, n0, n=n: vrt[:, n, j, :]), stores=[(d.rearrange(tok, p=P), vrt[:, n])])
                 for n, (o, d) in enumerate(((1024, v_a), (2048, v_b), (2560, r_b)))]
        jobs += [dict(w=w[:, 3072:3088], mode="F", epi=copy_to(lambda j, n0: gT[0:16, 0, :]))]
        project_split(nc, "p0", hT[:, :, 0:SEQ], SEQ, jobs)
        z = sb("z", [P, NT, 256])
        brow = sb("b_gate_row", [1, 256])
        load_all(nc, "gl", [(brow[:], a["gla_b_gate"].rearrange("(o c) -> o c", o=1))])
        project(nc, "gz", gT, SEQ, [dict(w=a["gla_w_gate_up"], mode="T", bias=brow[:], epi=copy_to(lambda j, n0: z[:, j, :]))], const={"ones": S.ones})
        gla_decay(nc, "gd", S, z, log_a)
    attention(nc, "at0", S, qk_a[0:8], qk_a[8:16], v_a, mixed[:, 0:512], 8, HD, HD ** -0.5, 3,
              slope0=-4.0, rel=a["dil_rel"], extra=a["dil_extra"])
    gla(nc, "gla", S, qk_b[0:4], qk_b[4:8], v_b, r_b, log_a, a["gla_tri"], a["gla_norm"], mixed, 512)
    mix_out(nc, "mo0", S, x_tiles, hT, mixed, a["ab_w_out"], a["norm_mix_post"][0])
    gated_ffn(nc, "f0", S, x_tiles, hT, c["norm_ffn_pre"][:, 0:KD], a["norm_ffn_post"][0], a["ffn_w_gate_up"][0], a["ffn_w_down"][0],
              a["ada_w_2"][0], lambda ada: modulation(nc, "mod0", S, ada, S.ada_cols[:, 0], S.second_cols[:, 0:KD], S.mod_cols[0], mods[0]))
    norm_transpose(nc, "n1", S, x_tiles, hT, cols=[(c["norm_mix_pre"][:, KD:2 * KD], None)] * NT)
    qk_c, v_c = dram(nc, "qk_c", [10, HD, SEQ]), dram(nc, "v_c", [SEQ, 128])
    qT_d, kT_d, v_d = dram(nc, "qT_d", [8, 96, SEQ]), dram(nc, "kT_d", [8, 96, SEQ]), dram(nc, "v_d", [SEQ, 512])
    w = a["cd_w_in"]
    with ExitStack() as mem:
        def sb(n, shape):
            return mem.enter_context(nc.sbuf_tensor(n, shape, F32))
        qkc = sb("qkc", [P, 5, SEQ])
        vq, kvr = sb("vq", [P, NT, 512]), sb("kvr", [P, NT, 288])
        two = "(j u) d t -> (u d) j t"
        jobs = [dict(w=w[:, 0:512], mode="F", epi=copy_to(lambda j, n0: qkc[:, j, :]), stores=[(qk_c[0:8].rearrange(two, u=2), qkc[:, 0:4])]),
                dict(w=w[:, 512:640], mode="F", epi=copy_to(lambda j, n0: qkc[:, 4, :]), stores=[(qk_c[8:10].rearrange(two, u=2), qkc[:, 4:5])]),
                dict(w=w[:, 640:1152], mode="T", epi=copy_to(lambda j, n0: vq[:, j, :]), stores=[(v_c.rearrange("(t p) c -> p t c", p=P), vq[:, :, 0:128])]),
                dict(w=w[:, 1152:1440], mode="T", epi=copy_to(lambda j, n0: kvr[:, j, :]))]
        project_split(nc, "p1", hT[:, :, 0:SEQ], SEQ, jobs)
        cqT, ckvT = sb("cqT", [P, 3, SEQ]), sb("ckvT", [P, 2, SEQ])
        norm_transpose(nc, "nq", S, [vq[:, t, 128:512] for t in range(NT)], cqT, cols=[(c["mla_q_norm"], None)] * NT)
        norm_transpose(nc, "nkv", S, [kvr[:, t, 0:256] for t in range(NT)], ckvT, cols=[(c["mla_kv_norm"], None)] * NT)
        q, kv = sb("q_d", [P, NT, 768]), sb("kv_d", [P, NT, 1024])
        project(nc, "uq", cqT, SEQ, [dict(w=a["mla_w_uq"][:, 384 * n:384 * n + 384], mode="T",
                                          epi=copy_to(lambda j, n0, n=n: q[:, j, 384 * n:384 * n + 384])) for n in range(2)])
        project(nc, "ukv", ckvT, SEQ, [dict(w=a["mla_w_ukv"][:, 512 * n:512 * n + 512], mode="T",
                                            epi=copy_to(lambda j, n0, n=n: kv[:, j, 512 * n:512 * n + 512])) for n in range(2)])
        mla_heads(nc, "mh", S, q, kv, kvr[:, :, 256:288], a["cos"], a["sin"], qT_d, kT_d, v_d)
    attention(nc, "at1", S, qk_c[0:8], qk_c[8:10], v_c, mixed[:, 0:512], 8, HD, HD ** -0.5, 1, group=4,
              slope0=-4.0, rel=a["swa_rel"], extra=a["zero_extra"], sinks=a["swa_sinks"])
    attention(nc, "at2", S, qT_d, kT_d, v_d, mixed[:, 512:1024], 8, 96, 96 ** -0.5, 3, causal=a["causal"])
    mix_out(nc, "mo1", S, x_tiles, hT, mixed, a["cd_w_out"], a["norm_mix_post"][1])
    gated_ffn(nc, "f1", S, x_tiles, hT, c["norm_ffn_pre"][:, KD:2 * KD], a["norm_ffn_post"][1], a["ffn_w_gate_up"][1], a["ffn_w_down"][1],
              a["ada_w_2"][1], lambda ada: modulation(nc, "mod1", S, ada, S.ada_cols[:, 1], S.rw_norm1, S.mod_cols[1], mods[1]))


def columns(v):
    return np.ascontiguousarray(np.asarray(v).reshape(-1, P).T)


def first_layout(inp):
    out = {n: np.ascontiguousarray(inp[n][0]) for n in ("ab_w_in", "ab_w_out", "gla_w_gate_up", "gla_b_gate", "gla_norm", "cd_w_in", "cd_w_out",
                                                        "swa_sinks", "mla_w_uq", "mla_w_ukv")}
    for n in ("norm_mix_post", "norm_ffn_post", "ffn_w_down"):
        out[n] = np.ascontiguousarray(inp[n])
    gu = np.stack([inp["ffn_w_gate"], inp["ffn_w_up"]], 1)
    out["ffn_w_gate_up"] = np.ascontiguousarray(gu.reshape(2, 2, KD, P, FT, P).transpose(0, 4, 3, 1, 2, 5))
    out["x"] = np.ascontiguousarray(inp["x"][0])
    out["first_cols"] = np.concatenate([columns(inp[n]) for n, _ in FIRST_COLS], 1)
    return out


N_MOD = 6
W_GMLP = 2048
GROUPS = 16
E_GROUPS, E_PER, N_EXP, HID = 4, 8, 32, 512


def modulation(nc, name, S, ada, bias_cols, gcol, cols, mods):
    N = N_MOD * KD
    with Stage(nc, name) as st:
        sums = st.sb("sums", [P, 2, N])
        rows = [st.sb(f"rows{w}", [N, P]) for w in range(2)]
        p_sum = [st.ps(f"p_sum{w}", [P, N]) for w in range(2)]
        p_row = [st.ps(f"p_row{w}", [N, P]) for w in range(2)]
        summed, biased, turned, copied, dve_step, stored = (st.sem(n) for n in ("summed", "biased", "turned", "copied", "dve_step", "stored"))
        with st.block() as block:
            @block.tensor
            def _(pe):
                for w in range(2):
                    for k in range(N):
                        mm = nc.tensor.matmul(p_sum[w][:, k:k + 1], ada[:, w, k * P:(k + 1) * P], S.ones[:, 0:1], start=True, stop=True)
                    mm.then_inc(summed, 1)
                for w in range(2):
                    pe.wait_ge(biased, w + 1)
                    nc.tensor.transpose(p_row[w][:], sums[:, w, :], S.ident[:]).then_inc(turned, 1)

            @block.vector
            def _(dve):
                steps = Chain(dve, dve_step)
                for w in range(2):
                    dve.wait_ge(summed, w + 1)
                    nc.vector.tensor_tensor(sums[:, w, :], p_sum[w][:], bias_cols, ALU.add).then_inc(biased, 1)
                for w, (gain, shift) in enumerate(cols):
                    dve.wait_ge(biased, w + 1)
                    steps.mark(nc.vector.scalar_tensor_tensor(out=gain, in0=sums[:, w, KD:2 * KD], scalar=1.0, in1=gcol, op0=ALU.add, op1=ALU.mult))
                    steps.mark(nc.vector.tensor_copy(shift, sums[:, w, 0:KD]))
                steps.wait()

            @block.scalar
            def _(act):
                for w in range(2):
                    act.wait_ge(turned, w + 1)
                    nc.scalar.activation(rows[w][:], p_row[w][:], ACT.Copy).then_inc(copied, 1)

            @block.sync
            def _(sp):
                for w in range(2):
                    sp.wait_ge(copied, w + 1)
                    sp.dma_start(mods[w].rearrange("(k p) -> k p", p=P), rows[w][:]).then_inc(stored, 16)
                sp.wait_ge(stored, 32)


def modulation_rows(nc, name, mods, g_row, out):
    with Stage(nc, name) as st:
        g = st.sb("g", [P, D])
        loaded, dve_step = st.sem("loaded"), st.sem("dve_step")
        with st.block() as block:
            @block.sync
            def _(sp):
                sp.dma_start(g[:], g_row.partition_broadcast(P)).then_inc(loaded, 16)
                for w in range(len(out)):
                    sp.dma_start(out[w][0], mods[w, 4 * D:5 * D].partition_broadcast(P)).then_inc(loaded, 16)
                    sp.dma_start(out[w][1], mods[w, 3 * D:4 * D].partition_broadcast(P)).then_inc(loaded, 16)
                sp.wait_ge(loaded, 16 * (1 + 2 * len(out)))

            @block.vector
            def _(dve):
                steps = Chain(dve, dve_step)
                dve.wait_ge(loaded, 16 * (1 + 2 * len(out)))
                for w in range(len(out)):
                    steps.mark(nc.vector.scalar_tensor_tensor(out=out[w][0], in0=out[w][0], scalar=1.0, in1=g[:], op0=ALU.add, op1=ALU.mult))
                steps.wait()


def gated_residual(x_tile, gate_row, tmp):
    def epi(which, engine, chain, j, n0, ps):
        chain.step(engine.tensor_tensor(tmp[:, j % 2], ps, gate_row(j), ALU.mult))
        return engine.tensor_tensor(x_tile(j), x_tile(j), tmp[:, j % 2], ALU.add)
    return epi


def spatial_gate(nc, name, S, uT, v, ln_rows, w_sT, b_s):
    with Stage(nc, name) as st:
        gain, shift = st.sb("gain", [P, W_GMLP]), st.sb("shift", [P, W_GMLP])
        ws = st.sb("w_s", [P, GROUPS, P])
        bs = st.sb("b_s", [1, GROUPS, P])
        stats = st.sb("stats", [P, W_GMLP // BANK, 6])
        mv = st.sb("mean_var", [P, 2])
        rms, rstd, variance = st.sb("rms", [P, 1]), st.sb("rstd", [P, 1]), st.sb("variance", [P, 1])
        banks = [st.ps(f"bank{b}", [P, 4, P]) for b in range(8)]
        loaded, normed, mixed, emptied = st.sem("loaded"), st.sem("normed"), st.sem("mixed"), st.sem("emptied")
        dve_step, var_ready, rms_ready = st.sem("dve_step"), st.sem("var_ready"), st.sem("rms_ready")
        nb = W_GMLP // BANK
        with st.block() as block:
            @block.sync
            def _(sp):
                sp.dma_start(gain[:], ln_rows[0].partition_broadcast(P)).then_inc(loaded, 16)
                sp.dma_start(shift[:], ln_rows[1].partition_broadcast(P)).then_inc(loaded, 16)
                sp.dma_start(ws[:], w_sT).then_inc(loaded, 16)
                sp.dma_start(bs[:], b_s).then_inc(loaded, 16)

            @block.vector
            def _(dve):
                steps = Chain(dve, dve_step)
                dve.wait_ge(loaded, 64)

                def gate(t):
                    for q in range(4):
                        dve.wait_ge(mixed, 4 * t + q + 1)
                        u = uT[:, 4 * q:4 * q + 4, t * P:(t + 1) * P]
                        nc.vector.tensor_tensor(u, u, banks[(4 * t + q) % 8][:], ALU.mult).then_inc(emptied, 1)

                for t in range(NA):
                    for b in range(nb):
                        steps.mark(nc.vector.bn_stats(stats[:, b, :], v[:, t, b * BANK:(b + 1) * BANK]))
                    steps.wait()
                    steps.mark(nc.vector.bn_aggr(mv[:], stats[:].rearrange("p b s -> p (b s)")))
                    steps.wait()
                    nc.vector.tensor_scalar(variance[:], mv[:, 1:2], 1.0, None, ALU.mult).then_inc(var_ready, 1)
                    dve.wait_ge(rms_ready, t + 1)
                    steps.step(nc.vector.reciprocal(rstd[:], rms[:]))
                    steps.step(nc.vector.tensor_scalar(v[:, t, :], v[:, t, :], mv[:, 0:1], rstd[:, 0:1], ALU.subtract, ALU.mult))
                    steps.step(nc.vector.tensor_tensor(v[:, t, :], v[:, t, :], gain[:], ALU.mult))
                    nc.vector.tensor_tensor(v[:, t, :], v[:, t, :], shift[:], ALU.add).then_inc(normed, 1)
                    if t:
                        gate(t - 1)
                gate(NA - 1)

            @block.scalar
            def _(act):
                for t in range(NA):
                    act.wait_ge(var_ready, t + 1)
                    nc.scalar.activation(rms[:], variance[:], ACT.Sqrt, bias=S.eps[:, 1:2]).then_inc(rms_ready, 1)

            @block.tensor
            def _(pe):
                pe.wait_ge(loaded, 64)
                for t in range(NA):
                    pe.wait_ge(normed, t + 1)
                    for q in range(4):
                        n = 4 * t + q
                        if n >= 8:
                            pe.wait_ge(emptied, n - 7)
                        for g in range(4):
                            gg = 4 * q + g
                            nc.tensor.matmul(banks[n % 8][:, g, :], v[:, t, gg * P:(gg + 1) * P], ws[:, gg, :], start=True, stop=False)
                            mm = nc.tensor.matmul(banks[n % 8][:, g, :], S.ones[0:1, :], bs[0:1, gg, :], start=False, stop=True)
                        mm.then_inc(mixed, 1)


def route(nc, name, S, logits, T, n_blocks, a, dest, weight, table, experts):
    cap = (n_blocks + 1) * P
    with Stage(nc, name) as st:
        def sb(n, shape, dt=F32):
            return st.sb(n, shape, dt)
        rank4, rank8 = sb("rank4", [P, 4]), sb("rank8", [P, 8])
        before, column = sb("before", [P, P]), sb("column", [P, 1])
        tokens, zeros = sb("tokens", [P, T], I32), sb("zeros", [P, n_blocks + 1], I32)
        gm, gsum, gtop = sb("gm", [P, T]), sb("gsum", [P, T]), sb("gtop", [P, T])
        gd, ge, gs, goh = (sb(n, [P, T, 4]) for n in ("gd", "ge", "gs", "goh"))
        part = sb("part", [P, T, 4, 8])
        el, el2, sc1 = sb("el", [P, T, 8]), sb("el2", [P, T, 8]), sb("sc1", [P, T, 8])
        oh = [sb(f"oh{n}", [P, T, 8]) for n in range(2)]
        top = [sb(f"top{n}", [P, T]) for n in range(2)]
        first = sb("first", [P, T])
        diff, ediff, den, share = sb("diff", [P, T]), sb("ediff", [P, T]), sb("den", [P, T]), sb("share", [P, T])
        E = [sb(f"E{n}", [P, T, 4, 8]) for n in range(2)]
        both = sb("both", [P, T, N_EXP])
        counts, blocks, ends, starts = sb("counts", [P, N_EXP]), sb("blocks", [P, N_EXP]), sb("ends", [P, N_EXP]), sb("starts", [P, N_EXP])
        place, picked = sb("place", [P, T, N_EXP]), sb("picked", [P, T, N_EXP])
        destf = sb("destf", [P, 2, T])
        past, owner, owner_i = sb("past", [P, N_EXP]), sb("owner", [P, 1]), sb("owner_i", [P, 1], I32)
        H = n_blocks // 2
        evens, begun = sb("evens", [P, H]), sb("begun", [P, H])
        pairs, pairs_i = sb("pairs", [P, 1]), sb("pairs_i", [P, 1], I32)
        p_pos, p_cnt = st.ps("p_pos", [P, T, N_EXP]), st.ps("p_cnt", [P, N_EXP])
        loaded, dve_step, exp_ready, counted = st.sem("loaded"), st.sem("dve_step"), st.sem("exp_ready"), st.sem("counted")
        stored, cleared, table_cleared = st.sem("stored"), st.sem("cleared"), st.sem("table_cleared")
        rank_ready, shifted, differed, placed, owned = (st.sem(n) for n in ("both_ready", "shifted", "differed", "placed", "owned"))
        scattered = S.scattered

        def bc(x, n):
            return x.rearrange("p (t o) -> p t o", o=1).broadcast_to([P, T, n])

        def table_row(x, n):
            return x.rearrange("p (o n) -> p o n", o=1).broadcast_to([P, T, n])

        with st.block() as block:
            @block.sync
            def _(sp):
                for dst, src in ((rank4, a["rank8"][:, 4:8]), (rank8, a["rank8"]), (before, a["before"]), (column, a["column"]),
                                 (tokens, a["token_ids"][:, 0:T]), (evens, a["evens"][:, 0:H])):
                    sp.dma_start(dst[:], src).then_inc(loaded, 16)
                sp.wait_ge(cleared, 1)
                sp.dma_start(table.rearrange("(p b) o -> p (b o)", p=P), zeros[:]).then_inc(table_cleared, 16)
                sp.wait_ge(owned, 1)
                sp.dma_start(experts[0:n_blocks].rearrange("(p o) -> p o", o=1), owner_i[0:n_blocks, :]).then_inc(stored, 16)
                sp.dma_start(experts[n_blocks:n_blocks + 1].rearrange("(p o) -> p o", o=1), pairs_i[0:1, :]).then_inc(stored, 16)
                sp.wait_ge(stored, 32)

            @block.gpsimd
            def _(pool):
                nc.gpsimd.memset(zeros[:], 0).then_inc(cleared, 1)
                pool.wait_ge(placed, 1)
                pool.wait_ge(table_cleared, 16)
                pool.wait_ge(loaded, 96)
                for n in range(2):
                    for t in range(T):
                        pool.indirect_dma_start(table, bass.IndirectOffsetOnAxis(dest[:, n, t:t + 1], 0), tokens[:, t:t + 1], None).then_inc(scattered, 16)
                pool.wait_ge(scattered, 16 * 2 * T)

            @block.scalar
            def _(act):
                act.wait_ge(shifted, 1)
                nc.scalar.activation(ge[:], gd[:], ACT.Exp).then_inc(exp_ready, 1)
                act.wait_ge(differed, 1)
                nc.scalar.activation(ediff[:], diff[:], ACT.Exp).then_inc(exp_ready, 1)

            @block.tensor
            def _(pe):
                pe.wait_ge(loaded, 96)
                pe.wait_ge(rank_ready, 1)
                for t in range(T):
                    for t2 in range(t + 1):
                        nc.tensor.matmul(p_pos[:, t, :], before[:] if t2 == t else S.ones[:], both[:, t2, :], start=(t2 == 0), stop=(t2 == t))
                for t in range(T):
                    mm = nc.tensor.matmul(p_cnt[:], S.ones[:], both[:, t, :], start=(t == 0), stop=(t == T - 1))
                mm.then_inc(counted, 1)

            @block.vector
            def _(dve):
                c = Chain(dve, dve_step)
                V = nc.vector
                dve.wait_ge(loaded, 96)
                gl = logits[:, :, 0:4]
                c.step(V.tensor_reduce(gm[:], gl, AX.X, ALU.max))
                V.tensor_tensor(gd[:], gl, bc(gm[:], 4), ALU.subtract).then_inc(shifted, 1)
                dve.wait_ge(exp_ready, 1)
                c.mark(V.tensor_reduce(gsum[:], ge[:], AX.X, ALU.add))
                c.step(V.tensor_scalar(gs[:], gd[:], 0.0, None, ALU.is_ge))
                c.step(V.tensor_tensor(gs[:], gs[:], table_row(rank4[:], 4), ALU.mult))
                c.step(V.tensor_reduce(gtop[:], gs[:], AX.X, ALU.max))
                c.step(V.tensor_tensor(goh[:], gs[:], bc(gtop[:], 4), ALU.is_equal))
                goh8 = goh[:].rearrange("p t (g o) -> p t g o", o=1).broadcast_to([P, T, 4, 8])
                c.step(V.tensor_tensor(part[:], logits[:, :, 4:36].rearrange("p t (g e) -> p t g e", g=4), goh8, ALU.mult))
                c.step(V.tensor_tensor(el[:], part[:, :, 0, :], part[:, :, 1, :], ALU.add))
                c.step(V.tensor_tensor(el[:], el[:], part[:, :, 2, :], ALU.add))
                c.step(V.tensor_tensor(el[:], el[:], part[:, :, 3, :], ALU.add))
                for n, src in enumerate((el, el2)):
                    if n:
                        c.step(V.scalar_tensor_tensor(out=el2[:], in0=oh[0][:], scalar=-BIG, in1=el[:], op0=ALU.mult, op1=ALU.add))
                    c.step(V.tensor_reduce(top[n][:], src[:], AX.X, ALU.max))
                    c.step(V.tensor_tensor(sc1[:], src[:], bc(top[n][:], 8), ALU.is_equal))
                    c.step(V.tensor_tensor(sc1[:], sc1[:], table_row(rank8[:], 8), ALU.mult))
                    c.step(V.tensor_reduce(first[:], sc1[:], AX.X, ALU.max))
                    c.step(V.tensor_tensor(oh[n][:], sc1[:], bc(first[:], 8), ALU.is_equal))
                    for t in range(T):
                        c.mark(V.tensor_tensor(E[n][:, t], goh[:, t, :].rearrange("p (g o) -> p g o", o=1).broadcast_to([P, 4, 8]),
                                               oh[n][:, t:t + 1, :].broadcast_to([P, 4, 8]), ALU.mult))
                    c.wait()
                V.tensor_tensor(both[:], E[0][:].rearrange("p t g e -> p t (g e)"), E[1][:].rearrange("p t g e -> p t (g e)"), ALU.add).then_inc(rank_ready, 1)
                V.tensor_tensor(diff[:], top[1][:], top[0][:], ALU.subtract).then_inc(differed, 1)
                dve.wait_ge(exp_ready, 2)
                c.step(V.tensor_scalar(den[:], ediff[:], 1.0, None, ALU.add))
                c.step(V.tensor_tensor(den[:], den[:], gsum[:], ALU.mult))
                c.step(V.reciprocal(weight[:, 0, :], den[:]))
                c.mark(V.tensor_tensor(weight[:, 1, :], weight[:, 0, :], ediff[:], ALU.mult))
                dve.wait_ge(counted, 1)
                c.mark(V.tensor_copy(counts[:], p_cnt[:]))
                c.step(V.memset(blocks[:], 0.0))
                for m in range(T):
                    c.step(V.scalar_tensor_tensor(out=blocks[:], in0=counts[:], scalar=float(P * m), in1=blocks[:], op0=ALU.is_gt, op1=ALU.add))
                c.step(V.tensor_tensor_scan(ends[:], S.ones[:, 0:N_EXP], blocks[:], 0.0, ALU.mult, ALU.add))
                c.step(V.tensor_tensor(starts[:], ends[:], blocks[:], ALU.subtract))
                c.step(V.tensor_scalar(starts[:], starts[:], float(P), None, ALU.mult))
                c.step(V.tensor_tensor(place[:], p_pos[:], table_row(starts[:], N_EXP), ALU.add))
                for n in range(2):
                    c.step(V.tensor_tensor(picked[:], place[:], E[n][:].rearrange("p t g e -> p t (g e)"), ALU.mult))
                    c.step(V.tensor_reduce(destf[:, n, :], picked[:], AX.X, ALU.add))
                V.tensor_copy(dest[:], destf[:]).then_inc(placed, 1)
                c.step(V.tensor_scalar(begun[:], evens[:], ends[:, N_EXP - 1:N_EXP], None, ALU.is_lt))
                c.step(V.tensor_reduce(pairs[:], begun[:], AX.X, ALU.add))
                c.step(V.tensor_copy(pairs_i[:], pairs[:]))
                c.step(V.tensor_scalar(past[:], ends[:], column[:, 0:1], None, ALU.is_le))
                c.step(V.tensor_reduce(owner[:], past[:], AX.X, ALU.add))
                c.step(V.tensor_scalar(owner[:], owner[:], float(N_EXP - 1), None, ALU.min))
                V.tensor_copy(owner_i[:], owner[:]).then_inc(owned, 1)
                dve.wait_ge(placed, 1)


def experts_run(nc, name, S, n_blocks, table, experts, h, w_gu, w_d, y):
    KH = HID // P
    with Stage(nc, name) as st:
        erow = st.sb("experts", [1, n_blocks + 1], I32)
        rows = [st.sb(f"rows{u}", [P, 1], I32) for u in range(2)]
        xg = [st.sb(f"xg{u}", [P, D]) for u in range(2)]
        xT = [st.sb(f"xT{u}", [P, KD, P]) for u in range(2)]
        wgu = [st.sb(f"wgu{u}", [P, 2, KD, HID]) for u in range(2)]
        wd = [st.sb(f"wd{u}", [P, KH, D]) for u in range(2)]
        sg, act_in = st.sb("gate", [P, HID]), st.sb("gated", [P, HID])
        aT = st.sb("gatedT", [P, KH, P])
        yo = [st.sb(f"y{u}", [P, D]) for u in range(2)]
        p_x = [st.ps(f"p_x{n}", [P, 4, P]) for n in range(2)]
        p_g, p_u, p_a = st.ps("p_g", [P, HID]), st.ps("p_u", [P, HID]), st.ps("p_a", [P, KH, P])
        p_y = [st.ps(f"p_y{n}", [P, BANK]) for n in range(2)]
        experts_loaded = st.sem("experts_loaded")
        rows_loaded = [st.sem(f"rows_loaded{u}") for u in range(2)]
        gathered = S.gathered
        gu_loaded, d_loaded = [st.sem(f"gu_loaded{u}") for u in range(2)], [st.sem(f"d_loaded{u}") for u in range(2)]
        x_turned, x_copied = st.sem("x_turned"), [st.sem("x_copied0"), st.sem("x_copied1")]
        gate_ready, up_ready, silu_ready, gated = st.sem("gate_ready"), st.sem("up_ready"), st.sem("silu_ready"), st.sem("gated")
        a_turned, a_copied, y_ready = st.sem("a_turned"), st.sem("a_copied"), st.sem("y_ready")
        y_copied = [st.sem("y_copied0"), st.sem("y_copied1")]
        stored = [st.sem(f"stored{u}") for u in range(2)]
        gather_free, tail_free, zeroed = st.sem("gather_free"), st.sem("tail_free"), st.sem("zeroed")
        zeros = st.sb("zeros", [P, D])
        H = n_blocks // 2

        def pairs_in_use(eng):
            eng.wait_ge(experts_loaded, 16)
            return eng.value_load(erow[0:1, n_blocks:n_blocks + 1], min_val=1, max_val=H)

        with st.block() as block:
            @block.sync
            def _(sp):
                sp.dma_start(erow[:], experts[0:n_blocks + 1].rearrange("(o b) -> o b", o=1)).then_inc(experts_loaded, 16)
                pairs = pairs_in_use(sp)

                def load_rows(b, u):
                    sp.dma_start(rows[u][:], table[bass.ds(b * P, P), :]).then_inc(rows_loaded[u], 16)

                def expert(b):
                    return sp.value_load(erow[0:1, bass.ds(b, 1)], min_val=0, max_val=N_EXP - 1)

                def load_gu(e, u):
                    sp.dma_start(wgu[u][:], w_gu[bass.ds(e, 1)].rearrange("a p g k f -> (a p) g k f")).then_inc(gu_loaded[u], 16)

                def load_d(e, u):
                    sp.dma_start(wd[u][:], w_d[bass.ds(e, 1)].rearrange("a p k f -> (a p) k f")).then_inc(d_loaded[u], 16)

                def store(b, u, done):
                    sp.wait_ge(y_copied[0], done)
                    sp.wait_ge(y_copied[1], done)
                    sp.dma_start(y[bass.ds(b * P, P), :], yo[u][:]).then_inc(stored[u], 16)

                load_rows(0, 0)
                load_rows(1, 1)
                for u in range(2):
                    sp.wait_ge(gathered[u], 16)
                for u in range(2):
                    e = expert(u)
                    load_gu(e, u)
                    load_d(e, u)
                sp.wait_ge(zeroed, 1)
                with sp.Fori(0, H - 1) as i:
                    with sp.If(i + 1 < pairs):
                        for u in range(2):
                            b = 2 * i + u
                            sp.wait_ge(gathered[u], 16 * i + 16)
                            load_rows(b + 2, u)
                            e = expert(b + 2)
                            sp.wait_ge(gated, b + 2)
                            load_gu(e, u)
                            store(b, u, b + 2)
                            sp.wait_ge(stored[u], 16 * i + 16)
                            load_d(e, u)
                    with sp.Else():
                        for u in range(2):
                            sp.dma_start(y[bass.ds((2 * i + 2 + u) * P, P), :], zeros[:]).then_inc(stored[u], 16)
                sp.wait_ge(gathered[0], 16 * pairs)
                sp.sem_inc(tail_free, 1)
                load_rows(2 * pairs, 0)
                for u in range(2):
                    store(2 * pairs - 2 + u, u, 2 * pairs + u)
                sp.wait_ge(rows_loaded[0], 16 * pairs + 16)
                sp.sem_inc(tail_free, 1)
                for u in range(2):
                    sp.wait_ge(stored[u], 16 * H)

            @block.gpsimd
            def _(pool):
                def gather(u):
                    pool.indirect_dma_start(xg[u][:], None, h, bass.IndirectOffsetOnAxis(rows[u][:, 0:1], 0)).then_inc(gathered[u], 16)

                for u in range(2):
                    pool.wait_ge(rows_loaded[u], 16)
                    gather(u)
                nc.gpsimd.memset(zeros[:], 0.0).then_inc(zeroed, 1)
                pairs = pairs_in_use(pool)
                with pool.Fori(0, H - 1) as i:
                    with pool.If(i + 1 < pairs):
                        for u in range(2):
                            pool.wait_ge(rows_loaded[u], 16 * i + 32)
                            pool.wait_ge(x_turned, 4 * i + 2 * u + 2)
                            pool.sem_inc(gather_free, 1)
                            gather(u)
                pool.wait_ge(rows_loaded[0], 16 * pairs + 16)
                pool.wait_ge(x_turned, 4 * pairs)
                pool.sem_inc(gather_free, 1)
                gather(0)
                pool.wait_ge(gathered[0], 16 * pairs + 16)

            @block.tensor
            def _(pe):
                def turn(b, u, i, first=False):
                    pe.wait_ge(gathered[u], 16 * i + 16)
                    for n in range(2):
                        if not first:
                            pe.wait_ge(x_copied[n], b)
                        for q in range(4):
                            d = 4 * n + q
                            mm = nc.tensor.transpose(p_x[n][:, q, :], xg[u][:, d * P:(d + 1) * P], S.ident[:, :])
                        mm.then_inc(x_turned, 1)

                pairs = pairs_in_use(pe)
                turn(0, 0, 0, True)
                pe.sem_inc(a_turned, 1)
                with pe.Fori(0, H) as i:
                    with pe.If(i < pairs):
                        for u in range(2):
                            b = 2 * i + u
                            pe.wait_ge(x_copied[0], b + 1)
                            pe.wait_ge(x_copied[1], b + 1)
                            pe.wait_ge(gu_loaded[u], 16 * i + 16)
                            pe.wait_ge(gated, b + 1)
                            for g, (p, ready) in enumerate(((p_g, gate_ready), (p_u, up_ready))):
                                for k in range(KD):
                                    mm = nc.tensor.matmul(p[:], xT[u][:, k, :], wgu[u][:, g, k, :], start=(k == 0), stop=(k == KD - 1))
                                mm.then_inc(ready, 1)
                            turn(b + 1, 1 - u, i + u)
                            pe.wait_ge(gated, b + 2)
                            pe.wait_ge(a_copied, b + 1)
                            for k in range(KH):
                                mm = nc.tensor.transpose(p_a[:, k, :], act_in[:, k * P:(k + 1) * P], S.ident[:, :])
                            mm.then_inc(a_turned, 1)
                            pe.wait_ge(a_copied, b + 2)
                            pe.wait_ge(d_loaded[u], 16 * i + 16)
                            for n in range(2):
                                pe.wait_ge(y_copied[n], b + 1)
                                for k in range(KH):
                                    mm = nc.tensor.matmul(p_y[n][:], aT[:, k, :], wd[u][:, k, n * BANK:(n + 1) * BANK], start=(k == 0), stop=(k == KH - 1))
                                mm.then_inc(y_ready, 1)

            @block.scalar
            def _(act):
                pairs = pairs_in_use(act)
                act.sem_inc(a_copied, 1)
                act.sem_inc(y_copied[0], 1)

                def copy_x(b, u):
                    act.wait_ge(x_turned, 2 * b + 1)
                    nc.scalar.activation(xT[u][:, 0:4, :], p_x[0][:], ACT.Copy).then_inc(x_copied[0], 1)

                copy_x(0, 0)
                with act.Fori(0, H) as i:
                    with act.If(i < pairs):
                        for u in range(2):
                            b = 2 * i + u
                            act.wait_ge(gate_ready, b + 1)
                            act.wait_ge(gated, b + 1)
                            nc.scalar.activation(sg[:], p_g[:], ACT.Silu).then_inc(silu_ready, 1)
                            copy_x(b + 1, 1 - u)
                            act.wait_ge(a_turned, b + 2)
                            nc.scalar.activation(aT[:], p_a[:], ACT.Copy).then_inc(a_copied, 1)
                            act.wait_ge(y_ready, 2 * b + 1)
                            nc.scalar.activation(yo[u][:, 0:BANK], p_y[0][:], ACT.Copy).then_inc(y_copied[0], 1)

            @block.vector
            def _(dve):
                pairs = pairs_in_use(dve)
                dve.sem_inc(gated, 1)
                dve.sem_inc(y_copied[1], 1)

                def copy_x(b, u):
                    dve.wait_ge(x_turned, 2 * b + 2)
                    nc.vector.tensor_copy(xT[u][:, 4:8, :], p_x[1][:]).then_inc(x_copied[1], 1)

                copy_x(0, 0)
                with dve.Fori(0, H) as i:
                    with dve.If(i < pairs):
                        for u in range(2):
                            b = 2 * i + u
                            dve.wait_ge(silu_ready, b + 1)
                            dve.wait_ge(up_ready, b + 1)
                            dve.wait_ge(a_turned, b + 1)
                            nc.vector.tensor_tensor(act_in[:], sg[:], p_u[:], ALU.mult).then_inc(gated, 1)
                            copy_x(b + 1, 1 - u)
                            dve.wait_ge(y_ready, 2 * b + 2)
                            nc.vector.tensor_copy(yo[u][:, BANK:D], p_y[1][:]).then_inc(y_copied[1], 1)


def combine(nc, name, S, streams, dest, weight, y):
    tiles = [(x, w) for w, (xs, _) in enumerate(streams) for x in xs]
    T = len(tiles)
    with Stage(nc, name) as st:
        row = [st.sb(f"gate{w}", [P, D]) for w in range(len(streams))]
        ya = [[st.sb(f"y{n}{u}", [P, D]) for u in range(2)] for n in range(2)]
        loaded, dve_step = st.sem("loaded"), st.sem("dve_step")
        fetched = S.fetched
        with st.block() as block:
            @block.sync
            def _(sp):
                for w, (_, gate_row) in enumerate(streams):
                    sp.dma_start(row[w][:], gate_row.partition_broadcast(P)).then_inc(loaded, 16)

            @block.gpsimd
            def _(pool):
                for t in range(T):
                    if t >= 2:
                        pool.wait_ge(dve_step, 4 * (t - 1))
                    for n in range(2):
                        pool.indirect_dma_start(ya[n][t % 2][:], None, y, bass.IndirectOffsetOnAxis(dest[:, n, t:t + 1], 0)).then_inc(fetched[t % 2], 16)
                for u in range(min(2, T)):
                    pool.wait_ge(fetched[u], 32 * ((T - u + 1) // 2))

            @block.vector
            def _(dve):
                steps = Chain(dve, dve_step)
                dve.wait_ge(loaded, 16 * len(streams))
                for t, (x, w) in enumerate(tiles):
                    dve.wait_ge(fetched[t % 2], 32 * (t // 2 + 1))
                    y0, y1 = ya[0][t % 2][:], ya[1][t % 2][:]
                    steps.step(nc.vector.tensor_scalar(y0, y0, weight[:, 0, t:t + 1], None, ALU.mult))
                    steps.step(nc.vector.scalar_tensor_tensor(out=y0, in0=y1, scalar=weight[:, 1, t:t + 1], in1=y0, op0=ALU.mult, op1=ALU.add))
                    steps.step(nc.vector.tensor_tensor(y0, y0, row[w][:], ALU.mult))
                    steps.step(nc.vector.tensor_tensor(x, x, y0, ALU.add))


def route_tables():
    i = np.arange(P)
    return {"rank8": np.tile(np.arange(8, 0, -1, dtype=np.float32), (P, 1)),
            "before": (i[:, None] < i[None, :]).astype(np.float32),
            "column": i[:, None].astype(np.float32), "evens": np.tile(np.arange(0, max(N_BLOCKS), 2, dtype=np.float32), (P, 1)),
            "token_ids": (np.arange(NA)[None, :] * P + i[:, None]).astype(np.int32)}


SECOND_COLS = (("norm1_g_2", 2 * KD), ("ga_b_in_2_u", W_GMLP // P))
N_BLOCKS = (44, 40)


def moe(nc, name, S, a, layer, streams, hT, mods):
    tiles = [(t, w) for ts, w in streams for t in ts]
    T = len(tiles)
    nb = N_BLOCKS[layer]
    assert nb % 2 == 0 and nb >= (2 * T * P + N_EXP * (P - 1)) // P
    h = dram(nc, name + "_h", [T * P, D])
    table, experts = dram(nc, name + "_table", [(nb + 1) * P, 1], I32), dram(nc, name + "_experts", [P], I32)
    y = dram(nc, name + "_y", [nb * P, D])
    with ExitStack() as mem:
        def sb(n, shape, dt=F32):
            return mem.enter_context(nc.sbuf_tensor(f"{name}_{n}", shape, dt))
        dest, weight = sb("dest", [P, 2, T], I32), sb("weight", [P, 2, T])
        with ExitStack() as mem2:
            rows = [[mem2.enter_context(nc.sbuf_tensor(f"{name}_row{w}{n}", [P, D], F32)) for n in range(2)] for w in range(len(streams))]
            modulation_rows(nc, name + "m", mods, a["norm2_g_2"][layer], [(r[0][:], r[1][:]) for r in rows])
            norm_transpose(nc, name + "n", S, [t for t, _ in tiles], hT, rows=[(rows[w][0][:], rows[w][1][:]) for _, w in tiles], h_dram=h)
            logits = mem2.enter_context(nc.sbuf_tensor(f"{name}_logits", [P, T, 36], F32))
            brow = mem2.enter_context(nc.sbuf_tensor(f"{name}_brow", [1, P], F32))
            load_all(nc, name + "b", [(brow[:], a["moe_b_2"][layer].rearrange("(o c) -> o c", o=1))])
            project(nc, name + "g", hT, T * P, [dict(w=a["moe_w_route_2"][layer], mode="T", bias=brow[:], epi=copy_to(lambda j, n0: logits[:, j, :], 36))],
                    const={"ones": S.ones})
            S.scattered = S.pool_sems[layer][0]
            route(nc, name + "r", S, logits, T, nb, a, dest, weight, table, experts)
        S.gathered = S.pool_sems[layer][1:3]
        experts_run(nc, name + "e", S, nb, table, experts, h, a["moe_w_gu_2"][layer], a["moe_w_down_2"][layer], y)
        S.fetched = S.pool_sems[layer][3:5]
        combine(nc, name + "c", S, [(ts, mods[w, 5 * D:6 * D]) for ts, w in streams], dest, weight, y)


def gmlp(nc, S, a, x_tiles, c_tiles, hT, mods):
    with ExitStack() as mem:
        def sb(n, shape):
            return mem.enter_context(nc.sbuf_tensor("gm_" + n, shape, F32))
        uT = sb("uT", [P, GROUPS, ALL])
        bias_u = S.second_cols[:, 2 * KD:2 * KD + W_GMLP // P]
        with ExitStack() as mem2:
            v = mem2.enter_context(nc.sbuf_tensor("gm_v", [P, NA, W_GMLP], F32))
            brow = mem2.enter_context(nc.sbuf_tensor("gm_brow", [1, W_GMLP], F32))
            load_all(nc, "gmb", [(brow[:], a["ga_b_in_2_v"].rearrange("(o c) -> o c", o=1))])

            def epi_u(c):
                def epi(which, engine, chain, j, n0, ps):
                    f = 4 * c + j
                    return engine.activation(uT[:, f, n0:n0 + ps.shape[1]], ps, ACT.Gelu, bias=bias_u[:, f:f + 1])
                return epi

            def epi_v(c):
                def epi(which, engine, chain, j, n0, ps):
                    return engine.activation(v[:, j, c * BANK:(c + 1) * BANK], ps, ACT.Gelu)
                return epi

            w = a["ga_w_in_2"]
            jobs = [dict(w=w[:, c * BANK:(c + 1) * BANK], mode="F", eng="act", epi=epi_u(c)) for c in range(4)]
            jobs += [dict(w=w[:, W_GMLP + c * BANK:W_GMLP + (c + 1) * BANK], mode="T", eng="act", bias=brow[0:1, c * BANK:(c + 1) * BANK], epi=epi_v(c)) for c in range(4)]
            project_split(nc, "gmi", hT, ALL, jobs, const={"ones": S.ones})
            spatial_gate(nc, "gms", S, uT, v, (a["ga_ln_g_2"], a["ga_ln_b_2"]), a["ga_w_sT_2"], a["ga_b_s_2"])
        brow = sb("brow_out", [1, D])
        gates = [sb(f"gate{w}", [P, D]) for w in range(2)]
        W = BANK
        tmp = sb("tmp", [P, 2, W])
        load_all(nc, "gmc", [(brow[:], a["ga_b_out_2"].rearrange("(o c) -> o c", o=1))] +
                 [(gates[w][:], mods[w, 2 * D:3 * D].partition_broadcast(P)) for w in range(2)])
        tiles = x_tiles + c_tiles
        jobs = []
        for c in range(D // W):
            s = slice(c * W, (c + 1) * W)
            jobs.append(dict(w=a["ga_w_out_2"][:, s], mode="T", eng="dve", bias=brow[0:1, s],
                             epi=gated_residual(lambda j, s=s: tiles[j][:, s], lambda j, s=s: gates[j >= NT][:, s], tmp)))
        project_split(nc, "gmo", uT, ALL, jobs, const={"ones": S.ones})


def second_block_a(nc, S, a, x_tiles, c_tiles, hT, mods):
    cols = S.mod_cols[0]
    norm_transpose(nc, "sn0", S, x_tiles + c_tiles, hT, cols=[cols[0]] * NT + [cols[1]] * (NA - NT))
    gmlp(nc, S, a, x_tiles, c_tiles, hT, mods[0])
    moe(nc, "moe0", S, a, 0, ((x_tiles, 0), (c_tiles, 1)), hT, mods[0])


def second_layout(inp):
    g = lambda n: np.asarray(inp[n])
    out = {n: np.ascontiguousarray(g(n)[0]) for n in ("ga_w_in_2", "ga_ln_g_2", "ga_ln_b_2", "ga_w_out_2", "ga_b_out_2")}
    for n in ("ada_w_2", "norm2_g_2"):
        out[n] = np.ascontiguousarray(g(n))
    out["ctx_2"] = np.ascontiguousarray(g("ctx_2")[0])
    out["ada_cols_2"] = np.ascontiguousarray(np.stack([columns(b) for b in g("ada_b_2")], 1))
    out["cT_2"] = np.ascontiguousarray(np.stack([columns(g("c_2")[0]), columns(g("c_ctx_2"))], 2))
    out["ga_w_sT_2"] = np.ascontiguousarray(g("ga_w_s_2")[0].transpose(2, 0, 1))
    out["ga_b_s_2"] = np.ascontiguousarray(g("ga_b_s_2")[0][None])
    out["ga_b_in_2_v"] = np.ascontiguousarray(g("ga_b_in_2")[0, W_GMLP:])
    out["moe_w_route_2"] = np.ascontiguousarray(np.concatenate([g("moe_w_grp_2"), g("moe_w_exp_2"), np.zeros((2, D, P - 36), np.float32)], 2))
    out["moe_b_2"] = np.ascontiguousarray(np.concatenate([g("moe_b_grp_2"), g("moe_b_exp_2"), np.zeros((2, P - 36), np.float32)], 1))
    gu = np.stack([g("moe_w_gate_2"), g("moe_w_up_2")], 2)
    out["moe_w_gu_2"] = np.ascontiguousarray(gu.reshape(2, N_EXP, 2, KD, P, HID).transpose(0, 1, 4, 2, 3, 5))
    out["moe_w_down_2"] = np.ascontiguousarray(g("moe_w_down_2").reshape(2, N_EXP, HID // P, P, D).transpose(0, 1, 3, 2, 4))
    out["second_cols"] = np.concatenate([columns(g("norm1_g_2")), columns(g("ga_b_in_2")[0, :W_GMLP])], 1)
    return out


HEADS, HK = 16, 64
CH = 64
STEPS = ALL // CH
CSTEPS = CTX // CH
GRID = 64
LEVELS = 5
LOG_DECAY = -math.exp(-0.5)


def token_shift(nc, name, hT, xx):
    rows = SEQ // GRID
    with Stage(nc, name) as st:
        dve_step = st.sem("dve_step")
        with st.block() as block:
            @block.vector
            def _(dve):
                steps = Chain(dve, dve_step)

                def sub(dst, shifted, here):
                    steps.mark(nc.vector.tensor_tensor(dst, shifted, here, ALU.subtract))

                def edge(dst, here):
                    steps.mark(nc.vector.tensor_scalar(dst, here, -1.0, None, ALU.mult))

                C = CTX
                b, f = slice(0, 4), slice(4, 8)
                sub(xx[:, b, 1:C], hT[:, b, 0:C - 1], hT[:, b, 1:C])
                edge(xx[:, b, 0:1], hT[:, b, 0:1])
                sub(xx[:, f, 0:C - 1], hT[:, f, 1:C], hT[:, f, 0:C - 1])
                edge(xx[:, f, C - 1:C], hT[:, f, C - 1:C])
                for k in range(0, 2):
                    g, o = (t[:, k, C:].rearrange("p (r c) -> p r c", c=GRID) for t in (hT, xx))
                    sub(o[:, :, 1:], g[:, :, :GRID - 1], g[:, :, 1:])
                    edge(o[:, :, 0:1], g[:, :, 0:1])
                for k in range(2, 4):
                    g, o = (t[:, k, C:].rearrange("p (r c) -> p r c", c=GRID) for t in (hT, xx))
                    sub(o[:, :, :GRID - 1], g[:, :, 1:], g[:, :, :GRID - 1])
                    edge(o[:, :, GRID - 1:], g[:, :, GRID - 1:])
                u, d = slice(4, 6), slice(6, 8)
                sub(xx[:, u, C + GRID:], hT[:, u, C:ALL - GRID], hT[:, u, C + GRID:])
                edge(xx[:, u, C:C + GRID], hT[:, u, C:C + GRID])
                sub(xx[:, d, C:ALL - GRID], hT[:, d, C + GRID:], hT[:, d, C:ALL - GRID])
                edge(xx[:, d, ALL - GRID:], hT[:, d, ALL - GRID:])
                steps.wait()


def backward(x):
    return x.rearrange("p (c t) -> p c t", t=CH)[:, ::-1, :]


def chunked(x):
    return x.rearrange("p (c t) -> p c t", t=CH)


def rwkv_scan(nc, name, S, a, kF, rF, sgF, aF, vS, yS, bS):
    NG = STEPS // 4
    NZ = LEVELS * NG
    lat = SEQ // CH
    assert CSTEPS == 4 and HEADS % 2 == 0
    WALK_PAIRS = [(2 * g, 2 * g + 1) for g in range(NG)]
    WALK_GROWTH = {n: 2 * NG + n for n in range(STEPS - 2 * NG)}
    KH_SLOTS = (7, 9)
    SLOTS = 14
    assert len(WALK_GROWTH) <= 8 and SLOTS < NZ
    with Stage(nc, name) as st:
        sb = st.sb
        masks = sb("masks", [P, 4, P])
        join = sb("join", [P, LEVELS + 1, P])
        join0 = sb("join0", [P, P])
        keep = sb("keep", [P, ALL])
        halves = sb("halves", [P, P])
        cols = sb("cols", [P, 4])
        k2, sg, aa = (sb(n, [P, ALL]) for n in ("k", "sg", "a"))
        r2 = sb("r", [P, SEQ])
        vs = [sb(f"v{u}", [P, STEPS, HK]) for u in range(2)]
        lw, L, G, G2, sq, kk, km, t1, e_neg = (sb(n, [P, ALL]) for n in ("lw", "L", "G", "G2", "sq", "kk", "km", "t1", "e_neg"))
        e_exc, e_inc, nrm = lw, L, sq
        em = sb("em", [P, STEPS])
        ee = [sb(f"ee{u}", [P, STEPS]) for u in range(2)]
        oneminus = sb("oneminus", [P, 1])
        at_ctx = [sb(f"at_ctx{u}", [P, CSTEPS, P]) for u in range(2)]
        at_rt = [sb(f"at_rt{u}", [P, lat, 2, P]) for u in range(2)]
        bh, kh = sb("bh", [P, STEPS, P]), sb("kh", [P, STEPS, P])
        pairs_ctx = [sb(f"pairs_ctx{u}", [P, CSTEPS, 2, P]) for u in range(2)]
        pairs_lat = [sb(f"pairs_lat{u}", [P, lat, 4, P]) for u in range(2)]
        bT, kT = ([sb(f"{n}{u}", [P, STEPS, P]) for u in range(2)] for n in ("bT", "kT"))
        T = sb("T", [P, STEPS, P])
        R = [sb(f"R{u}", [P, STEPS, P]) for u in range(2)]
        off = [sb(f"off{n}", [P, 4, P]) for n in range(2)]
        Z = [sb(f"Z{n}", [P, 4, P]) for n in range(2)]
        Sm, X, SA = sb("Sm", [P, HK]), sb("X", [P, HK]), sb("SA", [P, HK])
        yo, yb = sb("y", [P, lat, HK]), sb("yb", [P, lat, HK])
        bon = sb("bonus", [P, lat])
        rk = sb("rk", [P, lat, P])
        bank = [st.ps(f"bank{n}", [P, BANK]) for n in range(8)]
        pair_bank, pn_bank, tr_bank = bank[0:2], bank[2], bank[3:5]
        z_bank, tz_bank, zr_bank, ss_bank = bank[0:2], bank[2], bank[3], bank[4]
        x_twice, sa_twice, ds_twice, y_twice = (b.rearrange("p (o n) -> p o n", o=2) for b in (bank[5][:, 0:2 * HK], bank[5][:, 2 * HK:4 * HK], bank[6][:, 0:2 * HK], bank[7][:, 0:2 * HK]))
        x_psum, sa_psum, ds_psum, y_psum = (b[:, 0, :] for b in (x_twice, sa_twice, ds_twice, y_twice))
        names = ("lw_ready sq_ready g_ready ss_ready nrm_ready exp_ready cleared bd_ready pb_ready pb_masked pn_ready pn_masked tr_ready tr_copied "
                 "off_ready z_ready z_copied tz_ready tz_added zr_ready zr_added x_ready x_copied sa_ready sa_copied ds_ready sm_ready "
                 "y_ready y_copied bon_ready bon_read bonus_done dve_step kh_made factor_step const_loaded y_free bonus_free loaded stored_y stored_bonus").split()
        s = {n: st.sem(n) for n in names}
        v_loaded = [st.sem(f"v_loaded{u}") for u in range(2)]
        LOADS = 9
        lo, hi = slice(0, HK), slice(HK, P)

        def at(u, j):
            return at_ctx[u][:, j, :] if j < CSTEPS else at_rt[u][:, j - CSTEPS, 0, :]

        def pair(u, j, kind):
            return pairs_ctx[u][:, j, kind // 2, :] if j < CSTEPS else pairs_lat[u][:, j - CSTEPS, kind, :]

        def pairs_of_group(u, g):
            return pairs_ctx[u][:, :, 0, :] if g == 0 else pairs_lat[u][:, 4 * g - 4:4 * g, 0, :]

        def cs(x):
            return x[:].rearrange("p (c t) -> p c t", t=CH)

        def quad(x):
            return x.rearrange("p (c t) -> p c t", c=4)

        def over4(m):
            return m.rearrange("p (o t) -> p o t", o=1).broadcast_to([P, 4, P])

        def every_head(eng, factors, body):
            last = HEADS - 1
            factors(0)
            body(0, 0, 0, None, 1)
            with eng.Fori(0, HEADS // 2 - 1) as i:
                body(2 * i + 1, 1, i, (2 * i, 0, i), 2 * i + 2)
                body(2 * i + 2, 0, i + 1, (2 * i + 1, 1, i), 2 * i + 3)
            body(last, 1, last // 2, (last - 1, 0, last // 2), None)

        LAST = (HEADS - 1, 1, (HEADS - 1) // 2)

        with st.block() as block:
            @block.sync
            def _(sp):
                for dst, src in ((masks, "rw_masks"), (join, "rw_join"), (join0, "rw_join0"), (keep, "rw_keep"), (halves, "rw_halves")):
                    sp.dma_start(dst[:], a[src]).then_inc(s["const_loaded"], 16)

                def load(h):
                    hs = bass.ds(h * HK, HK)
                    for z, rows in ((0, lo), (1, hi)):
                        for dst, src in ((k2, kF), (r2, rF), (sg, sgF), (aa, aF)):
                            sp.dma_start(dst[rows, :], src[z][hs, :]).then_inc(s["loaded"], 16)
                    sp.dma_start(cols[:], a["rw_cols"][bass.ds(h, 1)].rearrange("a p c -> (a p) c")).then_inc(s["loaded"], 16)

                def load_v(h, u):
                    for z, rows in ((0, lo), (1, hi)):
                        sp.dma_start(vs[u][rows, :, :], vS[z].rearrange("s t c -> t s c")[:, :, bass.ds(h * HK, HK)]).then_inc(v_loaded[u], 16)

                def store(d, src, h, sem):
                    for z, rows in ((0, lo), (1, hi)):
                        sp.dma_start(d[z].rearrange("(c t) n -> t c n", t=CH)[:, :, bass.ds(h * HK, HK)], src[rows, :, :]).then_inc(sem, 16)

                def store_walk(walk):
                    sp.wait_ge(s["y_copied"], walk[0] * lat + lat)
                    store(yS, yo, walk[0], s["stored_y"])

                def factors(h):
                    load(h)
                    load_v(h, 0)
                    load_v(h + 1, 1)
                    sp.sem_inc(s["y_free"], 1)
                    sp.sem_inc(s["bonus_free"], 1)

                def body(h, u, k, walk, ahead):
                    if ahead is not None:
                        sp.wait_ge(s["bd_ready"], h + 1)
                        sp.wait_ge(s["kh_made"], 2 * h + 2)
                        load(ahead)
                    sp.wait_ge(s["bonus_done"], h + 1)
                    store(bS, yb, h, s["stored_bonus"])
                    if walk:
                        store_walk(walk)
                        if ahead is not None:
                            load_v(ahead, walk[1])
                    sp.wait_ge(s["stored_bonus"], h * 32 + 32)
                    sp.sem_inc(s["bonus_free"], 1)
                    if walk:
                        sp.wait_ge(s["stored_y"], walk[0] * 32 + 32)
                        sp.sem_inc(s["y_free"], 1)

                every_head(sp, factors, body)
                store_walk(LAST)
                sp.wait_ge(s["stored_y"], HEADS * 32)

            @block.gpsimd
            def _(pool):
                for x in (*at_ctx, *at_rt, bh, kh, rk):
                    nc.gpsimd.memset(x[:], 0.0).then_inc(s["cleared"], 1)
                pool.wait_ge(s["const_loaded"], 80)
                def factor_part(h, slot, before=None):
                    if slot in KH_SLOTS:
                        z = KH_SLOTS.index(slot)
                        rows, q = (lo, hi)[z], slice(z * CH, z * CH + CH)
                        if z == 0:
                            pool.wait_ge(s["exp_ready"], 7 * h + 7)
                            pool.wait_ge(s["factor_step"], h * FACTOR_STEPS + 5)
                        if before is not None:
                            pool.wait_ge(s["off_ready"], before)
                        nc.gpsimd.tensor_tensor(kh[rows, :, q], cs(km)[rows], cs(e_neg)[rows], ALU.mult).then_inc(s["kh_made"], 1)
                        pool.wait_ge(s["kh_made"], 2 * h + z + 1)

                def factors(h):
                    pool.wait_ge(s["cleared"], 7)
                    for slot in range(SLOTS):
                        factor_part(h, slot)

                def body(h, u, k, walk, ahead):
                    for n in range(NZ):
                        l, g = n // NG, n % NG
                        pool.wait_ge(s["pb_masked"], h * STEPS + 4 * g + 4)
                        if n >= 2:
                            pool.wait_ge(s["z_ready"], h * NZ + n - 1)
                        nc.gpsimd.tensor_tensor(off[n % 2][:], pairs_of_group(u, g), over4(join[:, l + 1, :]), ALU.mult).then_inc(s["off_ready"], 1)
                        if ahead is not None and n < SLOTS:
                            factor_part(ahead, n, h * NZ + n + 1)

                every_head(pool, factors, body)

            @block.scalar
            def _(act):
                A = nc.scalar.activation

                def walk_x(walk, j):
                    act.wait_ge(s["x_ready"], walk[0] * STEPS + j + 1)
                    A(X[:], x_psum, ACT.Copy).then_inc(s["x_copied"], 1)

                def walk_sa(walk, j):
                    act.wait_ge(s["sa_ready"], walk[0] * STEPS + j + 1)
                    A(SA[:], sa_psum, ACT.Copy).then_inc(s["sa_copied"], 1)

                def norm(h, n, c0, c1):
                    act.wait_ge(s["ss_ready"], 2 * h + n + 1)
                    A(nrm[:, c0:c1], ss_bank[:, 0:c1 - c0], ACT.Sqrt, bias=S.eps[:, 3:4]).then_inc(s["nrm_ready"], 1)

                def exps(*of):
                    for dst, rows, src, sign in of:
                        A(dst[rows, :], src[rows, :], ACT.Exp, scale=sign).then_inc(s["exp_ready"], 1)

                def factor_part(h, slot):
                    if slot == 0:
                        act.wait_ge(s["loaded"], h * 16 * LOADS + 16 * LOADS)
                        A(lw[:], sg[:], ACT.Copy, scale=LOG_DECAY).then_inc(s["lw_ready"], 1)
                        A(sq[:], k2[:], ACT.Square, scale=cols[:, 0:1]).then_inc(s["sq_ready"], 1)
                    if slot == 2:
                        norm(h, 0, 0, BANK)
                    if slot == 3:
                        act.wait_ge(s["g_ready"], h + 1)
                        A(em[:], cs(L)[:, :, CH - 1], ACT.Exp, scale=0.5).then_inc(s["exp_ready"], 1)
                        exps((e_exc, lo, G2, 1.0), (e_exc, hi, G, -1.0))
                    if slot == 4:
                        norm(h, 1, BANK, ALL)
                        exps((e_neg, lo, G, -1.0), (e_neg, hi, G2, 1.0))
                    if slot == 5:
                        act.wait_ge(s["exp_ready"], 7 * h + 1)
                        exps((e_inc, lo, G, 1.0), (e_inc, hi, G2, -1.0))

                def factors(h):
                    for slot in range(SLOTS):
                        factor_part(h, slot)

                def body(h, u, k, walk, ahead):
                    for g in range(NG):
                        if walk:
                            j0, j1 = WALK_PAIRS[g]
                            walk_x(walk, j0)
                            walk_sa(walk, j0)
                        for n, dst in enumerate((bT[u], kT[u])):
                            if walk:
                                (walk_x, walk_sa)[n](walk, j1)
                            act.wait_ge(s["tr_ready"], h * 2 * NG + 2 * g + n + 1)
                            A(dst[:, 4 * g:4 * g + 4, :], quad(tr_bank[n][:]), ACT.Copy).then_inc(s["tr_copied"], 1)

                    def copy_z(n):
                        act.wait_ge(s["z_ready"], h * NZ + n + 1)
                        if n >= 2:
                            act.wait_ge(s["zr_ready"], h * NZ + n - 1)
                        A(Z[n % 2][:], quad(z_bank[n % 2][:]), ACT.Copy).then_inc(s["z_copied"], 1)

                    copy_z(0)
                    for n in range(NZ):
                        if walk and n in WALK_GROWTH:
                            walk_x(walk, WALK_GROWTH[n])
                            walk_sa(walk, WALK_GROWTH[n])
                        if n + 1 < NZ:
                            copy_z(n + 1)
                        if ahead is not None and n < SLOTS:
                            factor_part(ahead, n)

                every_head(act, factors, body)
                for j in range(STEPS):
                    walk_x(LAST, j)
                    walk_sa(LAST, j)

            @block.vector
            def _(dve):
                dve.wait_ge(s["const_loaded"], 80)
                dve.wait_ge(s["cleared"], 7)
                V = nc.vector

                def walk_begin(walk):
                    dve.wait_ge(s["y_free"], walk[0] + 1)
                    V.memset(Sm[:], 0.0).then_inc(s["sm_ready"], 1)

                def walk_step(walk, j):
                    w, wu, _ = walk
                    if j < STEPS - 1:
                        dve.wait_ge(s["ds_ready"], w * (STEPS - 1) + j + 1)
                        V.tensor_scalar(Sm[:], ds_psum, ee[wu][:, j:j + 1], None, ALU.mult).then_inc(s["sm_ready"], 1)
                    if j >= CSTEPS:
                        n = j - CSTEPS
                        dve.wait_ge(s["y_ready"], w * lat + n + 1)
                        V.tensor_copy(yo[lo, n, :], y_psum[lo])
                        V.tensor_copy(yo[hi, lat - 1 - n, :], y_psum[hi]).then_inc(s["y_copied"], 1)

                def factor_part(c, h, u, slot):
                    if slot == 0:
                        dve.wait_ge(s["loaded"], h * 16 * LOADS + 16 * LOADS)
                    if slot == 1:
                        dve.wait_ge(s["lw_ready"], h + 1)
                        c.step(V.tensor_tensor_scan(L[:], keep[:], lw[:], 0.0, ALU.mult, ALU.add))
                    if slot == 2:
                        c.step(V.scalar_tensor_tensor(out=cs(G), in0=cs(L)[:, :, CH - 1:CH].broadcast_to([P, STEPS, CH]), scalar=-0.5, in1=cs(L), op0=ALU.mult, op1=ALU.add))
                        V.tensor_tensor(G2[:], G[:], lw[:], ALU.subtract).then_inc(s["g_ready"], 1)
                    if slot == 3:
                        c.step(V.tensor_scalar(oneminus[:], cols[:, 1:2], -1.0, 1.0, ALU.mult, ALU.add))
                        c.step(V.tensor_scalar(t1[:], aa[:], cols[:, 1:2], oneminus[:, 0:1], ALU.mult, ALU.add))
                    if slot == 4:
                        c.mark(V.tensor_tensor(km[:], k2[:], t1[:], ALU.mult))
                    if slot in (5, 6):
                        dve.wait_ge(s["nrm_ready"], 2 * h + 2)
                        part = slice((slot - 5) * (ALL // 2), (slot - 4) * (ALL // 2))
                        c.step(V.reciprocal(nrm[:, part], nrm[:, part]))
                    if slot == 7:
                        c.step(V.scalar_tensor_tensor(out=kk[:], in0=k2[:], scalar=cols[:, 0:1], in1=nrm[:], op0=ALU.mult, op1=ALU.mult))
                        c.step(V.tensor_tensor(t1[:], kk[:], aa[:], ALU.mult))
                    if slot >= 8:
                        z = (slot - 8) // 3
                        rows, q = (lo, hi)[z], slice(z * CH, z * CH + CH)
                    if slot in (8, 11):
                        dve.wait_ge(s["exp_ready"], 7 * h + 7)
                        V.scalar_tensor_tensor(out=at_ctx[u][rows, :, q], in0=cs(kk)[rows, 0:CSTEPS], scalar=-1.0, in1=cs(e_exc)[rows, 0:CSTEPS], op0=ALU.mult, op1=ALU.mult)
                        V.scalar_tensor_tensor(out=at_rt[u][rows, :, 0, q], in0=cs(kk)[rows, CSTEPS:], scalar=-1.0, in1=cs(e_exc)[rows, CSTEPS:], op0=ALU.mult, op1=ALU.mult)
                    if slot in (9, 12):
                        V.tensor_tensor(at_rt[u][rows, :, 1, q], cs(r2)[rows], cs(e_inc)[rows, CSTEPS:], ALU.mult)
                        V.tensor_tensor(bh[rows, :, q], cs(t1)[rows], cs(e_neg)[rows], ALU.mult)
                    if slot in (10, 13):
                        c.step(V.scalar_tensor_tensor(out=rk[rows, :, q], in0=cs(r2)[rows], scalar=cols[rows, 2:3], in1=cs(km)[rows, CSTEPS:], op0=ALU.mult, op1=ALU.mult))
                    if slot == 13:
                        V.tensor_tensor(ee[u][:, 0:STEPS - 1], em[:, 0:STEPS - 1], em[:, 1:STEPS], ALU.mult).then_inc(s["bd_ready"], 1)
                        assert c.n == FACTOR_STEPS, c.n

                def factors(h):
                    c = Chain(dve, s["factor_step"], 0)
                    for slot in range(SLOTS):
                        factor_part(c, h, 0, slot)

                def body(h, u, k, walk, ahead):
                    if walk:
                        walk_begin(walk)
                    c = Chain(dve, s["dve_step"], h * 2 * NG)
                    dve.wait_ge(s["bon_ready"], h + 1)
                    for n in range(2):
                        V.tensor_copy(bon[:, 4 * n:4 * n + 4], quad(tr_bank[n][:])[:, :, 0]).then_inc(s["bon_read"], 1)
                    for g in range(NG):
                        g4 = slice(4 * g, 4 * g + 4)
                        for j in range(4 * g, 4 * g + 4):
                            dve.wait_ge(s["pb_ready"], h * STEPS + j + 1)
                            if j < CSTEPS:
                                V.tensor_tensor(pairs_ctx[u][:, j], quad(pair_bank[j % 2][:])[:, 0::2, :], masks[:, 0::2, :], ALU.mult).then_inc(s["pb_masked"], 1)
                            else:
                                V.tensor_tensor(pairs_lat[u][:, j - CSTEPS], quad(pair_bank[j % 2][:]), masks[:], ALU.mult).then_inc(s["pb_masked"], 1)
                        if walk:
                            walk_step(walk, WALK_PAIRS[g][0])
                        dve.wait_ge(s["pn_ready"], h * NG + g + 1)
                        c.mark(V.tensor_tensor(T[:, g4, :], quad(pn_bank[:]), over4(join0[:]), ALU.mult))
                        dve.wait_ge(s["pb_masked"], h * STEPS + 4 * g + 4)
                        c.step(V.tensor_tensor(R[u][:, g4, :], pairs_of_group(u, g), over4(join[:, 0, :]), ALU.mult))
                        V.tensor_tensor(T[:, g4, :], T[:, g4, :], over4(S.ident[:]), ALU.add)
                        V.tensor_tensor(R[u][:, g4, :], R[u][:, g4, :], over4(S.ident[:]), ALU.add).then_inc(s["pn_masked"], 1)
                        if walk:
                            walk_step(walk, WALK_PAIRS[g][1])
                    dve.wait_ge(v_loaded[u], k * 32 + 32)
                    dve.wait_ge(s["bonus_free"], h + 1)
                    dve.wait_ge(s["bon_read"], 2 * h + 2)
                    V.tensor_tensor(yb[lo, :, :], vs[u][lo, CSTEPS:, :], bon[lo, :].rearrange("p (c o) -> p c o", o=1).broadcast_to([HK, lat, HK]), ALU.mult)
                    V.tensor_tensor(yb[hi, ::-1, :], vs[u][hi, CSTEPS:, :], bon[hi, :].rearrange("p (c o) -> p c o", o=1).broadcast_to([HK, lat, HK]), ALU.mult).then_inc(s["bonus_done"], 1)
                    if ahead is not None:
                        fc = Chain(dve, s["factor_step"], ahead * FACTOR_STEPS)
                    for n in range(NZ):
                        l, g = n // NG, n % NG
                        g4 = slice(4 * g, 4 * g + 4)
                        if l < LEVELS - 1:
                            dve.wait_ge(s["tz_ready"], h * (NZ - NG) + n + 1)
                            V.tensor_tensor(T[:, g4, :], T[:, g4, :], quad(tz_bank[:]), ALU.add).then_inc(s["tz_added"], 1)
                        dve.wait_ge(s["zr_ready"], h * NZ + n + 1)
                        V.tensor_tensor(R[u][:, g4, :], R[u][:, g4, :], quad(zr_bank[:]), ALU.add).then_inc(s["zr_added"], 1)
                        if walk and n in WALK_GROWTH:
                            walk_step(walk, WALK_GROWTH[n])
                        if ahead is not None and n < SLOTS:
                            factor_part(fc, ahead, 1 - u, n)
                    assert c.n == 2 * NG

                every_head(dve, factors, body)
                walk_begin(LAST)
                for j in range(STEPS):
                    walk_step(LAST, j)

            @block.tensor
            def _(pe):
                pe.wait_ge(s["const_loaded"], 80)
                mmul = nc.tensor.matmul

                def walk_state(walk, j):
                    w, wu, wk = walk
                    v, state = twice(vs[wu][:, j, :]), twice(Sm[:])
                    if j == 0:
                        pe.wait_ge(v_loaded[wu], wk * 32 + 32)
                    mmul(x_twice, pair(wu, j, 2), v, start=True, stop=False)
                    pe.wait_ge(s["sm_ready"], w * STEPS + j + 1)
                    mmul(x_twice, at(wu, j), state, start=False, stop=True).then_inc(s["x_ready"], 1)
                    if j < STEPS - 1:
                        mmul(ds_twice, S.ident[:], state, start=True, stop=False)
                        mmul(ds_twice, kT[wu][:, j, :], v, start=False, stop=False)
                    if j >= CSTEPS:
                        if j > CSTEPS:
                            pe.wait_ge(s["y_copied"], w * lat + j - CSTEPS)
                        mmul(y_twice, at_rt[wu][:, j - CSTEPS, 1, :], state, start=True, stop=False)
                        mmul(y_twice, pair(wu, j, 3), v, start=False, stop=False)

                def walk_solve(walk, j):
                    w, wu, _ = walk
                    pe.wait_ge(s["x_copied"], w * STEPS + j + 1)
                    mmul(sa_twice, R[wu][:, j, :], twice(X[:]), start=True, stop=True).then_inc(s["sa_ready"], 1)

                def walk_share(walk, j):
                    w, wu, _ = walk
                    pe.wait_ge(s["sa_copied"], w * STEPS + j + 1)
                    if j < STEPS - 1:
                        mmul(ds_twice, bT[wu][:, j, :], twice(SA[:]), start=False, stop=True).then_inc(s["ds_ready"], 1)
                    if j >= CSTEPS:
                        mmul(y_twice, pair(wu, j, 1), twice(SA[:]), start=False, stop=True).then_inc(s["y_ready"], 1)

                def factor_part(h, slot):
                    if slot == 1:
                        pe.wait_ge(s["sq_ready"], h + 1)
                        mmul(ss_bank[:], halves[:], sq[:, 0:BANK], start=True, stop=True).then_inc(s["ss_ready"], 1)
                    if slot == 3:
                        pe.wait_ge(s["nrm_ready"], 2 * h + 1)
                        mmul(ss_bank[:, 0:ALL - BANK], halves[:], sq[:, BANK:ALL], start=True, stop=True).then_inc(s["ss_ready"], 1)

                def factors(h):
                    for slot in range(SLOTS):
                        factor_part(h, slot)

                def body(h, u, k, walk, ahead):
                    def part(what, j):
                        if walk and j is not None:
                            what(walk, j)

                    pe.wait_ge(s["bd_ready"], h + 1)
                    pe.wait_ge(s["kh_made"], 2 * h + 2)
                    for n in range(lat):
                        mm = mmul(tr_bank[n // 4][:, (n % 4) * P:(n % 4 + 1) * P], rk[:, n, :], S.ones[:], start=True, stop=True)
                    mm.then_inc(s["bon_ready"], 1)
                    for g in range(NG):
                        j0, j1 = WALK_PAIRS[g]
                        for j in range(4 * g, 4 * g + 4):
                            if j == 4 * g + 2:
                                part(walk_state, j0)
                            if j >= 2:
                                pe.wait_ge(s["pb_masked"], h * STEPS + j - 1)
                            b = pair_bank[j % 2]
                            if j < CSTEPS:
                                w, rhs = P, at_ctx[u][:, j, :]
                            else:
                                w, rhs = 2 * P, at_rt[u][:, j - CSTEPS].rearrange("p a t -> p (a t)")
                            mmul(b[:, 0:w], bh[:, j, :], rhs, start=True, stop=True)
                            mmul(b[:, 2 * P:2 * P + w], kh[:, j, :], rhs, start=True, stop=True).then_inc(s["pb_ready"], 1)
                        part(walk_solve, j0)
                        if g >= 1:
                            pe.wait_ge(s["pn_masked"], h * NG + g)
                        for j in range(4 * g, 4 * g + 4):
                            mm = mmul(pn_bank[:, (j % 4) * P:(j % 4 + 1) * P], at(u, j), bh[:, j, :], start=True, stop=True)
                        mm.then_inc(s["pn_ready"], 1)
                        part(walk_share, j0)
                        for n, src in enumerate((bh, kh)):
                            if g >= 1:
                                pe.wait_ge(s["tr_copied"], h * 2 * NG + 2 * g - 1 + n)
                            else:
                                pe.wait_ge(s["bon_read"], 2 * h + n + 1)
                            for j in range(4 * g, 4 * g + 4):
                                mm = nc.tensor.transpose(tr_bank[n][:, (j % 4) * P:(j % 4 + 1) * P], src[:, j, :], S.ident[:])
                            mm.then_inc(s["tr_ready"], 1)
                            part((walk_state, walk_solve)[n], j1)
                        part(walk_share, j1)
                    pe.wait_ge(s["tr_copied"], h * 2 * NG + 2 * NG)

                    def grow_z(n):
                        l, g = n // NG, n % NG
                        pe.wait_ge(s["off_ready"], h * NZ + n + 1)
                        if l == 0:
                            pe.wait_ge(s["pn_masked"], h * NG + NG)
                        else:
                            pe.wait_ge(s["tz_added"], h * (NZ - NG) + (l - 1) * NG + g + 1)
                        if n >= 2:
                            pe.wait_ge(s["z_copied"], h * NZ + n - 1)
                        for q in range(4):
                            mm = mmul(z_bank[n % 2][:, q * P:(q + 1) * P], off[n % 2][:, q, :], T[:, 4 * g + q, :], start=True, stop=True)
                        mm.then_inc(s["z_ready"], 1)

                    grow_z(0)
                    for n in range(NZ):
                        l, g = n // NG, n % NG
                        j = WALK_GROWTH[n] if n in WALK_GROWTH else None
                        part(walk_state, j)
                        if n + 1 < NZ:
                            grow_z(n + 1)
                        part(walk_solve, j)
                        pe.wait_ge(s["z_copied"], h * NZ + n + 1)
                        if l < LEVELS - 1:
                            if l > 0:
                                pe.wait_ge(s["zr_added"], h * NZ + n - NG + 1)
                            if n >= 1:
                                pe.wait_ge(s["tz_added"], h * (NZ - NG) + n)
                            for q in range(4):
                                mm = mmul(tz_bank[:, q * P:(q + 1) * P], R[u][:, 4 * g + q, :], Z[n % 2][:, q, :], start=True, stop=True)
                            mm.then_inc(s["tz_ready"], 1)
                        if n >= 1:
                            pe.wait_ge(s["zr_added"], h * NZ + n)
                        for q in range(4):
                            mm = mmul(zr_bank[:, q * P:(q + 1) * P], Z[n % 2][:, q, :], R[u][:, 4 * g + q, :], start=True, stop=True)
                        mm.then_inc(s["zr_ready"], 1)
                        part(walk_share, j)
                        if ahead is not None and n < SLOTS:
                            factor_part(ahead, n)
                    pe.wait_ge(s["zr_added"], h * NZ + NZ)

                every_head(pe, factors, body)
                for j in range(STEPS):
                    for what in (walk_state, walk_solve, walk_share):
                        what(LAST, j)


FACTOR_STEPS = 11


def rwkv_tables():
    i = np.arange(CH)
    z1 = np.zeros((CH, CH))
    f = np.float32

    def bd(fwd, bwd):
        return np.block([[fwd, z1], [z1, bwd]]).astype(f)

    early, same = i[:, None] < i[None, :], i[:, None] == i[None, :]
    strict = bd(early, early.T)
    incl = bd(early | same, early.T | same)
    joins = []
    for l in range(LEVELS + 1):
        m = 1 << l
        b = (i[:, None] // (2 * m) == i[None, :] // (2 * m)) & (i[:, None] % (2 * m) < m) & (i[None, :] % (2 * m) >= m)
        joins.append(bd(b, b.T))
    keep = np.ones((P, ALL), f)
    keep[:, ::CH] = 0.0
    return {"rw_masks": np.ascontiguousarray(np.stack([strict, incl, strict, incl], 1)),
            "rw_join": np.ascontiguousarray(np.stack(joins, 1)), "rw_join0": np.ascontiguousarray(joins[0].T),
            "rw_keep": keep, "rw_halves": bd(np.ones((CH, CH)), np.ones((CH, CH)))}


def rwkv_join(nc, name, S, a, yS, bS, gate, out):
    with Stage(nc, name) as st:
        y = [[st.sb(f"y{n}{u}", [P, D]) for n in range(4)] for u in range(2)]
        gain, shift = st.sb("gain", [P, D]), st.sb("shift", [P, D])
        g = [st.sb(f"gate{u}", [P, D]) for u in range(2)]
        mean, var, rms = st.sb("mean", [P, HEADS]), st.sb("var", [P, HEADS]), st.sb("rms", [P, HEADS])
        sq = st.sb("sq", [P, D])
        const_loaded, loaded = st.sem("const_loaded"), [st.sem(f"loaded{u}") for u in range(2)]
        dve_step, squared, var_ready, rms_ready, centred = (st.sem(n) for n in ("dve_step", "squared", "var_ready", "rms_ready", "centred"))
        pool_step, summed, bonus_ready = st.sem("pool_step"), st.sem("summed"), st.sem("bonus_ready")

        def hv(x):
            return x[:].rearrange("p (h c) -> p h c", c=HK)

        def per_head(x):
            return x[:].rearrange("p (h o) -> p h o", o=1).broadcast_to([P, HEADS, HK])

        SV = 7
        with st.block() as block:
            @block.sync
            def _(sp):
                sp.dma_start(gain[:], a["rw_ln_g_2"].partition_broadcast(P)).then_inc(const_loaded, 16)
                sp.dma_start(shift[:], a["rw_ln_b_2"].partition_broadcast(P)).then_inc(const_loaded, 16)
                for t in range(NT):
                    if t >= 2:
                        sp.wait_ge(dve_step, SV * (t - 1))
                    rows = slice(t * P, (t + 1) * P)
                    for n, src in enumerate((yS[0], yS[1], bS[0], bS[1])):
                        sp.dma_start(y[t % 2][n][:], src[rows, :]).then_inc(loaded[t % 2], 16)
                    sp.dma_start(g[t % 2][:], gate[rows, :]).then_inc(loaded[t % 2], 16)

            @block.scalar
            def _(act):
                for t in range(NT):
                    act.wait_ge(centred, t + 1)
                    nc.scalar.activation(sq[:], y[t % 2][0][:], ACT.Square).then_inc(squared, 1)
                    act.wait_ge(var_ready, t + 1)
                    nc.scalar.activation(rms[:], var[:], ACT.Sqrt, scale=1.0 / HK, bias=S.eps[:, 2:3]).then_inc(rms_ready, 1)

            @block.gpsimd
            def _(pool):
                pool.wait_ge(const_loaded, 32)
                c = Chain(pool, pool_step)
                for t in range(NT):
                    y0, y1, b0, b1 = y[t % 2]
                    pool.wait_ge(loaded[t % 2], 80 * (t // 2 + 1))
                    nc.gpsimd.tensor_tensor(y0[:], y0[:], y1[:], ALU.add).then_inc(summed, 1)
                    c.step(nc.gpsimd.tensor_tensor(b0[:], b0[:], b1[:], ALU.add))
                    nc.gpsimd.tensor_tensor(b0[:], b0[:], shift[:], ALU.add).then_inc(bonus_ready, 1)

            @block.vector
            def _(dve):
                V = nc.vector
                dve.wait_ge(const_loaded, 32)
                for t in range(NT):
                    c = Chain(dve, dve_step, t * SV)
                    y0, y1, b0, b1 = y[t % 2]
                    dve.wait_ge(loaded[t % 2], 80 * (t // 2 + 1))
                    dve.wait_ge(summed, t + 1)
                    c.step(V.tensor_reduce(mean[:], hv(y0), AX.X, ALU.add))
                    c.step(V.tensor_scalar(mean[:], mean[:], 1.0 / HK, None, ALU.mult))
                    V.tensor_tensor(hv(y0), hv(y0), per_head(mean), ALU.subtract).then_inc(centred, 1)
                    dve.wait_ge(squared, t + 1)
                    V.tensor_reduce(var[:], hv(sq), AX.X, ALU.add).then_inc(var_ready, 1)
                    dve.wait_ge(rms_ready, t + 1)
                    c.step(V.reciprocal(rms[:], rms[:]))
                    c.step(V.tensor_tensor(hv(y0), hv(y0), per_head(rms), ALU.mult))
                    c.step(V.tensor_tensor(y0[:], y0[:], gain[:], ALU.mult))
                    dve.wait_ge(bonus_ready, t + 1)
                    c.step(V.tensor_tensor(y0[:], y0[:], b0[:], ALU.add))
                    c.step(V.tensor_tensor(out[:, t, :], y0[:], g[t % 2][:], ALU.mult))
                    while c.n < SV:
                        c.mark(V.nop())
                    c.wait()
                    assert c.n == SV, c.n


RW_COLS = (("mu", 6 * KD), ("w0", 2 * KD), ("a0", 2 * KD), ("norm1", KD))


def rwkv(nc, S, a, x_tiles, c_tiles, hT, mods):
    c = {}
    at = 0
    for n, w in RW_COLS:
        c[n] = S.rw_cols[:, at:at + w]
        at += w
    cols = S.mod_cols[1]
    norm_transpose(nc, "sn1", S, c_tiles + x_tiles, hT, cols=[cols[1]] * (NA - NT) + [cols[0]] * NT)
    kF, sgF, aF = ([dram(nc, f"rw_{n}{z}", [D, ALL]) for z in range(2)] for n in ("k", "sg", "a"))
    rF = [dram(nc, f"rw_r{z}", [D, SEQ]) for z in range(2)]
    vS = [dram(nc, f"rw_v{z}", [STEPS, CH, D]) for z in range(2)]
    yS, bS = ([dram(nc, f"rw_{n}{z}", [SEQ, D]) for z in range(2)] for n in ("y", "bon"))
    gate = dram(nc, "rw_gate", [SEQ, D])
    parts = ((0, CTX), (CTX, SEQ))
    fdram = "(k p) t -> p k t"
    with ExitStack() as mem:
        xx = mem.enter_context(nc.sbuf_tensor("rw_xx", [P, KD, ALL], F32))
        mix = mem.enter_context(nc.sbuf_tensor("rw_mix", [P, KD, ALL], F32))
        token_shift(nc, "rws", hT, xx)

        def mixed(j):
            return hT, xx, c["mu"][:, j * KD:(j + 1) * KD]

        def both_orders(fwd, bwd, lead):
            def epi(which, engine, chain, j, n0, ps):
                w = ps.shape[1]
                o = slice(n0 - lead, n0 - lead + w)
                copy = (lambda d, s_: engine.activation(d, s_, ACT.Copy)) if which == "act" else engine.tensor_copy
                copy(fwd(j)[:, o], ps)
                return copy(backward(bwd(j)[:, o]), chunked(ps))
            return epi

        def rows(t, q):
            return t.rearrange(fdram, p=P)[:, 4 * q:4 * q + 4, :]

        with ExitStack() as m2:
            f, b = (m2.enter_context(nc.sbuf_tensor(f"rw_rf{z}", [P, KD, SEQ], F32)) for z in range(2))
            project_split(nc, "rp0", mix, SEQ, [dict(w=a["rw_wr_2"][:, q * BANK:(q + 1) * BANK], mode="F",
                                              epi=both_orders(lambda j, q=q: f[:, 4 * q + j, :], lambda j, q=q: b[:, 4 * q + j, :], CTX),
                                              stores=[(rows(d, q), x[:, 4 * q:4 * q + 4]) for d, x in zip(rF, (f, b))]) for q in range(2)],
                    parts=parts[1:], mix=mixed(0))
        with ExitStack() as m2:
            f, b = (m2.enter_context(nc.sbuf_tensor(f"rw_kf{z}", [P, KD, ALL], F32)) for z in range(2))
            project_split(nc, "rp2", mix, ALL, [dict(w=a["rw_wk_2"][:, q * BANK:(q + 1) * BANK], mode="F",
                                              epi=both_orders(lambda j, q=q: f[:, 4 * q + j, :], lambda j, q=q: b[:, 4 * q + j, :], 0),
                                              stores=[(rows(d, q), x[:, 4 * q:4 * q + 4]) for d, x in zip(kF, (f, b))]) for q in range(2)],
                    parts=parts, mix=mixed(2))
        with ExitStack() as m2:
            v = m2.enter_context(nc.sbuf_tensor("rw_vt", [P, NA, D], F32))

            def v_stores(o):
                out = [(vS[0].rearrange("(q s) t c -> (s t) q c", s=2)[:, :, o], v[:, :, o])]
                for j in range(STEPS):
                    step = CSTEPS - 1 - j if j < CSTEPS else STEPS - 1 - (j - CSTEPS)
                    out.append((vS[1][step][:, o], v[CH * (j % 2):CH * (j % 2) + CH, j // 2, o]))
                return out

            project_split(nc, "rp3", mix, ALL, [dict(w=a["rw_wv_2"][:, q * BANK:(q + 1) * BANK], mode="T",
                                              epi=copy_to(lambda j, n0, q=q: v[:, j, q * BANK:(q + 1) * BANK]),
                                              stores=v_stores(slice(q * BANK, (q + 1) * BANK))) for q in range(2)], mix=mixed(3))
        for j, n, func, w1, w2, base, outF in ((1, "w", ACT.Tanh, "rw_w1_2", "rw_w2_2", c["w0"], sgF), (4, "a", ACT.Copy, "rw_a1_2", "rw_a2_2", c["a0"], aF)):
            with ExitStack() as m2:
                low = [m2.enter_context(nc.sbuf_tensor(f"rw_low{n}{z}", [HK, 1, ALL], F32)) for z in range(2)]
                f = [m2.enter_context(nc.sbuf_tensor(f"rw_out{n}{z}", [P, KD, ALL], F32)) for z in range(2)]

                def squash(z, func=func):
                    def epi(which, engine, chain, j, n0, ps):
                        return engine.activation(low[z][:, 0, n0:n0 + ps.shape[1]], ps, func)
                    return epi

                def sigmoid(z, q, base=base):
                    def epi(which, engine, chain, j, n0, ps):
                        d = 4 * q + j
                        o = slice(n0, n0 + ps.shape[1])
                        bias = base[:, z * KD + d:z * KD + d + 1]
                        if z == 0:
                            return engine.activation(f[0][:, d, o], ps, ACT.Sigmoid, bias=bias)
                        return engine.activation(backward(f[1][:, d, o]), chunked(ps), ACT.Sigmoid, bias=bias)
                    return epi

                project(nc, f"rl{n}", mix, ALL, [dict(w=a[w1][z], mode="F", eng="act", epi=squash(z)) for z in range(2)], parts=parts, mix=mixed(j))
                project(nc, f"ro{n}", low[0], ALL, [dict(w=a[w2][z][:, q * BANK:(q + 1) * BANK], x=low[z], mode="F", eng="act", epi=sigmoid(z, q),
                                                        stores=[(rows(outF[z], q), f[z][:, 4 * q:4 * q + 4])]) for z in range(2) for q in range(2)], parts=parts)
        with ExitStack() as m2:
            low = m2.enter_context(nc.sbuf_tensor("rw_glow", [P, 2, SEQ], F32))
            g = m2.enter_context(nc.sbuf_tensor("rw_gt", [P, NT, D], F32))

            def squash_g(which, engine, chain, j, n0, ps):
                return engine.activation(low[0:ps.shape[0], j, 0:SEQ], ps, ACT.Sigmoid)

            project(nc, "rg1", mix, SEQ, [dict(w=a["rw_g1_2"], mode="F", eng="act", epi=squash_g)], parts=parts[1:], mix=mixed(5))
            project(nc, "rg2", low, SEQ, [dict(w=a["rw_g2_2"][:, q * BANK:(q + 1) * BANK], mode="T",
                                              epi=copy_to(lambda j, n0, q=q: g[:, j, q * BANK:(q + 1) * BANK]),
                                              stores=[(gate.rearrange("(t p) c -> p t c", p=P)[:, :, q * BANK:(q + 1) * BANK], g[:, :, q * BANK:(q + 1) * BANK])])
                                         for q in range(2)])
    S.free_hT()
    rwkv_scan(nc, "scan", S, a, kF, rF, sgF, aF, vS, yS, bS)
    hT = S.take_hT()
    with ExitStack() as mem:
        o = mem.enter_context(nc.sbuf_tensor("rw_o", [P, NT, D], F32))
        row = mem.enter_context(nc.sbuf_tensor("rw_gaterow", [P, D], F32))
        tmp = mem.enter_context(nc.sbuf_tensor("rw_tmp", [P, 2, BANK], F32))
        rwkv_join(nc, "rwj", S, a, yS, bS, gate, o)
        load_all(nc, "rwl", [(row[:], mods[0, 2 * D:3 * D].partition_broadcast(P))])
        norm_transpose(nc, "rwt", S, [o[:, t, :] for t in range(NT)], hT, scaled=False)
        project_split(nc, "rwo", hT[:, :, 0:SEQ], SEQ, [dict(w=a["rw_wo_2"][:, q * BANK:(q + 1) * BANK], mode="T", eng="dve",
                                         epi=gated_residual(lambda j, q=q: x_tiles[j][:, q * BANK:(q + 1) * BANK], lambda j, q=q: row[:, q * BANK:(q + 1) * BANK], tmp)) for q in range(2)])
    return hT


def final_norm(nc, S, x_tiles, gain, out):
    T = len(x_tiles)
    with Stage(nc, "fin") as st:
        row, junk = st.sb("row", [P, D]), st.sb("squares", [P, D])
        ss, rms, rstd = st.sb("sum_sq", [P, T]), st.sb("rms", [P, T]), st.sb("rstd", [P, T])
        y = st.sb("y", [P, T, D])
        row_loaded, rms_ready, scaled, act_step, dve_step = (st.sem(n) for n in ("row_loaded", "rms_ready", "scaled", "act_step", "dve_step"))
        stored = st.sem("stored")
        with st.block() as block:
            @block.sync
            def _(sp):
                sp.dma_start(row[:], gain.partition_broadcast(P)).then_inc(row_loaded, 16)
                for t in range(T):
                    sp.wait_ge(scaled, t + 1)
                    sp.dma_start(out[t * P:(t + 1) * P, :], y[:, t, :]).then_inc(stored, 16)
                sp.wait_ge(stored, 16 * T)

            @block.scalar
            def _(act):
                steps = Chain(act, act_step)
                for t in range(T):
                    steps.step(nc.scalar.activation(junk[:], x_tiles[t], ACT.Square, accum_out=ss[:, t:t + 1]))
                nc.scalar.activation(rms[:], ss[:], ACT.Sqrt, scale=1.0 / D, bias=S.eps6[:, 0:1]).then_inc(rms_ready, 1)

            @block.vector
            def _(dve):
                steps = Chain(dve, dve_step)
                dve.wait_ge(rms_ready, 1)
                steps.step(nc.vector.reciprocal(rstd[:], rms[:]))
                dve.wait_ge(row_loaded, 16)
                for t in range(T):
                    nc.vector.scalar_tensor_tensor(out=y[:, t, :], in0=x_tiles[t], scalar=rstd[:, t:t + 1], in1=row[:], op0=ALU.mult, op1=ALU.mult).then_inc(scaled, 1)


def second_block_b(nc, S, a, x_tiles, c_tiles, hT, mods, out):
    hT = rwkv(nc, S, a, x_tiles, c_tiles, hT, mods[1])
    moe(nc, "moe1", S, a, 1, ((x_tiles, 0),), hT, mods[1])
    final_norm(nc, S, x_tiles, a["final_g_2"], out)


def rwkv_layout(inp):
    g = lambda n: np.asarray(inp[n])
    out = {n: np.ascontiguousarray(g(n)[0]) for n in ("rw_wr_2", "rw_wk_2", "rw_wv_2", "rw_wo_2", "rw_w1_2", "rw_w2_2", "rw_a1_2", "rw_a2_2", "rw_g1_2", "rw_g2_2", "rw_ln_g_2", "rw_ln_b_2")}
    out["final_g_2"] = np.ascontiguousarray(g("final_g_2"))
    out["rwkv_cols"] = np.concatenate([columns(g("rw_mu_2")), columns(g("rw_w0_2")), columns(g("rw_a0_2")), columns(g("norm1_g_2")[1])], 1)
    per = np.stack([g("rw_k_k_2")[0].reshape(HEADS, HK), g("rw_k_a_2")[0].reshape(HEADS, HK), g("rw_r_k_2")[0], g("rw_r_k_2")[0]], 2)
    out["rw_cols"] = np.ascontiguousarray(np.concatenate([per, per], 1))
    return out



def network(nc, a, out):
    Stage.zeroed = []
    S = Shared()
    with ExitStack() as mem:
        def sb(n, shape):
            return mem.enter_context(nc.sbuf_tensor(n, shape, F32))
        S.pool_sems = [[nc.alloc_semaphore(f"pool_dma{l}{n}") for n in range(7)] for l in range(2)]
        S.ident, S.ones, S.eps = sb("identity", [P, P]), sb("ones", [P, P]), sb("epsilons", [P, 4])
        S.eps6 = S.eps[:, 0:1]
        S.first_cols, S.second_cols, S.rw_cols = sb("first_columns", [P, 37]), sb("second_columns", [P, 32]), sb("rwkv_columns", [P, 88])
        mod_cols = sb("mod_columns", [P, 2, 4, KD])
        S.mod_cols = [[(mod_cols[:, l, 0], mod_cols[:, l, 1]), (mod_cols[:, l, 2], mod_cols[:, l, 3])] for l in range(2)]
        S.ada_cols, S.cond = sb("ada_columns", [P, 2, N_MOD * KD]), sb("condition", [P, KD, 2])
        S.rw_norm1 = S.rw_cols[:, 10 * KD:11 * KD]
        x = sb("x", [P, NT, D])
        hT_mem = ExitStack()
        taken = []

        def take_hT():
            taken.append(1)
            return hT_mem.enter_context(nc.sbuf_tensor(f"hT{len(taken)}", [P, KD, ALL], F32))

        S.take_hT, S.free_hT = take_hT, hT_mem.close
        mods = dram(nc, "mods", [2, 2, N_MOD * D])
        tok = "(t p) d -> p t d"
        load_all(nc, "consts", [(S.ada_cols[:], a["ada_cols_2"]), (S.cond[:], a["cT_2"]), (S.ident[:], a["ident"]), (S.ones[:], a["ones"]), (S.eps[:], a["eps"]), (S.first_cols[:], a["first_cols"]),
                                (S.second_cols[:], a["second_cols"]), (S.rw_cols[:], a["rwkv_cols"]), (x[:], a["x"].rearrange(tok, p=P))])
        with Stage(nc, "cond") as st:
            done = st.sem("done")
            with st.block() as block:
                @block.scalar
                def _(act):
                    nc.scalar.activation(S.cond[:], S.cond[:], ACT.Silu).then_inc(done, 1)
                    act.wait_ge(done, 1)
        x_tiles = [x[:, t, :] for t in range(NT)]
        with ExitStack() as first:
            first_block(nc, S, a, x_tiles, first.enter_context(nc.sbuf_tensor("first_hT", [P, KD, SEQ], F32)), mods)
        xc = hT_mem.enter_context(nc.sbuf_tensor("xc", [P, NA - NT, D], F32))
        c_tiles = [xc[:, t, :] for t in range(NA - NT)]
        hT = take_hT()
        load_all(nc, "context", [(xc[:], a["ctx_2"].rearrange(tok, p=P))])
        second_block_a(nc, S, a, x_tiles, c_tiles, hT, mods)
        second_block_b(nc, S, a, x_tiles, c_tiles, hT, mods, out)
        hT_mem.close()


def kernel(**inputs):
    import concourse.bacc as bacc
    from concourse.bass_utils import run_bass_kernel_spmd

    inp = {n: np.asarray(v) for n, v in inputs.items()}
    arrays = {}
    for part in (first_layout(inp), second_layout(inp), rwkv_layout(inp), constants(), attention_tables(), gla_tables(),
                 rope_tables(), route_tables(), rwkv_tables()):
        arrays.update(part)
    nc = bacc.Bacc("TRN2", target_bir_lowering=False, num_devices=1)
    a = {n: nc.dram_tensor(f"in_{n}_dram", v.shape, mybir.dt.from_np(v.dtype), kind="ExternalInput").ap() for n, v in arrays.items()}
    out = nc.dram_tensor("out_0_dram", (1, SEQ, D), F32, kind="ExternalOutput").ap()
    network(nc, a, out[0])
    r = run_bass_kernel_spmd(nc, [{f"in_{n}_dram": v for n, v in arrays.items()}], core_ids=[0])
    return r.results[0]["out_0_dram"]
```
